# Optimizing a Trainium2 kernel written in Bass

```python
import jax
import jax.numpy as jnp
from jax import lax
import numpy as np

D_MODEL = 1024
BATCH = 1
SEQ = 128
DEPTH = 2
DEC_BATCH = 1
DEC_SEQ = 256
PAST_LEN = 128

GRID_W = 64
N_EVEN = (DEPTH + 1) // 2
N_ODD = DEPTH // 2
HEAD_DIM = 64
ML_HEADS = 4
ML_DK = 128
ML_DV = 128
ML_CHUNK = 64
WIN_Q_HEADS = 8
WIN_KV_HEADS = 2
WIN_GROUP = WIN_Q_HEADS // WIN_KV_HEADS
WIN = 128
WIN_BLOCK = 128
MLA_HEADS = 8
MLA_NOPE = 64
MLA_ROPE = 32
MLA_V = 64
MLA_Q_LORA = 256
MLA_KV_LORA = 128
NAT_HEADS = 8
NAT_ROWS = 8
NAT_COLS = 16
N_GROUPS = 4
EXPERTS_PER_GROUP = 8
N_EXPERTS = N_GROUPS * EXPERTS_PER_GROUP
TOP_K = 2
EXPERT_FF = 512
MOE_BLOCK = 128

Q_BLOCK = 128
ROPE_BASE = 10000.0
EPS = 1e-6

EVEN_SPLITS = (ML_HEADS * ML_DK, ML_HEADS * ML_DK, ML_HEADS * ML_DV, ML_HEADS * ML_DV, 4 * ML_HEADS,
               WIN_Q_HEADS * HEAD_DIM, WIN_KV_HEADS * HEAD_DIM, WIN_KV_HEADS * HEAD_DIM)
EVEN_IN = sum(EVEN_SPLITS)
EVEN_MIX = ML_HEADS * ML_DV + WIN_Q_HEADS * HEAD_DIM
ODD_SPLITS = (MLA_Q_LORA, MLA_KV_LORA, MLA_ROPE,
              NAT_HEADS * HEAD_DIM, NAT_HEADS * HEAD_DIM, NAT_HEADS * HEAD_DIM)
ODD_IN = sum(ODD_SPLITS)
ODD_MIX = MLA_HEADS * MLA_V + NAT_HEADS * HEAD_DIM

kernel_name = 'hybrid_diffusion_mlstm_win_mla_nat_hmoe_step'

def rmsnorm(x, g):
    x32 = x.astype(jnp.float32)
    y = x32 * lax.rsqrt(jnp.mean(x32 * x32, axis=-1, keepdims=True) + EPS)
    return y.astype(x.dtype) * g

def split_cols(z, sizes):
    return jnp.split(z, np.cumsum(sizes)[:-1].tolist(), axis=-1)

def adaln(cvec, w, b):
    return jnp.split(jax.nn.silu(cvec) @ w + b, 6, axis=-1)

def axial_rope(x):
    T, R = x.shape[1], x.shape[-1]
    half = R // 2
    nf = half // 2
    t = jnp.arange(T)
    inv = ROPE_BASE ** (-jnp.arange(nf, dtype=jnp.float32) / nf)

    def rot(xp, pos):
        ang = pos.astype(jnp.float32)[:, None] * inv[None, :]
        cos = jnp.cos(ang)[None, :, None, :].astype(x.dtype)
        sin = jnp.sin(ang)[None, :, None, :].astype(x.dtype)
        x1, x2 = xp[..., :nf], xp[..., nf:]
        return jnp.concatenate([x1 * cos - x2 * sin, x1 * sin + x2 * cos], axis=-1)

    return jnp.concatenate([rot(x[..., :half], t // GRID_W), rot(x[..., half:], t % GRID_W)], axis=-1)

def dense_attention(q, k, v, sink=None):
    B, Tq, HKV, G, Dq = q.shape
    scale = Dq ** -0.5
    qb = jnp.moveaxis(q.reshape(B, Tq // Q_BLOCK, Q_BLOCK, HKV, G, Dq), 1, 0)

    def block(qblk):
        s = jnp.einsum('bqhgd,bkhd->bhgqk', qblk, k).astype(jnp.float32) * scale
        if sink is None:
            p = jax.nn.softmax(s, axis=-1)
        else:
            sk = jnp.broadcast_to(sink.astype(jnp.float32)[None, :, :, None, None], s.shape[:-1] + (1,))
            p = jax.nn.softmax(jnp.concatenate([s, sk], axis=-1), axis=-1)[..., :-1]
        return jnp.einsum('bhgqk,bkhe->bqhge', p.astype(v.dtype), v)

    out = lax.map(block, qb)
    return jnp.moveaxis(out, 0, 1).reshape(B, Tq, -1)

def window_attention_latent(q, k, v, k_ctx, v_ctx, sink):
    B, T, HQ, Dh = q.shape
    HKV = k.shape[2]
    G = HQ // HKV
    NB = T // WIN_BLOCK
    S = k_ctx.shape[1]
    scale = Dh ** -0.5
    qb = q.reshape(B, NB, WIN_BLOCK, HKV, G, Dh)

    def band(a):
        ap = jnp.pad(a, ((0, 0), (WIN_BLOCK, WIN_BLOCK), (0, 0), (0, 0)))
        return jnp.concatenate(
            [ap[:, o * WIN_BLOCK:o * WIN_BLOCK + T].reshape(B, NB, WIN_BLOCK, HKV, a.shape[-1]) for o in range(3)],
            axis=2)

    kb, vb = band(k), band(v)
    qpos = jnp.arange(NB)[:, None, None] * WIN_BLOCK + jnp.arange(WIN_BLOCK)[None, :, None]
    kpos = (jnp.arange(NB)[:, None, None] - 1) * WIN_BLOCK + jnp.arange(3 * WIN_BLOCK)[None, None, :]
    valid = (jnp.abs(qpos - kpos) <= WIN) & (kpos >= 0) & (kpos < T)
    s_loc = jnp.einsum('bnqhgd,bnkhd->bhgnqk', qb, kb).astype(jnp.float32) * scale
    s_loc = jnp.where(valid, s_loc, -jnp.inf)
    s_ctx = jnp.einsum('bnqhgd,bshd->bhgnqs', qb, k_ctx).astype(jnp.float32) * scale
    sk = jnp.broadcast_to(sink.astype(jnp.float32)[None, :, :, None, None, None], s_ctx.shape[:-1] + (1,))
    p = jax.nn.softmax(jnp.concatenate([s_ctx, s_loc, sk], axis=-1), axis=-1).astype(v.dtype)
    out = (jnp.einsum('bhgnqs,bshd->bnqhgd', p[..., :S], v_ctx)
           + jnp.einsum('bhgnqk,bnkhd->bnqhgd', p[..., S:S + 3 * WIN_BLOCK], vb))
    return out.reshape(B, T, HQ * Dh)

def neighbourhood_attention(q, k, v, k_ctx, v_ctx, rpb):
    B, T, H, Dh = q.shape
    R = T // GRID_W
    KH = min(NAT_ROWS, R)
    S = k_ctx.shape[1]
    scale = Dh ** -0.5
    rows = jnp.arange(R)
    cols = jnp.arange(GRID_W)
    row_idx = jnp.clip(rows - KH // 2, 0, R - KH)[:, None] + jnp.arange(KH)[None, :]
    col_start = jnp.clip(cols - NAT_COLS // 2, 0, GRID_W - NAT_COLS)
    col_ok = (cols[None, :] >= col_start[:, None]) & (cols[None, :] < col_start[:, None] + NAT_COLS)
    grid = lambda a: a.reshape(B, R, GRID_W, H, a.shape[-1])
    qg = grid(q)
    kg = grid(k)[:, row_idx]
    vg = grid(v)[:, row_idx]
    dr = row_idx - rows[:, None] + (NAT_ROWS - 1)
    dc = jnp.clip(cols[None, :] - cols[:, None], -(NAT_COLS - 1), NAT_COLS - 1) + (NAT_COLS - 1)
    bias = rpb.astype(jnp.float32)[:, dr[:, None, :, None], dc[None, :, None, :]]
    s_loc = jnp.einsum('brqhd,brkwhd->bhrqkw', qg, kg).astype(jnp.float32) * scale + bias[None]
    s_loc = jnp.where(col_ok[None, None, None, :, None, :], s_loc, -jnp.inf)
    s_ctx = jnp.einsum('brqhd,bshd->bhrqs', qg, k_ctx).astype(jnp.float32) * scale
    logits = jnp.concatenate([s_ctx, s_loc.reshape(B, H, R, GRID_W, KH * GRID_W)], axis=-1)
    p = jax.nn.softmax(logits, axis=-1).astype(v.dtype)
    p_loc = p[..., S:].reshape(B, H, R, GRID_W, KH, GRID_W)
    out = (jnp.einsum('bhrqs,bshd->brqhd', p[..., :S], v_ctx)
           + jnp.einsum('bhrqkw,brkwhd->brqhd', p_loc, vg))
    return out.reshape(B, T, H * Dh)

def mlstm_prepare(zq, zk, zv, zg, gate_b):
    B, T, _ = zq.shape
    heads = lambda z, d: jnp.swapaxes(z.reshape(B, T, ML_HEADS, d), 1, 2).astype(jnp.float32)
    q = heads(zq, ML_DK)
    k = heads(zk, ML_DK) * (ML_DK ** -0.5)
    v = heads(zv, ML_DV)
    g = (zg.astype(jnp.float32) + gate_b.astype(jnp.float32)).reshape(B, T, 4, ML_HEADS)
    g = jnp.swapaxes(jnp.moveaxis(g, 2, 0), 2, 3)
    return q, k, v, g[0], jax.nn.log_sigmoid(g[1]), g[2], jax.nn.log_sigmoid(g[3])

def mlstm_scan(q, k, v, ig, lf, c0, n0, m0):
    B, H, T, _ = q.shape
    NC = T // ML_CHUNK
    chunks = lambda a: jnp.moveaxis(a.reshape(B, H, NC, ML_CHUNK, *a.shape[3:]), 2, 0)
    tril = jnp.tril(jnp.ones((ML_CHUNK, ML_CHUNK), dtype=bool))

    def step(carry, xs):
        C, n, m = carry
        qc, kc, vc, ic, fc = xs
        b = jnp.cumsum(fc, axis=-1)
        log_d = jnp.where(tril, b[..., :, None] - b[..., None, :] + ic[..., None, :], -jnp.inf)
        m_prev = b + m[..., None]
        m_t = jnp.maximum(m_prev, jnp.max(log_d, axis=-1))
        dmat = jnp.exp(log_d - m_t[..., None])
        w_prev = jnp.exp(m_prev - m_t)
        s = jnp.einsum('bhtd,bhsd->bhts', qc, kc) * dmat
        num = jnp.einsum('bhts,bhsv->bhtv', s, vc) + w_prev[..., None] * jnp.einsum('bhtd,bhdv->bhtv', qc, C)
        den = jnp.sum(s, axis=-1) + w_prev * jnp.einsum('bhtd,bhd->bht', qc, n)
        h = num / jnp.maximum(jnp.abs(den), jnp.exp(-m_t))[..., None]
        b_last = b[..., -1]
        log_w = b_last[..., None] - b + ic
        m_new = jnp.maximum(b_last + m, jnp.max(log_w, axis=-1))
        w = jnp.exp(log_w - m_new[..., None])
        decay = jnp.exp(b_last + m - m_new)
        C_new = decay[..., None, None] * C + jnp.einsum('bhs,bhsd,bhsv->bhdv', w, kc, vc)
        n_new = decay[..., None] * n + jnp.einsum('bhs,bhsd->bhd', w, kc)
        return (C_new, n_new, m_new), h

    (C, n, m), h = lax.scan(step, (c0, n0, m0), (chunks(q), chunks(k), chunks(v), chunks(ig), chunks(lf)))
    return jnp.moveaxis(h, 0, 2).reshape(B, H, T, -1), C, n, m

def mlstm_bidir(q, k, v, i_f, lf_f, i_b, lf_b, c0, n0, m0):
    f32 = jnp.float32
    c0, n0, m0 = c0.astype(f32), n0.astype(f32), m0.astype(f32)
    h_f, c_f, n_f, m_f = mlstm_scan(q, k, v, i_f, lf_f, c0[:, 0], n0[:, 0], m0[:, 0])
    rev = lambda a: jnp.flip(a, axis=2)
    h_b, c_b, n_b, m_b = mlstm_scan(rev(q), rev(k), rev(v), rev(i_b), rev(lf_b), c0[:, 1], n0[:, 1], m0[:, 1])
    return (h_f + rev(h_b), jnp.stack([c_f, c_b], axis=1), jnp.stack([n_f, n_b], axis=1),
            jnp.stack([m_f, m_b], axis=1))

def mlstm_output(h, zo, g):
    B, H, T, DV = h.shape
    h = rmsnorm(h, g.astype(jnp.float32))
    h = jnp.swapaxes(h, 1, 2).reshape(B, T, H * DV)
    return (h * jax.nn.sigmoid(zo.astype(jnp.float32))).astype(zo.dtype)

def mla_queries(zq, q_a_g, w_q_up, q_g, rotate):
    B, T, _ = zq.shape
    q = (rmsnorm(zq, q_a_g) @ w_q_up).reshape(B, T, MLA_HEADS, MLA_NOPE + MLA_ROPE)
    q = rmsnorm(q, q_g)
    if rotate:
        q = jnp.concatenate([q[..., :MLA_NOPE], axial_rope(q[..., MLA_NOPE:])], axis=-1)
    return q

def mla_keys(ckv, kpe, w_kv_up, k_g, rotate):
    B, T, _ = ckv.shape
    kv = (ckv @ w_kv_up).reshape(B, T, MLA_HEADS, MLA_NOPE + MLA_V)
    k = jnp.concatenate([kv[..., :MLA_NOPE],
                         jnp.broadcast_to(kpe[:, :, None, :], (B, T, MLA_HEADS, MLA_ROPE))], axis=-1)
    k = rmsnorm(k, k_g)
    if rotate:
        k = jnp.concatenate([k[..., :MLA_NOPE], axial_rope(k[..., MLA_NOPE:])], axis=-1)
    return k, kv[..., MLA_NOPE:]

def even_mixer(h, j, P, cache):
    B, T, _ = h.shape
    zq, zk, zv, zo, zg, wq, wk, wv = split_cols(h @ P['even_w_in'][j], EVEN_SPLITS)
    q, k, v, i_f, lf_f, i_b, lf_b = mlstm_prepare(zq, zk, zv, zg, P['ml_gate_b'][j])
    wq = rmsnorm(wq.reshape(B, T, WIN_Q_HEADS, HEAD_DIM), P['win_q_g'][j])
    wk = rmsnorm(wk.reshape(B, T, WIN_KV_HEADS, HEAD_DIM), P['win_k_g'][j])
    wv = wv.reshape(B, T, WIN_KV_HEADS, HEAD_DIM)
    sink = P['win_sink'][j].reshape(WIN_KV_HEADS, WIN_GROUP)
    if cache is None:
        c0 = jnp.zeros((B, 2, ML_HEADS, ML_DK, ML_DV), jnp.float32)
        n0 = jnp.zeros((B, 2, ML_HEADS, ML_DK), jnp.float32)
        m0 = jnp.zeros((B, 2, ML_HEADS), jnp.float32)
        y_win = dense_attention(wq.reshape(B, T, WIN_KV_HEADS, WIN_GROUP, HEAD_DIM), wk, wv, sink)
    else:
        c0, n0, m0, k_ctx, v_ctx = cache
        y_win = window_attention_latent(axial_rope(wq), axial_rope(wk), wv, k_ctx, v_ctx, sink)
    h_ml, c_fin, n_fin, m_fin = mlstm_bidir(q, k, v, i_f, lf_f, i_b, lf_b, c0, n0, m0)
    y_ml = mlstm_output(h_ml, zo, P['ml_out_g'][j])
    out = jnp.concatenate([y_ml, y_win], axis=-1) @ P['even_w_out'][j]
    new = (c_fin, n_fin, m_fin, wk, wv) if cache is None else None
    return out, new

def odd_mixer(h, j, P, cache):
    B, T, _ = h.shape
    zq, zkv, zpe, nq, nk, nv = split_cols(h @ P['odd_w_in'][j], ODD_SPLITS)
    latent = cache is not None
    ckv = rmsnorm(zkv, P['mla_kv_a_g'][j])
    q = mla_queries(zq, P['mla_q_a_g'][j], P['mla_w_q_up'][j], P['mla_q_g'][j], latent)
    k, v = mla_keys(ckv, zpe, P['mla_w_kv_up'][j], P['mla_k_g'][j], latent)
    nq = rmsnorm(nq.reshape(B, T, NAT_HEADS, HEAD_DIM), P['nat_q_g'][j])
    nk = rmsnorm(nk.reshape(B, T, NAT_HEADS, HEAD_DIM), P['nat_k_g'][j])
    nv = nv.reshape(B, T, NAT_HEADS, HEAD_DIM)
    if not latent:
        y_mla = dense_attention(q[:, :, :, None], k, v)
        y_nat = dense_attention(nq[:, :, :, None], nk, nv)
        new = (ckv, zpe, nk, nv)
    else:
        ckv_c, kpe_c, nk_c, nv_c = cache
        k_c, v_c = mla_keys(ckv_c, kpe_c, P['mla_w_kv_up'][j], P['mla_k_g'][j], False)
        y_mla = dense_attention(q[:, :, :, None], jnp.concatenate([k_c, k], axis=1),
                                jnp.concatenate([v_c, v], axis=1))
        y_nat = neighbourhood_attention(nq, nk, nv, nk_c, nv_c, P['nat_rpb'][j])
        new = None
    out = jnp.concatenate([y_mla, y_nat], axis=-1) @ P['odd_w_out'][j]
    return out, new

def moe_experts(xt, expert_id, weight, w_gate, w_up, w_down):
    N, Dm = xt.shape
    M = N * TOP_K
    flat_e = expert_id.reshape(M)
    order = jnp.argsort(flat_e)
    sorted_e = flat_e[order]
    tok = (order // TOP_K).astype(jnp.int32)
    counts = jnp.bincount(flat_e, length=N_EXPERTS)
    padded = (counts + MOE_BLOCK - 1) // MOE_BLOCK * MOE_BLOCK
    pad_end = jnp.cumsum(padded)
    pad_start = pad_end - padded
    seg_start = jnp.cumsum(counts) - counts
    dest = pad_start[sorted_e] + jnp.arange(M) - seg_start[sorted_e]
    n_blocks = -(-M // MOE_BLOCK) + N_EXPERTS
    cap = n_blocks * MOE_BLOCK
    buf_tok = jnp.full((cap,), N, jnp.int32).at[dest].set(tok)
    xbuf = jnp.concatenate([xt, jnp.zeros((1, Dm), xt.dtype)], axis=0)[buf_tok].reshape(n_blocks, MOE_BLOCK, Dm)
    block_e = jnp.minimum(jnp.searchsorted(pad_end, jnp.arange(n_blocks) * MOE_BLOCK, side='right'), N_EXPERTS - 1)

    def run(args):
        xb, e = args
        return (jax.nn.silu(xb @ w_gate[e]) * (xb @ w_up[e])) @ w_down[e]

    ybuf = lax.map(run, (xbuf, block_e)).reshape(cap, Dm)
    y = ybuf[dest] * weight.reshape(M)[order][:, None].astype(xt.dtype)
    return jnp.zeros_like(xt).at[tok].add(y)

def hier_moe(h, l, P):
    B, T, Dm = h.shape
    xt = h.reshape(B * T, Dm)
    pg = jax.nn.softmax((xt @ P['moe_w_group'][l]).astype(jnp.float32)
                        + P['moe_b_group'][l].astype(jnp.float32), axis=-1)
    pg_top, g_idx = lax.top_k(pg, 1)
    el = ((xt @ P['moe_w_expert'][l]).astype(jnp.float32) + P['moe_b_expert'][l].astype(jnp.float32))
    el = el.reshape(B * T, N_GROUPS, EXPERTS_PER_GROUP)
    el_g = jnp.take_along_axis(el, g_idx[:, :, None], axis=1)[:, 0]
    ev, ei = lax.top_k(el_g, TOP_K)
    weight = pg_top * jax.nn.softmax(ev, axis=-1)
    expert_id = g_idx * EXPERTS_PER_GROUP + ei
    y = moe_experts(xt, expert_id, weight, P['moe_w_gate'][l], P['moe_w_up'][l], P['moe_w_down'][l])
    return y.reshape(B, T, Dm)

def trunk_layer(x, l, mod, P, cache):
    sh1, sc1, g1, sh2, sc2, g2 = mod
    h = rmsnorm(x, P['norm1_g'][l]) * (1 + sc1) + sh1
    if l % 2 == 0:
        out, new = even_mixer(h, l // 2, P, cache)
    else:
        out, new = odd_mixer(h, l // 2, P, cache)
    x = x + g1 * out
    h = rmsnorm(x, P['norm2_g'][l]) * (1 + sc2) + sh2
    x = x + g2 * hier_moe(h, l, P)
    return x, new

def setup_inputs(seed: int = 0) -> dict:
    key = jax.random.key(seed)
    ks = iter(jax.random.split(key, 64))
    nrm = lambda shape, scale=1.0: jax.random.normal(next(ks), shape, jnp.float32) * scale
    gain = lambda shape: 1.0 + 0.02 * nrm(shape)
    D = D_MODEL
    gate_base = jnp.repeat(jnp.array([0.0, 3.0, 0.0, 3.0], jnp.float32), ML_HEADS)
    return {
        'x_prompt': nrm((BATCH, SEQ, D)),
        'x_sample': nrm((DEC_BATCH, DEC_SEQ, D)),
        'state_ml_c': nrm((DEC_BATCH, N_EVEN, 2, ML_HEADS, ML_DK, ML_DV), 0.1),
        'state_ml_n': nrm((DEC_BATCH, N_EVEN, 2, ML_HEADS, ML_DK), 0.1),
        'state_ml_m': nrm((DEC_BATCH, N_EVEN, 2, ML_HEADS)),
        'cache_win_k': nrm((DEC_BATCH, N_EVEN, PAST_LEN, WIN_KV_HEADS, HEAD_DIM)),
        'cache_win_v': nrm((DEC_BATCH, N_EVEN, PAST_LEN, WIN_KV_HEADS, HEAD_DIM)),
        'cache_mla_ckv': nrm((DEC_BATCH, N_ODD, PAST_LEN, MLA_KV_LORA)),
        'cache_mla_kpe': nrm((DEC_BATCH, N_ODD, PAST_LEN, MLA_ROPE)),
        'cache_nat_k': nrm((DEC_BATCH, N_ODD, PAST_LEN, NAT_HEADS, HEAD_DIM)),
        'cache_nat_v': nrm((DEC_BATCH, N_ODD, PAST_LEN, NAT_HEADS, HEAD_DIM)),
        'c': nrm((DEC_BATCH, D)),
        'c_ctx': nrm((D,)),
        'ada_w': nrm((DEPTH, D, 6 * D), 0.5 * D ** -0.5),
        'ada_b': nrm((DEPTH, 6 * D), 0.02),
        'norm1_g': gain((DEPTH, D)),
        'norm2_g': gain((DEPTH, D)),
        'even_w_in': nrm((N_EVEN, D, EVEN_IN), D ** -0.5),
        'ml_gate_b': gate_base[None, :] + nrm((N_EVEN, 4 * ML_HEADS), 0.1),
        'ml_out_g': gain((N_EVEN, ML_DV)),
        'win_q_g': gain((N_EVEN, HEAD_DIM)),
        'win_k_g': gain((N_EVEN, HEAD_DIM)),
        'win_sink': nrm((N_EVEN, WIN_Q_HEADS), 0.5),
        'even_w_out': nrm((N_EVEN, EVEN_MIX, D), EVEN_MIX ** -0.5),
        'odd_w_in': nrm((N_ODD, D, ODD_IN), D ** -0.5),
        'mla_q_a_g': gain((N_ODD, MLA_Q_LORA)),
        'mla_kv_a_g': gain((N_ODD, MLA_KV_LORA)),
        'mla_w_q_up': nrm((N_ODD, MLA_Q_LORA, MLA_HEADS * (MLA_NOPE + MLA_ROPE)), MLA_Q_LORA ** -0.5),
        'mla_w_kv_up': nrm((N_ODD, MLA_KV_LORA, MLA_HEADS * (MLA_NOPE + MLA_V)), MLA_KV_LORA ** -0.5),
        'mla_q_g': gain((N_ODD, MLA_NOPE + MLA_ROPE)),
        'mla_k_g': gain((N_ODD, MLA_NOPE + MLA_ROPE)),
        'nat_q_g': gain((N_ODD, HEAD_DIM)),
        'nat_k_g': gain((N_ODD, HEAD_DIM)),
        'nat_rpb': nrm((N_ODD, NAT_HEADS, 2 * NAT_ROWS - 1, 2 * NAT_COLS - 1), 0.5),
        'odd_w_out': nrm((N_ODD, ODD_MIX, D), ODD_MIX ** -0.5),
        'moe_w_group': nrm((DEPTH, D, N_GROUPS), D ** -0.5),
        'moe_b_group': nrm((DEPTH, N_GROUPS), 0.01),
        'moe_w_expert': nrm((DEPTH, D, N_EXPERTS), D ** -0.5),
        'moe_b_expert': nrm((DEPTH, N_EXPERTS), 0.01),
        'moe_w_gate': nrm((DEPTH, N_EXPERTS, D, EXPERT_FF), D ** -0.5),
        'moe_w_up': nrm((DEPTH, N_EXPERTS, D, EXPERT_FF), D ** -0.5),
        'moe_w_down': nrm((DEPTH, N_EXPERTS, EXPERT_FF, D), EXPERT_FF ** -0.5),
    }

def reference(x_prompt, x_sample, state_ml_c, state_ml_n, state_ml_m, cache_win_k, cache_win_v,
              cache_mla_ckv, cache_mla_kpe, cache_nat_k, cache_nat_v, c, c_ctx, ada_w, ada_b,
              norm1_g, norm2_g, even_w_in, ml_gate_b, ml_out_g, win_q_g, win_k_g, win_sink, even_w_out,
              odd_w_in, mla_q_a_g, mla_kv_a_g, mla_w_q_up, mla_w_kv_up, mla_q_g, mla_k_g, nat_q_g, nat_k_g,
              nat_rpb, odd_w_out, moe_w_group, moe_b_group, moe_w_expert, moe_b_expert, moe_w_gate,
              moe_w_up, moe_w_down):
    P = dict(norm1_g=norm1_g, norm2_g=norm2_g, even_w_in=even_w_in, ml_gate_b=ml_gate_b,
             ml_out_g=ml_out_g, win_q_g=win_q_g, win_k_g=win_k_g, win_sink=win_sink,
             even_w_out=even_w_out, odd_w_in=odd_w_in, mla_q_a_g=mla_q_a_g, mla_kv_a_g=mla_kv_a_g,
             mla_w_q_up=mla_w_q_up, mla_w_kv_up=mla_w_kv_up, mla_q_g=mla_q_g, mla_k_g=mla_k_g,
             nat_q_g=nat_q_g, nat_k_g=nat_k_g, nat_rpb=nat_rpb, odd_w_out=odd_w_out,
             moe_w_group=moe_w_group, moe_b_group=moe_b_group, moe_w_expert=moe_w_expert,
             moe_b_expert=moe_b_expert, moe_w_gate=moe_w_gate, moe_w_up=moe_w_up, moe_w_down=moe_w_down)

    x = x_prompt
    ctx_even, ctx_odd = [], []
    for l in range(DEPTH):
        mod = adaln(c_ctx, ada_w[l], ada_b[l])
        x, new = trunk_layer(x, l, mod, P, None)
        if l % 2 == 0:
            ctx_even.append(new)
        else:
            ctx_odd.append(new)
    y_prompt = x
    new_state_ml_c = jnp.stack([s[0] for s in ctx_even], axis=1)
    new_state_ml_n = jnp.stack([s[1] for s in ctx_even], axis=1)
    new_state_ml_m = jnp.stack([s[2] for s in ctx_even], axis=1)
    new_cache_win_k = jnp.stack([s[3] for s in ctx_even], axis=1)
    new_cache_win_v = jnp.stack([s[4] for s in ctx_even], axis=1)
    new_cache_mla_ckv = jnp.stack([s[0] for s in ctx_odd], axis=1)
    new_cache_mla_kpe = jnp.stack([s[1] for s in ctx_odd], axis=1)
    new_cache_nat_k = jnp.stack([s[2] for s in ctx_odd], axis=1)
    new_cache_nat_v = jnp.stack([s[3] for s in ctx_odd], axis=1)

    x = x_sample
    for l in range(DEPTH):
        mod = [m[:, None, :] for m in adaln(c, ada_w[l], ada_b[l])]
        j = l // 2
        if l % 2 == 0:
            cache = (state_ml_c[:, j], state_ml_n[:, j], state_ml_m[:, j], cache_win_k[:, j], cache_win_v[:, j])
        else:
            cache = (cache_mla_ckv[:, j], cache_mla_kpe[:, j], cache_nat_k[:, j], cache_nat_v[:, j])
        x, _ = trunk_layer(x, l, mod, P, cache)
    y_sample = x

    return (y_prompt, y_sample, new_state_ml_c, new_state_ml_n, new_state_ml_m, new_cache_win_k,
            new_cache_win_v, new_cache_mla_ckv, new_cache_mla_kpe, new_cache_nat_k, new_cache_nat_v)


_drawn_inputs = setup_inputs


def setup_inputs(seed=0):
    import zlib

    import numpy as np

    out = dict(_drawn_inputs(seed))
    spreads = {}
    factors = {'state_ml_c': 4.463,
     'state_ml_n': 7.003,
     'state_ml_m': 5.379,
     'cache_win_k': 4.593,
     'cache_win_v': 3.537,
     'cache_mla_ckv': 4.899,
     'cache_mla_kpe': 8.0,
     'cache_nat_k': 3.307,
     'cache_nat_v': 2.767,
     'norm2_g': 2.687,
     'ml_out_g': 8.0,
     'win_q_g': 8.0,
     'win_k_g': 3.628,
     'win_sink': 8.0,
     'mla_q_a_g': 8.0,
     'mla_kv_a_g': 3.097,
     'mla_q_g': 8.0,
     'mla_k_g': 8.0,
     'nat_q_g': 8.0,
     'nat_k_g': 2.898,
     'nat_rpb': 5.754,
     'moe_b_group': 6.474,
     'moe_b_expert': 8.0}
    for name, (base, spread) in spreads.items():
        noise = np.random.default_rng([zlib.crc32(name.encode()), seed]).standard_normal(out[name].shape)
        drawn = base * np.exp(spread * noise) if base else spread * noise
        out[name] = jnp.asarray(drawn.astype(out[name].dtype))
    for name, factor in factors.items():
        out[name] = (out[name] * factor).astype(out[name].dtype)
    return out
```

```python
from contextlib import ExitStack, contextmanager

import numpy as np

import concourse.bass as bass
from concourse import mybir

F32 = mybir.dt.float32
I32 = mybir.dt.int32
U32 = mybir.dt.uint32
ALU = mybir.AluOpType
ACT = mybir.ActivationFunctionType
AX = mybir.AxisListType.X

P = 128
D = 1024
KC = D // P
NT = 3
SEQ, LAT = 128, 256
TOK = SEQ + LAT
GRID_W = 64
EPS = 1e-6
BIG = 1e30
N_EXP, N_GRP, PER_GRP, FF = 32, 4, 8, 512
HEADS, HD = 8, 64
ML_H, ML_D = 4, 128
MLA_QK, MLA_NOPE, MLA_ROPE = 96, 64, 32

RING = 6
UNIT = 4096
BLK = 64
MAX_BLK = -(-TOK // BLK)
OVER = (2 * TOK - 2) // BLK
N_BLK = N_EXP + OVER

EVEN_COLS, ODD_COLS = 2832, 1952
WQ0, WK0, WV0, ZG0 = 2064, 2576, 2704, 2048
ZKV0, ZPE0, NQ0, NK0, NV0 = 256, 384, 416, 928, 1440

CONST = {}
_at = 0
for _name, _width in (("ident", P), ("flip", P), ("tri", P), ("ones", P), ("win", 2 * 384), ("nat", 2 * 256),
                      ("ml_f", P), ("ml_b", P), ("cos64", 2 * 64), ("sin64", 2 * 64),
                      ("cos32", 2 * 32), ("sin32", 2 * 32), ("token", NT), ("iota", 64),
                      ("sel", 4 * P), ("half", 64), ("thr", N_EXP * (MAX_BLK - 1))):
    CONST[_name] = (_at, _width)
    _at += _width
N_CONST = _at


def constants():
    c = np.zeros((P, N_CONST), np.float32)

    def put(name, a):
        at, w = CONST[name]
        c[:, at:at + w] = np.asarray(a, np.float32).reshape(-1, w)

    r = np.arange(P)
    put("ident", np.eye(P))
    put("flip", r[:, None] // GRID_W * GRID_W + GRID_W - 1 - r[:, None] % GRID_W == r[None, :])
    put("tri", r[:, None] < r[None, :])
    put("ones", np.ones((P, P)))
    t = np.arange(LAT)
    near = np.abs(t[:, None] - t[None, :]) <= 128
    win = np.concatenate([np.zeros((LAT, P)), np.where(near, 0, -BIG)], 1)
    put("win", win.reshape(2, P, 384).transpose(1, 0, 2))
    col = t % GRID_W
    start = np.clip(col - 8, 0, GRID_W - 16)
    ok = (col[None, :] >= start[:, None]) & (col[None, :] < start[:, None] + 16)
    put("nat", np.where(ok, 0, -BIG).reshape(2, P, 256).transpose(1, 0, 2))
    put("ml_f", np.where(r[:, None] <= r[None, :], 0, BIG))
    put("ml_b", np.where(r[:, None] >= r[None, :], 0, BIG))
    for width in (64, 32):
        nf = width // 4
        inv = 10000.0 ** (-np.arange(nf, dtype=np.float32) / nf)
        cos, sin = [], []
        for pos in (t // GRID_W, t % GRID_W):
            ang = pos.astype(np.float32)[:, None] * inv[None, :].astype(np.float32)
            cos += [np.cos(ang), np.cos(ang)]
            sin += [-np.sin(ang), np.sin(ang)]
        put(f"cos{width}", np.concatenate(cos, 1).reshape(2, P, width).transpose(1, 0, 2))
        put(f"sin{width}", np.concatenate(sin, 1).reshape(2, P, width).transpose(1, 0, 2))
    put("token", r[:, None] + P * np.arange(NT)[None, :])
    put("iota", np.broadcast_to(np.arange(64), (P, 64)))
    sel = np.zeros((P, 4, P))
    for h in range(4):
        sel[h, h] = 1
    put("sel", sel)
    put("half", np.full((P, 64), -0.5))
    over = BLK * (1 + np.arange(MAX_BLK - 1)) - 0.0
    put("thr", np.broadcast_to(over, (P, N_EXP, MAX_BLK - 1)))
    return c


class Counter:

    def __init__(self, nc, ctx, name):
        self.sem = ctx.enter_context(nc.semaphore(name))
        self.base = self.made = 0

    def adds(self, n):
        self.made += n
        return n

    def at(self, n):
        return self.base + n

    def now(self):
        return self.base + self.made


def weight_units(I):
    units = []
    for l in range(2):
        cols = 6 * D
        units += [(I["ada_w"][l].rearrange("(p c) n -> p c n", c=KC)[:, :, n:n + 512], 512)
                  for n in range(0, cols, 512)]
        w_in = I["odd_w_in" if l else "even_w_in"][0].rearrange("(p c) n -> p c n", c=KC)
        total = ODD_COLS if l else EVEN_COLS
        units += [(w_in[:, :, n:min(n + 512, total)], min(512, total - n)) for n in range(0, total, 512)]
        w_out = I["odd_w_out" if l else "even_w_out"][0].rearrange("(p c) n -> p c n", c=KC)
        units += [(w_out[:, :, n:n + 512], 512) for n in (0, 512)]
        units += [("experts", l)] * (3 * N_EXP)
    return units


class Trunk:

    def __init__(self, nc, ctx, I, O):
        self.nc, self.ctx, self.I, self.O = nc, ctx, I, O
        self.counters = {}
        sb = self.sb
        self.const = sb(ctx, "const", [P, N_CONST])
        self.x = sb(ctx, "x", [P, NT, D])
        self.ring = sb(ctx, "ring", [P, RING, UNIT])
        self.ps = ctx.enter_context(nc.psum_tensor("ps", [P, 8, 512], F32))
        self.units = weight_units(I)
        self.landed = [self.counter(f"landed{i}") for i in range(RING)]
        self.unit_used = self.counter("unit_used")
        dram = lambda name, shape: nc.dram_tensor(name, shape, F32, kind="Internal").ap()
        self.mod_dram = dram("mod_rows", (2, 2, 6 * D))
        self.h_dram = dram("h_rows", (TOK, D))
        self.y_dram = dram("expert_rows", (N_BLK * BLK, D))

    def sb(self, ctx, name, shape, dt=F32):
        return ctx.enter_context(self.nc.sbuf_tensor(name, shape, dt))

    def counter(self, name):
        if name not in self.counters:
            self.counters[name] = Counter(self.nc, self.ctx, name)
        return self.counters[name]

    def c(self, name, parts=P):
        at, w = CONST[name]
        return self.const[0:parts, at:at + w]

    @contextmanager
    def loop(self, engine, start, end):
        before = {name: s.made for name, s in self.counters.items()}
        with engine.Fori(start, end) as i:
            yield i
        for name, s in self.counters.items():
            s.made += (s.made - before.get(name, 0)) * (end - start - 1)

    def end_stage(self):
        for s in self.counters.values():
            s.base += s.made
            s.made = 0

    def unit(self, u):
        n = self.units[u][1]
        return self.ring[:, u % RING, 0:KC * n].rearrange("p (c n) -> p c n", c=KC)

    def load_unit(self, sp, u, i=0):
        slot = u % RING
        if u >= RING:
            sp.wait_ge(self.unit_used.sem, u - RING + 1 + i * RING)
        if self.units[u][0] == "experts":
            l = self.units[u][1]
            first = self.units.index(("experts", l))
            e, part = divmod(u - first, 3)
            src = self.expert_source(l, e + 2 * i, part)
            dst = self.ring[:, slot, :].rearrange("p (c n) -> p c n", c=KC if part < 2 else FF // P)
        else:
            src, _ = self.units[u]
            dst = self.unit(u)
        sp.dma_start(dst, src).then_inc(self.landed[slot].sem, 16)

    def expert_source(self, l, e, part):
        w = self.I[("moe_w_gate", "moe_w_up", "moe_w_down")[part]][l]
        one = w[bass.ds(e, 1)]
        if part < 2:
            return one.rearrange("o (p c) n -> p (o c) n", c=KC)
        return one.rearrange("o (j p) n -> p (o j) n", p=P)

    def load_ahead(self, sp, first, end):
        if first == 0:
            for u in range(min(RING, len(self.units))):
                self.load_unit(sp, u)
        for u in range(first + RING, min(end + RING, len(self.units))):
            self.load_unit(sp, u)

    def used_at(self, u, i=0):
        return u + 1 + i * RING

    def landing(self, u):
        return self.landed[u % RING].sem

    def landed_at(self, u, i=0):
        return (u // RING + 1 + i) * 16


def spread(ap, parts=P):
    return ap.partition_broadcast(parts)


class Turns:

    BANKS = 2

    def __init__(self, T, groups):
        self.T, self.groups = T, groups
        self.done = T.counter("turned")
        self.copied = (T.counter("turned_act"), T.counter("turned_dve"))

    def bank(self, g):
        return self.T.ps[:, g % self.BANKS, :]

    def tensor(self, pe, first=0, end=None):
        T = self.T
        for g in range(first, len(self.groups) if end is None else end):
            sources, _, ready = self.groups[g]
            if ready is not None:
                producer, n = ready
                pe.wait_ge(producer.sem, producer.at(n))
            if g >= self.BANKS:
                self.wait_copied(pe, g - self.BANKS)
            for k, s in enumerate(sources):
                rows, cols = s.shape[0], int(np.prod(s.shape[1:]))
                ins = T.nc.tensor.transpose(self.bank(g)[0:cols, k * rows:(k + 1) * rows], s,
                                            T.c("ident")[0:rows, 0:rows])
            ins.then_inc(self.done.sem, self.done.adds(1))

    def wait_copied(self, engine, g):
        engine.wait_ge(self.copied[g % 2].sem, self.copied[g % 2].at(g // 2 + 1))

    def wait_all(self, engine):
        n = len(self.groups)
        for g in (n - 2, n - 1):
            if g >= 0:
                self.wait_copied(engine, g)

    def copy_out(self, engine, copy, parity, first=0, end=None):
        for g in range(first, len(self.groups) if end is None else end):
            if g % 2 == parity:
                sources, out, _ = self.groups[g]
                rows, cols = sources[0].shape[0], int(np.prod(sources[0].shape[1:]))
                engine.wait_ge(self.done.sem, self.done.at(g + 1))
                src = self.bank(g)[0:cols, 0:rows * len(sources)]
                if len(out.shape) == 3:
                    src = src.rearrange("p (k r) -> p k r", k=len(sources))
                copy(out, src).then_inc(self.copied[parity].sem, self.copied[parity].adds(1))


def stage_modulation(T, l, first):
    nc, I = T.nc, T.I
    n_units = 12
    with ExitStack() as ctx:
        cv = T.sb(ctx, f"cv{l}", [P, 2, KC])
        ce = T.sb(ctx, f"ce{l}", [P, 2, KC])
        rows = T.sb(ctx, f"mod{l}", [2, 6 * D])
        bias = T.sb(ctx, f"ada_b{l}", [2, 6 * D])
        gain = T.sb(ctx, f"gain{l}", [2, 2, D])
        loads, exp, silu = T.counter("loads_act"), T.counter("act_done"), T.counter("dve_done")
        row_done, stored = T.counter("row_done"), T.counter("stored_act")
        const_in = T.counter("const_in")
        blank, blank_out = T.counter("blank"), T.counter("blank_stored")
        extra_rows = T.y_dram[N_EXP * BLK:, :].rearrange("(b p) d -> p b d", p=BLK)
        if l == 0:
            zeros = T.sb(ctx, "zeros", [BLK, D])
        block = ctx.enter_context(nc.Block())

        @block.sync
        def _(sp):
            T.load_ahead(sp, first, first + n_units)

        if l == 0:
            @block.gpsimd
            def _(pool):
                nc.gpsimd.memset(zeros[:, :], 0.0).then_inc(blank.sem, blank.adds(1))
                pool.wait_ge(blank.sem, blank.now())
                pool.dma_start(extra_rows, zeros[:, :].unsqueeze(1).broadcast_to([BLK, OVER, D])).then_inc(blank_out.sem, blank_out.adds(16))
                pool.wait_ge(blank_out.sem, blank_out.at(16))

        @block.scalar
        def _(act):
            act.dma_start(cv[:, 0, :], I["c_ctx"].rearrange("(p c) -> p c", c=KC)).then_inc(loads.sem, loads.adds(16))
            act.dma_start(cv[:, 1, :], I["c"][0].rearrange("(p c) -> p c", c=KC)).then_inc(loads.sem, loads.adds(16))
            act.dma_start(bias[:, :], spread(I["ada_b"][l], 2)).then_inc(loads.sem, loads.adds(16))
            for k, name in enumerate(("norm1_g", "norm2_g")):
                act.dma_start(gain[:, k, :], spread(I[name][l], 2)).then_inc(loads.sem, loads.adds(16))
            if l == 0:
                act.dma_start(T.const[:, :], I["const"]).then_inc(const_in.sem, const_in.adds(16))
                act.dma_start(T.x[:, 0, :], I["x_prompt"][0]).then_inc(const_in.sem, const_in.adds(16))
                act.dma_start(T.x[:, 1:3, :], I["x_sample"][0].rearrange("(t p) d -> p t d", p=P)).then_inc(const_in.sem, const_in.adds(16))
            act.wait_ge(loads.sem, loads.at(32 + 48))
            act.activation(ce[:, :, :], cv[:, :, :], ACT.Exp, scale=-1.0).then_inc(exp.sem, exp.adds(1))
            act.wait_ge(row_done.sem, row_done.at(n_units + 2))
            act.dma_start(T.mod_dram[l], rows[:, :]).then_inc(stored.sem, stored.adds(16))
            act.wait_ge(stored.sem, stored.at(16))
            if l == 0:
                act.wait_ge(const_in.sem, const_in.at(48))

        @block.vector
        def _(dve):
            dve.wait_ge(exp.sem, exp.at(1))
            nc.vector.tensor_scalar(ce[:, :, :], ce[:, :, :], 1.0, None, ALU.add).then_inc(silu.sem, silu.adds(1))
            dve.wait_ge(silu.sem, silu.now())
            nc.vector.reciprocal(ce[:, :, :], ce[:, :, :]).then_inc(silu.sem, silu.adds(1))
            dve.wait_ge(silu.sem, silu.now())
            nc.vector.tensor_tensor(cv[:, :, :], cv[:, :, :], ce[:, :, :], ALU.mult).then_inc(silu.sem, silu.adds(1))
            dve.wait_ge(loads.sem, loads.at(80))
            for n in range(n_units):
                dve.wait_ge(T.unit_used.sem, T.used_at(first + n))
                cols = slice(n * 512, n * 512 + 512)
                nc.vector.tensor_tensor(rows[:, cols], T.ps[0:2, n % 2, :], bias[:, cols], ALU.add).then_inc(row_done.sem, row_done.adds(1))
            dve.wait_ge(row_done.sem, row_done.at(n_units))
            for k, at in ((0, D), (1, 4 * D)):
                r = rows[:, at:at + D]
                nc.vector.scalar_tensor_tensor(out=r, in0=r, scalar=1.0, in1=gain[:, k, :],
                                                           op0=ALU.add, op1=ALU.mult).then_inc(row_done.sem, row_done.adds(1))

        @block.tensor
        def _(pe):
            pe.wait_ge(silu.sem, silu.at(3))
            for n in range(n_units):
                u = first + n
                pe.wait_ge(T.landing(u), T.landed_at(u))
                if n >= 2:
                    pe.wait_ge(row_done.sem, row_done.at(n - 1))
                for c in range(KC):
                    ins = nc.tensor.matmul(T.ps[0:2, n % 2, :], cv[:, :, c], T.unit(u)[:, c, :],
                                           start=(c == 0), stop=(c == KC - 1))
                ins.then_inc(T.unit_used.sem, T.unit_used.adds(1))
    T.end_stage()


def stage_projection(T, l, first, z):
    nc = T.nc
    total = ODD_COLS if l else EVEN_COLS
    n_units = -(-total // 512)
    with ExitStack() as ctx:
        scale = T.sb(ctx, f"scale{l}", [P, 2, D])
        shift = T.sb(ctx, f"shift{l}", [P, 2, D])
        h = T.sb(ctx, f"h{l}", [P, 2, D])
        hT = T.sb(ctx, f"hT{l}", [P, KC, TOK])
        stat = T.sb(ctx, f"stat{l}", [P, 2, NT])
        loads, squares, rstd, row = T.counter("loads_act"), T.counter("squares"), T.counter("rstd"), T.counter("rows")
        product, out = T.counter("product"), (T.counter("z_act"), T.counter("z_dve"))
        steps = T.counter("dve_done")
        groups = []
        for t in range(NT):
            for k in range(2):
                src = [h[:, t % 2, c::KC] for c in range(4 * k, 4 * k + 4)]
                ready = (row, t + 1) if k == 0 else None
                groups.append((src, hT[:, 4 * k:4 * k + 4, t * P:(t + 1) * P], ready))
        turns = Turns(T, groups)
        block = ctx.enter_context(nc.Block())

        def z_out(engine, copy, parity):
            for e in range(n_units * NT):
                if e % 2 != parity:
                    continue
                n, t = divmod(e, NT)
                cols = min(512, total - n * 512)
                if t < NT - 1:
                    engine.wait_ge(product.sem, product.at(n * (NT - 1) + t + 1))
                else:
                    engine.wait_ge(T.unit_used.sem, T.used_at(first + n))
                copy(z[:, t, n * 512:n * 512 + cols], T.ps[:, 4 + e % 4, 0:cols]).then_inc(out[parity].sem, out[parity].adds(1))

        @block.sync
        def _(sp):
            T.load_ahead(sp, first, first + n_units)

        @block.scalar
        def _(act):
            for buf, k in ((scale, 1), (shift, 0)):
                act.dma_start(buf[:, :, :], spread(T.mod_dram[l, :, k * D:(k + 1) * D])).then_inc(loads.sem, loads.adds(16))
            for t in range(NT):
                if t >= 1:
                    act.wait_ge(squares.sem, squares.at(t))
                act.activation(hT[:, 0:KC, 0:P], T.x[:, t, :].rearrange("p (c n) -> p c n", c=KC),
                                          ACT.Square, accum_out=stat[:, 0, t:t + 1]).then_inc(squares.sem, squares.adds(1))
            act.wait_ge(squares.sem, squares.at(NT))
            turns.copy_out(act, nc.scalar.copy, 0)
            z_out(act, nc.scalar.copy, 0)

        @block.gpsimd
        def _(pool):
            pool.wait_ge(squares.sem, squares.at(NT))
            nc.gpsimd.tensor_scalar(stat[:, 0, :], stat[:, 0, :], 1.0 / D, EPS, ALU.mult, ALU.add).then_inc(rstd.sem, rstd.adds(1))
            pool.wait_ge(rstd.sem, rstd.now())
            nc.gpsimd.tensor_tensor(stat[:, 1, :], stat[:, 0, :], T.c("half")[:, 0:NT], ALU.pow).then_inc(rstd.sem, rstd.adds(1))

        @block.vector
        def _(dve):
            dve.wait_ge(loads.sem, loads.at(32))
            dve.wait_ge(rstd.sem, rstd.at(2))
            for t in range(NT):
                if t >= 2:
                    dve.wait_ge(turns.done.sem, turns.done.at(2 * (t - 1)))
                g = min(t, 1)
                nc.vector.scalar_tensor_tensor(
                    out=h[:, t % 2, :], in0=T.x[:, t, :], scalar=stat[:, 1, t:t + 1], in1=scale[:, g, :],
                    op0=ALU.mult, op1=ALU.mult).then_inc(steps.sem, steps.adds(1))
                dve.wait_ge(steps.sem, steps.now())
                nc.vector.tensor_tensor(h[:, t % 2, :], h[:, t % 2, :], shift[:, g, :], ALU.add).then_inc(row.sem, row.adds(1))
                if t >= 1:
                    turns.copy_out(dve, nc.vector.tensor_copy, 1, 2 * (t - 1), 2 * t)
            turns.copy_out(dve, nc.vector.tensor_copy, 1, 2 * NT - 2)
            z_out(dve, nc.vector.tensor_copy, 1)

        @block.tensor
        def _(pe):
            turns.tensor(pe)
            turns.wait_all(pe)
            for n in range(n_units):
                cols = min(512, total - n * 512)
                pe.wait_ge(T.landing(first + n), T.landed_at(first + n))
                for t in range(NT):
                    e = n * NT + t
                    if e >= 4:
                        pe.wait_ge(out[(e - 4) % 2].sem, out[(e - 4) % 2].at((e - 4) // 2 + 1))
                    for c in range(KC):
                        ins = nc.tensor.matmul(T.ps[:, 4 + e % 4, 0:cols], hT[:, c, t * P:(t + 1) * P],
                                               T.unit(first + n)[:, c, :], start=(c == 0), stop=(c == KC - 1))
                    if t < NT - 1:
                        ins.then_inc(product.sem, product.adds(1))
                    else:
                        ins.then_inc(T.unit_used.sem, T.unit_used.adds(1))
    T.end_stage()


def stage_output(T, l, first, mix):
    nc = T.nc
    with ExitStack() as ctx:
        mixT = T.sb(ctx, f"mixT{l}", [P, KC, TOK])
        part = T.sb(ctx, f"part{l}", [P, 2, 512])
        gate = T.sb(ctx, f"gate{l}", [P, 2, D])
        loads = T.counter("loads_act")
        product, used, steps = T.counter("product"), T.counter("row_done"), T.counter("dve_done")
        groups = [([mix[:, t, c::KC] for c in range(4 * k, 4 * k + 4)],
                   mixT[:, 4 * k:4 * k + 4, t * P:(t + 1) * P], None) for t in range(NT) for k in range(2)]
        turns = Turns(T, groups)
        block = ctx.enter_context(nc.Block())

        @block.sync
        def _(sp):
            T.load_ahead(sp, first, first + 2)

        @block.scalar
        def _(act):
            act.dma_start(gate[:, :, :], spread(T.mod_dram[l, :, 2 * D:3 * D])).then_inc(loads.sem, loads.adds(16))
            turns.copy_out(act, nc.scalar.copy, 0)

        @block.vector
        def _(dve):
            turns.copy_out(dve, nc.vector.tensor_copy, 1)
            dve.wait_ge(loads.sem, loads.at(16))
            for e in range(2 * NT):
                n, t = divmod(e, NT)
                if t < NT - 1:
                    dve.wait_ge(product.sem, product.at(n * (NT - 1) + t + 1))
                else:
                    dve.wait_ge(T.unit_used.sem, T.used_at(first + n))
                cols = slice(n * 512, n * 512 + 512)
                nc.vector.tensor_tensor(part[:, e % 2, :], T.ps[:, 4 + e % 4, :],
                                                       gate[:, min(t, 1), cols], ALU.mult).then_inc(used.sem, used.adds(1))
                dve.wait_ge(used.sem, used.now())
                nc.vector.tensor_tensor(T.x[:, t, cols], T.x[:, t, cols], part[:, e % 2, :], ALU.add).then_inc(steps.sem, steps.adds(1))
                if e >= 1:
                    dve.wait_ge(steps.sem, steps.at(e))

        @block.tensor
        def _(pe):
            turns.tensor(pe)
            turns.wait_all(pe)
            for n in range(2):
                pe.wait_ge(T.landing(first + n), T.landed_at(first + n))
                for t in range(NT):
                    e = n * NT + t
                    if e >= 4:
                        pe.wait_ge(used.sem, used.at(e - 3))
                    for c in range(KC):
                        ins = nc.tensor.matmul(T.ps[:, 4 + e % 4, :], mixT[:, c, t * P:(t + 1) * P],
                                               T.unit(first + n)[:, c, :], start=(c == 0), stop=(c == KC - 1))
                    if t < NT - 1:
                        ins.then_inc(product.sem, product.adds(1))
                    else:
                        ins.then_inc(T.unit_used.sem, T.unit_used.adds(1))
    T.end_stage()



class Attention:

    def __init__(self, T, ctx, name, groups):
        self.T, self.groups = T, groups
        self.units = [u for g in groups for u in g[0]]
        n = len(self.units)
        self.masked = T.sb(ctx, name + "_masked", [P, 2, 384])
        self.prob = T.sb(ctx, name + "_prob", [P, 2, 384])
        self.probT = T.sb(ctx, name + "_probT", [P, 2, 384])
        self.top = T.sb(ctx, name + "_top", [P, n])
        self.shift = T.sb(ctx, name + "_shift", [P, n])
        self.sum = T.sb(ctx, name + "_sum", [P, n])
        self.sink = T.sb(ctx, name + "_sink_exp", [P, n])
        names = ("score", "shift", "prob", "turn", "out", "sink_in", "sink_out", "group")
        (self.s_score, self.s_shift, self.s_prob, self.s_turn, self.s_out, self.s_sink_in, self.s_sink_out,
         self.s_group) = (T.counter("att_" + s) for s in names)
        self.copied = (T.counter("att_copied_act"), T.counter("att_copied_dve"))

    def tensor(self, pe):
        T, nc, n = self.T, self.T.nc, len(self.units)
        for i in range(n + 2):
            if i < n:
                q, k = self.units[i][:2]
                if i >= 2:
                    pe.wait_ge(self.s_prob.sem, self.s_prob.at(i - 1))
                nc.tensor.matmul(T.ps[:, i % 2, 0:k.shape[1]], q, k, start=True, stop=True).then_inc(self.s_score.sem, self.s_score.adds(1))
            if 1 <= i < n + 1:
                u = i - 1
                keys = self.units[u][1].shape[1]
                pe.wait_ge(self.s_prob.sem, self.s_prob.at(u + 1))
                if u >= 2:
                    pe.wait_ge(self.copied[u % 2].sem, self.copied[u % 2].at(u // 2))
                for j in range(keys // P):
                    ins = nc.tensor.transpose(T.ps[:, 2 + u % 2, j * P:(j + 1) * P],
                                              self.prob[:, u % 2, j * P:(j + 1) * P], T.c("ident"))
                ins.then_inc(self.s_turn.sem, self.s_turn.adds(1))
            if i >= 2:
                u = i - 2
                g, h = self.place(u)
                values = self.units[u][2]
                pe.wait_ge(self.copied[u % 2].sem, self.copied[u % 2].at(u // 2 + 1))
                if h == 0 and g >= 2:
                    pe.wait_ge(self.s_group.sem, self.s_group.at(g - 1))
                for j, v in enumerate(values):
                    ins = nc.tensor.matmul(T.ps[:, 4 + g % 2, h * HD:(h + 1) * HD],
                                           self.probT[:, u % 2, j * P:(j + 1) * P], v,
                                           start=(j == 0), stop=(j == len(values) - 1))
                ins.then_inc(self.s_out.sem, self.s_out.adds(1))

    def place(self, u):
        return u // HEADS, u % HEADS

    def copy_out(self, engine, copy, u):
        if 0 <= u < len(self.units):
            keys = self.units[u][1].shape[1]
            engine.wait_ge(self.s_turn.sem, self.s_turn.at(u + 1))
            if u >= 2:
                engine.wait_ge(self.s_out.sem, self.s_out.at(u - 1))
            copy(self.probT[:, u % 2, 0:keys], self.T.ps[:, 2 + u % 2, 0:keys]).then_inc(self.copied[u % 2].sem, self.copied[u % 2].adds(1))

    def sinks(self):
        return [g for g in range(len(self.groups)) if self.groups[g][2] is not None]

    def scalar(self, act):
        nc, n = self.T.nc, len(self.units)
        for i in range(n + 3):
            if i < n:
                q, k, _, mask, scale = self.units[i]
                keys = k.shape[1]
                act.wait_ge(self.s_shift.sem, self.s_shift.at(i + 1))
                if i >= 2:
                    act.wait_ge(self.s_turn.sem, self.s_turn.at(i - 1))
                src = self.T.ps[:, i % 2, 0:keys] if mask is None else self.masked[:, i % 2, 0:keys]
                act.activation(self.prob[:, i % 2, 0:keys], src, ACT.Exp, bias=self.shift[:, i:i + 1],
                                              scale=scale, accum_out=self.sum[:, i:i + 1]).then_inc(self.s_prob.sem, self.s_prob.adds(1))
            if i >= 1 and (i - 1) % 2 == 0:
                self.copy_out(act, nc.scalar.copy, i - 1)
            g = (i - 2) // HEADS
            if i >= 2 and (i - 2) % HEADS == HEADS - 1 and self.groups[g][2] is not None:
                act.wait_ge(self.s_sink_in.sem, self.s_sink_in.at(self.sinks().index(g) + 1))
                cols = self.sink[:, g * HEADS:(g + 1) * HEADS]
                act.activation(cols, cols, ACT.Exp).then_inc(self.s_sink_out.sem, self.s_sink_out.adds(1))

    def vector(self, dve):
        nc, T, n = self.T.nc, self.T, len(self.units)
        steps = T.counter("dve_done")
        for i in range(n + 3):
            if i < n:
                g, h = self.place(i)
                q, k, _, mask, scale = self.units[i]
                keys = k.shape[1]
                dve.wait_ge(self.s_score.sem, self.s_score.at(i + 1))
                scores = T.ps[:, i % 2, 0:keys]
                top = self.top[:, i:i + 1]
                if mask is None:
                    nc.vector.reduce_max(top, scores, AX).then_inc(steps.sem, steps.adds(1))
                    dve.wait_ge(steps.sem, steps.now())
                else:
                    if i >= 2:
                        dve.wait_ge(self.s_prob.sem, self.s_prob.at(i - 1))
                    nc.vector.tensor_tensor_reduce(
                        out=self.masked[:, i % 2, 0:keys], in0=scores, in1=mask, scale=1.0, scalar=-3e38,
                        op0=ALU.add, op1=ALU.max, accum_out=top).then_inc(steps.sem, steps.adds(1))
                    dve.wait_ge(steps.sem, steps.now())
                sink = self.groups[g][2]
                if sink is None:
                    nc.vector.tensor_scalar(self.shift[:, i:i + 1], top, -scale, None, ALU.mult).then_inc(self.s_shift.sem, self.s_shift.adds(1))
                else:
                    nc.vector.tensor_scalar(self.shift[:, i:i + 1], top, -scale,
                                                            sink[:, HEADS + h:HEADS + h + 1], ALU.mult, ALU.min).then_inc(self.s_shift.sem, self.s_shift.adds(1))
            if i >= 1 and (i - 1) % 2 == 1:
                self.copy_out(dve, nc.vector.tensor_copy, i - 1)
            if i >= 2 and (i - 2) % HEADS == HEADS - 1:
                g = (i - 2) // HEADS
                _, out, sink = self.groups[g]
                cols = slice(g * HEADS, (g + 1) * HEADS)
                dve.wait_ge(self.s_prob.sem, self.s_prob.at((g + 1) * HEADS))
                if sink is not None:
                    nc.vector.tensor_tensor(self.sink[:, cols], self.shift[:, cols],
                                                              sink[:, 0:HEADS], ALU.add).then_inc(self.s_sink_in.sem, self.s_sink_in.adds(1))
                    dve.wait_ge(self.s_sink_out.sem, self.s_sink_out.at(self.sinks().index(g) + 1))
                    nc.vector.tensor_tensor(self.sum[:, cols], self.sum[:, cols],
                                                            self.sink[:, cols], ALU.add).then_inc(steps.sem, steps.adds(1))
                    dve.wait_ge(steps.sem, steps.now())
                nc.vector.reciprocal(self.sum[:, cols], self.sum[:, cols]).then_inc(steps.sem, steps.adds(1))
                dve.wait_ge(steps.sem, steps.now())
                dve.wait_ge(self.s_out.sem, self.s_out.at((g + 1) * HEADS))
                each = self.sum[:, cols].unsqueeze(2).broadcast_to([P, HEADS, HD])
                nc.vector.tensor_tensor(
                    out, T.ps[:, 4 + g % 2, 0:HEADS * HD].rearrange("p (h d) -> p h d", h=HEADS), each, ALU.mult).then_inc(self.s_group.sem, self.s_group.adds(1))


def key_order(kT):
    return kT[..., 0:P], kT[..., P:4 * P]


def stage_window(T, z, mix):
    nc, I, O = T.nc, T.I, T.O
    qk_heads = 10
    with ExitStack() as ctx:
        sq = mix[:, :, 0:qk_heads * HD]
        rot = z[:, 1:3, WQ0:WQ0 + qk_heads * HD]
        stat = T.sb(ctx, "win_stat", [P, 2, NT * qk_heads])
        gains = T.sb(ctx, "win_gain", [P, 2, HD])
        sink = T.sb(ctx, "win_sink", [P, 2 * HEADS])
        kc = T.sb(ctx, "win_kc", [P, P])
        vc = T.sb(ctx, "win_vc", [P, P])
        qT = T.sb(ctx, "win_qT", [P, 4, TOK])
        kT = T.sb(ctx, "win_kT", [P, 4 * P])
        loads, squares, sums, rstd = T.counter("loads_act"), T.counter("squares"), T.counter("sums"), T.counter("rstd")
        steps, ready, rotated, stored = (T.counter("dve_done"), T.counter("rows"), T.counter("pool_done"),
                                         T.counter("stored_act"))
        normed = T.counter("normed")
        qk = z[:, :, WQ0:WQ0 + qk_heads * HD]
        by_head = qk.rearrange("p t (h d) -> p t h d", d=HD)
        paired = T.sb(ctx, "win_paired", [P, NT, qk_heads * HD])
        paired_heads = paired[:, :, :].rearrange("p t (h d) -> p t h d", d=HD)
        groups = [([paired[:, t, 2 * j * HD:2 * (j + 1) * HD] for t in range(NT)], qT[:, j, :],
                   (ready, 1) if j == 0 else None) for j in range(4)]
        keys = paired[:, :, HEADS * HD:]
        groups.append(([keys[:, 0, :], kc[:, :], keys[:, 1, :], keys[:, 2, :]],
                       kT[:, :], (loads, 5 * 16)))
        turns = Turns(T, groups)

        att_groups = []
        for t in range(NT):
            units = []
            for h in range(HEADS):
                kv = h // 4
                rows = slice(kv * HD, kv * HD + HD)
                k = key_order(kT[rows, :])[min(t, 1)]
                own = [z[:, s, WV0 + kv * HD:WV0 + (kv + 1) * HD] for s in range(NT)]
                values = own[0:1] if t == 0 else [vc[:, kv * HD:(kv + 1) * HD]] + own[1:]
                mask = None if t == 0 else T.c("win")[:, (t - 1) * 384:t * 384]
                units.append((qT[rows, h % 4, t * P:(t + 1) * P], k, values, mask, HD ** -0.5))
            out = mix[:, t, 512:1024].rearrange("p (h d) -> p h d", d=HD)
            att_groups.append((units, out, sink))
        att = Attention(T, ctx, "win", att_groups)
        block = ctx.enter_context(nc.Block())

        @block.scalar
        def _(act):
            for dst, src in ((gains[:, 0, :], spread(I["win_q_g"][0])), (gains[:, 1, :], spread(I["win_k_g"][0])),
                             (sink[:, 0:HEADS], spread(I["win_sink"][0])),
                             (kc[:, :], I["cache_win_k"][0, 0].rearrange("s h d -> s (h d)")),
                             (vc[:, :], I["cache_win_v"][0, 0].rearrange("s h d -> s (h d)"))):
                act.dma_start(dst, src).then_inc(loads.sem, loads.adds(16))
            act.activation(sq[:, :, :], qk, ACT.Square).then_inc(squares.sem, squares.adds(1))
            turns.copy_out(act, nc.scalar.copy, 0)
            att.scalar(act)
            act.wait_ge(normed.sem, normed.at(1))
            act.dma_start(O["win_k"][0, 0].rearrange("s h d -> s (h d)"), keys[:, 0, :]).then_inc(stored.sem, stored.adds(16))
            act.dma_start(O["win_v"][0, 0].rearrange("s h d -> s (h d)"), z[:, 0, WV0:WV0 + P]).then_inc(stored.sem, stored.adds(16))
            act.wait_ge(stored.sem, stored.at(32))

        @block.gpsimd
        def _(pool):
            pool.wait_ge(sums.sem, sums.at(1))
            nc.gpsimd.tensor_scalar(stat[:, 0, :], stat[:, 0, :], 1.0 / HD, EPS, ALU.mult, ALU.add).then_inc(rstd.sem, rstd.adds(1))
            pool.wait_ge(rstd.sem, rstd.now())
            nc.gpsimd.tensor_tensor(stat[:, 1, :], stat[:, 0, :], T.c("half")[:, 0:NT * qk_heads], ALU.pow).then_inc(rstd.sem, rstd.adds(1))
            pool.wait_ge(normed.sem, normed.at(1))
            for t in range(2):
                cos = T.c("cos64")[:, t * HD:(t + 1) * HD].unsqueeze(1).broadcast_to([P, qk_heads, HD])
                nc.gpsimd.tensor_tensor(rot[:, t, :].rearrange("p (h d) -> p h d", d=HD),
                                                   paired_heads[:, t + 1], cos, ALU.mult).then_inc(rotated.sem, rotated.adds(1))

        @block.vector
        def _(dve):
            dve.wait_ge(squares.sem, squares.at(1))
            nc.vector.reduce_sum(stat[:, 0, :].rearrange("p (t h) -> p t h", t=NT),
                                         sq[:, :, :].rearrange("p t (h d) -> p t h d", d=HD), AX).then_inc(sums.sem, sums.adds(1))
            dve.wait_ge(loads.sem, loads.at(5 * 16))
            nc.vector.tensor_scalar(sink[:, HEADS:], sink[:, 0:HEADS], -1.0, None, ALU.mult).then_inc(steps.sem, steps.adds(1))
            dve.wait_ge(steps.sem, steps.now())
            dve.wait_ge(rstd.sem, rstd.at(2))
            each = stat[:, 1, :].rearrange("p (t h) -> p t h", t=NT).unsqueeze(3).broadcast_to([P, NT, qk_heads, HD])
            nc.vector.tensor_tensor(by_head, by_head, each, ALU.mult).then_inc(steps.sem, steps.adds(1))
            dve.wait_ge(steps.sem, steps.now())
            for t in range(NT):
                gain = gains[:, 0, :].unsqueeze(1).unsqueeze(1).broadcast_to([P, 2, 4, HD])
                nc.vector.tensor_tensor(
                    paired[:, t, 0:512].rearrange("p (j a d) -> p a j d", a=2, d=HD),
                    z[:, t, WQ0:WQ0 + 512].rearrange("p (a j d) -> p a j d", a=2, d=HD), gain, ALU.mult).then_inc(steps.sem, steps.adds(1))
            gain = gains[:, 1, :].unsqueeze(1).unsqueeze(1).broadcast_to([P, NT, 2, HD])
            dve.wait_ge(steps.sem, steps.at(steps.made))
            nc.vector.tensor_tensor(paired_heads[:, :, 8:10, :], by_head[:, :, 8:10, :], gain, ALU.mult).then_inc(normed.sem, normed.adds(1))
            dve.wait_ge(normed.sem, normed.now())
            rope(T, dve, paired_heads[:, 1:3], sq, rot, (rotated, 2), qk_heads, HD, ready)
            turns.copy_out(dve, nc.vector.tensor_copy, 1)
            att.vector(dve)

        @block.tensor
        def _(pe):
            turns.tensor(pe)
            turns.wait_all(pe)
            att.tensor(pe)
    T.end_stage()


def rope(T, dve, x, swapped, straight, straight_ready, heads, width, done):
    nc, steps = T.nc, T.counter("dve_done")
    q = width // 4
    for t in range(2):
        src = x[:, t].rearrange("p h (a b d) -> p h a b d", a=2, b=2)
        dst = swapped[:, t, 0:heads * width].rearrange("p (h a b d) -> p h a b d", h=heads, a=2, b=2)
        sin = T.c(f"sin{width}")[:, t * width:(t + 1) * width].rearrange("p (a b d) -> p a b d", a=2, b=2)
        for b in range(2):
            s = sin[:, :, b, :].unsqueeze(1).broadcast_to([P, heads, 2, q])
            ins = nc.vector.tensor_tensor(dst[:, :, :, b, :], src[:, :, :, 1 - b, :], s, ALU.mult)
            ins.then_inc(steps.sem, steps.adds(1))
    dve.wait_ge(steps.sem, steps.at(steps.made))
    dve.wait_ge(straight_ready[0].sem, straight_ready[0].at(straight_ready[1]))
    ins = nc.vector.tensor_tensor(x, straight[:, :, 0:heads * width].rearrange("p t (h d) -> p t h d", d=width),
                                  swapped[:, 0:2, 0:heads * width].rearrange("p t (h d) -> p t h d", d=width), ALU.add)
    ins.then_inc(done.sem, done.adds(1))



def stage_mlstm(T, z, mix):
    nc, I, O = T.nc, T.I, T.O
    pairs = [(h, d) for h in range(ML_H) for d in range(2)]
    W = ML_D + 1
    k_scale = ML_D ** -0.5
    with ExitStack() as ctx:
        sb = lambda name, shape: T.sb(ctx, "ml_" + name, shape)
        area = sb("area", [P, 4 * TOK])
        gates = area[0:4, :].rearrange("p (k t) -> p k t", k=4)
        decay = area[:, 0:1024].rearrange("p (b n) -> p b n", b=2)
        run = sb("run", [4, 2, 2, TOK])
        gate_b = sb("gate_b", [4, 4])
        m0_row, m0_all = sb("m0_row", [4, 2]), sb("m0_all", [P, 2 * ML_H])
        cols = sb("cols", [P, NT, 3, 2 * ML_H])
        w_prev = sb("w_prev", [P, 2, 2 * ML_H])
        floor = sb("floor", [P, NT, 2 * ML_H])
        qT, kT = sb("qT", [P, 2, TOK]), sb("kT", [P, 2, TOK])
        v1 = z[:, :, WQ0:WQ0 + ML_H * W].rearrange("p t (h n) -> p t h n", h=ML_H)
        c0 = sb("c0", [P, 2 * ML_H, W])
        prob = sb("prob", [P, 2, 512])
        kw = sb("kw", [P, 2, P])
        own = sb("own", [P, 2, NT, W])
        state = sb("state", [P, 2, W])
        den = sb("den", [P, 2, NT])
        stat = sb("stat", [P, 2, NT * ML_H])
        gain = sb("gain", [P, ML_D])
        squares_at = z[:, :, 0:512]

        loads, steps, act_steps, pool_steps = (T.counter("loads_act"), T.counter("dve_done"), T.counter("act_done"),
                                               T.counter("pool_done"))
        gates_turned, gates_in, logs, rows = (T.counter("ml_" + n) for n in ("gates_turned", "gates_in", "logs", "rows"))
        cols_turned, cols_in, factors = (T.counter("ml_" + n) for n in ("cols_turned", "cols_in", "factors"))
        score, spread_m, log_d, exp_d, prob_in, kw_in = (
            T.counter("ml_" + n) for n in ("score", "spread", "log_d", "exp_d", "prob", "kw"))
        num, num_out, c_out, combined = (T.counter("ml_" + n) for n in ("num", "num_out", "c_out", "combined"))
        stored, v_in, squares, sums, rstd = (T.counter("stored_act"), T.counter("ml_v"), T.counter("squares"),
                                             T.counter("sums"), T.counter("rstd"))
        state_stored = [T.counter(f"ml_state_stored{i}") for i in range(2)]
        groups = []
        for h in range(ML_H):
            for base, buf in ((0, qT), (512, kT)):
                groups.append(([z[:, t, base + h * P:base + (h + 1) * P] for t in range(NT)], buf[:, h % 2, :], None))
        turns = Turns(T, groups)
        tiles = [(0, 0), (1, 1), (2, 2), (1, 2), (2, 1)]
        gates_ps = T.ps[0:4, 4:7, :].rearrange("p a b -> p (a b)")
        cols_ps = T.ps[:, 7, 0:NT * 24].rearrange("p (t w n) -> p t w n", t=NT, w=3)
        c_ps = T.ps[:, 7, 2 * W:3 * W]
        block = ctx.enter_context(nc.Block())

        def tile(a, t):
            return a[:, t * P:(t + 1) * P]

        @block.scalar
        def _(act):
            with nc.allow_non_contiguous_dma(reason="small vectors"):
                for dst, src in ((gate_b[:, :], I["ml_gate_b"][0].rearrange("(k h) -> h k", k=4)),
                                 (m0_row[:, :], I["state_ml_m"][0, 0].rearrange("d h -> h d")),
                                 (m0_all[:, :], spread(I["state_ml_m"][0, 0].rearrange("d h -> (d h)"))),
                                 (gain[:, :], spread(I["ml_out_g"][0])),
                                 (c0[:, :, 0:ML_D], I["state_ml_c"][0, 0].rearrange("d h k v -> k (d h) v")),
                                 (c0[:, :, ML_D], I["state_ml_n"][0, 0].rearrange("d h k -> k (d h)"))):
                    act.dma_start(dst, src).then_inc(loads.sem, loads.adds(16))
            turns.copy_out(act, nc.scalar.copy, 0, 0, 2)
            act.wait_ge(gates_in.sem, gates_in.at(4))
            f = gates[:, 1::2, :]
            tmp = run[:, 1, :, :]
            act.activation(tmp, f, ACT.Abs).then_inc(act_steps.sem, act_steps.adds(1))
            act.wait_ge(act_steps.sem, act_steps.now())
            act.activation(tmp, tmp, ACT.Exp, scale=-1.0).then_inc(act_steps.sem, act_steps.adds(1))
            act.wait_ge(act_steps.sem, act_steps.now())
            act.activation(tmp, tmp, ACT.Ln, bias=1.0).then_inc(logs.sem, logs.adds(1))
            zo = z[:, :, 1536:2048]
            act.activation(zo, zo, ACT.Exp, scale=-1.0).then_inc(act_steps.sem, act_steps.adds(1))
            act.wait_ge(rows.sem, rows.at(1))
            with nc.allow_non_contiguous_dma(reason="four numbers"):
                for d in range(2):
                    last = SEQ - 1 if d == 0 else 0
                    act.dma_start(O["ml_m"][0, 0, d].rearrange("(h o) -> h o", o=1),
                                            gates[:, 2 * d + 1, last:last + 1]).then_inc(stored.sem, stored.adds(16))
            act.wait_ge(cols_in.sem, cols_in.at(2))
            act.activation(w_prev[:, :, :], w_prev[:, :, :], ACT.Exp).then_inc(factors.sem, factors.adds(1))
            act.activation(floor[:, :, :], cols[:, :, 2, :], ACT.Exp, scale=-1.0).then_inc(factors.sem, factors.adds(1))
            for i in range(len(pairs) + 1):
                if i < len(pairs):
                    act.wait_ge(log_d.sem, log_d.at(i + 1))
                    act.activation(decay[:, i % 2, :], decay[:, i % 2, :], ACT.Exp, scale=-1.0).then_inc(exp_d.sem, exp_d.adds(1))
                if i >= 1:
                    w = i - 1
                    h, d = pairs[w]
                    act.wait_ge(num.sem, num.at(w + 1))
                    if w >= 2:
                        act.wait_ge(combined.sem, combined.at(w - 1))
                    nc.scalar.copy(own[:, w % 2, :, :], T.ps[:, 6, 0:NT * W].rearrange("p (t n) -> p t n", t=NT)).then_inc(num_out.sem, num_out.adds(1))
                    act.wait_ge(c_out.sem, c_out.at(w + 1))
                    with nc.allow_non_contiguous_dma(reason="n, one number per partition"):
                        act.dma_start(O["ml_c"][0, 0, d, h], state[:, w % 2, 0:ML_D]).then_inc(state_stored[w % 2].sem, state_stored[w % 2].adds(16))
                        act.dma_start(O["ml_n"][0, 0, d, h].rearrange("(k o) -> k o", o=1),
                                                            state[:, w % 2, ML_D:W]).then_inc(state_stored[w % 2].sem, state_stored[w % 2].adds(16))
                if i % 2 == 1 and i + 1 < len(pairs):
                    turns.copy_out(act, nc.scalar.copy, 0, i + 1, i + 3)
            act.wait_ge(combined.sem, combined.at(len(pairs)))
            act.activation(squares_at, mix[:, :, 0:512], ACT.Square).then_inc(squares.sem, squares.adds(1))
            for half in range(2):
                act.wait_ge(state_stored[half].sem, state_stored[half].at(32 * len(pairs) // 2))

        @block.gpsimd
        def _(pool):
            for h in range(ML_H):
                nc.gpsimd.tensor_copy(v1[:, :, h, 0:ML_D], z[:, :, 1024 + h * P:1024 + (h + 1) * P]).then_inc(v_in.sem, v_in.adds(1))
            nc.gpsimd.memset(v1[:, :, :, ML_D:W], 1.0).then_inc(v_in.sem, v_in.adds(1))
            pool.wait_ge(sums.sem, sums.at(1))
            nc.gpsimd.tensor_scalar(stat[:, 0, :], stat[:, 0, :], 1.0 / ML_D, EPS, ALU.mult, ALU.add).then_inc(rstd.sem, rstd.adds(1))
            pool.wait_ge(rstd.sem, rstd.now())
            nc.gpsimd.tensor_tensor(stat[:, 1, :], stat[:, 0, :], T.c("half")[:, 0:NT * ML_H], ALU.pow).then_inc(rstd.sem, rstd.adds(1))

        @block.vector
        def _(dve):
            turns.copy_out(dve, nc.vector.tensor_copy, 1, 0, 2)
            dve.wait_ge(loads.sem, loads.at(6 * 16))
            dve.wait_ge(gates_turned.sem, gates_turned.at(1))
            for k in range(4):
                nc.vector.tensor_scalar(gates[:, k, :], gates_ps[:, k * TOK:(k + 1) * TOK],
                                                    gate_b[:, k:k + 1], None, ALU.add).then_inc(gates_in.sem, gates_in.adds(1))
            dve.wait_ge(logs.sem, logs.at(1))
            f, i_gate = gates[:, 1::2, :], gates[:, 0::2, :]
            nc.vector.scalar_tensor_tensor(out=f, in0=f, scalar=0.0, in1=run[:, 1, :, :],
                                                           op0=ALU.min, op1=ALU.subtract).then_inc(steps.sem, steps.adds(1))
            dve.wait_ge(steps.sem, steps.now())
            spans = (slice(0, SEQ), slice(SEQ, TOK))
            ones = T.c("ones", 4)[:, 0:1]

            def scan(out, src, first, op):
                for d in range(2):
                    for n, span in enumerate(spans):
                        o, s = out[:, d, span], src(d)[:, span]
                        width = span.stop - span.start
                        if d:
                            o, s = o[:, ::-1], s[:, ::-1]
                        nc.vector.tensor_tensor_scan(o, ones.broadcast_to([4, width]), s, first(d, n), ALU.mult, op).then_inc(steps.sem, steps.adds(1))
                dve.wait_ge(steps.sem, steps.at(steps.made))

            scan(run[:, 0], lambda d: gates[:, 2 * d + 1, :], lambda d, n: 0.0, ALU.add)
            nc.vector.tensor_tensor(i_gate, i_gate, run[:, 0], ALU.subtract).then_inc(steps.sem, steps.adds(1))
            dve.wait_ge(steps.sem, steps.now())
            scan(run[:, 1], lambda d: gates[:, 2 * d, :], lambda d, n: m0_row[:, d:d + 1] if n else 0.0, ALU.max)
            nc.vector.tensor_tensor(f, run[:, 0], run[:, 1], ALU.add).then_inc(rows.sem, rows.adds(1))
            dve.wait_ge(cols_turned.sem, cols_turned.at(1))
            nc.vector.tensor_copy(cols[:, :, :, :], cols_ps).then_inc(cols_in.sem, cols_in.adds(1))
            dve.wait_ge(cols_in.sem, cols_in.now())
            m0 = m0_all[:, :].unsqueeze(1).broadcast_to([P, 2, 2 * ML_H])
            nc.vector.tensor_tensor(w_prev[:, :, :], m0, cols[:, 1:3, 1, :], ALU.subtract).then_inc(cols_in.sem, cols_in.adds(1))
            dve.wait_ge(stored.sem, stored.at(32))

            def combine(w):
                h, d = pairs[w]
                o = own[:, w % 2]
                dve.wait_ge(num.sem, num.at(w + 1))
                if w >= 2:
                    dve.wait_ge(state_stored[w % 2].sem, state_stored[w % 2].at(32 * (w // 2)))
                nc.vector.tensor_copy(state[:, w % 2, :], c_ps).then_inc(c_out.sem, c_out.adds(1))
                dve.wait_ge(num_out.sem, num_out.at(w + 1))
                dve.wait_ge(factors.sem, factors.at(2))
                for t in (1, 2):
                    nc.vector.scalar_tensor_tensor(
                        out=o[:, t, :], in0=T.ps[:, 7, (t - 1) * W:t * W], scalar=w_prev[:, t - 1, d * ML_H + h:d * ML_H + h + 1],
                        in1=o[:, t, :], op0=ALU.mult, op1=ALU.add).then_inc(steps.sem, steps.adds(1))
                dve.wait_ge(steps.sem, steps.at(steps.made))
                n = den[:, w % 2, :]
                nc.vector.scalar_tensor_tensor(out=n, in0=o[:, :, ML_D], scalar=-1.0,
                                                               in1=floor[:, :, d * ML_H + h], op0=ALU.mult, op1=ALU.max).then_inc(steps.sem, steps.adds(1))
                dve.wait_ge(steps.sem, steps.now())
                nc.vector.tensor_tensor(n, n, o[:, :, ML_D], ALU.max).then_inc(steps.sem, steps.adds(1))
                dve.wait_ge(steps.sem, steps.now())
                nc.vector.reciprocal(n, n).then_inc(steps.sem, steps.adds(1))
                dve.wait_ge(steps.sem, steps.now())
                each = n.unsqueeze(2).broadcast_to([P, NT, ML_D])
                out = mix[:, :, h * P:(h + 1) * P]
                if d == 0:
                    nc.vector.tensor_tensor(out, o[:, :, 0:ML_D], each, ALU.mult).then_inc(combined.sem, combined.adds(1))
                    dve.wait_ge(combined.sem, combined.now())
                else:
                    nc.vector.tensor_tensor(o[:, :, 0:ML_D], o[:, :, 0:ML_D], each, ALU.mult).then_inc(steps.sem, steps.adds(1))
                    dve.wait_ge(steps.sem, steps.now())
                    nc.vector.tensor_tensor(out, out, o[:, :, 0:ML_D], ALU.add).then_inc(combined.sem, combined.adds(1))
                    dve.wait_ge(combined.sem, combined.now())

            for i in range(len(pairs) + 2):
                if i < len(pairs):
                    h, d = pairs[i]
                    m_all = T.ps[:, 4 + i % 2, 0:TOK]
                    mask = T.c("ml_b" if d else "ml_f")
                    dve.wait_ge(spread_m.sem, spread_m.at(i + 1))
                    if i >= 2:
                        dve.wait_ge(kw_in.sem, kw_in.at(i - 1))
                        dve.wait_ge(prob_in.sem, prob_in.at(i - 1))
                    dec = decay[:, i % 2, :]
                    for slot, (s, t) in enumerate(tiles[0:3] + [tiles[3 + d]]):
                        a = cols[:, s, 0, d * ML_H + h:d * ML_H + h + 1]
                        if slot < 3:
                            ins = nc.vector.scalar_tensor_tensor(out=tile(dec, slot), in0=tile(m_all, t), scalar=a,
                                                                 in1=mask, op0=ALU.subtract, op1=ALU.max)
                        else:
                            ins = nc.vector.tensor_scalar(tile(dec, slot), tile(m_all, t), a, 0.0, ALU.subtract, ALU.max)
                        done = log_d if slot == 3 else steps
                        ins.then_inc(done.sem, done.adds(1))
                if i >= 2:
                    combine(i - 2)
                if i < len(pairs):
                    dve.wait_ge(exp_d.sem, exp_d.at(i + 1))
                    dve.wait_ge(score.sem, score.at(h + 1))
                    pr = prob[:, i % 2, :]
                    if i >= 2:
                        dve.wait_ge(num.sem, num.at(i - 1))
                    same = 4 if d == 0 else 3
                    ins = nc.vector.scalar_tensor_tensor(out=pr[:, 0:same * P], in0=dec[:, 0:same * P], scalar=k_scale,
                                                         in1=T.ps[:, 2, 0:same * P], op0=ALU.mult, op1=ALU.mult)
                    if d:
                        ins.then_inc(steps.sem, steps.adds(1))
                        dve.wait_ge(steps.sem, steps.now())
                        ins = nc.vector.scalar_tensor_tensor(out=pr[:, 3 * P:], in0=dec[:, 3 * P:], scalar=k_scale,
                                                             in1=T.ps[:, 3, 0:P], op0=ALU.mult, op1=ALU.mult)
                    ins.then_inc(prob_in.sem, prob_in.adds(1))
                    last = SEQ - 1 if d == 0 else 0
                    nc.vector.tensor_scalar(kw[:, i % 2, :], z[:, 0, 512 + h * P:512 + (h + 1) * P],
                                                     dec[:, last:last + 1], k_scale, ALU.mult, ALU.mult).then_inc(kw_in.sem, kw_in.adds(1))
                if i % 2 == 1 and i + 1 < len(pairs):
                    turns.copy_out(dve, nc.vector.tensor_copy, 1, i + 1, i + 3)
            dve.wait_ge(act_steps.sem, act_steps.at(3))
            zo = z[:, :, 1536:2048]
            nc.vector.tensor_scalar(zo, zo, 1.0, None, ALU.add).then_inc(steps.sem, steps.adds(1))
            dve.wait_ge(steps.sem, steps.now())
            nc.vector.reciprocal(zo, zo).then_inc(steps.sem, steps.adds(1))
            dve.wait_ge(steps.sem, steps.now())
            dve.wait_ge(squares.sem, squares.at(1))
            heads = lambda a: a.rearrange("p t (h d) -> p t h d", h=ML_H)
            nc.vector.reduce_sum(stat[:, 0, :].rearrange("p (t h) -> p t h", t=NT), heads(squares_at), AX).then_inc(sums.sem, sums.adds(1))
            out = mix[:, :, 0:512]
            g = gain[:, :].unsqueeze(1).unsqueeze(1).broadcast_to([P, NT, ML_H, ML_D])
            nc.vector.tensor_tensor(heads(zo), heads(zo), g, ALU.mult).then_inc(steps.sem, steps.adds(1))
            dve.wait_ge(steps.sem, steps.now())
            nc.vector.tensor_tensor(out, out, zo, ALU.mult).then_inc(steps.sem, steps.adds(1))
            dve.wait_ge(steps.sem, steps.now())
            dve.wait_ge(rstd.sem, rstd.at(2))
            each = stat[:, 1, :].rearrange("p (t h) -> p t h", t=NT).unsqueeze(3).broadcast_to([P, NT, ML_H, ML_D])
            nc.vector.tensor_tensor(heads(out), heads(out), each, ALU.mult).then_inc(steps.sem, steps.adds(1))

        @block.tensor
        def _(pe):
            for k in range(4):
                for t in range(NT):
                    ins = nc.tensor.transpose(gates_ps[:, k * TOK + t * P:k * TOK + (t + 1) * P],
                                              z[:, t, ZG0 + 4 * k:ZG0 + 4 * k + 4], T.c("ident"))
            ins.then_inc(gates_turned.sem, gates_turned.adds(1))
            turns.tensor(pe, 0, 2)
            pe.wait_ge(rows.sem, rows.at(1))
            for t in range(NT):
                for w, of in enumerate((lambda d: gates[:, 2 * d, :], lambda d: run[:, 1, d, :],
                                        lambda d: gates[:, 2 * d + 1, :])):
                    for d in range(2):
                        ins = nc.tensor.transpose(cols_ps[:, t, w, d * ML_H:(d + 1) * ML_H],
                                                  of(d)[:, t * P:(t + 1) * P], T.c("ident", 4)[:, 0:4])
            ins.then_inc(cols_turned.sem, cols_turned.adds(1))
            pe.wait_ge(cols_in.sem, cols_in.at(1))
            pe.wait_ge(loads.sem, loads.at(6 * 16))
            pe.wait_ge(v_in.sem, v_in.at(5))
            for i in range(len(pairs) + 1):
                if i < len(pairs):
                    h, d = pairs[i]
                    if i >= 2:
                        pe.wait_ge(log_d.sem, log_d.at(i - 1))
                    nc.tensor.matmul(T.ps[:, 4 + i % 2, 0:TOK], T.c("sel", 4)[:, h * P:(h + 1) * P],
                                                 run[:, 1, d, :], start=True, stop=True).then_inc(spread_m.sem, spread_m.adds(1))
                    if d == 0:
                        turns.wait_copied(pe, 2 * h)
                        turns.wait_copied(pe, 2 * h + 1)
                        if i:
                            pe.wait_ge(prob_in.sem, prob_in.at(i))
                        for slot, (s, t) in enumerate(tiles):
                            at = T.ps[:, 2 + slot // 4, (slot % 4) * P:(slot % 4 + 1) * P]
                            ins = nc.tensor.matmul(at, tile(kT[:, h % 2, :], s), tile(qT[:, h % 2, :], t),
                                                   start=True, stop=True)
                        ins.then_inc(score.sem, score.adds(1))
                if i >= 1:
                    w = i - 1
                    h, d = pairs[w]
                    if w >= 1:
                        pe.wait_ge(combined.sem, combined.at(w))
                        pe.wait_ge(num_out.sem, num_out.at(w))
                        pe.wait_ge(c_out.sem, c_out.at(w))
                    for t in (1, 2):
                        nc.tensor.matmul(T.ps[:, 7, (t - 1) * W:t * W], tile(qT[:, h % 2, :], t), c0[:, d * ML_H + h, :],
                                         start=True, stop=True)
                    pe.wait_ge(kw_in.sem, kw_in.at(w + 1))
                    nc.tensor.matmul(c_ps, kw[:, w % 2, :], v1[:, 0, h, :], start=True, stop=True)
                    for t in range(NT):
                        own_slots = [slot for slot in (0, 1, 2, 3) if (tiles[0:3] + [tiles[3 + d]])[slot][1] == t]
                        for n, slot in enumerate(own_slots):
                            s = (tiles[0:3] + [tiles[3 + d]])[slot][0]
                            ins = nc.tensor.matmul(T.ps[:, 6, t * W:(t + 1) * W], tile(prob[:, w % 2, :], slot),
                                                   v1[:, s, h, :], start=(n == 0), stop=(n == len(own_slots) - 1))
                    ins.then_inc(num.sem, num.adds(1))
                if i % 2 == 1 and i + 1 < len(pairs):
                    turns.tensor(pe, i + 1, i + 3)
    T.end_stage()



def stage_mla_heads(T, z, mix, qT, kT, v):
    nc, I, O = T.nc, T.I, T.O
    QW, KVW = HEADS * MLA_QK, HEADS * 2 * HD
    with ExitStack() as ctx:
        sb = lambda name, shape: T.sb(ctx, "mla_" + name, shape)
        k = sb("k", [P, 4, QW])
        stat = sb("stat", [P, 2, 6])
        stat_q, stat_k = sb("stat_q", [P, 2, NT * HEADS]), sb("stat_k", [P, 2, 4 * HEADS])
        q = mix[:, :, 0:QW]
        q_heads = q.rearrange("p t (h d) -> p t h d", h=HEADS)
        k_heads = k[:, :, :].rearrange("p t (h d) -> p t h d", h=HEADS)
        q_room, k_room = qT.rearrange("p h t -> p (h t)"), kT.rearrange("p h t -> p (h t)")
        w_q = k_room[:, 0:2 * QW].rearrange("p (c n) -> p c n", c=2)
        qaT = k_room[:, 2 * QW:2 * QW + 2 * TOK].rearrange("p (c t) -> p c t", c=2)
        ckvT = k_room[:, 2 * QW + 2 * TOK:2 * QW + 2 * TOK + 4 * P]
        w_kv = k_room[:, 4 * QW:4 * QW + KVW]
        g_qa, g_kv, ckv_c = mix[:, 0, QW:D], mix[:, 1, QW:QW + P], mix[:, 1, QW + P:D]
        g_heads = mix[:, 2, QW:QW + 2 * MLA_QK].rearrange("p (a d) -> p a d", a=2)
        kpe_c = mix[:, 2, QW + 2 * MLA_QK:QW + 2 * MLA_QK + MLA_ROPE]
        low = z[:, :, 0:384]
        loads, steps, pool_steps = T.counter("loads_act"), T.counter("dve_done"), T.counter("pool_done")
        squares, sums, rstd, normed = T.counter("squares"), T.counter("sums"), T.counter("rstd"), T.counter("normed")
        straight, ready, product = T.counter("straight"), T.counter("rows"), T.counter("product")
        out = (T.counter("z_act"), T.counter("z_dve"))
        stored = T.counter("stored_act")
        groups = [([z[:, t, c:256:2] for t in range(NT)], qaT[:, c, :],
                   (normed, 1) if c == 0 else None) for c in range(2)]
        groups.append(([z[:, 0, ZKV0:ZKV0 + P], ckv_c, z[:, 1, ZKV0:ZKV0 + P], z[:, 2, ZKV0:ZKV0 + P]],
                       ckvT, (loads, 9 * 16)))
        for h in range(HEADS):
            groups.append(([q[:, t, h * MLA_QK:(h + 1) * MLA_QK] for t in range(NT)], qT[0:MLA_QK, h, :],
                           (ready, 1) if h == 0 else None))
        for h in range(HEADS):
            groups.append(([k[:, t, h * MLA_QK:(h + 1) * MLA_QK] for t in range(4)], kT[0:MLA_QK, h, :],
                           (ready, 2) if h == 0 else None))
        turns = Turns(T, groups)
        jobs = [("q", t, half) for t in range(NT) for half in range(2)]
        jobs += [("kv", t, half) for t in range(4) for half in range(2)]
        block = ctx.enter_context(nc.Block())

        def products_out(engine, copy, parity):
            for e, (what, t, half) in enumerate(jobs):
                if e % 2 != parity:
                    continue
                engine.wait_ge(product.sem, product.at(e + 1))
                bank = T.ps[:, 4 + e % 4, :]
                if what == "q":
                    copy(q[:, t, half * 384:(half + 1) * 384], bank[:, 0:384]).then_inc(out[parity].sem, out[parity].adds(1))
                else:
                    both = bank.rearrange("p (h n) -> p h n", h=4)
                    heads = slice(4 * half, 4 * half + 4)
                    copy(k_heads[:, t, heads, 0:HD], both[:, :, 0:HD]).then_inc(T.counter("aside").sem, 1)
                    T.counter("aside").made += 1
                    copy(v[:, t, half * 256:(half + 1) * 256].rearrange("p (h n) -> p h n", h=4),
                                        both[:, :, HD:2 * HD]).then_inc(out[parity].sem, out[parity].adds(1))

        @block.scalar
        def _(act):
            for dst, src in ((g_qa, spread(I["mla_q_a_g"][0])), (g_kv, spread(I["mla_kv_a_g"][0])),
                             (ckv_c, I["cache_mla_ckv"][0, 0]), (kpe_c, I["cache_mla_kpe"][0, 0]),
                             (w_q[:, :, :], I["mla_w_q_up"][0].rearrange("(p c) n -> p c n", c=2)),
                             (w_kv, I["mla_w_kv_up"][0]),
                             (g_heads[:, 0, :], spread(I["mla_q_g"][0])), (g_heads[:, 1, :], spread(I["mla_k_g"][0])),
                             (O["mla_kpe"][0, 0], z[:, 0, ZPE0:ZPE0 + MLA_ROPE])):
                act.dma_start(dst, src).then_inc(loads.sem, loads.adds(16))
            act.activation(q_room[:, 0:NT * 384].rearrange("p (t n) -> p t n", t=NT), low, ACT.Square).then_inc(squares.sem, squares.adds(1))
            turns.copy_out(act, nc.scalar.copy, 0, 0, 3)
            products_out(act, nc.scalar.copy, 0)
            for parity in range(2):
                act.wait_ge(out[parity].sem, out[parity].at(3))
            act.wait_ge(sums.sem, sums.at(2))
            act.activation(q_room[:, 0:NT * QW].rearrange("p (t n) -> p t n", t=NT), q, ACT.Square).then_inc(squares.sem, squares.adds(1))
            for parity in range(2):
                act.wait_ge(out[parity].sem, out[parity].at(7))
            act.wait_ge(pool_steps.sem, pool_steps.at(4))
            act.activation(k_room[:, 0:4 * QW].rearrange("p (t n) -> p t n", t=4), k[:, :, :], ACT.Square).then_inc(squares.sem, squares.adds(1))
            turns.copy_out(act, nc.scalar.copy, 0, 3)
            act.dma_start(O["mla_ckv"][0, 0], z[:, 0, ZKV0:ZKV0 + P]).then_inc(stored.sem, stored.adds(16))
            act.wait_ge(stored.sem, stored.at(16))

        def rotate(pool, n, heads, room):
            pool.wait_ge(normed.sem, normed.at(n))
            for t in range(2):
                cos = T.c("cos32")[:, t * 32:(t + 1) * 32].unsqueeze(1).broadcast_to([P, HEADS, 32])
                nc.gpsimd.tensor_tensor(room[:, t].rearrange("p (h d) -> p h d", h=HEADS),
                                                    heads[:, t, :, MLA_NOPE:], cos, ALU.mult).then_inc(straight.sem, straight.adds(1))

        def power(pool, s, ready_at, scales):
            pool.wait_ge(sums.sem, sums.at(ready_at))
            for cols, n in scales:
                nc.gpsimd.tensor_scalar(s[:, 0, cols], s[:, 0, cols], 1.0 / n, EPS, ALU.mult, ALU.add).then_inc(rstd.sem, rstd.adds(1))
                pool.wait_ge(rstd.sem, rstd.now())
            width = s.shape[2]
            nc.gpsimd.tensor_tensor(s[:, 1, :], s[:, 0, :], T.c("half")[:, 0:width], ALU.pow).then_inc(rstd.sem, rstd.adds(1))

        @block.gpsimd
        def _(pool):
            power(pool, stat, 2, ((slice(0, 3), 256), (slice(3, 6), P)))
            pool.wait_ge(loads.sem, loads.at(9 * 16))
            for t, pe_row in enumerate((z[:, 0, ZPE0:ZPE0 + MLA_ROPE], kpe_c, z[:, 1, ZPE0:ZPE0 + MLA_ROPE],
                                        z[:, 2, ZPE0:ZPE0 + MLA_ROPE])):
                nc.gpsimd.tensor_copy(k_heads[:, t, :, MLA_NOPE:],
                                                    pe_row.unsqueeze(1).broadcast_to([P, HEADS, MLA_ROPE])).then_inc(pool_steps.sem, pool_steps.adds(1))
            power(pool, stat_q, 3, ((slice(0, NT * HEADS), MLA_QK),))
            rotate(pool, 2, q_heads[:, 1:3], z[:, 0:2, 0:256])
            power(pool, stat_k, 4, ((slice(0, 4 * HEADS), MLA_QK),))
            rotate(pool, 3, k_heads[:, 2:4], k_room[:, 0:512].rearrange("p (t n) -> p t n", t=2))

        @block.vector
        def _(dve):
            dve.wait_ge(squares.sem, squares.at(1))
            sq = q_room[:, 0:NT * 384].rearrange("p (t n) -> p t n", t=NT)
            nc.vector.reduce_sum(stat[:, 0, 0:3], sq[:, :, 0:256], AX).then_inc(sums.sem, sums.adds(1))
            nc.vector.reduce_sum(stat[:, 0, 3:6], sq[:, :, 256:384], AX).then_inc(sums.sem, sums.adds(1))
            dve.wait_ge(loads.sem, loads.at(9 * 16))
            dve.wait_ge(rstd.sem, rstd.at(3))
            for t in range(NT):
                for at, n, g, col in ((0, 256, g_qa, t), (256, P, g_kv, 3 + t)):
                    x = z[:, t, at:at + n]
                    nc.vector.scalar_tensor_tensor(out=x, in0=x, scalar=stat[:, 1, col:col + 1], in1=g[:, :],
                                                            op0=ALU.mult, op1=ALU.mult).then_inc(steps.sem, steps.adds(1))
            dve.wait_ge(steps.sem, steps.at(steps.made))
            nc.vector.tensor_copy(stat[:, 0, 0:1], stat[:, 1, 0:1]).then_inc(normed.sem, normed.adds(1))
            turns.copy_out(dve, nc.vector.tensor_copy, 1, 0, 3)
            products_out(dve, nc.vector.tensor_copy, 1)
            for n, (x, tiles, s, room, g, last) in enumerate((
                    (q_heads, NT, stat_q, q_room, 0, 3), (k_heads, 4, stat_k, k_room, 1, 5))):
                dve.wait_ge(squares.sem, squares.at(2 + n))
                nc.vector.reduce_sum(s[:, 0, :].rearrange("p (t h) -> p t h", t=tiles),
                                             room[:, 0:tiles * QW].rearrange("p (t h d) -> p t h d", t=tiles, h=HEADS), AX).then_inc(sums.sem, sums.adds(1))
                dve.wait_ge(rstd.sem, rstd.at(5 + 2 * n))
                each = s[:, 1, :].rearrange("p (t h) -> p t h", t=tiles).unsqueeze(3).broadcast_to([P, tiles, HEADS, MLA_QK])
                nc.vector.tensor_tensor(x, x, each, ALU.mult).then_inc(steps.sem, steps.adds(1))
                dve.wait_ge(steps.sem, steps.now())
                gain = g_heads[:, g, :].unsqueeze(1).unsqueeze(1).broadcast_to([P, tiles, HEADS, MLA_QK])
                nc.vector.tensor_tensor(x, x, gain, ALU.mult).then_inc(normed.sem, normed.adds(1))
                dve.wait_ge(normed.sem, normed.now())
                turned = x[:, tiles - 2:tiles, :, MLA_NOPE:]
                plain = z[:, 0:2, 0:256] if n == 0 else room[:, 0:512].rearrange("p (t n) -> p t n", t=2)
                spare = room[:, 1024:1536].rearrange("p (t n) -> p t n", t=2)
                rope(T, dve, turned, spare, plain, (straight, 2 * (n + 1)), HEADS, MLA_ROPE, ready)
            turns.copy_out(dve, nc.vector.tensor_copy, 1, 3)

        @block.tensor
        def _(pe):
            turns.tensor(pe, 0, 3)
            for g in range(3):
                turns.wait_copied(pe, g)
            for e, (what, t, half) in enumerate(jobs):
                if e >= 4:
                    pe.wait_ge(out[e % 2].sem, out[e % 2].at((e - 4) // 2 + 1))
                bank = T.ps[:, 4 + e % 4, :]
                if what == "q":
                    for c in range(2):
                        ins = nc.tensor.matmul(bank[:, 0:384], qaT[:, c, t * P:(t + 1) * P],
                                               w_q[:, c, half * 384:(half + 1) * 384], start=(c == 0), stop=(c == 1))
                else:
                    ins = nc.tensor.matmul(bank, ckvT[:, t * P:(t + 1) * P], w_kv[:, half * 512:(half + 1) * 512],
                                           start=True, stop=True)
                ins.then_inc(product.sem, product.adds(1))
            turns.tensor(pe, 3)
    T.end_stage()


def stage_mla_attention(T, mix, qT, kT, v):
    nc = T.nc
    with ExitStack() as ctx:
        groups = []
        for t in range(NT):
            units = []
            for h in range(HEADS):
                k = key_order(kT[0:MLA_QK, h, :])[min(t, 1)]
                tiles = (0,) if t == 0 else (1, 2, 3)
                values = [v[:, s, h * HD:(h + 1) * HD] for s in tiles]
                units.append((qT[0:MLA_QK, h, t * P:(t + 1) * P], k, values, None, MLA_QK ** -0.5))
            groups.append((units, mix[:, t, 0:512].rearrange("p (h d) -> p h d", d=HD), None))
        att = Attention(T, ctx, "mla", groups)
        block = ctx.enter_context(nc.Block())

        @block.scalar
        def _(act):
            att.scalar(act)

        @block.vector
        def _(dve):
            att.vector(dve)

        @block.tensor
        def _(pe):
            att.tensor(pe)
    T.end_stage()


def stage_neighbourhood(T, z, mix):
    nc, I, O = T.nc, T.I, T.O
    ROWS, RPB_COLS = LAT // GRID_W, 31
    with ExitStack() as ctx:
        sb = lambda name, shape: T.sb(ctx, "nat_" + name, shape)
        qT, kT = sb("qT", [P, 4, TOK]), sb("kT", [P, 4, 4 * P])
        kc, vc = sb("kc", [P, 512]), sb("vc", [P, 512])
        bias = sb("bias", [P, 2, HEADS, 384])
        gains = sb("gains", [P, 2, HD])
        stat = sb("stat", [P, 2, 2, NT * HEADS])
        loads, tables, steps = T.counter("loads_act"), T.counter("loads_pool"), T.counter("dve_done")
        squares, sums, rstd, ready = T.counter("squares"), T.counter("sums"), T.counter("rstd"), T.counter("rows")
        zeroed, stored = T.counter("pool_done"), T.counter("stored_act")
        flipped, biased = T.counter("nat_flipped"), T.counter("nat_biased")
        room = mix[:, :, 512:1024], kT[:, 0:3, :]
        parts = [z[:, :, at:at + 512] for at in (NQ0, NK0)]
        heads = lambda a: a.rearrange("p t (h d) -> p t h d", h=HEADS)
        groups = [([z[:, t, NQ0 + j * P:NQ0 + (j + 1) * P] for t in range(NT)], qT[:, j, :],
                   (ready, 2) if j == 0 else None) for j in range(4)]
        for j in range(4):
            at = slice(NK0 + j * P, NK0 + (j + 1) * P)
            groups.append(([z[:, 0, at], kc[:, j * P:(j + 1) * P], z[:, 1, at], z[:, 2, at]], kT[:, j, :],
                           (loads, 4 * 16) if j == 0 else None))
        turns = Turns(T, groups)
        att_groups = []
        for t in range(NT):
            units = []
            for h in range(HEADS):
                rows = slice((h % 2) * HD, (h % 2) * HD + HD)
                k = key_order(kT[rows, h // 2, :])[min(t, 1)]
                own = [z[:, s, NV0 + h * HD:NV0 + (h + 1) * HD] for s in range(NT)]
                values = own[0:1] if t == 0 else [vc[:, h * HD:(h + 1) * HD]] + own[1:]
                mask = None if t == 0 else bias[:, t - 1, h, :]
                units.append((qT[rows, h // 2, t * P:(t + 1) * P], k, values, mask, HD ** -0.5))
            att_groups.append((units, mix[:, t, 512:1024].rearrange("p (h d) -> p h d", d=HD), None))
        att = Attention(T, ctx, "nat", att_groups)
        block = ctx.enter_context(nc.Block())

        @block.scalar
        def _(act):
            for dst, src in ((gains[:, 0, :], spread(I["nat_q_g"][0])), (gains[:, 1, :], spread(I["nat_k_g"][0])),
                             (kc[:, :], I["cache_nat_k"][0, 0].rearrange("s h d -> s (h d)")),
                             (vc[:, :], I["cache_nat_v"][0, 0].rearrange("s h d -> s (h d)"))):
                act.dma_start(dst, src).then_inc(loads.sem, loads.adds(16))
            for n in range(2):
                act.activation(room[n], parts[n], ACT.Square).then_inc(squares.sem, squares.adds(1))
            turns.copy_out(act, nc.scalar.copy, 0)
            att.scalar(act)
            act.dma_start(O["nat_k"][0, 0].rearrange("s h d -> s (h d)"), z[:, 0, NK0:NK0 + 512]).then_inc(stored.sem, stored.adds(16))
            act.dma_start(O["nat_v"][0, 0].rearrange("s h d -> s (h d)"), z[:, 0, NV0:NV0 + 512]).then_inc(stored.sem, stored.adds(16))
            act.wait_ge(stored.sem, stored.at(32))

        @block.sync
        def _(sp):
            rpb = I["nat_rpb"]
            for h in range(HEADS):
                for r in range(ROWS):
                    first = (h * 15 + 7 - r) * RPB_COLS + 15 - (GRID_W - 1)
                    src = bass.AP(tensor=rpb.tensor, offset=rpb.offset + first,
                                  ap=[[1, GRID_W], [RPB_COLS, ROWS], [1, GRID_W]])
                    part = slice((r % 2) * GRID_W, (r % 2 + 1) * GRID_W)
                    dst = bias[part, r // 2, h, P:].rearrange("p (k c) -> p k c", k=ROWS)
                    sp.dma_start(dst, src).then_inc(tables.sem, tables.adds(16))

        @block.gpsimd
        def _(pool):
            nc.gpsimd.memset(bias[:, :, :, 0:P], 0.0).then_inc(zeroed.sem, zeroed.adds(1))
            pool.wait_ge(sums.sem, sums.at(2))
            flat = stat[:, :, :, :].rearrange("p a b n -> p a (b n)")
            nc.gpsimd.tensor_scalar(flat[:, 0, :], flat[:, 0, :], 1.0 / HD, EPS, ALU.mult, ALU.add).then_inc(rstd.sem, rstd.adds(1))
            pool.wait_ge(rstd.sem, rstd.now())
            nc.gpsimd.tensor_tensor(flat[:, 1, :], flat[:, 0, :], T.c("half")[:, 0:2 * NT * HEADS], ALU.pow).then_inc(rstd.sem, rstd.adds(1))

        @block.vector
        def _(dve):
            for n in range(2):
                dve.wait_ge(squares.sem, squares.at(n + 1))
                nc.vector.reduce_sum(stat[:, 0, n, :].rearrange("p (t h) -> p t h", t=NT), heads(room[n]), AX).then_inc(sums.sem, sums.adds(1))
            dve.wait_ge(rstd.sem, rstd.at(2))
            dve.wait_ge(loads.sem, loads.at(4 * 16))
            for n in range(2):
                x = heads(parts[n])
                each = stat[:, 1, n, :].rearrange("p (t h) -> p t h", t=NT).unsqueeze(3).broadcast_to([P, NT, HEADS, HD])
                nc.vector.tensor_tensor(x, x, each, ALU.mult).then_inc(steps.sem, steps.adds(1))
                dve.wait_ge(steps.sem, steps.now())
                gain = gains[:, n, :].unsqueeze(1).unsqueeze(1).broadcast_to([P, NT, HEADS, HD])
                nc.vector.tensor_tensor(x, x, gain, ALU.mult).then_inc(ready.sem, ready.adds(1))
            for n in range(2 * HEADS // 2):
                t, h = divmod(2 * n, HEADS)
                dve.wait_ge(flipped.sem, flipped.at(n + 1))
                mask = T.c("nat")[:, t * LAT:(t + 1) * LAT].unsqueeze(1).broadcast_to([P, 2, LAT])
                nc.vector.scalar_tensor_tensor(
                    out=bias[:, t, h:h + 2, P:], in0=T.ps[:, 6 + n % 2, :].rearrange("p (h k) -> p h k", h=2),
                    scalar=HD ** 0.5, in1=mask, op0=ALU.mult, op1=ALU.add).then_inc(biased.sem, biased.adds(1))
            dve.wait_ge(biased.sem, biased.at(HEADS))
            dve.wait_ge(zeroed.sem, zeroed.at(1))
            turns.copy_out(dve, nc.vector.tensor_copy, 1)
            att.vector(dve)

        @block.tensor
        def _(pe):
            pe.wait_ge(tables.sem, tables.at(16 * HEADS * ROWS))
            for n in range(2 * HEADS // 2):
                t, h = divmod(2 * n, HEADS)
                if n >= 2:
                    pe.wait_ge(biased.sem, biased.at(n - 1))
                nc.tensor.matmul(T.ps[:, 6 + n % 2, :], T.c("flip"), bias[:, t, h:h + 2, P:],
                                            start=True, stop=True).then_inc(flipped.sem, flipped.adds(1))
            turns.tensor(pe)
            turns.wait_all(pe)
            att.tensor(pe)
    T.end_stage()


def stage_router(T, l, plan):
    nc, I = T.nc, T.I
    R = N_GRP + N_EXP
    with ExitStack() as ctx:
        sb = lambda name, shape: T.sb(ctx, f"r{l}_" + name, shape)
        scale, shift = sb("scale", [P, 2, D]), sb("shift", [P, 2, D])
        h, hT = sb("h", [P, NT, D]), sb("hT", [P, KC, TOK])
        w, bias = sb("w", [P, KC, R]), sb("bias", [P, R])
        stat = sb("stat", [P, 2, NT])
        logit = sb("logit", [P, NT, R])
        top, least = sb("top", [P, 3, NT]), sb("least", [P, 3, NT])
        cand, chosen_g = sb("cand", [P, NT, N_EXP]), sb("chosen_g", [P, NT, N_GRP])
        g_exp, p_top, ratio = sb("g_exp", [P, NT, N_GRP]), sb("p_top", [P, NT]), sb("ratio", [P, 2, NT])
        left = sb("left", [P, NT, N_EXP])
        chosen, both = sb("chosen", [P, 2, NT, N_EXP]), sb("both", [P, NT, N_EXP])
        rank = sb("rank", [P, NT + 1, N_EXP])
        above = sb("above", [P, N_EXP * (MAX_BLK - 1)])
        extra, upto, start = sb("extra", [P, N_EXP]), sb("upto", [P, N_EXP]), sb("start", [P, N_EXP])
        picked = sb("picked", [P, NT, N_EXP])
        r, base, q, row, blk, tmp = (sb(n, [P, 2 * NT]) for n in ("rk", "base", "q", "row", "blk", "tmp"))
        row_hot, blk_hot = sb("row_hot", [P, 2 * NT, BLK]), sb("blk_hot", [P, 2 * NT, N_BLK])
        before, over = sb("before", [1, OVER, N_EXP]), sb("over", [1, OVER + 1])
        loads, squares, rstd, rows = T.counter("loads_act"), T.counter("squares"), T.counter("rstd"), T.counter("rows")
        steps, stored, product = T.counter("dve_done"), T.counter("stored_act"), T.counter("product")
        shifted, exps, marked = T.counter("r_shifted"), T.counter("r_exps"), T.counter("r_marked")
        groups = [([h[:, t, c::KC] for c in range(4 * k, 4 * k + 4)], hT[:, 4 * k:4 * k + 4, t * P:(t + 1) * P],
                   (rows, t + 1) if k == 0 else None) for t in range(NT) for k in range(2)]
        turns = Turns(T, groups)
        block = ctx.enter_context(nc.Block())

        @block.scalar
        def _(act):
            with nc.allow_non_contiguous_dma(reason="the router's narrow weights"):
                for dst, src in ((scale[:, :, :], spread(T.mod_dram[l, :, 4 * D:5 * D])),
                                 (shift[:, :, :], spread(T.mod_dram[l, :, 3 * D:4 * D])),
                                 (w[:, :, 0:N_GRP], I["moe_w_group"][l].rearrange("(p c) n -> p c n", c=KC)),
                                 (w[:, :, N_GRP:], I["moe_w_expert"][l].rearrange("(p c) n -> p c n", c=KC)),
                                 (bias[:, 0:N_GRP], spread(I["moe_b_group"][l])),
                                 (bias[:, N_GRP:], spread(I["moe_b_expert"][l]))):
                    act.dma_start(dst, src).then_inc(loads.sem, loads.adds(16))
            for t in range(NT):
                if t >= 1:
                    act.wait_ge(squares.sem, squares.at(t))
                act.activation(hT[:, 0:KC, 0:P], T.x[:, t, :].rearrange("p (c n) -> p c n", c=KC),
                                          ACT.Square, accum_out=stat[:, 0, t:t + 1]).then_inc(squares.sem, squares.adds(1))
            act.wait_ge(squares.sem, squares.at(NT))
            turns.copy_out(act, nc.scalar.copy, 0)
            act.wait_ge(rows.sem, rows.at(NT))
            act.dma_start(T.h_dram.rearrange("(t p) d -> p t d", p=P), h[:, :, :]).then_inc(stored.sem, stored.adds(16))
            act.wait_ge(shifted.sem, shifted.at(1))
            act.activation(g_exp[:, :, :], g_exp[:, :, :], ACT.Exp).then_inc(exps.sem, exps.adds(1))
            act.wait_ge(shifted.sem, shifted.at(2))
            act.activation(ratio[:, 0, :], ratio[:, 0, :], ACT.Exp).then_inc(exps.sem, exps.adds(1))
            act.wait_ge(stored.sem, stored.at(16))

        @block.gpsimd
        def _(pool):
            pool.wait_ge(squares.sem, squares.at(NT))
            nc.gpsimd.tensor_scalar(stat[:, 0, :], stat[:, 0, :], 1.0 / D, EPS, ALU.mult, ALU.add).then_inc(rstd.sem, rstd.adds(1))
            pool.wait_ge(rstd.sem, rstd.now())
            nc.gpsimd.tensor_tensor(stat[:, 1, :], stat[:, 0, :], T.c("half")[:, 0:NT], ALU.pow).then_inc(rstd.sem, rstd.adds(1))

        @block.vector
        def _(dve):
            v = nc.vector

            def wide(a, n):
                return a.unsqueeze(len(a.shape)).broadcast_to(list(a.shape) + [n])

            dve.wait_ge(loads.sem, loads.at(6 * 16))
            dve.wait_ge(rstd.sem, rstd.at(2))
            for t in range(NT):
                g = min(t, 1)
                v.scalar_tensor_tensor(out=h[:, t, :], in0=T.x[:, t, :], scalar=stat[:, 1, t:t + 1],
                                          in1=scale[:, g, :], op0=ALU.mult, op1=ALU.mult).then_inc(steps.sem, steps.adds(1))
                dve.wait_ge(steps.sem, steps.now())
                v.tensor_tensor(h[:, t, :], h[:, t, :], shift[:, g, :], ALU.add).then_inc(rows.sem, rows.adds(1))
                if t >= 1:
                    turns.copy_out(dve, v.tensor_copy, 1, 2 * (t - 1), 2 * t)
            turns.copy_out(dve, v.tensor_copy, 1, 2 * NT - 2)
            dve.wait_ge(product.sem, product.at(1))
            v.tensor_tensor(logit[:, :, :], T.ps[:, 4, 0:NT * R].rearrange("p (t n) -> p t n", t=NT),
                               bias[:, :].unsqueeze(1).broadcast_to([P, NT, R]), ALU.add).then_inc(steps.sem, steps.adds(1))
            dve.wait_ge(steps.sem, steps.now())

            def first_largest(x, n, k, out):
                c = cand[:, :, 0:n]
                v.reduce_max(top[:, k, :], x, AX).then_inc(steps.sem, steps.adds(1))
                dve.wait_ge(steps.sem, steps.now())
                v.tensor_tensor(c, x, wide(top[:, k, :], n), ALU.is_equal).then_inc(steps.sem, steps.adds(1))
                dve.wait_ge(steps.sem, steps.now())
                v.scalar_tensor_tensor(out=c, in0=c, scalar=-64.0,
                                          in1=T.c("iota")[:, 0:n].unsqueeze(1).broadcast_to([P, NT, n]),
                                          op0=ALU.mult, op1=ALU.add).then_inc(steps.sem, steps.adds(1))
                dve.wait_ge(steps.sem, steps.now())
                v.tensor_reduce(least[:, k, :], c, AX, ALU.min).then_inc(steps.sem, steps.adds(1))
                dve.wait_ge(steps.sem, steps.now())
                v.tensor_tensor(out, c, wide(least[:, k, :], n), ALU.is_equal).then_inc(steps.sem, steps.adds(1))
                dve.wait_ge(steps.sem, steps.now())

            group, expert = logit[:, :, 0:N_GRP], logit[:, :, N_GRP:]
            first_largest(group, N_GRP, 0, chosen_g[:, :, :])
            v.tensor_tensor(g_exp[:, :, :], group, wide(top[:, 0, :], N_GRP), ALU.subtract).then_inc(shifted.sem, shifted.adds(1))
            dve.wait_ge(shifted.sem, shifted.now())
            v.tensor_scalar(chosen_g[:, :, :], chosen_g[:, :, :], -1.0, BIG, ALU.add, ALU.mult).then_inc(steps.sem, steps.adds(1))
            dve.wait_ge(steps.sem, steps.now())
            by_group = lambda a: a.rearrange("p t (g e) -> p t g e", g=N_GRP)
            v.tensor_tensor(by_group(left[:, :, :]), by_group(expert), wide(chosen_g[:, :, :], PER_GRP), ALU.add).then_inc(steps.sem, steps.adds(1))
            dve.wait_ge(steps.sem, steps.now())
            first_largest(left[:, :, :], N_EXP, 1, chosen[:, 0])
            v.scalar_tensor_tensor(out=left[:, :, :], in0=chosen[:, 0], scalar=-3.0 * BIG, in1=left[:, :, :],
                                      op0=ALU.mult, op1=ALU.add).then_inc(steps.sem, steps.adds(1))
            dve.wait_ge(steps.sem, steps.now())
            first_largest(left[:, :, :], N_EXP, 2, chosen[:, 1])
            v.tensor_tensor(ratio[:, 0, :], top[:, 2, :], top[:, 1, :], ALU.subtract).then_inc(shifted.sem, shifted.adds(1))
            dve.wait_ge(shifted.sem, shifted.now())
            v.tensor_tensor(both[:, :, :], chosen[:, 0], chosen[:, 1], ALU.add).then_inc(marked.sem, marked.adds(1))
            dve.wait_ge(marked.sem, marked.now())
            dve.wait_ge(exps.sem, exps.at(2))
            v.reduce_sum(p_top[:, :], g_exp[:, :, :], AX).then_inc(steps.sem, steps.adds(1))
            dve.wait_ge(steps.sem, steps.now())
            v.tensor_scalar(ratio[:, 1, :], ratio[:, 0, :], 1.0, None, ALU.add).then_inc(steps.sem, steps.adds(1))
            dve.wait_ge(steps.sem, steps.now())
            v.tensor_tensor(p_top[:, :], p_top[:, :], ratio[:, 1, :], ALU.mult).then_inc(steps.sem, steps.adds(1))
            dve.wait_ge(steps.sem, steps.now())
            v.reciprocal(plan.weight[:, 0, :], p_top[:, :]).then_inc(steps.sem, steps.adds(1))
            dve.wait_ge(steps.sem, steps.now())
            v.tensor_tensor(plan.weight[:, 1, :], plan.weight[:, 0, :], ratio[:, 0, :], ALU.mult).then_inc(steps.sem, steps.adds(1))
            dve.wait_ge(steps.sem, steps.now())
            dve.wait_ge(product.sem, product.at(2))
            v.tensor_copy(rank[:, :, :], T.ps[:, 5, 0:(NT + 1) * N_EXP].rearrange("p (t n) -> p t n", n=N_EXP)).then_inc(steps.sem, steps.adds(1))
            dve.wait_ge(steps.sem, steps.now())
            count = rank[:, NT, :]
            n_thr = MAX_BLK - 1
            by_expert = above[:, :].rearrange("p (e m) -> p e m", m=n_thr)
            v.tensor_tensor(by_expert, wide(count, n_thr), T.c("thr").rearrange("p (e m) -> p e m", m=n_thr), ALU.is_gt).then_inc(steps.sem, steps.adds(1))
            dve.wait_ge(steps.sem, steps.now())
            v.reduce_sum(extra[:, :], by_expert, AX).then_inc(steps.sem, steps.adds(1))
            dve.wait_ge(steps.sem, steps.now())
            v.tensor_tensor_scan(upto[:, :], T.c("ones")[:, 0:N_EXP], extra[:, :], 0.0, ALU.mult, ALU.add).then_inc(steps.sem, steps.adds(1))
            dve.wait_ge(steps.sem, steps.now())
            v.tensor_tensor(start[:, :], upto[:, :], extra[:, :], ALU.subtract).then_inc(steps.sem, steps.adds(1))
            dve.wait_ge(steps.sem, steps.now())
            for k in range(2):
                part = slice(k * NT, (k + 1) * NT)
                v.tensor_tensor(picked[:, :, :], chosen[:, k], rank[:, 0:NT, :], ALU.mult).then_inc(steps.sem, steps.adds(1))
                dve.wait_ge(steps.sem, steps.now())
                v.reduce_sum(r[:, part], picked[:, :, :], AX).then_inc(steps.sem, steps.adds(1))
                dve.wait_ge(steps.sem, steps.now())
                v.tensor_tensor(picked[:, :, :], chosen[:, k], start[:, :].unsqueeze(1).broadcast_to([P, NT, N_EXP]),
                                   ALU.mult).then_inc(steps.sem, steps.adds(1))
                dve.wait_ge(steps.sem, steps.now())
                v.reduce_sum(base[:, part], picked[:, :, :], AX).then_inc(steps.sem, steps.adds(1))
                dve.wait_ge(steps.sem, steps.now())
            quot = above[:, 0:2 * NT * n_thr].rearrange("p (n m) -> p n m", m=n_thr)
            v.tensor_tensor(quot, wide(r[:, :], n_thr), T.c("thr")[:, 0:n_thr].unsqueeze(1).broadcast_to([P, 2 * NT, n_thr]),
                               ALU.is_ge).then_inc(steps.sem, steps.adds(1))
            dve.wait_ge(steps.sem, steps.now())
            v.reduce_sum(q[:, :], quot, AX).then_inc(steps.sem, steps.adds(1))
            dve.wait_ge(steps.sem, steps.now())
            v.scalar_tensor_tensor(out=row[:, :], in0=q[:, :], scalar=-float(BLK), in1=r[:, :], op0=ALU.mult, op1=ALU.add).then_inc(steps.sem, steps.adds(1))
            dve.wait_ge(steps.sem, steps.now())
            e = least[:, 1:3, :].rearrange("p k t -> p (k t)")
            v.tensor_scalar(e, e, 64.0, None, ALU.add).then_inc(steps.sem, steps.adds(1))
            dve.wait_ge(steps.sem, steps.now())
            v.tensor_tensor(base[:, :], base[:, :], q[:, :], ALU.add).then_inc(steps.sem, steps.adds(1))
            dve.wait_ge(steps.sem, steps.now())
            v.scalar_tensor_tensor(out=tmp[:, :], in0=base[:, :], scalar=N_EXP - 1.0, in1=e, op0=ALU.add, op1=ALU.subtract).then_inc(steps.sem, steps.adds(1))
            dve.wait_ge(steps.sem, steps.now())
            v.tensor_scalar(q[:, :], q[:, :], 1.0, None, ALU.min).then_inc(steps.sem, steps.adds(1))
            dve.wait_ge(steps.sem, steps.now())
            v.tensor_tensor(tmp[:, :], tmp[:, :], q[:, :], ALU.mult).then_inc(steps.sem, steps.adds(1))
            dve.wait_ge(steps.sem, steps.now())
            v.tensor_tensor(blk[:, :], tmp[:, :], e, ALU.add).then_inc(steps.sem, steps.adds(1))
            dve.wait_ge(steps.sem, steps.now())
            v.scalar_tensor_tensor(out=tmp[:, :], in0=blk[:, :], scalar=float(BLK), in1=row[:, :], op0=ALU.mult, op1=ALU.add).then_inc(steps.sem, steps.adds(1))
            dve.wait_ge(steps.sem, steps.now())
            v.tensor_copy(plan.slot[:, :], tmp[:, :]).then_inc(steps.sem, steps.adds(1))
            dve.wait_ge(steps.sem, steps.now())
            iota = T.c("iota")
            v.tensor_tensor(row_hot[:, :, :], iota.unsqueeze(1).broadcast_to([P, 2 * NT, BLK]), wide(row[:, :], BLK),
                               ALU.is_equal).then_inc(steps.sem, steps.adds(1))
            dve.wait_ge(steps.sem, steps.now())
            v.tensor_tensor(blk_hot[:, :, :], iota[:, 0:N_BLK].unsqueeze(1).broadcast_to([P, 2 * NT, N_BLK]),
                               wide(blk[:, :], N_BLK), ALU.is_equal).then_inc(steps.sem, steps.adds(1))
            dve.wait_ge(steps.sem, steps.now())
            for k in range(2):
                b = blk_hot[:, k * NT:(k + 1) * NT, :]
                ins = v.tensor_tensor(b, b, wide(T.c("token"), N_BLK), ALU.mult)
                if k == 0:
                    ins.then_inc(steps.sem, steps.adds(1))
                    dve.wait_ge(steps.sem, steps.now())
                else:
                    ins.then_inc(marked.sem, marked.adds(1))
                    dve.wait_ge(marked.sem, marked.now())
            v.tensor_tensor(before[:, :, :], wide(iota[0:1, 0:OVER], N_EXP),
                               upto[0:1, :].unsqueeze(1).broadcast_to([1, OVER, N_EXP]), ALU.is_ge).then_inc(steps.sem, steps.adds(1))
            dve.wait_ge(steps.sem, steps.now())
            v.reduce_sum(over[:, 0:OVER], before[:, :, :], AX).then_inc(steps.sem, steps.adds(1))
            dve.wait_ge(steps.sem, steps.now())
            v.tensor_scalar(over[:, 0:OVER], over[:, 0:OVER], N_EXP - 1.0, None, ALU.min).then_inc(steps.sem, steps.adds(1))
            dve.wait_ge(steps.sem, steps.now())
            v.tensor_copy(over[:, OVER:], upto[0:1, N_EXP - 1:N_EXP]).then_inc(steps.sem, steps.adds(1))
            dve.wait_ge(steps.sem, steps.now())
            v.tensor_copy(plan.over[:, :], over[:, :]).then_inc(steps.sem, steps.adds(1))
            dve.wait_ge(steps.sem, steps.now())
            dve.wait_ge(product.sem, product.at(3))
            v.tensor_copy(plan.table[:, :], T.ps[0:BLK, 6, 0:N_BLK]).then_inc(steps.sem, steps.adds(1))

        @block.tensor
        def _(pe):
            turns.tensor(pe)
            turns.wait_all(pe)
            pe.wait_ge(loads.sem, loads.at(6 * 16))
            for t in range(NT):
                for c in range(KC):
                    ins = nc.tensor.matmul(T.ps[:, 4, t * R:(t + 1) * R], hT[:, c, t * P:(t + 1) * P], w[:, c, :],
                                           start=(c == 0), stop=(c == KC - 1))
            ins.then_inc(product.sem, product.adds(1))
            pe.wait_ge(marked.sem, marked.at(1))
            for t in range(NT + 1):
                out = T.ps[:, 5, t * N_EXP:(t + 1) * N_EXP]
                earlier = list(range(t))
                for n, s in enumerate(earlier):
                    ins = nc.tensor.matmul(out, T.c("ones"), both[:, s, :], start=(n == 0), stop=(t == NT and n == NT - 1))
                if t < NT:
                    ins = nc.tensor.matmul(out, T.c("tri"), both[:, t, :], start=(t == 0), stop=True)
            ins.then_inc(product.sem, product.adds(1))
            pe.wait_ge(marked.sem, marked.at(2))
            for n in range(2 * NT):
                ins = nc.tensor.matmul(T.ps[0:BLK, 6, 0:N_BLK], row_hot[:, n, :], blk_hot[:, n, :],
                                       start=(n == 0), stop=(n == 2 * NT - 1))
            ins.then_inc(product.sem, product.adds(1))
    T.end_stage()


def stage_experts(T, l, first, plan):
    nc = T.nc
    pairs = N_EXP // 2
    FC = FF // P
    tag = f"e{l}_"
    with ExitStack() as ctx:
        sb = lambda name, shape: T.sb(ctx, tag + name, shape)
        x_in, xT = sb("x", [BLK, 2, D]), sb("xT", [P, 2, KC * BLK])
        sig, hid = sb("sig", [P, FC * BLK]), sb("hid", [P, FC * BLK])
        y = sb("y", [BLK, 2, D])
        over_w = sb("over_w", [P, 2, UNIT])
        over_x = sb("over_x", [BLK, D])
        over_idx = T.sb(ctx, tag + "over_idx", [BLK, 1], U32)
        gathered = [T.counter(f"gathered{i}") for i in range(2)]
        stored = [T.counter(f"y_stored{i}") for i in range(2)]
        turned, turned_out, sigmoid = T.counter("x_turned"), T.counter("x_turned_out"), T.counter("sigmoid")
        silu, hidden, y_act, y_dve = T.counter("silu"), T.counter("hidden"), T.counter("y_act"), T.counter("y_dve")
        o = {n: T.counter(f"o{l}_{n}") for n in ("turn", "x", "idx", "index_read", "x_seen", "w", "down_w", "turned", "xT", "gate", "up",
                                                "sig", "silu", "hidden", "down", "y", "stored")}
        block = ctx.enter_context(nc.Block())

        def each_pair(engine, step):
            for s in range(2):
                step(0, s)
            with T.loop(engine, 1, pairs) as i:
                for s in range(2):
                    step(i, s)

        def each_extra(engine, step):
            n = engine.value_load(plan.over[0:1, OVER:OVER + 1], min_val=0, max_val=OVER)
            with engine.Fori(0, OVER) as i:
                with engine.If(i < n):
                    step(i)

        def count(i, s, k=0):
            return i * 2 + (s + k)

        def turn(pe, x, bank):
            for c in range(KC):
                ins = nc.tensor.transpose(bank[:, c * BLK:(c + 1) * BLK], x[:, c::KC], T.c("ident", BLK)[:, 0:BLK])
            return ins

        def up(pe, weights, xt, bank):
            for j in range(FC):
                for c in range(KC):
                    ins = nc.tensor.matmul(bank[:, j * BLK:(j + 1) * BLK], weights[:, c, j * P:(j + 1) * P],
                                           xt[:, c * BLK:(c + 1) * BLK], start=(c == 0), stop=(c == KC - 1))
            return ins

        def down(pe, weights):
            for n in range(2):
                for j in range(FC):
                    ins = nc.tensor.matmul(T.ps[0:BLK, 3 + n, :], hid[:, j * BLK:(j + 1) * BLK],
                                           weights[:, j, n * 512:(n + 1) * 512], start=(j == 0), stop=(j == FC - 1))
            return ins

        def as_up(w):
            return w.rearrange("p (c n) -> p c n", c=KC)

        def as_down(w):
            return w.rearrange("p (j n) -> p j n", j=FC)

        def slot(u):
            return T.ring[:, u % RING, :]

        gate_ps, up_ps = T.ps[:, 1, 0:FC * BLK], T.ps[:, 2, 0:FC * BLK]

        @block.sync
        def _(sp):
            with sp.Fori(0, pairs - 1) as i:
                for k in range(RING):
                    T.load_unit(sp, first + RING + k, i)
            T.load_ahead(sp, first + 3 * N_EXP - RING, first + 3 * N_EXP)

            def extra(i):
                e = sp.value_load(plan.over[0:1, bass.ds(i, 1)], min_val=0, max_val=N_EXP - 1)
                sp.wait_ge(o["turn"].sem, i + 1)
                for part in range(2):
                    sp.dma_start(over_w[:, part, :].rearrange("p (c n) -> p c n", c=KC),
                                 T.expert_source(l, e, part)).then_inc(o["w"].sem, 16)
                sp.wait_ge(o["gate"].sem, i + 1)
                sp.dma_start(over_w[:, 0, :].rearrange("p (j n) -> p j n", j=FC),
                             T.expert_source(l, e, 2)).then_inc(o["down_w"].sem, 16)

            each_extra(sp, extra)

        @block.gpsimd
        def _(pool):
            for b in range(N_EXP + 1):
                if b >= 2:
                    pool.wait_ge(turned.sem, turned.at(b - 1))
                nc.gpsimd.indirect_dma_start(
                    out=x_in[:, b % 2, :], out_offset=None, in_=T.h_dram,
                    in_offset=bass.IndirectOffsetOnAxis(ap=plan.table[:, b:b + 1], axis=0)).then_inc(gathered[b % 2].sem, gathered[b % 2].adds(16))
            pool.wait_ge(gathered[N_EXP % 2].sem, gathered[N_EXP % 2].at(16 * (N_EXP // 2 + 1)))

            def extra(i):
                pool.wait_ge(o["turn"].sem, i + 1)
                nc.gpsimd.tensor_copy(over_idx[:, :], plan.table[:, bass.ds(i + N_EXP, 1)]).then_inc(o["idx"].sem, 1)
                pool.wait_ge(o["idx"].sem, i + 1)
                pool.sem_inc(o["index_read"].sem, 1)
                nc.gpsimd.indirect_dma_start(
                    out=over_x[:, :], out_offset=None, in_=T.h_dram,
                    in_offset=bass.IndirectOffsetOnAxis(ap=over_idx[:, :], axis=0)).then_inc(o["x"].sem, 16)

            each_extra(pool, extra)

        @block.tensor
        def _(pe):
            def turn_next(s):
                turn(pe, x_in[:, s, :], T.ps[:, 0, :]).then_inc(turned.sem, turned.adds(1))

            def step(i, s):
                u = first + 3 * s
                peeled = isinstance(i, int)
                pe.wait_ge(turned_out.sem, turned_out.at(count(i, s, 1)))
                pe.wait_ge(T.landing(u), T.landed_at(u, i))
                up(pe, as_up(slot(u)), xT[:, s, :], gate_ps).then_inc(T.unit_used.sem, T.unit_used.adds(1))
                pe.wait_ge(gathered[1 - s].sem, gathered[1 - s].at((i + s) * 16 + 16))
                pe.wait_ge(T.landing(u + 1), T.landed_at(u + 1, i))
                up(pe, as_up(slot(u + 1)), xT[:, s, :], up_ps).then_inc(T.unit_used.sem, T.unit_used.adds(1))
                turn_next(1 - s)
                pe.wait_ge(hidden.sem, hidden.at(count(i, s, 1)))
                if not (peeled and s == 0):
                    pe.wait_ge(y_act.sem, y_act.at(count(i, s)))
                    pe.wait_ge(y_dve.sem, y_dve.at(count(i, s)))
                pe.wait_ge(T.landing(u + 2), T.landed_at(u + 2, i))
                down(pe, as_down(slot(u + 2))).then_inc(T.unit_used.sem, T.unit_used.adds(1))

            pe.wait_ge(gathered[0].sem, gathered[0].at(16))
            turn_next(0)
            each_pair(pe, step)
            pe.wait_ge(y_act.sem, y_act.at(N_EXP))
            pe.wait_ge(y_dve.sem, y_dve.at(N_EXP))
            pe.wait_ge(turned_out.sem, turned_out.at(N_EXP + 1))

            def extra(i):
                pe.wait_ge(o["x"].sem, i * 16 + 16)
                pe.sem_inc(o["x_seen"].sem, 1)
                turn(pe, over_x[:, :], T.ps[:, 0, :]).then_inc(o["turned"].sem, 1)
                pe.wait_ge(o["xT"].sem, i + 1)
                pe.wait_ge(o["w"].sem, i * 32 + 32)
                up(pe, as_up(over_w[:, 0, :]), xT[:, 0, :], gate_ps).then_inc(o["gate"].sem, 1)
                up(pe, as_up(over_w[:, 1, :]), xT[:, 0, :], up_ps).then_inc(o["up"].sem, 1)
                pe.wait_ge(o["hidden"].sem, i + 1)
                pe.wait_ge(o["down_w"].sem, i * 16 + 16)
                down(pe, as_down(over_w[:, 0, :])).then_inc(o["down"].sem, 1)

            each_extra(pe, extra)

        @block.scalar
        def _(act):
            def copy_turned(i, s):
                act.wait_ge(turned.sem, turned.at(count(i, s, 1)))
                nc.scalar.copy(xT[:, s, :], T.ps[:, 0, :]).then_inc(turned_out.sem, turned_out.adds(1))

            def step(i, s):
                u = first + 3 * s
                peeled = isinstance(i, int)
                act.wait_ge(T.unit_used.sem, T.used_at(u, i))
                if not (peeled and s == 0):
                    act.wait_ge(hidden.sem, hidden.at(count(i, s)))
                nc.scalar.activation(sig[:, :], gate_ps, ACT.Exp, scale=-1.0).then_inc(sigmoid.sem, sigmoid.adds(1))
                copy_turned(i + s, 1 - s)
                act.wait_ge(T.unit_used.sem, T.used_at(u + 2, i))
                if not peeled:
                    act.wait_ge(stored[s].sem, stored[s].at(i * 16))
                nc.scalar.copy(y[:, s, 0:512], T.ps[0:BLK, 3, :]).then_inc(y_act.sem, y_act.adds(1))
                act.wait_ge(y_act.sem, y_act.at(count(i, s, 1)))
                act.wait_ge(y_dve.sem, y_dve.at(count(i, s, 1)))
                rows = T.y_dram[bass.ds(count(i, s) * BLK, BLK), :]
                act.dma_start(rows, y[:, s, :]).then_inc(stored[s].sem, stored[s].adds(16))

            copy_turned(0, 0)
            each_pair(act, step)
            for s in range(2):
                act.wait_ge(stored[s].sem, stored[s].at(16 * pairs))
            act.sem_inc(o["turn"].sem, 1)

            def extra(i):
                act.wait_ge(o["turned"].sem, i + 1)
                nc.scalar.copy(xT[:, 0, :], T.ps[:, 0, :]).then_inc(o["xT"].sem, 1)
                act.wait_ge(o["gate"].sem, i + 1)
                nc.scalar.activation(sig[:, :], gate_ps, ACT.Exp, scale=-1.0).then_inc(o["sig"].sem, 1)
                act.wait_ge(o["down"].sem, i + 1)
                for n in range(2):
                    nc.scalar.copy(y[:, 0, n * 512:(n + 1) * 512], T.ps[0:BLK, 3 + n, :]).then_inc(o["y"].sem, 1)
                act.wait_ge(o["y"].sem, i * 2 + 2)
                rows = T.y_dram[bass.ds((i + N_EXP) * BLK, BLK), :]
                act.dma_start(rows, y[:, 0, :]).then_inc(o["stored"].sem, 16)
                act.wait_ge(o["stored"].sem, i * 16 + 16)
                act.sem_inc(o["turn"].sem, 1)

            each_extra(act, extra)

        @block.vector
        def _(dve):
            v = nc.vector

            def step(i, s):
                u = first + 3 * s
                n = count(i, s) * 3
                dve.wait_ge(sigmoid.sem, sigmoid.at(count(i, s, 1)))
                v.tensor_scalar(sig[:, :], sig[:, :], 1.0, None, ALU.add).then_inc(silu.sem, silu.adds(1))
                dve.wait_ge(silu.sem, silu.at(n + 1))
                v.reciprocal(sig[:, :], sig[:, :]).then_inc(silu.sem, silu.adds(1))
                dve.wait_ge(silu.sem, silu.at(n + 2))
                v.tensor_tensor(sig[:, :], sig[:, :], gate_ps, ALU.mult).then_inc(silu.sem, silu.adds(1))
                dve.wait_ge(silu.sem, silu.at(n + 3))
                dve.wait_ge(T.unit_used.sem, T.used_at(u + 1, i))
                v.tensor_tensor(hid[:, :], sig[:, :], up_ps, ALU.mult).then_inc(hidden.sem, hidden.adds(1))
                dve.wait_ge(T.unit_used.sem, T.used_at(u + 2, i))
                if not isinstance(i, int):
                    dve.wait_ge(stored[s].sem, stored[s].at(i * 16))
                v.tensor_copy(y[:, s, 512:D], T.ps[0:BLK, 4, :]).then_inc(y_dve.sem, y_dve.adds(1))

            each_pair(dve, step)

            def extra(i):
                silu_n = i * 3
                dve.wait_ge(o["sig"].sem, i + 1)
                v.tensor_scalar(sig[:, :], sig[:, :], 1.0, None, ALU.add).then_inc(o["silu"].sem, 1)
                dve.wait_ge(o["silu"].sem, silu_n + 1)
                v.reciprocal(sig[:, :], sig[:, :]).then_inc(o["silu"].sem, 1)
                dve.wait_ge(o["silu"].sem, silu_n + 2)
                v.tensor_tensor(sig[:, :], sig[:, :], gate_ps, ALU.mult).then_inc(o["silu"].sem, 1)
                dve.wait_ge(o["silu"].sem, silu_n + 3)
                dve.wait_ge(o["up"].sem, i + 1)
                v.tensor_tensor(hid[:, :], sig[:, :], up_ps, ALU.mult).then_inc(o["hidden"].sem, 1)

            each_extra(dve, extra)
    T.end_stage()


def stage_combine(T, l, plan):
    nc, O = T.nc, T.O
    with ExitStack() as ctx:
        gate = T.sb(ctx, f"gate2_{l}", [P, 2, D])
        rows = T.sb(ctx, f"rows{l}", [P, 2 * NT, D])
        loads, steps, added = T.counter("loads_act"), T.counter("dve_done"), T.counter("rows")
        fetched = [T.counter(f"fetched{n}") for n in range(2 * NT)]
        stored = T.counter("stored_act")
        block = ctx.enter_context(nc.Block())

        @block.gpsimd
        def _(pool):
            for t in range(NT):
                for k in range(2):
                    n = k * NT + t
                    nc.gpsimd.indirect_dma_start(
                        out=rows[:, n, :], out_offset=None, in_=T.y_dram,
                        in_offset=bass.IndirectOffsetOnAxis(ap=plan.slot[:, n:n + 1], axis=0)).then_inc(fetched[n].sem, fetched[n].adds(16))
            for n in range(2 * NT):
                pool.wait_ge(fetched[n].sem, fetched[n].at(16))

        @block.scalar
        def _(act):
            act.dma_start(gate[:, :, :], spread(T.mod_dram[l, :, 5 * D:6 * D])).then_inc(loads.sem, loads.adds(16))
            if l == 1:
                for t in range(NT):
                    act.wait_ge(added.sem, added.at(t + 1))
                    out = O["y_sample"][0, (t - 1) * P:t * P, :] if t else O["y_prompt"][0]
                    act.dma_start(out, T.x[:, t, :]).then_inc(stored.sem, stored.adds(16))
                act.wait_ge(stored.sem, stored.at(16 * NT))

        @block.vector
        def _(dve):
            v = nc.vector
            dve.wait_ge(loads.sem, loads.at(16))
            for t in range(NT):
                a, b = rows[:, t, :], rows[:, NT + t, :]
                dve.wait_ge(fetched[t].sem, fetched[t].at(16))
                v.tensor_scalar(a, a, plan.weight[:, 0, t:t + 1], None, ALU.mult).then_inc(steps.sem, steps.adds(1))
                dve.wait_ge(steps.sem, steps.now())
                dve.wait_ge(fetched[NT + t].sem, fetched[NT + t].at(16))
                v.scalar_tensor_tensor(out=a, in0=b, scalar=plan.weight[:, 1, t:t + 1], in1=a,
                                                       op0=ALU.mult, op1=ALU.add).then_inc(steps.sem, steps.adds(1))
                dve.wait_ge(steps.sem, steps.now())
                v.tensor_tensor(a, a, gate[:, min(t, 1), :], ALU.mult).then_inc(steps.sem, steps.adds(1))
                dve.wait_ge(steps.sem, steps.now())
                v.tensor_tensor(T.x[:, t, :], T.x[:, t, :], a, ALU.add).then_inc(added.sem, added.adds(1))
    T.end_stage()


class Plan:

    def __init__(self, T, ctx, l):
        self.table = T.sb(ctx, f"table{l}", [BLK, N_BLK], U32)
        self.slot = T.sb(ctx, f"slot{l}", [P, 2 * NT], U32)
        self.over = T.sb(ctx, f"over{l}", [1, OVER + 1], I32)
        self.weight = T.sb(ctx, f"weight{l}", [P, 2, NT])


def program(nc, I, O):
    with ExitStack() as ctx:
        T = Trunk(nc, ctx, I, O)
        first = 0
        for l in range(2):
            total = ODD_COLS if l else EVEN_COLS
            n_in = -(-total // 512)
            stage_modulation(T, l, first)
            first += 12
            with ExitStack() as mixer:
                z = T.sb(mixer, f"z{l}", [P, NT, total])
                stage_projection(T, l, first, z)
                first += n_in
                mix = T.sb(mixer, f"mix{l}", [P, NT, D])
                if l == 0:
                    stage_window(T, z, mix)
                    stage_mlstm(T, z, mix)
                else:
                    with ExitStack() as heads:
                        qT = T.sb(heads, "mla_qT", [P, HEADS, TOK])
                        kT = T.sb(heads, "mla_kT", [P, HEADS, 4 * P])
                        v = T.sb(heads, "mla_v", [P, 4, HEADS * HD])
                        stage_mla_heads(T, z, mix, qT[:, :, :], kT[:, :, :], v[:, :, :])
                        stage_mla_attention(T, mix, qT, kT, v)
                    stage_neighbourhood(T, z, mix)
                stage_output(T, l, first, mix)
                first += 2
            with ExitStack() as moe:
                plan = Plan(T, moe, l)
                stage_router(T, l, plan)
                stage_experts(T, l, first, plan)
                first += 3 * N_EXP
                stage_combine(T, l, plan)


OUTPUTS = (("y_prompt", (1, SEQ, D)), ("y_sample", (1, LAT, D)), ("ml_c", (1, 1, 2, ML_H, ML_D, ML_D)),
           ("ml_n", (1, 1, 2, ML_H, ML_D)), ("ml_m", (1, 1, 2, ML_H)),
           ("win_k", (1, 1, SEQ, 2, HD)), ("win_v", (1, 1, SEQ, 2, HD)), ("mla_ckv", (1, 1, SEQ, P)),
           ("mla_kpe", (1, 1, SEQ, MLA_ROPE)), ("nat_k", (1, 1, SEQ, HEADS, HD)),
           ("nat_v", (1, 1, SEQ, HEADS, HD)))
INPUTS = ("x_prompt", "x_sample", "state_ml_c", "state_ml_n", "state_ml_m", "cache_win_k", "cache_win_v",
          "cache_mla_ckv", "cache_mla_kpe", "cache_nat_k", "cache_nat_v", "c", "c_ctx", "ada_w", "ada_b",
          "norm1_g", "norm2_g", "even_w_in", "ml_gate_b", "ml_out_g", "win_q_g", "win_k_g", "win_sink",
          "even_w_out", "odd_w_in", "mla_q_a_g", "mla_kv_a_g", "mla_w_q_up", "mla_w_kv_up", "mla_q_g",
          "mla_k_g", "nat_q_g", "nat_k_g", "nat_rpb", "odd_w_out", "moe_w_group", "moe_b_group",
          "moe_w_expert", "moe_b_expert", "moe_w_gate", "moe_w_up", "moe_w_down")


def kernel(**inputs):
    import concourse.bacc as bacc
    from concourse.bass_utils import run_bass_kernel_spmd

    nc = bacc.Bacc("TRN2", target_bir_lowering=False, num_devices=1)
    arrays = {name: np.ascontiguousarray(inputs[name]) for name in INPUTS}
    arrays["const"] = constants()
    I = {name: nc.dram_tensor("in_" + name, a.shape, mybir.dt.from_np(a.dtype), kind="ExternalInput").ap()
         for name, a in arrays.items()}
    O = {name: nc.dram_tensor("out_" + name, shape, F32, kind="ExternalOutput").ap() for name, shape in OUTPUTS}
    program(nc, I, O)
    got = run_bass_kernel_spmd(nc, [{"in_" + name: a for name, a in arrays.items()}], core_ids=[0]).results[0]
    return tuple(got["out_" + name] for name, _ in OUTPUTS)
```

```python
from contextlib import ExitStack, contextmanager

import numpy as np

import concourse.bass as bass
from concourse import mybir

F32 = mybir.dt.float32
I32 = mybir.dt.int32
U32 = mybir.dt.uint32
ALU = mybir.AluOpType
ACT = mybir.ActivationFunctionType
AX = mybir.AxisListType.X

P = 128
D = 1024
KC = D // P
NT = 3
SEQ, LAT = 128, 256
TOK = SEQ + LAT
GRID_W = 64
EPS = 1e-6
BIG = 1e30
N_EXP, N_GRP, PER_GRP, FF = 32, 4, 8, 512
HEADS, HD = 8, 64
ML_H, ML_D = 4, 128
MLA_QK, MLA_NOPE, MLA_ROPE = 96, 64, 32

RING = 6
UNIT = 4096
BLK = 64
MAX_BLK = -(-TOK // BLK)
OVER = (2 * TOK - 2) // BLK
N_BLK = N_EXP + OVER
NO_ROW = 1024

EVEN_COLS, ODD_COLS = 2832, 1952
WQ0, WK0, WV0, ZG0 = 2064, 2576, 2704, 2048
ZKV0, ZPE0, NQ0, NK0, NV0 = 256, 384, 416, 928, 1440

CONST = {}
_at = 0
for _name, _width in (("ident", P), ("flip", P), ("tri", P), ("ones", P), ("win", 2 * 384), ("nat", 2 * 256),
                      ("ml_f", P), ("ml_b", P), ("cos64", 2 * 64), ("sin64", 2 * 64),
                      ("cos32", 2 * 32), ("sin32", 2 * 32), ("token", 4 * NT), ("iota", 64),
                      ("sel", 4 * P), ("half", 64), ("thr", N_EXP * (MAX_BLK - 1))):
    CONST[_name] = (_at, _width)
    _at += _width
N_CONST = _at


def constants():
    c = np.zeros((P, N_CONST), np.float32)

    def put(name, a):
        at, w = CONST[name]
        c[:, at:at + w] = np.asarray(a, np.float32).reshape(-1, w)

    r = np.arange(P)
    put("ident", np.eye(P))
    put("flip", r[:, None] // GRID_W * GRID_W + GRID_W - 1 - r[:, None] % GRID_W == r[None, :])
    put("tri", r[:, None] < r[None, :])
    put("ones", np.ones((P, P)))
    t = np.arange(LAT)
    near = np.abs(t[:, None] - t[None, :]) <= 128
    win = np.concatenate([np.zeros((LAT, P)), np.where(near, 0, -BIG)], 1)
    put("win", win.reshape(2, P, 384).transpose(1, 0, 2))
    col = t % GRID_W
    start = np.clip(col - 8, 0, GRID_W - 16)
    ok = (col[None, :] >= start[:, None]) & (col[None, :] < start[:, None] + 16)
    put("nat", np.where(ok, 0, -BIG).reshape(2, P, 256).transpose(1, 0, 2))
    put("ml_f", np.where(r[:, None] <= r[None, :], 0, BIG))
    put("ml_b", np.where(r[:, None] >= r[None, :], 0, BIG))
    for width in (64, 32):
        nf = width // 4
        inv = 10000.0 ** (-np.arange(nf, dtype=np.float32) / nf)
        cos, sin = [], []
        for pos in (t // GRID_W, t % GRID_W):
            ang = pos.astype(np.float32)[:, None] * inv[None, :].astype(np.float32)
            cos += [np.cos(ang), np.cos(ang)]
            sin += [-np.sin(ang), np.sin(ang)]
        put(f"cos{width}", np.concatenate(cos, 1).reshape(2, P, width).transpose(1, 0, 2))
        put(f"sin{width}", np.concatenate(sin, 1).reshape(2, P, width).transpose(1, 0, 2))
    token = np.broadcast_to(r[:, None, None] + P * np.arange(NT), (P, 2, NT))
    put("token", np.stack([token, token + TOK * np.arange(2)[:, None]], -1) - NO_ROW)
    put("iota", np.broadcast_to(np.arange(64), (P, 64)))
    sel = np.zeros((P, 4, P))
    for h in range(4):
        sel[h, h] = 1
    put("sel", sel)
    put("half", np.full((P, 64), -0.5))
    over = BLK * (1 + np.arange(MAX_BLK - 1)) - 0.0
    put("thr", np.broadcast_to(over, (P, N_EXP, MAX_BLK - 1)))
    return c


class Counter:

    def __init__(self, nc, ctx, name):
        self.sem = ctx.enter_context(nc.semaphore(name))
        self.base = self.made = 0

    def adds(self, n):
        self.made += n
        return n

    def at(self, n):
        return self.base + n

    def now(self):
        return self.base + self.made


def weight_units(I):
    units = []

    def modulation(l):
        w = I["ada_w"][l].rearrange("(p c) n -> p c n", c=KC)
        return [(w[:, :, n:n + 512], 512) for n in range(0, 6 * D, 512)]

    units += modulation(0)
    for l in range(2):
        w_in = I["odd_w_in" if l else "even_w_in"][0].rearrange("(p c) n -> p c n", c=KC)
        total = ODD_COLS if l else EVEN_COLS
        units += [(w_in[:, :, n:min(n + 512, total)], min(512, total - n)) for n in range(0, total, 512)]
        if l == 0:
            units += modulation(1)
        w_out = I["odd_w_out" if l else "even_w_out"][0].rearrange("(p c) n -> p c n", c=KC)
        units += [(w_out[:, :, n:n + 512], 512) for n in (0, 512)]
        units += [("experts", l)] * (3 * N_EXP)
    return units


class Trunk:

    def __init__(self, nc, ctx, I, O):
        self.nc, self.ctx, self.I, self.O = nc, ctx, I, O
        self.counters = {}
        sb = self.sb
        self.const = sb(ctx, "const", [P, N_CONST])
        self.x = sb(ctx, "x", [P, NT, D])
        self.cond = sb(ctx, "cond", [P, 2, KC])
        self.ring = sb(ctx, "ring", [P, RING, UNIT])
        self.ps = ctx.enter_context(nc.psum_tensor("ps", [P, 8, 512], F32))
        self.units = weight_units(I)
        self.landed = [self.counter(f"landed{i}") for i in range(RING)]
        self.unit_used = self.counter("unit_used")
        dram = lambda name, shape: nc.dram_tensor(name, shape, F32, kind="Internal").ap()
        self.mod_dram = dram("mod_rows", (2, 2, 6 * D))
        self.raw_dram = dram("raw_mod_rows", (2, 6 * D))
        self.h_dram = dram("h_rows", (TOK, D))
        self.y_dram = dram("expert_rows", (2 * TOK, D))

    def sb(self, ctx, name, shape, dt=F32):
        return ctx.enter_context(self.nc.sbuf_tensor(name, shape, dt))

    def counter(self, name):
        if name not in self.counters:
            self.counters[name] = Counter(self.nc, self.ctx, name)
        return self.counters[name]

    def c(self, name, parts=P):
        at, w = CONST[name]
        return self.const[0:parts, at:at + w]

    @contextmanager
    def loop(self, engine, start, end):
        before = {name: s.made for name, s in self.counters.items()}
        with engine.Fori(start, end) as i:
            yield i
        for name, s in self.counters.items():
            s.made += (s.made - before.get(name, 0)) * (end - start - 1)

    def end_stage(self):
        for s in self.counters.values():
            s.base += s.made
            s.made = 0

    def unit(self, u):
        n = self.units[u][1]
        return self.ring[:, u % RING, 0:KC * n].rearrange("p (c n) -> p c n", c=KC)

    def load_unit(self, sp, u, i=0):
        slot = u % RING
        if u >= RING:
            sp.wait_ge(self.unit_used.sem, u - RING + 1 + i * RING)
        if self.units[u][0] == "experts":
            l = self.units[u][1]
            first = self.units.index(("experts", l))
            e, part = divmod(u - first, 3)
            src = self.expert_source(l, e + 2 * i, part)
            dst = self.ring[:, slot, :].rearrange("p (c n) -> p c n", c=KC if part < 2 else FF // P)
        else:
            src, _ = self.units[u]
            dst = self.unit(u)
        sp.dma_start(dst, src).then_inc(self.landed[slot].sem, 16)

    def expert_source(self, l, e, part):
        w = self.I[("moe_w_gate", "moe_w_up", "moe_w_down")[part]][l]
        one = w[bass.ds(e, 1)]
        if part < 2:
            return one.rearrange("o (p c) n -> p (o c) n", c=KC)
        return one.rearrange("o (j p) n -> p (o j) n", p=P)

    def load_ahead(self, sp, first, end):
        if first == 0:
            for u in range(min(RING, len(self.units))):
                self.load_unit(sp, u)
        for u in range(first + RING, min(end + RING, len(self.units))):
            self.load_unit(sp, u)

    def used_at(self, u, i=0):
        return u + 1 + i * RING

    def landing(self, u):
        return self.landed[u % RING].sem

    def landed_at(self, u, i=0):
        return (u // RING + 1 + i) * 16


def spread(ap, parts=P):
    return ap.partition_broadcast(parts)


class Modulated:

    def __init__(self, T, columns):
        self.T, self.columns = T, columns

    def scalars(self, c, t):
        g = min(t, 1)
        return self.columns[:, 1, g, c:c + 1], self.columns[:, 0, g, c:c + 1]

    def scalar(self, out, src, c, t):
        scale, shift = self.scalars(c, t)
        return self.T.nc.scalar.activation(out, src, ACT.Identity, bias=shift, scale=scale)

    def vector(self, out, src, c, t):
        scale, shift = self.scalars(c, t)
        return self.T.nc.vector.tensor_scalar(out, src, scale, shift, ALU.mult, ALU.add)

    def copy_out(self, engine, turns, hT, modulate, parity, first=0, end=None):
        for g in range(first, len(turns.groups) if end is None else end):
            if g % 2 == parity:
                t, half = divmod(g, 2)
                engine.wait_ge(turns.done.sem, turns.done.at(g + 1))
                for k in range(4):
                    c = 4 * half + k
                    ins = modulate(hT[:, c, t * P:(t + 1) * P], turns.bank(g)[:, k * P:(k + 1) * P], c, t)
                ins.then_inc(turns.copied[parity].sem, turns.copied[parity].adds(1))


class Turns:

    BANKS = 2

    def __init__(self, T, groups):
        self.T, self.groups = T, groups
        self.done = T.counter("turned")
        self.copied = (T.counter("turned_act"), T.counter("turned_dve"))

    def bank(self, g):
        return self.T.ps[:, g % self.BANKS, :]

    def tensor(self, pe, first=0, end=None):
        T = self.T
        for g in range(first, len(self.groups) if end is None else end):
            sources, _, ready = self.groups[g]
            if ready is not None:
                producer, n = ready
                pe.wait_ge(producer.sem, producer.at(n))
            if g >= self.BANKS:
                self.wait_copied(pe, g - self.BANKS)
            for k, s in enumerate(sources):
                rows, cols = s.shape[0], int(np.prod(s.shape[1:]))
                ins = T.nc.tensor.transpose(self.bank(g)[0:cols, k * rows:(k + 1) * rows], s,
                                            T.c("ident")[0:rows, 0:rows])
            ins.then_inc(self.done.sem, self.done.adds(1))

    def wait_copied(self, engine, g):
        engine.wait_ge(self.copied[g % 2].sem, self.copied[g % 2].at(g // 2 + 1))

    def wait_all(self, engine):
        n = len(self.groups)
        for g in (n - 2, n - 1):
            if g >= 0:
                self.wait_copied(engine, g)

    def copy_out(self, engine, copy, parity, first=0, end=None):
        for g in range(first, len(self.groups) if end is None else end):
            if g % 2 == parity:
                sources, out, _ = self.groups[g]
                rows, cols = sources[0].shape[0], int(np.prod(sources[0].shape[1:]))
                engine.wait_ge(self.done.sem, self.done.at(g + 1))
                src = self.bank(g)[0:cols, 0:rows * len(sources)]
                if len(out.shape) == 3:
                    src = src.rearrange("p (k r) -> p k r", k=len(sources))
                copy(out, src).then_inc(self.copied[parity].sem, self.copied[parity].adds(1))


MOD_UNITS = 6 * D // 512


WIN_MOD = 5


class Modulation:

    BUFFERS = 4

    def __init__(self, T, ctx, first, start, end, banks):
        self.T, self.first, self.start, self.end, self.banks = T, first, start, end, banks
        self.rows = T.sb(ctx, f"mod{start}_rows", [2, self.BUFFERS, 512])
        self.copied = T.counter("mod_copied")
        self.stored = [T.counter(f"mod_stored{i}") for i in range(self.BUFFERS)]

    def tensor(self, pe, n, chunks=range(KC)):
        T, u = self.T, self.first + n
        if chunks[0] == 0:
            pe.wait_ge(T.landing(u), T.landed_at(u))
            k = n - self.start
            last = [j for j in range(k) if self.banks[j] == self.banks[k]]
            if last:
                pe.wait_ge(self.copied.sem, self.copied.at(last[-1] + 1))
        for c in chunks:
            ins = T.nc.tensor.matmul(T.ps[0:2, self.banks[n - self.start], :], T.cond[:, :, c], T.unit(u)[:, c, :],
                                     start=(c == 0), stop=(c == KC - 1))
        if chunks[-1] == KC - 1:
            ins.then_inc(T.unit_used.sem, T.unit_used.adds(1))

    def scalar(self, act, n):
        T, k = self.T, n - self.start
        stored, row = self.stored[k % self.BUFFERS], self.rows[:, k % self.BUFFERS, :]
        act.wait_ge(T.unit_used.sem, T.used_at(self.first + n))
        if k >= self.BUFFERS:
            act.wait_ge(stored.sem, stored.now())
        act.copy(row, T.ps[0:2, self.banks[k], :]).then_inc(self.copied.sem, self.copied.adds(1))
        act.wait_ge(self.copied.sem, self.copied.now())
        act.dma_start(T.raw_dram[:, n * 512:(n + 1) * 512], row).then_inc(stored.sem, stored.adds(16))

    def finish(self, act):
        for stored in self.stored:
            act.wait_ge(stored.sem, stored.now())


class FinishModulation:

    HALF = 3 * D

    def __init__(self, T, ctx):
        self.T = T
        self.rows, self.bias, self.gain = (T.sb(ctx, "finish_" + n, [2, w])
                                           for n, w in (("rows", self.HALF), ("bias", self.HALF), ("gain", D)))
        self.loaded, self.done, self.stored = (T.counter("finish_" + n) for n in ("loaded", "done", "stored"))

    def load(self, pool, half):
        T, I = self.T, self.T.I
        cols = slice(half * self.HALF, (half + 1) * self.HALF)
        if half:
            pool.wait_ge(self.stored.sem, self.stored.at(16))
        for dst, src in ((self.rows, T.raw_dram[:, cols]), (self.bias, spread(I["ada_b"][1, cols], 2)),
                         (self.gain, spread(I[("norm1_g", "norm2_g")[half]][1], 2))):
            pool.dma_start(dst[:, :], src).then_inc(self.loaded.sem, self.loaded.adds(16))

    def finish(self, pool, half):
        T, nc = self.T, self.T.nc
        rows, bias, gain = self.rows[:, :], self.bias[:, :], self.gain[:, :]
        pool.wait_ge(self.loaded.sem, self.loaded.at(48 * (half + 1)))
        nc.gpsimd.tensor_tensor(rows, rows, bias, ALU.add).then_inc(self.done.sem, self.done.adds(1))
        pool.wait_ge(self.done.sem, self.done.now())
        scale = rows[:, D:2 * D]
        nc.gpsimd.tensor_scalar(scale, scale, 1.0, None, ALU.add).then_inc(self.done.sem, self.done.adds(1))
        pool.wait_ge(self.done.sem, self.done.now())
        nc.gpsimd.tensor_tensor(scale, scale, gain, ALU.mult).then_inc(self.done.sem, self.done.adds(1))
        pool.wait_ge(self.done.sem, self.done.now())
        pool.dma_start(T.mod_dram[1, :, half * self.HALF:(half + 1) * self.HALF], rows).then_inc(
            self.stored.sem, self.stored.adds(16))


def stage_modulation(T, first):
    nc, I = T.nc, T.I
    with ExitStack() as ctx:
        ce = T.sb(ctx, "ce", [P, 2, KC])
        rows = T.sb(ctx, "even_rows", [2, 6 * D])
        bias = T.sb(ctx, "even_bias", [2, 6 * D])
        gain = T.sb(ctx, "even_gain", [2, 2, D])
        loads, exp, silu = T.counter("loads_act"), T.counter("act_done"), T.counter("dve_done")
        bias_in, row_done, stored = T.counter("bias_in"), T.counter("row_done"), T.counter("stored_act")
        const_in = T.counter("const_in")
        block = ctx.enter_context(nc.Block())

        @block.sync
        def _(sp):
            sp.wait_ge(loads.sem, loads.at(32))
            T.load_ahead(sp, first, first + MOD_UNITS - RING + 2)

        @block.scalar
        def _(act):
            act.dma_start(T.cond[:, 0, :], I["c_ctx"].rearrange("(p c) -> p c", c=KC)).then_inc(loads.sem, loads.adds(16))
            act.dma_start(T.cond[:, 1, :], I["c"][0].rearrange("(p c) -> p c", c=KC)).then_inc(loads.sem, loads.adds(16))
            act.dma_start(bias[:, :], spread(I["ada_b"][0], 2)).then_inc(bias_in.sem, bias_in.adds(16))
            for k, name in enumerate(("norm1_g", "norm2_g")):
                act.dma_start(gain[:, k, :], spread(I[name][0], 2)).then_inc(bias_in.sem, bias_in.adds(16))
            act.wait_ge(loads.sem, loads.at(32))
            act.activation(ce[:, :, :], T.cond[:, :, :], ACT.Exp, scale=-1.0).then_inc(exp.sem, exp.adds(1))
            act.wait_ge(T.unit_used.sem, T.used_at(first))
            act.dma_start(T.const[:, :], I["const"]).then_inc(const_in.sem, const_in.adds(16))
            act.dma_start(T.x[:, 0, :], I["x_prompt"][0]).then_inc(const_in.sem, const_in.adds(16))
            act.dma_start(T.x[:, 1:3, :], I["x_sample"][0].rearrange("(t p) d -> p t d", p=P)).then_inc(
                const_in.sem, const_in.adds(16))
            act.wait_ge(row_done.sem, row_done.at(MOD_UNITS + 2))
            act.dma_start(T.mod_dram[0], rows[:, :]).then_inc(stored.sem, stored.adds(16))
            act.wait_ge(stored.sem, stored.at(16))
            act.wait_ge(const_in.sem, const_in.at(48))

        @block.vector
        def _(dve):
            cond = T.cond[:, :, :]
            dve.wait_ge(exp.sem, exp.at(1))
            nc.vector.tensor_scalar(ce[:, :, :], ce[:, :, :], 1.0, None, ALU.add).then_inc(silu.sem, silu.adds(1))
            dve.wait_ge(silu.sem, silu.now())
            nc.vector.reciprocal(ce[:, :, :], ce[:, :, :]).then_inc(silu.sem, silu.adds(1))
            dve.wait_ge(silu.sem, silu.now())
            nc.vector.tensor_tensor(cond, cond, ce[:, :, :], ALU.mult).then_inc(silu.sem, silu.adds(1))
            dve.wait_ge(bias_in.sem, bias_in.at(48))
            for n in range(MOD_UNITS):
                dve.wait_ge(T.unit_used.sem, T.used_at(first + n))
                cols = slice(n * 512, n * 512 + 512)
                nc.vector.tensor_tensor(rows[:, cols], T.ps[0:2, n % 2, :], bias[:, cols], ALU.add).then_inc(
                    row_done.sem, row_done.adds(1))
            dve.wait_ge(row_done.sem, row_done.at(MOD_UNITS))
            for k, at in ((0, D), (1, 4 * D)):
                r = rows[:, at:at + D]
                nc.vector.scalar_tensor_tensor(out=r, in0=r, scalar=1.0, in1=gain[:, k, :], op0=ALU.add,
                                               op1=ALU.mult).then_inc(row_done.sem, row_done.adds(1))

        @block.tensor
        def _(pe):
            pe.wait_ge(silu.sem, silu.at(3))
            for n in range(MOD_UNITS):
                u = first + n
                pe.wait_ge(T.landing(u), T.landed_at(u))
                if n >= 2:
                    pe.wait_ge(row_done.sem, row_done.at(n - 1))
                for c in range(KC):
                    ins = nc.tensor.matmul(T.ps[0:2, n % 2, :], T.cond[:, :, c], T.unit(u)[:, c, :],
                                           start=(c == 0), stop=(c == KC - 1))
                ins.then_inc(T.unit_used.sem, T.unit_used.adds(1))
    T.end_stage()


def stage_projection(T, l, first, z):
    nc = T.nc
    total = ODD_COLS if l else EVEN_COLS
    n_units = -(-total // 512)
    with ExitStack() as ctx:
        columns = T.sb(ctx, f"columns{l}", [P, 2, 2, KC])
        h = T.sb(ctx, f"h{l}", [P, 2, D])
        hT = T.sb(ctx, f"hT{l}", [P, KC, TOK])
        stat = T.sb(ctx, f"stat{l}", [P, 2, NT])
        loads, squares, rstd, row = T.counter("loads_act"), T.counter("squares"), T.counter("rstd"), T.counter("rows")
        product, out = T.counter("product"), (T.counter("z_act"), T.counter("z_dve"))
        groups = []
        for t in range(NT):
            for k in range(2):
                src = [h[:, t % 2, c::KC] for c in range(4 * k, 4 * k + 4)]
                ready = (row, t + 1) if k == 0 else None
                groups.append((src, hT[:, 4 * k:4 * k + 4, t * P:(t + 1) * P], ready))
        turns = Turns(T, groups)
        modulated = Modulated(T, columns)
        block = ctx.enter_context(nc.Block())

        def z_out(engine, copy, parity):
            for e in range(n_units * NT):
                if e % 2 != parity:
                    continue
                n, t = divmod(e, NT)
                cols = min(512, total - n * 512)
                if t < NT - 1:
                    engine.wait_ge(product.sem, product.at(n * (NT - 1) + t + 1))
                else:
                    engine.wait_ge(T.unit_used.sem, T.used_at(first + n))
                copy(z[:, t, n * 512:n * 512 + cols], T.ps[:, 4 + e % 4, 0:cols]).then_inc(out[parity].sem, out[parity].adds(1))

        @block.sync
        def _(sp):
            if l == 0:
                sp.wait_ge(loads.sem, loads.at(32))
                T.load_ahead(sp, first + 2 - RING, first)
            T.load_ahead(sp, first, first + n_units)

        @block.scalar
        def _(act):
            for g in range(2):
                act.dma_start(columns[:, :, g, :],
                              T.mod_dram[l, g, 0:2 * D].rearrange("(k p c) -> p k c", k=2, c=KC)).then_inc(
                                  loads.sem, loads.adds(16))
            for t in range(NT):
                if t >= 1:
                    act.wait_ge(squares.sem, squares.at(t))
                act.activation(hT[:, 0:KC, 0:P], T.x[:, t, :].rearrange("p (c n) -> p c n", c=KC),
                                          ACT.Square, accum_out=stat[:, 0, t:t + 1]).then_inc(squares.sem, squares.adds(1))
            act.wait_ge(squares.sem, squares.at(NT))
            act.wait_ge(loads.sem, loads.at(32))
            modulated.copy_out(act, turns, hT, modulated.scalar, 0)
            z_out(act, nc.scalar.copy, 0)

        @block.gpsimd
        def _(pool):
            for t in range(NT):
                one = slice(t, t + 1)
                pool.wait_ge(squares.sem, squares.at(t + 1))
                nc.gpsimd.tensor_scalar(stat[:, 0, one], stat[:, 0, one], 1.0 / D, EPS, ALU.mult, ALU.add).then_inc(
                    rstd.sem, rstd.adds(1))
                pool.wait_ge(rstd.sem, rstd.now())
                nc.gpsimd.tensor_tensor(stat[:, 1, one], stat[:, 0, one], T.c("half")[:, 0:1], ALU.pow).then_inc(
                    rstd.sem, rstd.adds(1))

        @block.vector
        def _(dve):
            for t in range(NT):
                dve.wait_ge(rstd.sem, rstd.at(2 * t + 2))
                if t >= 2:
                    dve.wait_ge(turns.done.sem, turns.done.at(2 * (t - 1)))
                nc.vector.tensor_scalar(h[:, t % 2, :], T.x[:, t, :], stat[:, 1, t:t + 1], None, ALU.mult).then_inc(
                    row.sem, row.adds(1))
                if t == 0:
                    dve.wait_ge(loads.sem, loads.at(32))
                    dve.wait_ge(squares.sem, squares.at(NT))
                else:
                    modulated.copy_out(dve, turns, hT, modulated.vector, 1, 2 * (t - 1), 2 * t)
            modulated.copy_out(dve, turns, hT, modulated.vector, 1, 2 * NT - 2)
            z_out(dve, nc.vector.tensor_copy, 1)

        @block.tensor
        def _(pe):
            turns.tensor(pe)
            turns.wait_all(pe)
            for n in range(n_units):
                cols = min(512, total - n * 512)
                pe.wait_ge(T.landing(first + n), T.landed_at(first + n))
                for t in range(NT):
                    e = n * NT + t
                    if e >= 4:
                        pe.wait_ge(out[(e - 4) % 2].sem, out[(e - 4) % 2].at((e - 4) // 2 + 1))
                    for c in range(KC):
                        ins = nc.tensor.matmul(T.ps[:, 4 + e % 4, 0:cols], hT[:, c, t * P:(t + 1) * P],
                                               T.unit(first + n)[:, c, :], start=(c == 0), stop=(c == KC - 1))
                    if t < NT - 1:
                        ins.then_inc(product.sem, product.adds(1))
                    else:
                        ins.then_inc(T.unit_used.sem, T.unit_used.adds(1))
    T.end_stage()


def stage_output(T, l, first, mix):
    nc = T.nc
    with ExitStack() as ctx:
        mixT = T.sb(ctx, f"mixT{l}", [P, KC, TOK])
        part = T.sb(ctx, f"part{l}", [P, 2, 512])
        gate = T.sb(ctx, f"gate{l}", [P, 2, D])
        loads = T.counter("loads_act")
        product, used, steps = T.counter("product"), T.counter("row_done"), T.counter("dve_done")
        groups = [([mix[:, t, c::KC] for c in range(4 * k, 4 * k + 4)],
                   mixT[:, 4 * k:4 * k + 4, t * P:(t + 1) * P], None) for t in range(NT) for k in range(2)]
        turns = Turns(T, groups)
        block = ctx.enter_context(nc.Block())

        @block.sync
        def _(sp):
            T.load_ahead(sp, first, first + 2)

        @block.scalar
        def _(act):
            act.dma_start(gate[:, :, :], spread(T.mod_dram[l, :, 2 * D:3 * D])).then_inc(loads.sem, loads.adds(16))
            turns.copy_out(act, nc.scalar.copy, 0)

        @block.vector
        def _(dve):
            turns.copy_out(dve, nc.vector.tensor_copy, 1)
            dve.wait_ge(loads.sem, loads.at(16))
            for e in range(2 * NT):
                n, t = divmod(e, NT)
                if t < NT - 1:
                    dve.wait_ge(product.sem, product.at(n * (NT - 1) + t + 1))
                else:
                    dve.wait_ge(T.unit_used.sem, T.used_at(first + n))
                cols = slice(n * 512, n * 512 + 512)
                nc.vector.tensor_tensor(part[:, e % 2, :], T.ps[:, 4 + e % 4, :],
                                                       gate[:, min(t, 1), cols], ALU.mult).then_inc(used.sem, used.adds(1))
                dve.wait_ge(used.sem, used.now())
                nc.vector.tensor_tensor(T.x[:, t, cols], T.x[:, t, cols], part[:, e % 2, :], ALU.add).then_inc(steps.sem, steps.adds(1))
                if e >= 1:
                    dve.wait_ge(steps.sem, steps.at(e))

        @block.tensor
        def _(pe):
            turns.tensor(pe)
            turns.wait_all(pe)
            for n in range(2):
                pe.wait_ge(T.landing(first + n), T.landed_at(first + n))
                for t in range(NT):
                    e = n * NT + t
                    if e >= 4:
                        pe.wait_ge(used.sem, used.at(e - 3))
                    for c in range(KC):
                        ins = nc.tensor.matmul(T.ps[:, 4 + e % 4, :], mixT[:, c, t * P:(t + 1) * P],
                                               T.unit(first + n)[:, c, :], start=(c == 0), stop=(c == KC - 1))
                    if t < NT - 1:
                        ins.then_inc(product.sem, product.adds(1))
                    else:
                        ins.then_inc(T.unit_used.sem, T.unit_used.adds(1))
    T.end_stage()



class Attention:

    def __init__(self, T, ctx, name, groups):
        self.T, self.groups = T, groups
        self.units = [u for g in groups for u in g[0]]
        n = len(self.units)
        self.masked = T.sb(ctx, name + "_masked", [P, 2, 384])
        self.prob = T.sb(ctx, name + "_prob", [P, 2, 384])
        self.probT = T.sb(ctx, name + "_probT", [P, 2, 384])
        self.top = T.sb(ctx, name + "_top", [P, n])
        self.shift = T.sb(ctx, name + "_shift", [P, n])
        self.sum = T.sb(ctx, name + "_sum", [P, n])
        if self.sinks():
            self.sink = T.sb(ctx, name + "_sink_exp", [P, n])
        names = ("score", "shift", "prob", "turn", "out", "sink_in", "sink_out", "group")
        (self.s_score, self.s_shift, self.s_prob, self.s_turn, self.s_out, self.s_sink_in, self.s_sink_out,
         self.s_group) = (T.counter("att_" + s) for s in names)
        self.copied = (T.counter("att_copied_act"), T.counter("att_copied_dve"))

    def tensor(self, pe, between=None):
        T, nc, n = self.T, self.T.nc, len(self.units)
        for i in range(n + 2):
            if i < n:
                q, k = self.units[i][:2]
                if i >= 2:
                    pe.wait_ge(self.s_prob.sem, self.s_prob.at(i - 1))
                nc.tensor.matmul(T.ps[:, i % 2, 0:k.shape[1]], q, k, start=True, stop=True).then_inc(self.s_score.sem, self.s_score.adds(1))
            if 1 <= i < n + 1:
                u = i - 1
                keys = self.units[u][1].shape[1]
                pe.wait_ge(self.s_prob.sem, self.s_prob.at(u + 1))
                if u >= 2:
                    pe.wait_ge(self.copied[u % 2].sem, self.copied[u % 2].at(u // 2))
                for j in range(keys // P):
                    ins = nc.tensor.transpose(T.ps[:, 2 + u % 2, j * P:(j + 1) * P],
                                              self.prob[:, u % 2, j * P:(j + 1) * P], T.c("ident"))
                ins.then_inc(self.s_turn.sem, self.s_turn.adds(1))
            if i >= 2:
                u = i - 2
                g, h = self.place(u)
                values = self.units[u][2]
                pe.wait_ge(self.copied[u % 2].sem, self.copied[u % 2].at(u // 2 + 1))
                if h == 0 and g >= 2:
                    pe.wait_ge(self.s_group.sem, self.s_group.at(g - 1))
                for j, v in enumerate(values):
                    ins = nc.tensor.matmul(T.ps[:, 4 + g % 2, h * HD:(h + 1) * HD],
                                           self.probT[:, u % 2, j * P:(j + 1) * P], v,
                                           start=(j == 0), stop=(j == len(values) - 1))
                ins.then_inc(self.s_out.sem, self.s_out.adds(1))
            if between is not None:
                between(i)

    def place(self, u):
        return u // HEADS, u % HEADS

    def copy_out(self, engine, copy, u):
        if 0 <= u < len(self.units):
            keys = self.units[u][1].shape[1]
            engine.wait_ge(self.s_turn.sem, self.s_turn.at(u + 1))
            if u >= 2:
                engine.wait_ge(self.s_out.sem, self.s_out.at(u - 1))
            copy(self.probT[:, u % 2, 0:keys], self.T.ps[:, 2 + u % 2, 0:keys]).then_inc(self.copied[u % 2].sem, self.copied[u % 2].adds(1))

    def sinks(self):
        return [g for g in range(len(self.groups)) if self.groups[g][2] is not None]

    def scalar(self, act):
        nc, n = self.T.nc, len(self.units)
        for i in range(n + 3):
            if i < n:
                q, k, _, mask, scale = self.units[i]
                keys = k.shape[1]
                act.wait_ge(self.s_shift.sem, self.s_shift.at(i + 1))
                if i >= 2:
                    act.wait_ge(self.s_turn.sem, self.s_turn.at(i - 1))
                src = self.T.ps[:, i % 2, 0:keys] if mask is None else self.masked[:, i % 2, 0:keys]
                act.activation(self.prob[:, i % 2, 0:keys], src, ACT.Exp, bias=self.shift[:, i:i + 1],
                                              scale=scale, accum_out=self.sum[:, i:i + 1]).then_inc(self.s_prob.sem, self.s_prob.adds(1))
            if i >= 1 and (i - 1) % 2 == 0:
                self.copy_out(act, nc.scalar.copy, i - 1)
            g = (i - 2) // HEADS
            if i >= 2 and (i - 2) % HEADS == HEADS - 1 and self.groups[g][2] is not None:
                act.wait_ge(self.s_sink_in.sem, self.s_sink_in.at(self.sinks().index(g) + 1))
                cols = self.sink[:, g * HEADS:(g + 1) * HEADS]
                act.activation(cols, cols, ACT.Exp).then_inc(self.s_sink_out.sem, self.s_sink_out.adds(1))

    def vector(self, dve):
        nc, T, n = self.T.nc, self.T, len(self.units)
        steps = T.counter("dve_done")
        for i in range(n + 3):
            if i < n:
                g, h = self.place(i)
                q, k, _, mask, scale = self.units[i]
                keys = k.shape[1]
                dve.wait_ge(self.s_score.sem, self.s_score.at(i + 1))
                scores = T.ps[:, i % 2, 0:keys]
                top = self.top[:, i:i + 1]
                if mask is None:
                    nc.vector.reduce_max(top, scores, AX).then_inc(steps.sem, steps.adds(1))
                    dve.wait_ge(steps.sem, steps.now())
                else:
                    if i >= 2:
                        dve.wait_ge(self.s_prob.sem, self.s_prob.at(i - 1))
                    nc.vector.tensor_tensor_reduce(
                        out=self.masked[:, i % 2, 0:keys], in0=scores, in1=mask, scale=1.0, scalar=-3e38,
                        op0=ALU.add, op1=ALU.max, accum_out=top).then_inc(steps.sem, steps.adds(1))
                    dve.wait_ge(steps.sem, steps.now())
                sink = self.groups[g][2]
                if sink is None:
                    nc.vector.tensor_scalar(self.shift[:, i:i + 1], top, -scale, None, ALU.mult).then_inc(self.s_shift.sem, self.s_shift.adds(1))
                else:
                    nc.vector.tensor_scalar(self.shift[:, i:i + 1], top, -scale,
                                                            sink[:, HEADS + h:HEADS + h + 1], ALU.mult, ALU.min).then_inc(self.s_shift.sem, self.s_shift.adds(1))
            if i >= 1 and (i - 1) % 2 == 1:
                self.copy_out(dve, nc.vector.tensor_copy, i - 1)
            if i >= 2 and (i - 2) % HEADS == HEADS - 1:
                g = (i - 2) // HEADS
                _, out, sink = self.groups[g]
                cols = slice(g * HEADS, (g + 1) * HEADS)
                dve.wait_ge(self.s_prob.sem, self.s_prob.at((g + 1) * HEADS))
                if sink is not None:
                    nc.vector.tensor_tensor(self.sink[:, cols], self.shift[:, cols],
                                                              sink[:, 0:HEADS], ALU.add).then_inc(self.s_sink_in.sem, self.s_sink_in.adds(1))
                    dve.wait_ge(self.s_sink_out.sem, self.s_sink_out.at(self.sinks().index(g) + 1))
                    nc.vector.tensor_tensor(self.sum[:, cols], self.sum[:, cols],
                                                            self.sink[:, cols], ALU.add).then_inc(steps.sem, steps.adds(1))
                    dve.wait_ge(steps.sem, steps.now())
                nc.vector.reciprocal(self.sum[:, cols], self.sum[:, cols]).then_inc(steps.sem, steps.adds(1))
                dve.wait_ge(steps.sem, steps.now())
                dve.wait_ge(self.s_out.sem, self.s_out.at((g + 1) * HEADS))
                each = self.sum[:, cols].unsqueeze(2).broadcast_to([P, HEADS, HD])
                nc.vector.tensor_tensor(
                    out, T.ps[:, 4 + g % 2, 0:HEADS * HD].rearrange("p (h d) -> p h d", h=HEADS), each, ALU.mult).then_inc(self.s_group.sem, self.s_group.adds(1))


def key_order(kT):
    return kT[..., 0:P], kT[..., P:4 * P]


def stage_window(T, first, z, mix):
    nc, I, O = T.nc, T.I, T.O
    qk_heads = 10
    with ExitStack() as ctx:
        sq = mix[:, :, 0:qk_heads * HD]
        rot = z[:, 1:3, WQ0:WQ0 + qk_heads * HD]
        stat = T.sb(ctx, "win_stat", [P, 2, NT * qk_heads])
        gains = T.sb(ctx, "win_gain", [P, 2, HD])
        sink = T.sb(ctx, "win_sink", [P, 2 * HEADS])
        kc = T.sb(ctx, "win_kc", [P, P])
        vc = T.sb(ctx, "win_vc", [P, P])
        qT = T.sb(ctx, "win_qT", [P, 4, TOK])
        kT = T.sb(ctx, "win_kT", [P, 4 * P])
        loads, squares, sums, rstd = T.counter("loads_act"), T.counter("squares"), T.counter("sums"), T.counter("rstd")
        steps, ready, rotated, stored = (T.counter("dve_done"), T.counter("rows"), T.counter("pool_done"),
                                         T.counter("stored_act"))
        normed = T.counter("normed")
        qk = z[:, :, WQ0:WQ0 + qk_heads * HD]
        by_head = qk.rearrange("p t (h d) -> p t h d", d=HD)
        paired = T.sb(ctx, "win_paired", [P, NT, qk_heads * HD])
        paired_heads = paired[:, :, :].rearrange("p t (h d) -> p t h d", d=HD)
        groups = [([paired[:, t, 2 * j * HD:2 * (j + 1) * HD] for t in range(NT)], qT[:, j, :],
                   (ready, 1) if j == 0 else None) for j in range(4)]
        keys = paired[:, :, HEADS * HD:]
        groups.append(([keys[:, 0, :], kc[:, :], keys[:, 1, :], keys[:, 2, :]],
                       kT[:, :], (loads, 5 * 16)))
        turns = Turns(T, groups)

        att_groups = []
        for t in range(NT):
            units = []
            for h in range(HEADS):
                kv = h // 4
                rows = slice(kv * HD, kv * HD + HD)
                k = key_order(kT[rows, :])[min(t, 1)]
                own = [z[:, s, WV0 + kv * HD:WV0 + (kv + 1) * HD] for s in range(NT)]
                values = own[0:1] if t == 0 else [vc[:, kv * HD:(kv + 1) * HD]] + own[1:]
                mask = None if t == 0 else T.c("win")[:, (t - 1) * 384:t * 384]
                units.append((qT[rows, h % 4, t * P:(t + 1) * P], k, values, mask, HD ** -0.5))
            out = mix[:, t, 512:1024].rearrange("p (h d) -> p h d", d=HD)
            att_groups.append((units, out, sink))
        att = Attention(T, ctx, "win", att_groups)
        mod = Modulation(T, ctx, first, 0, WIN_MOD, [6, 7] * WIN_MOD)
        early = range(WIN_MOD - 1)
        block = ctx.enter_context(nc.Block())

        @block.sync
        def _(sp):
            T.load_ahead(sp, first, first + WIN_MOD)

        @block.scalar
        def _(act):
            for dst, src in ((gains[:, 0, :], spread(I["win_q_g"][0])), (gains[:, 1, :], spread(I["win_k_g"][0])),
                             (sink[:, 0:HEADS], spread(I["win_sink"][0])),
                             (kc[:, :], I["cache_win_k"][0, 0].rearrange("s h d -> s (h d)")),
                             (vc[:, :], I["cache_win_v"][0, 0].rearrange("s h d -> s (h d)"))):
                act.dma_start(dst, src).then_inc(loads.sem, loads.adds(16))
            act.activation(sq[:, :, :], qk, ACT.Square).then_inc(squares.sem, squares.adds(1))
            for n in early:
                mod.scalar(act, n)
            turns.copy_out(act, nc.scalar.copy, 0)
            att.scalar(act)
            mod.scalar(act, WIN_MOD - 1)
            mod.finish(act)
            act.wait_ge(normed.sem, normed.at(1))
            act.dma_start(O["win_k"][0, 0].rearrange("s h d -> s (h d)"), keys[:, 0, :]).then_inc(stored.sem, stored.adds(16))
            act.dma_start(O["win_v"][0, 0].rearrange("s h d -> s (h d)"), z[:, 0, WV0:WV0 + P]).then_inc(stored.sem, stored.adds(16))
            act.wait_ge(stored.sem, stored.at(32))

        @block.gpsimd
        def _(pool):
            pool.wait_ge(sums.sem, sums.at(1))
            nc.gpsimd.tensor_scalar(stat[:, 0, :], stat[:, 0, :], 1.0 / HD, EPS, ALU.mult, ALU.add).then_inc(rstd.sem, rstd.adds(1))
            pool.wait_ge(rstd.sem, rstd.now())
            nc.gpsimd.tensor_tensor(stat[:, 1, :], stat[:, 0, :], T.c("half")[:, 0:NT * qk_heads], ALU.pow).then_inc(rstd.sem, rstd.adds(1))
            pool.wait_ge(normed.sem, normed.at(1))
            for t in range(2):
                cos = T.c("cos64")[:, t * HD:(t + 1) * HD].unsqueeze(1).broadcast_to([P, qk_heads, HD])
                nc.gpsimd.tensor_tensor(rot[:, t, :].rearrange("p (h d) -> p h d", d=HD),
                                                   paired_heads[:, t + 1], cos, ALU.mult).then_inc(rotated.sem, rotated.adds(1))

        @block.vector
        def _(dve):
            dve.wait_ge(squares.sem, squares.at(1))
            nc.vector.reduce_sum(stat[:, 0, :].rearrange("p (t h) -> p t h", t=NT),
                                         sq[:, :, :].rearrange("p t (h d) -> p t h d", d=HD), AX).then_inc(sums.sem, sums.adds(1))
            dve.wait_ge(loads.sem, loads.at(5 * 16))
            nc.vector.tensor_scalar(sink[:, HEADS:], sink[:, 0:HEADS], -1.0, None, ALU.mult).then_inc(steps.sem, steps.adds(1))
            dve.wait_ge(steps.sem, steps.now())
            dve.wait_ge(rstd.sem, rstd.at(2))
            each = stat[:, 1, :].rearrange("p (t h) -> p t h", t=NT).unsqueeze(3).broadcast_to([P, NT, qk_heads, HD])
            nc.vector.tensor_tensor(by_head, by_head, each, ALU.mult).then_inc(steps.sem, steps.adds(1))
            dve.wait_ge(steps.sem, steps.now())
            for t in range(NT):
                gain = gains[:, 0, :].unsqueeze(1).unsqueeze(1).broadcast_to([P, 2, 4, HD])
                nc.vector.tensor_tensor(
                    paired[:, t, 0:512].rearrange("p (j a d) -> p a j d", a=2, d=HD),
                    z[:, t, WQ0:WQ0 + 512].rearrange("p (a j d) -> p a j d", a=2, d=HD), gain, ALU.mult).then_inc(steps.sem, steps.adds(1))
            gain = gains[:, 1, :].unsqueeze(1).unsqueeze(1).broadcast_to([P, NT, 2, HD])
            dve.wait_ge(steps.sem, steps.at(steps.made))
            nc.vector.tensor_tensor(paired_heads[:, :, 8:10, :], by_head[:, :, 8:10, :], gain, ALU.mult).then_inc(normed.sem, normed.adds(1))
            dve.wait_ge(normed.sem, normed.now())
            rope(T, dve, paired_heads[:, 1:3], sq, rot, (rotated, 2), qk_heads, HD, ready)
            turns.copy_out(dve, nc.vector.tensor_copy, 1)
            att.vector(dve)

        @block.tensor
        def _(pe):
            for n in early:
                mod.tensor(pe, n)
            turns.tensor(pe)
            turns.wait_all(pe)

            def between(i):
                if i % 3 == 2 and i // 3 < KC:
                    mod.tensor(pe, WIN_MOD - 1, range(i // 3, i // 3 + 1))

            att.tensor(pe, between)
    T.end_stage()


def rope(T, dve, x, swapped, straight, straight_ready, heads, width, done):
    nc, steps = T.nc, T.counter("dve_done")
    q = width // 4
    for t in range(2):
        src = x[:, t].rearrange("p h (a b d) -> p h a b d", a=2, b=2)
        dst = swapped[:, t, 0:heads * width].rearrange("p (h a b d) -> p h a b d", h=heads, a=2, b=2)
        sin = T.c(f"sin{width}")[:, t * width:(t + 1) * width].rearrange("p (a b d) -> p a b d", a=2, b=2)
        for b in range(2):
            s = sin[:, :, b, :].unsqueeze(1).broadcast_to([P, heads, 2, q])
            ins = nc.vector.tensor_tensor(dst[:, :, :, b, :], src[:, :, :, 1 - b, :], s, ALU.mult)
            ins.then_inc(steps.sem, steps.adds(1))
    dve.wait_ge(steps.sem, steps.at(steps.made))
    dve.wait_ge(straight_ready[0].sem, straight_ready[0].at(straight_ready[1]))
    ins = nc.vector.tensor_tensor(x, straight[:, :, 0:heads * width].rearrange("p t (h d) -> p t h d", d=width),
                                  swapped[:, 0:2, 0:heads * width].rearrange("p t (h d) -> p t h d", d=width), ALU.add)
    ins.then_inc(done.sem, done.adds(1))



def stage_mlstm(T, first, z, mix):
    nc, I, O = T.nc, T.I, T.O
    pairs = [(h, d) for h in range(ML_H) for d in range(2)]
    W = ML_D + 1
    k_scale = ML_D ** -0.5
    with ExitStack() as ctx:
        sb = lambda name, shape: T.sb(ctx, "ml_" + name, shape)
        area = sb("area", [P, 4 * TOK])
        gates = area[0:4, :].rearrange("p (k t) -> p k t", k=4)
        decay = area[:, 0:1024].rearrange("p (b n) -> p b n", b=2)
        run = sb("run", [4, 2, 2, TOK])
        gate_b = sb("gate_b", [4, 4])
        m0_row, m0_all = sb("m0_row", [4, 2]), sb("m0_all", [P, 2 * ML_H])
        cols = sb("cols", [P, NT, 3, 2 * ML_H])
        w_prev = sb("w_prev", [P, 2, 2 * ML_H])
        floor = sb("floor", [P, NT, 2 * ML_H])
        qT, kT = sb("qT", [P, 2, TOK]), sb("kT", [P, 2, TOK])
        v1 = z[:, :, WQ0:WQ0 + ML_H * W].rearrange("p t (h n) -> p t h n", h=ML_H)
        c0 = sb("c0", [P, 2 * ML_H, W])
        prob = sb("prob", [P, 2, 512])
        kw = sb("kw", [P, 2, P])
        own = sb("own", [P, 2, NT, W])
        state = sb("state", [P, 2, W])
        den = sb("den", [P, 2, NT])
        stat = sb("stat", [P, 2, NT * ML_H])
        gain = sb("gain", [P, ML_D])
        squares_at = z[:, :, 0:512]

        loads, steps, act_steps, pool_steps = (T.counter("loads_act"), T.counter("dve_done"), T.counter("act_done"),
                                               T.counter("pool_done"))
        gates_turned, gates_in, logs, rows = (T.counter("ml_" + n) for n in ("gates_turned", "gates_in", "logs", "rows"))
        cols_turned, cols_in, factors = (T.counter("ml_" + n) for n in ("cols_turned", "cols_in", "factors"))
        score, spread_m, log_d, exp_d, prob_in, kw_in = (
            T.counter("ml_" + n) for n in ("score", "spread", "log_d", "exp_d", "prob", "kw"))
        num, num_out, c_out, combined = (T.counter("ml_" + n) for n in ("num", "num_out", "c_out", "combined"))
        stored, v_in, squares, sums, rstd = (T.counter("stored_act"), T.counter("ml_v"), T.counter("squares"),
                                             T.counter("sums"), T.counter("rstd"))
        state_stored = [T.counter(f"ml_state_stored{i}") for i in range(2)]
        groups = []
        for h in range(ML_H):
            for base, buf in ((0, qT), (512, kT)):
                groups.append(([z[:, t, base + h * P:base + (h + 1) * P] for t in range(NT)], buf[:, h % 2, :], None))
        turns = Turns(T, groups)
        tiles = [(0, 0), (1, 1), (2, 2), (1, 2), (2, 1)]
        gates_ps = T.ps[0:4, 4:7, :].rearrange("p a b -> p (a b)")
        cols_ps = T.ps[:, 7, 0:NT * 24].rearrange("p (t w n) -> p t w n", t=NT, w=3)
        c_ps = T.ps[:, 7, 2 * W:3 * W]
        mod = Modulation(T, ctx, first, WIN_MOD, MOD_UNITS, [3, 2] + [3] * MOD_UNITS)
        early, late = range(WIN_MOD, MOD_UNITS - 4), range(MOD_UNITS - 4, MOD_UNITS)
        block = ctx.enter_context(nc.Block())

        @block.sync
        def _(sp):
            T.load_ahead(sp, first + WIN_MOD, first + MOD_UNITS)

        def tile(a, t):
            return a[:, t * P:(t + 1) * P]

        @block.scalar
        def _(act):
            with nc.allow_non_contiguous_dma(reason="small vectors"):
                for dst, src in ((gate_b[:, :], I["ml_gate_b"][0].rearrange("(k h) -> h k", k=4)),
                                 (m0_row[:, :], I["state_ml_m"][0, 0].rearrange("d h -> h d")),
                                 (m0_all[:, :], spread(I["state_ml_m"][0, 0].rearrange("d h -> (d h)"))),
                                 (gain[:, :], spread(I["ml_out_g"][0])),
                                 (c0[:, :, 0:ML_D], I["state_ml_c"][0, 0].rearrange("d h k v -> k (d h) v")),
                                 (c0[:, :, ML_D], I["state_ml_n"][0, 0].rearrange("d h k -> k (d h)"))):
                    act.dma_start(dst, src).then_inc(loads.sem, loads.adds(16))
            turns.copy_out(act, nc.scalar.copy, 0, 0, 2)
            act.wait_ge(gates_in.sem, gates_in.at(4))
            f = gates[:, 1::2, :]
            tmp = run[:, 1, :, :]
            act.activation(tmp, f, ACT.Abs).then_inc(act_steps.sem, act_steps.adds(1))
            act.wait_ge(act_steps.sem, act_steps.now())
            act.activation(tmp, tmp, ACT.Exp, scale=-1.0).then_inc(act_steps.sem, act_steps.adds(1))
            act.wait_ge(act_steps.sem, act_steps.now())
            act.activation(tmp, tmp, ACT.Ln, bias=1.0).then_inc(logs.sem, logs.adds(1))
            for n in early:
                mod.scalar(act, n)
            zo = z[:, :, 1536:2048]
            act.activation(zo, zo, ACT.Exp, scale=-1.0).then_inc(act_steps.sem, act_steps.adds(1))
            act.wait_ge(rows.sem, rows.at(1))
            with nc.allow_non_contiguous_dma(reason="four numbers"):
                for d in range(2):
                    last = SEQ - 1 if d == 0 else 0
                    act.dma_start(O["ml_m"][0, 0, d].rearrange("(h o) -> h o", o=1),
                                            gates[:, 2 * d + 1, last:last + 1]).then_inc(stored.sem, stored.adds(16))
            act.wait_ge(cols_in.sem, cols_in.at(2))
            act.activation(w_prev[:, :, :], w_prev[:, :, :], ACT.Exp).then_inc(factors.sem, factors.adds(1))
            act.activation(floor[:, :, :], cols[:, :, 2, :], ACT.Exp, scale=-1.0).then_inc(factors.sem, factors.adds(1))
            for i in range(len(pairs) + 1):
                if i % 2 == 0 and i >= 2:
                    mod.scalar(act, late[i // 2 - 1])
                if i < len(pairs):
                    act.wait_ge(log_d.sem, log_d.at(i + 1))
                    act.activation(decay[:, i % 2, :], decay[:, i % 2, :], ACT.Exp, scale=-1.0).then_inc(exp_d.sem, exp_d.adds(1))
                if i >= 1:
                    w = i - 1
                    h, d = pairs[w]
                    act.wait_ge(num.sem, num.at(w + 1))
                    if w >= 2:
                        act.wait_ge(combined.sem, combined.at(w - 1))
                    nc.scalar.copy(own[:, w % 2, :, :], T.ps[:, 6, 0:NT * W].rearrange("p (t n) -> p t n", t=NT)).then_inc(num_out.sem, num_out.adds(1))
                    act.wait_ge(c_out.sem, c_out.at(w + 1))
                    with nc.allow_non_contiguous_dma(reason="n, one number per partition"):
                        act.dma_start(O["ml_c"][0, 0, d, h], state[:, w % 2, 0:ML_D]).then_inc(state_stored[w % 2].sem, state_stored[w % 2].adds(16))
                        act.dma_start(O["ml_n"][0, 0, d, h].rearrange("(k o) -> k o", o=1),
                                                            state[:, w % 2, ML_D:W]).then_inc(state_stored[w % 2].sem, state_stored[w % 2].adds(16))
                if i % 2 == 1 and i + 1 < len(pairs):
                    turns.copy_out(act, nc.scalar.copy, 0, i + 1, i + 3)
            act.wait_ge(combined.sem, combined.at(len(pairs)))
            act.activation(squares_at, mix[:, :, 0:512], ACT.Square).then_inc(squares.sem, squares.adds(1))
            mod.finish(act)
            for half in range(2):
                act.wait_ge(state_stored[half].sem, state_stored[half].at(32 * len(pairs) // 2))

        @block.gpsimd
        def _(pool):
            for h in range(ML_H):
                nc.gpsimd.tensor_copy(v1[:, :, h, 0:ML_D], z[:, :, 1024 + h * P:1024 + (h + 1) * P]).then_inc(v_in.sem, v_in.adds(1))
            nc.gpsimd.memset(v1[:, :, :, ML_D:W], 1.0).then_inc(v_in.sem, v_in.adds(1))
            pool.wait_ge(sums.sem, sums.at(1))
            nc.gpsimd.tensor_scalar(stat[:, 0, :], stat[:, 0, :], 1.0 / ML_D, EPS, ALU.mult, ALU.add).then_inc(rstd.sem, rstd.adds(1))
            pool.wait_ge(rstd.sem, rstd.now())
            nc.gpsimd.tensor_tensor(stat[:, 1, :], stat[:, 0, :], T.c("half")[:, 0:NT * ML_H], ALU.pow).then_inc(rstd.sem, rstd.adds(1))

        @block.vector
        def _(dve):
            turns.copy_out(dve, nc.vector.tensor_copy, 1, 0, 2)
            dve.wait_ge(loads.sem, loads.at(6 * 16))
            dve.wait_ge(gates_turned.sem, gates_turned.at(1))
            for k in range(4):
                nc.vector.tensor_scalar(gates[:, k, :], gates_ps[:, k * TOK:(k + 1) * TOK],
                                                    gate_b[:, k:k + 1], None, ALU.add).then_inc(gates_in.sem, gates_in.adds(1))
            dve.wait_ge(logs.sem, logs.at(1))
            f, i_gate = gates[:, 1::2, :], gates[:, 0::2, :]
            nc.vector.scalar_tensor_tensor(out=f, in0=f, scalar=0.0, in1=run[:, 1, :, :],
                                                           op0=ALU.min, op1=ALU.subtract).then_inc(steps.sem, steps.adds(1))
            dve.wait_ge(steps.sem, steps.now())
            spans = (slice(0, SEQ), slice(SEQ, TOK))
            ones = T.c("ones", 4)[:, 0:1]

            def scan(out, src, first, op):
                for d in range(2):
                    for n, span in enumerate(spans):
                        o, s = out[:, d, span], src(d)[:, span]
                        width = span.stop - span.start
                        if d:
                            o, s = o[:, ::-1], s[:, ::-1]
                        nc.vector.tensor_tensor_scan(o, ones.broadcast_to([4, width]), s, first(d, n), ALU.mult, op).then_inc(steps.sem, steps.adds(1))
                dve.wait_ge(steps.sem, steps.at(steps.made))

            scan(run[:, 0], lambda d: gates[:, 2 * d + 1, :], lambda d, n: 0.0, ALU.add)
            nc.vector.tensor_tensor(i_gate, i_gate, run[:, 0], ALU.subtract).then_inc(steps.sem, steps.adds(1))
            dve.wait_ge(steps.sem, steps.now())
            scan(run[:, 1], lambda d: gates[:, 2 * d, :], lambda d, n: m0_row[:, d:d + 1] if n else 0.0, ALU.max)
            nc.vector.tensor_tensor(f, run[:, 0], run[:, 1], ALU.add).then_inc(rows.sem, rows.adds(1))
            dve.wait_ge(cols_turned.sem, cols_turned.at(1))
            nc.vector.tensor_copy(cols[:, :, :, :], cols_ps).then_inc(cols_in.sem, cols_in.adds(1))
            dve.wait_ge(cols_in.sem, cols_in.now())
            m0 = m0_all[:, :].unsqueeze(1).broadcast_to([P, 2, 2 * ML_H])
            nc.vector.tensor_tensor(w_prev[:, :, :], m0, cols[:, 1:3, 1, :], ALU.subtract).then_inc(cols_in.sem, cols_in.adds(1))
            dve.wait_ge(stored.sem, stored.at(32))

            def combine(w):
                h, d = pairs[w]
                o = own[:, w % 2]
                dve.wait_ge(num.sem, num.at(w + 1))
                if w >= 2:
                    dve.wait_ge(state_stored[w % 2].sem, state_stored[w % 2].at(32 * (w // 2)))
                nc.vector.tensor_copy(state[:, w % 2, :], c_ps).then_inc(c_out.sem, c_out.adds(1))
                dve.wait_ge(num_out.sem, num_out.at(w + 1))
                dve.wait_ge(factors.sem, factors.at(2))
                for t in (1, 2):
                    nc.vector.scalar_tensor_tensor(
                        out=o[:, t, :], in0=T.ps[:, 7, (t - 1) * W:t * W], scalar=w_prev[:, t - 1, d * ML_H + h:d * ML_H + h + 1],
                        in1=o[:, t, :], op0=ALU.mult, op1=ALU.add).then_inc(steps.sem, steps.adds(1))
                dve.wait_ge(steps.sem, steps.at(steps.made))
                n = den[:, w % 2, :]
                nc.vector.scalar_tensor_tensor(out=n, in0=o[:, :, ML_D], scalar=-1.0,
                                                               in1=floor[:, :, d * ML_H + h], op0=ALU.mult, op1=ALU.max).then_inc(steps.sem, steps.adds(1))
                dve.wait_ge(steps.sem, steps.now())
                nc.vector.tensor_tensor(n, n, o[:, :, ML_D], ALU.max).then_inc(steps.sem, steps.adds(1))
                dve.wait_ge(steps.sem, steps.now())
                nc.vector.reciprocal(n, n).then_inc(steps.sem, steps.adds(1))
                dve.wait_ge(steps.sem, steps.now())
                each = n.unsqueeze(2).broadcast_to([P, NT, ML_D])
                out = mix[:, :, h * P:(h + 1) * P]
                if d == 0:
                    nc.vector.tensor_tensor(out, o[:, :, 0:ML_D], each, ALU.mult).then_inc(combined.sem, combined.adds(1))
                    dve.wait_ge(combined.sem, combined.now())
                else:
                    nc.vector.tensor_tensor(o[:, :, 0:ML_D], o[:, :, 0:ML_D], each, ALU.mult).then_inc(steps.sem, steps.adds(1))
                    dve.wait_ge(steps.sem, steps.now())
                    nc.vector.tensor_tensor(out, out, o[:, :, 0:ML_D], ALU.add).then_inc(combined.sem, combined.adds(1))
                    dve.wait_ge(combined.sem, combined.now())

            for i in range(len(pairs) + 2):
                if i < len(pairs):
                    h, d = pairs[i]
                    m_all = T.ps[:, 4 + i % 2, 0:TOK]
                    mask = T.c("ml_b" if d else "ml_f")
                    dve.wait_ge(spread_m.sem, spread_m.at(i + 1))
                    if i >= 2:
                        dve.wait_ge(kw_in.sem, kw_in.at(i - 1))
                        dve.wait_ge(prob_in.sem, prob_in.at(i - 1))
                    dec = decay[:, i % 2, :]
                    for slot, (s, t) in enumerate(tiles[0:3] + [tiles[3 + d]]):
                        a = cols[:, s, 0, d * ML_H + h:d * ML_H + h + 1]
                        if slot < 3:
                            ins = nc.vector.scalar_tensor_tensor(out=tile(dec, slot), in0=tile(m_all, t), scalar=a,
                                                                 in1=mask, op0=ALU.subtract, op1=ALU.max)
                        else:
                            ins = nc.vector.tensor_scalar(tile(dec, slot), tile(m_all, t), a, 0.0, ALU.subtract, ALU.max)
                        done = log_d if slot == 3 else steps
                        ins.then_inc(done.sem, done.adds(1))
                if i >= 2:
                    combine(i - 2)
                if i < len(pairs):
                    dve.wait_ge(exp_d.sem, exp_d.at(i + 1))
                    dve.wait_ge(score.sem, score.at(h + 1))
                    pr = prob[:, i % 2, :]
                    if i >= 2:
                        dve.wait_ge(num.sem, num.at(i - 1))
                    same = 4 if d == 0 else 3
                    ins = nc.vector.scalar_tensor_tensor(out=pr[:, 0:same * P], in0=dec[:, 0:same * P], scalar=k_scale,
                                                         in1=T.ps[:, 2, 0:same * P], op0=ALU.mult, op1=ALU.mult)
                    if d:
                        ins.then_inc(steps.sem, steps.adds(1))
                        dve.wait_ge(steps.sem, steps.now())
                        ins = nc.vector.scalar_tensor_tensor(out=pr[:, 3 * P:], in0=dec[:, 3 * P:], scalar=k_scale,
                                                             in1=T.ps[:, 5, TOK:], op0=ALU.mult, op1=ALU.mult)
                    ins.then_inc(prob_in.sem, prob_in.adds(1))
                    last = SEQ - 1 if d == 0 else 0
                    nc.vector.tensor_scalar(kw[:, i % 2, :], z[:, 0, 512 + h * P:512 + (h + 1) * P],
                                                     dec[:, last:last + 1], k_scale, ALU.mult, ALU.mult).then_inc(kw_in.sem, kw_in.adds(1))
                if i % 2 == 1 and i + 1 < len(pairs):
                    turns.copy_out(dve, nc.vector.tensor_copy, 1, i + 1, i + 3)
            dve.wait_ge(act_steps.sem, act_steps.at(3))
            zo = z[:, :, 1536:2048]
            nc.vector.tensor_scalar(zo, zo, 1.0, None, ALU.add).then_inc(steps.sem, steps.adds(1))
            dve.wait_ge(steps.sem, steps.now())
            nc.vector.reciprocal(zo, zo).then_inc(steps.sem, steps.adds(1))
            dve.wait_ge(steps.sem, steps.now())
            dve.wait_ge(squares.sem, squares.at(1))
            heads = lambda a: a.rearrange("p t (h d) -> p t h d", h=ML_H)
            nc.vector.reduce_sum(stat[:, 0, :].rearrange("p (t h) -> p t h", t=NT), heads(squares_at), AX).then_inc(sums.sem, sums.adds(1))
            out = mix[:, :, 0:512]
            g = gain[:, :].unsqueeze(1).unsqueeze(1).broadcast_to([P, NT, ML_H, ML_D])
            nc.vector.tensor_tensor(heads(zo), heads(zo), g, ALU.mult).then_inc(steps.sem, steps.adds(1))
            dve.wait_ge(steps.sem, steps.now())
            nc.vector.tensor_tensor(out, out, zo, ALU.mult).then_inc(steps.sem, steps.adds(1))
            dve.wait_ge(steps.sem, steps.now())
            dve.wait_ge(rstd.sem, rstd.at(2))
            each = stat[:, 1, :].rearrange("p (t h) -> p t h", t=NT).unsqueeze(3).broadcast_to([P, NT, ML_H, ML_D])
            nc.vector.tensor_tensor(heads(out), heads(out), each, ALU.mult).then_inc(steps.sem, steps.adds(1))

        @block.tensor
        def _(pe):
            for k in range(4):
                for t in range(NT):
                    ins = nc.tensor.transpose(gates_ps[:, k * TOK + t * P:k * TOK + (t + 1) * P],
                                              z[:, t, ZG0 + 4 * k:ZG0 + 4 * k + 4], T.c("ident"))
            ins.then_inc(gates_turned.sem, gates_turned.adds(1))
            turns.tensor(pe, 0, 2)
            for n in early:
                mod.tensor(pe, n)
            pe.wait_ge(rows.sem, rows.at(1))
            for t in range(NT):
                for w, of in enumerate((lambda d: gates[:, 2 * d, :], lambda d: run[:, 1, d, :],
                                        lambda d: gates[:, 2 * d + 1, :])):
                    for d in range(2):
                        ins = nc.tensor.transpose(cols_ps[:, t, w, d * ML_H:(d + 1) * ML_H],
                                                  of(d)[:, t * P:(t + 1) * P], T.c("ident", 4)[:, 0:4])
            ins.then_inc(cols_turned.sem, cols_turned.adds(1))
            pe.wait_ge(cols_in.sem, cols_in.at(1))
            pe.wait_ge(loads.sem, loads.at(6 * 16))
            pe.wait_ge(v_in.sem, v_in.at(5))
            pe.wait_ge(mod.copied.sem, mod.copied.at(len(early)))
            for i in range(len(pairs) + 1):
                if i < len(pairs):
                    h, d = pairs[i]
                    if i >= 2:
                        pe.wait_ge(log_d.sem, log_d.at(i - 1))
                        pe.wait_ge(prob_in.sem, prob_in.at(i - 1))
                    ins = nc.tensor.matmul(T.ps[:, 4 + i % 2, 0:TOK], T.c("sel", 4)[:, h * P:(h + 1) * P],
                                           run[:, 1, d, :], start=True, stop=True)
                    if d:
                        s, t = tiles[4]
                        ins = nc.tensor.matmul(T.ps[:, 5, TOK:], tile(kT[:, h % 2, :], s), tile(qT[:, h % 2, :], t),
                                               start=True, stop=True)
                    ins.then_inc(spread_m.sem, spread_m.adds(1))
                    if d == 0:
                        turns.wait_copied(pe, 2 * h)
                        turns.wait_copied(pe, 2 * h + 1)
                        if i:
                            pe.wait_ge(prob_in.sem, prob_in.at(i))
                        for slot, (s, t) in enumerate(tiles[0:4]):
                            ins = nc.tensor.matmul(T.ps[:, 2, slot * P:(slot + 1) * P], tile(kT[:, h % 2, :], s),
                                                   tile(qT[:, h % 2, :], t), start=True, stop=True)
                        ins.then_inc(score.sem, score.adds(1))
                    mod.tensor(pe, late[i // 2], range(i % 2 * KC // 2, (i % 2 + 1) * KC // 2))
                if i >= 1:
                    w = i - 1
                    h, d = pairs[w]
                    if w >= 1:
                        pe.wait_ge(combined.sem, combined.at(w))
                        pe.wait_ge(num_out.sem, num_out.at(w))
                        pe.wait_ge(c_out.sem, c_out.at(w))
                    for t in (1, 2):
                        nc.tensor.matmul(T.ps[:, 7, (t - 1) * W:t * W], tile(qT[:, h % 2, :], t), c0[:, d * ML_H + h, :],
                                         start=True, stop=True)
                    pe.wait_ge(kw_in.sem, kw_in.at(w + 1))
                    nc.tensor.matmul(c_ps, kw[:, w % 2, :], v1[:, 0, h, :], start=True, stop=True)
                    for t in range(NT):
                        own_slots = [slot for slot in (0, 1, 2, 3) if (tiles[0:3] + [tiles[3 + d]])[slot][1] == t]
                        for n, slot in enumerate(own_slots):
                            s = (tiles[0:3] + [tiles[3 + d]])[slot][0]
                            ins = nc.tensor.matmul(T.ps[:, 6, t * W:(t + 1) * W], tile(prob[:, w % 2, :], slot),
                                                   v1[:, s, h, :], start=(n == 0), stop=(n == len(own_slots) - 1))
                    ins.then_inc(num.sem, num.adds(1))
                if i % 2 == 1 and i + 1 < len(pairs):
                    turns.tensor(pe, i + 1, i + 3)
    T.end_stage()



def stage_mla_heads(T, z, mix, qT, kT, v):
    nc, I, O = T.nc, T.I, T.O
    QW, KVW = HEADS * MLA_QK, HEADS * 2 * HD
    with ExitStack() as ctx:
        sb = lambda name, shape: T.sb(ctx, "mla_" + name, shape)
        k = sb("k", [P, 4, QW])
        stat = sb("stat", [P, 2, 6])
        stat_q, stat_k = sb("stat_q", [P, 2, NT * HEADS]), sb("stat_k", [P, 2, 4 * HEADS])
        q = mix[:, :, 0:QW]
        q_heads = q.rearrange("p t (h d) -> p t h d", h=HEADS)
        k_heads = k[:, :, :].rearrange("p t (h d) -> p t h d", h=HEADS)
        q_room, k_room = qT.rearrange("p h t -> p (h t)"), kT.rearrange("p h t -> p (h t)")
        w_q = k_room[:, 0:2 * QW].rearrange("p (c n) -> p c n", c=2)
        qaT = k_room[:, 2 * QW:2 * QW + 2 * TOK].rearrange("p (c t) -> p c t", c=2)
        ckvT = k_room[:, 2 * QW + 2 * TOK:2 * QW + 2 * TOK + 4 * P]
        w_kv = k_room[:, 4 * QW:4 * QW + KVW]
        g_qa, g_kv, ckv_c = mix[:, 0, QW:D], mix[:, 1, QW:QW + P], mix[:, 1, QW + P:D]
        g_heads = mix[:, 2, QW:QW + 2 * MLA_QK].rearrange("p (a d) -> p a d", a=2)
        kpe_c = mix[:, 2, QW + 2 * MLA_QK:QW + 2 * MLA_QK + MLA_ROPE]
        low = z[:, :, 0:384]
        loads, steps, pool_steps = T.counter("loads_act"), T.counter("dve_done"), T.counter("pool_done")
        squares, sums, rstd, normed = T.counter("squares"), T.counter("sums"), T.counter("rstd"), T.counter("normed")
        straight, ready, product = T.counter("straight"), T.counter("rows"), T.counter("product")
        out = (T.counter("z_act"), T.counter("z_dve"))
        stored = T.counter("stored_act")
        groups = [([z[:, t, c:256:2] for t in range(NT)], qaT[:, c, :],
                   (normed, 1) if c == 0 else None) for c in range(2)]
        groups.append(([z[:, 0, ZKV0:ZKV0 + P], ckv_c, z[:, 1, ZKV0:ZKV0 + P], z[:, 2, ZKV0:ZKV0 + P]],
                       ckvT, (loads, 9 * 16)))
        for h in range(HEADS):
            groups.append(([q[:, t, h * MLA_QK:(h + 1) * MLA_QK] for t in range(NT)], qT[0:MLA_QK, h, :],
                           (ready, 1) if h == 0 else None))
        for h in range(HEADS):
            groups.append(([k[:, t, h * MLA_QK:(h + 1) * MLA_QK] for t in range(4)], kT[0:MLA_QK, h, :],
                           (ready, 2) if h == 0 else None))
        turns = Turns(T, groups)
        jobs = [("q", t, half) for t in range(NT) for half in range(2)]
        jobs += [("kv", t, half) for t in range(4) for half in range(2)]
        block = ctx.enter_context(nc.Block())

        def products_out(engine, copy, parity):
            for e, (what, t, half) in enumerate(jobs):
                if e % 2 != parity:
                    continue
                engine.wait_ge(product.sem, product.at(e + 1))
                bank = T.ps[:, 4 + e % 4, :]
                if what == "q":
                    copy(q[:, t, half * 384:(half + 1) * 384], bank[:, 0:384]).then_inc(out[parity].sem, out[parity].adds(1))
                else:
                    both = bank.rearrange("p (h n) -> p h n", h=4)
                    heads = slice(4 * half, 4 * half + 4)
                    copy(k_heads[:, t, heads, 0:HD], both[:, :, 0:HD]).then_inc(T.counter("aside").sem, 1)
                    T.counter("aside").made += 1
                    copy(v[:, t, half * 256:(half + 1) * 256].rearrange("p (h n) -> p h n", h=4),
                                        both[:, :, HD:2 * HD]).then_inc(out[parity].sem, out[parity].adds(1))

        @block.scalar
        def _(act):
            for dst, src in ((g_qa, spread(I["mla_q_a_g"][0])), (g_kv, spread(I["mla_kv_a_g"][0])),
                             (ckv_c, I["cache_mla_ckv"][0, 0]), (kpe_c, I["cache_mla_kpe"][0, 0]),
                             (w_q[:, :, :], I["mla_w_q_up"][0].rearrange("(p c) n -> p c n", c=2)),
                             (w_kv, I["mla_w_kv_up"][0]),
                             (g_heads[:, 0, :], spread(I["mla_q_g"][0])), (g_heads[:, 1, :], spread(I["mla_k_g"][0])),
                             (O["mla_kpe"][0, 0], z[:, 0, ZPE0:ZPE0 + MLA_ROPE])):
                act.dma_start(dst, src).then_inc(loads.sem, loads.adds(16))
            act.activation(q_room[:, 0:NT * 384].rearrange("p (t n) -> p t n", t=NT), low, ACT.Square).then_inc(squares.sem, squares.adds(1))
            turns.copy_out(act, nc.scalar.copy, 0, 0, 3)
            products_out(act, nc.scalar.copy, 0)
            for parity in range(2):
                act.wait_ge(out[parity].sem, out[parity].at(3))
            act.wait_ge(sums.sem, sums.at(2))
            act.activation(q_room[:, 0:NT * QW].rearrange("p (t n) -> p t n", t=NT), q, ACT.Square).then_inc(squares.sem, squares.adds(1))
            for parity in range(2):
                act.wait_ge(out[parity].sem, out[parity].at(7))
            act.wait_ge(pool_steps.sem, pool_steps.at(4))
            act.activation(k_room[:, 0:4 * QW].rearrange("p (t n) -> p t n", t=4), k[:, :, :], ACT.Square).then_inc(squares.sem, squares.adds(1))
            turns.copy_out(act, nc.scalar.copy, 0, 3)
            act.dma_start(O["mla_ckv"][0, 0], z[:, 0, ZKV0:ZKV0 + P]).then_inc(stored.sem, stored.adds(16))
            act.wait_ge(stored.sem, stored.at(16))

        def rotate(pool, n, heads, room):
            pool.wait_ge(normed.sem, normed.at(n))
            for t in range(2):
                cos = T.c("cos32")[:, t * 32:(t + 1) * 32].unsqueeze(1).broadcast_to([P, HEADS, 32])
                nc.gpsimd.tensor_tensor(room[:, t].rearrange("p (h d) -> p h d", h=HEADS),
                                                    heads[:, t, :, MLA_NOPE:], cos, ALU.mult).then_inc(straight.sem, straight.adds(1))

        def power(pool, s, ready_at, scales):
            pool.wait_ge(sums.sem, sums.at(ready_at))
            for cols, n in scales:
                nc.gpsimd.tensor_scalar(s[:, 0, cols], s[:, 0, cols], 1.0 / n, EPS, ALU.mult, ALU.add).then_inc(rstd.sem, rstd.adds(1))
                pool.wait_ge(rstd.sem, rstd.now())
            width = s.shape[2]
            nc.gpsimd.tensor_tensor(s[:, 1, :], s[:, 0, :], T.c("half")[:, 0:width], ALU.pow).then_inc(rstd.sem, rstd.adds(1))

        @block.gpsimd
        def _(pool):
            power(pool, stat, 2, ((slice(0, 3), 256), (slice(3, 6), P)))
            pool.wait_ge(loads.sem, loads.at(9 * 16))
            for t, pe_row in enumerate((z[:, 0, ZPE0:ZPE0 + MLA_ROPE], kpe_c, z[:, 1, ZPE0:ZPE0 + MLA_ROPE],
                                        z[:, 2, ZPE0:ZPE0 + MLA_ROPE])):
                nc.gpsimd.tensor_copy(k_heads[:, t, :, MLA_NOPE:],
                                                    pe_row.unsqueeze(1).broadcast_to([P, HEADS, MLA_ROPE])).then_inc(pool_steps.sem, pool_steps.adds(1))
            power(pool, stat_q, 3, ((slice(0, NT * HEADS), MLA_QK),))
            rotate(pool, 2, q_heads[:, 1:3], z[:, 0:2, 0:256])
            power(pool, stat_k, 4, ((slice(0, 4 * HEADS), MLA_QK),))
            rotate(pool, 3, k_heads[:, 2:4], k_room[:, 0:512].rearrange("p (t n) -> p t n", t=2))

        @block.vector
        def _(dve):
            dve.wait_ge(squares.sem, squares.at(1))
            sq = q_room[:, 0:NT * 384].rearrange("p (t n) -> p t n", t=NT)
            nc.vector.reduce_sum(stat[:, 0, 0:3], sq[:, :, 0:256], AX).then_inc(sums.sem, sums.adds(1))
            nc.vector.reduce_sum(stat[:, 0, 3:6], sq[:, :, 256:384], AX).then_inc(sums.sem, sums.adds(1))
            dve.wait_ge(loads.sem, loads.at(9 * 16))
            dve.wait_ge(rstd.sem, rstd.at(3))
            for t in range(NT):
                for at, n, g, col in ((0, 256, g_qa, t), (256, P, g_kv, 3 + t)):
                    x = z[:, t, at:at + n]
                    nc.vector.scalar_tensor_tensor(out=x, in0=x, scalar=stat[:, 1, col:col + 1], in1=g[:, :],
                                                            op0=ALU.mult, op1=ALU.mult).then_inc(steps.sem, steps.adds(1))
            dve.wait_ge(steps.sem, steps.at(steps.made))
            nc.vector.tensor_copy(stat[:, 0, 0:1], stat[:, 1, 0:1]).then_inc(normed.sem, normed.adds(1))
            turns.copy_out(dve, nc.vector.tensor_copy, 1, 0, 3)
            products_out(dve, nc.vector.tensor_copy, 1)
            for n, (x, tiles, s, room, g, last) in enumerate((
                    (q_heads, NT, stat_q, q_room, 0, 3), (k_heads, 4, stat_k, k_room, 1, 5))):
                dve.wait_ge(squares.sem, squares.at(2 + n))
                nc.vector.reduce_sum(s[:, 0, :].rearrange("p (t h) -> p t h", t=tiles),
                                             room[:, 0:tiles * QW].rearrange("p (t h d) -> p t h d", t=tiles, h=HEADS), AX).then_inc(sums.sem, sums.adds(1))
                dve.wait_ge(rstd.sem, rstd.at(5 + 2 * n))
                each = s[:, 1, :].rearrange("p (t h) -> p t h", t=tiles).unsqueeze(3).broadcast_to([P, tiles, HEADS, MLA_QK])
                nc.vector.tensor_tensor(x, x, each, ALU.mult).then_inc(steps.sem, steps.adds(1))
                dve.wait_ge(steps.sem, steps.now())
                gain = g_heads[:, g, :].unsqueeze(1).unsqueeze(1).broadcast_to([P, tiles, HEADS, MLA_QK])
                nc.vector.tensor_tensor(x, x, gain, ALU.mult).then_inc(normed.sem, normed.adds(1))
                dve.wait_ge(normed.sem, normed.now())
                turned = x[:, tiles - 2:tiles, :, MLA_NOPE:]
                plain = z[:, 0:2, 0:256] if n == 0 else room[:, 0:512].rearrange("p (t n) -> p t n", t=2)
                spare = room[:, 1024:1536].rearrange("p (t n) -> p t n", t=2)
                rope(T, dve, turned, spare, plain, (straight, 2 * (n + 1)), HEADS, MLA_ROPE, ready)
            turns.copy_out(dve, nc.vector.tensor_copy, 1, 3)

        @block.tensor
        def _(pe):
            turns.tensor(pe, 0, 3)
            for g in range(3):
                turns.wait_copied(pe, g)
            for e, (what, t, half) in enumerate(jobs):
                if e >= 4:
                    pe.wait_ge(out[e % 2].sem, out[e % 2].at((e - 4) // 2 + 1))
                bank = T.ps[:, 4 + e % 4, :]
                if what == "q":
                    for c in range(2):
                        ins = nc.tensor.matmul(bank[:, 0:384], qaT[:, c, t * P:(t + 1) * P],
                                               w_q[:, c, half * 384:(half + 1) * 384], start=(c == 0), stop=(c == 1))
                else:
                    ins = nc.tensor.matmul(bank, ckvT[:, t * P:(t + 1) * P], w_kv[:, half * 512:(half + 1) * 512],
                                           start=True, stop=True)
                ins.then_inc(product.sem, product.adds(1))
            turns.tensor(pe, 3)
    T.end_stage()


def stage_mla_attention(T, mix, qT, kT, v):
    nc = T.nc
    with ExitStack() as ctx:
        groups = []
        for t in range(NT):
            units = []
            for h in range(HEADS):
                k = key_order(kT[0:MLA_QK, h, :])[min(t, 1)]
                tiles = (0,) if t == 0 else (1, 2, 3)
                values = [v[:, s, h * HD:(h + 1) * HD] for s in tiles]
                units.append((qT[0:MLA_QK, h, t * P:(t + 1) * P], k, values, None, MLA_QK ** -0.5))
            groups.append((units, mix[:, t, 0:512].rearrange("p (h d) -> p h d", d=HD), None))
        att = Attention(T, ctx, "mla", groups)
        block = ctx.enter_context(nc.Block())

        @block.scalar
        def _(act):
            att.scalar(act)

        @block.vector
        def _(dve):
            att.vector(dve)

        @block.tensor
        def _(pe):
            att.tensor(pe)
    T.end_stage()


def stage_neighbourhood(T, z, mix):
    nc, I, O = T.nc, T.I, T.O
    ROWS, RPB_COLS = LAT // GRID_W, 31
    with ExitStack() as ctx:
        sb = lambda name, shape: T.sb(ctx, "nat_" + name, shape)
        qT, kT = sb("qT", [P, 4, TOK]), sb("kT", [P, 4, 4 * P])
        kc, vc = sb("kc", [P, 512]), sb("vc", [P, 512])
        bias = sb("bias", [P, 2, HEADS, 384])
        gains = sb("gains", [P, 2, HD])
        stat = sb("stat", [P, 2, 2, NT * HEADS])
        loads, tables, steps = T.counter("loads_act"), T.counter("loads_pool"), T.counter("dve_done")
        squares, sums, rstd, ready = T.counter("squares"), T.counter("sums"), T.counter("rstd"), T.counter("rows")
        zeroed, stored = T.counter("pool_done"), T.counter("stored_act")
        flipped, biased = T.counter("nat_flipped"), T.counter("nat_biased")
        room = mix[:, :, 512:1024], kT[:, 0:3, :]
        parts = [z[:, :, at:at + 512] for at in (NQ0, NK0)]
        heads = lambda a: a.rearrange("p t (h d) -> p t h d", h=HEADS)
        groups = [([z[:, t, NQ0 + j * P:NQ0 + (j + 1) * P] for t in range(NT)], qT[:, j, :],
                   (ready, 2) if j == 0 else None) for j in range(4)]
        for j in range(4):
            at = slice(NK0 + j * P, NK0 + (j + 1) * P)
            groups.append(([z[:, 0, at], kc[:, j * P:(j + 1) * P], z[:, 1, at], z[:, 2, at]], kT[:, j, :],
                           (loads, 4 * 16) if j == 0 else None))
        turns = Turns(T, groups)
        att_groups = []
        for t in range(NT):
            units = []
            for h in range(HEADS):
                rows = slice((h % 2) * HD, (h % 2) * HD + HD)
                k = key_order(kT[rows, h // 2, :])[min(t, 1)]
                own = [z[:, s, NV0 + h * HD:NV0 + (h + 1) * HD] for s in range(NT)]
                values = own[0:1] if t == 0 else [vc[:, h * HD:(h + 1) * HD]] + own[1:]
                mask = None if t == 0 else bias[:, t - 1, h, :]
                units.append((qT[rows, h // 2, t * P:(t + 1) * P], k, values, mask, HD ** -0.5))
            att_groups.append((units, mix[:, t, 512:1024].rearrange("p (h d) -> p h d", d=HD), None))
        att = Attention(T, ctx, "nat", att_groups)
        block = ctx.enter_context(nc.Block())

        @block.scalar
        def _(act):
            for dst, src in ((gains[:, 0, :], spread(I["nat_q_g"][0])), (gains[:, 1, :], spread(I["nat_k_g"][0])),
                             (kc[:, :], I["cache_nat_k"][0, 0].rearrange("s h d -> s (h d)")),
                             (vc[:, :], I["cache_nat_v"][0, 0].rearrange("s h d -> s (h d)"))):
                act.dma_start(dst, src).then_inc(loads.sem, loads.adds(16))
            for n in range(2):
                act.activation(room[n], parts[n], ACT.Square).then_inc(squares.sem, squares.adds(1))
            turns.copy_out(act, nc.scalar.copy, 0)
            att.scalar(act)
            act.dma_start(O["nat_k"][0, 0].rearrange("s h d -> s (h d)"), z[:, 0, NK0:NK0 + 512]).then_inc(stored.sem, stored.adds(16))
            act.dma_start(O["nat_v"][0, 0].rearrange("s h d -> s (h d)"), z[:, 0, NV0:NV0 + 512]).then_inc(stored.sem, stored.adds(16))
            act.wait_ge(stored.sem, stored.at(32))

        @block.sync
        def _(sp):
            rpb = I["nat_rpb"]
            for h in range(HEADS):
                for r in range(ROWS):
                    first = (h * 15 + 7 - r) * RPB_COLS + 15 - (GRID_W - 1)
                    src = bass.AP(tensor=rpb.tensor, offset=rpb.offset + first,
                                  ap=[[1, GRID_W], [RPB_COLS, ROWS], [1, GRID_W]])
                    part = slice((r % 2) * GRID_W, (r % 2 + 1) * GRID_W)
                    dst = bias[part, r // 2, h, P:].rearrange("p (k c) -> p k c", k=ROWS)
                    sp.dma_start(dst, src).then_inc(tables.sem, tables.adds(16))

        @block.gpsimd
        def _(pool):
            nc.gpsimd.memset(bias[:, :, :, 0:P], 0.0).then_inc(zeroed.sem, zeroed.adds(1))
            pool.wait_ge(sums.sem, sums.at(2))
            flat = stat[:, :, :, :].rearrange("p a b n -> p a (b n)")
            nc.gpsimd.tensor_scalar(flat[:, 0, :], flat[:, 0, :], 1.0 / HD, EPS, ALU.mult, ALU.add).then_inc(rstd.sem, rstd.adds(1))
            pool.wait_ge(rstd.sem, rstd.now())
            nc.gpsimd.tensor_tensor(flat[:, 1, :], flat[:, 0, :], T.c("half")[:, 0:2 * NT * HEADS], ALU.pow).then_inc(rstd.sem, rstd.adds(1))

        @block.vector
        def _(dve):
            for n in range(2):
                dve.wait_ge(squares.sem, squares.at(n + 1))
                nc.vector.reduce_sum(stat[:, 0, n, :].rearrange("p (t h) -> p t h", t=NT), heads(room[n]), AX).then_inc(sums.sem, sums.adds(1))
            dve.wait_ge(rstd.sem, rstd.at(2))
            dve.wait_ge(loads.sem, loads.at(4 * 16))
            for n in range(2):
                x = heads(parts[n])
                each = stat[:, 1, n, :].rearrange("p (t h) -> p t h", t=NT).unsqueeze(3).broadcast_to([P, NT, HEADS, HD])
                nc.vector.tensor_tensor(x, x, each, ALU.mult).then_inc(steps.sem, steps.adds(1))
                dve.wait_ge(steps.sem, steps.now())
                gain = gains[:, n, :].unsqueeze(1).unsqueeze(1).broadcast_to([P, NT, HEADS, HD])
                nc.vector.tensor_tensor(x, x, gain, ALU.mult).then_inc(ready.sem, ready.adds(1))
            for n in range(2 * HEADS // 2):
                t, h = divmod(2 * n, HEADS)
                dve.wait_ge(flipped.sem, flipped.at(n + 1))
                mask = T.c("nat")[:, t * LAT:(t + 1) * LAT].unsqueeze(1).broadcast_to([P, 2, LAT])
                nc.vector.scalar_tensor_tensor(
                    out=bias[:, t, h:h + 2, P:], in0=T.ps[:, 6 + n % 2, :].rearrange("p (h k) -> p h k", h=2),
                    scalar=HD ** 0.5, in1=mask, op0=ALU.mult, op1=ALU.add).then_inc(biased.sem, biased.adds(1))
            dve.wait_ge(biased.sem, biased.at(HEADS))
            dve.wait_ge(zeroed.sem, zeroed.at(1))
            turns.copy_out(dve, nc.vector.tensor_copy, 1)
            att.vector(dve)

        @block.tensor
        def _(pe):
            pe.wait_ge(tables.sem, tables.at(16 * HEADS * ROWS))
            for n in range(2 * HEADS // 2):
                t, h = divmod(2 * n, HEADS)
                if n >= 2:
                    pe.wait_ge(biased.sem, biased.at(n - 1))
                nc.tensor.matmul(T.ps[:, 6 + n % 2, :], T.c("flip"), bias[:, t, h:h + 2, P:],
                                            start=True, stop=True).then_inc(flipped.sem, flipped.adds(1))
            turns.tensor(pe)
            turns.wait_all(pe)
            att.tensor(pe)
    T.end_stage()


def stage_router(T, l, plan):
    nc, I = T.nc, T.I
    R = N_GRP + N_EXP
    with ExitStack() as ctx:
        sb = lambda name, shape: T.sb(ctx, f"r{l}_" + name, shape)
        scale, shift = sb("scale", [P, 2, D]), sb("shift", [P, 2, D])
        h, hT = sb("h", [P, NT, D]), sb("hT", [P, KC, TOK])
        w, bias = sb("w", [P, KC, R]), sb("bias", [P, R])
        stat = sb("stat", [P, 2, NT])
        logit = sb("logit", [P, NT, R])
        top, least = sb("top", [P, 3, NT]), sb("least", [P, 3, NT])
        cand, chosen_g = sb("cand", [P, NT, N_EXP]), sb("chosen_g", [P, NT, N_GRP])
        g_exp, p_top, ratio = sb("g_exp", [P, NT, N_GRP]), sb("p_top", [P, NT]), sb("ratio", [P, 2, NT])
        left = sb("left", [P, NT, N_EXP])
        chosen, both = sb("chosen", [P, 2, NT, N_EXP]), sb("both", [P, NT, N_EXP])
        rank = sb("rank", [P, NT + 1, N_EXP])
        above = sb("above", [P, N_EXP * (MAX_BLK - 1)])
        extra, upto, start = sb("extra", [P, N_EXP]), sb("upto", [P, N_EXP]), sb("start", [P, N_EXP])
        picked = sb("picked", [P, NT, N_EXP])
        r, base, q, row, blk, tmp = (sb(n, [P, 2 * NT]) for n in ("rk", "base", "q", "row", "blk", "tmp"))
        row_hot, blk_hot = sb("row_hot", [P, 2 * NT, BLK]), sb("blk_hot", [P, 2 * NT, N_BLK])
        marks = sb("marks", [P, 2 * NT, 2, N_BLK])
        table = sb("table", [BLK, 2 * N_BLK])
        before, over = sb("before", [1, OVER, N_EXP]), sb("over", [1, OVER + 1])
        columns = sb("columns", [P, 2, 2, KC])
        rows_in = T.counter("rows_in")
        loads, squares, rstd, rows = T.counter("loads_act"), T.counter("squares"), T.counter("rstd"), T.counter("rows")
        steps, stored, product = T.counter("dve_done"), T.counter("stored_act"), T.counter("product")
        blank = T.counter("blank")
        shifted, exps, marked = T.counter("r_shifted"), T.counter("r_exps"), T.counter("r_marked")
        groups = [([h[:, t, c::KC] for c in range(4 * k, 4 * k + 4)], hT[:, 4 * k:4 * k + 4, t * P:(t + 1) * P],
                   (rows, t + 1) if k == 0 else None) for t in range(NT) for k in range(2)]
        turns = Turns(T, groups)
        modulated = Modulated(T, columns)
        modulated_rows = T.counter("modulated_rows")
        block = ctx.enter_context(nc.Block())

        @block.scalar
        def _(act):
            with nc.allow_non_contiguous_dma(reason="the router's narrow weights"):
                by_feature = T.mod_dram[l, :, 3 * D:5 * D].rearrange("g (k p c) -> g p k c", k=2, c=KC)
                for dst, src in ((columns[:, :, 0, :], by_feature[0]), (columns[:, :, 1, :], by_feature[1]),
                                 (w[:, :, 0:N_GRP], I["moe_w_group"][l].rearrange("(p c) n -> p c n", c=KC)),
                                 (w[:, :, N_GRP:], I["moe_w_expert"][l].rearrange("(p c) n -> p c n", c=KC)),
                                 (bias[:, 0:N_GRP], spread(I["moe_b_group"][l])),
                                 (bias[:, N_GRP:], spread(I["moe_b_expert"][l]))):
                    act.dma_start(dst, src).then_inc(loads.sem, loads.adds(16))
                for dst, src in ((scale[:, :, :], spread(T.mod_dram[l, :, 4 * D:5 * D])),
                                 (shift[:, :, :], spread(T.mod_dram[l, :, 3 * D:4 * D]))):
                    act.dma_start(dst, src).then_inc(rows_in.sem, rows_in.adds(16))
            for t in range(NT):
                if t >= 1:
                    act.wait_ge(squares.sem, squares.at(t))
                act.activation(hT[:, 0:KC, 0:P], T.x[:, t, :].rearrange("p (c n) -> p c n", c=KC),
                                          ACT.Square, accum_out=stat[:, 0, t:t + 1]).then_inc(squares.sem, squares.adds(1))
            act.wait_ge(squares.sem, squares.at(NT))
            act.wait_ge(loads.sem, loads.at(6 * 16))
            modulated.copy_out(act, turns, hT, modulated.scalar, 0)
            act.wait_ge(shifted.sem, shifted.at(1))
            act.activation(g_exp[:, :, :], g_exp[:, :, :], ACT.Exp).then_inc(exps.sem, exps.adds(1))
            act.wait_ge(shifted.sem, shifted.at(2))
            act.activation(ratio[:, 0, :], ratio[:, 0, :], ACT.Exp).then_inc(exps.sem, exps.adds(1))
            act.wait_ge(modulated_rows.sem, modulated_rows.at(2 * NT))
            act.dma_start(T.h_dram.rearrange("(t p) d -> p t d", p=P), h[:, :, :]).then_inc(stored.sem, stored.adds(16))
            act.wait_ge(stored.sem, stored.at(16))

        @block.gpsimd
        def _(pool):
            nc.gpsimd.memset(plan.x_in[:, :, :], 0.0).then_inc(blank.sem, blank.adds(1))
            for t in range(NT):
                one = slice(t, t + 1)
                pool.wait_ge(squares.sem, squares.at(t + 1))
                nc.gpsimd.tensor_scalar(stat[:, 0, one], stat[:, 0, one], 1.0 / D, EPS, ALU.mult, ALU.add).then_inc(
                    rstd.sem, rstd.adds(1))
                pool.wait_ge(rstd.sem, rstd.now())
                nc.gpsimd.tensor_tensor(stat[:, 1, one], stat[:, 0, one], T.c("half")[:, 0:1], ALU.pow).then_inc(
                    rstd.sem, rstd.adds(1))
            pool.wait_ge(rows_in.sem, rows_in.at(32))
            for t in range(NT):
                g = min(t, 1)
                pool.wait_ge(turns.done.sem, turns.done.at(2 * t + 2))
                nc.gpsimd.tensor_tensor(h[:, t, :], h[:, t, :], scale[:, g, :], ALU.mult).then_inc(
                    modulated_rows.sem, modulated_rows.adds(1))
                pool.wait_ge(modulated_rows.sem, modulated_rows.now())
                nc.gpsimd.tensor_tensor(h[:, t, :], h[:, t, :], shift[:, g, :], ALU.add).then_inc(
                    modulated_rows.sem, modulated_rows.adds(1))

        @block.vector
        def _(dve):
            v = nc.vector

            def wide(a, n):
                return a.unsqueeze(len(a.shape)).broadcast_to(list(a.shape) + [n])

            for t in range(NT):
                dve.wait_ge(rstd.sem, rstd.at(2 * t + 2))
                v.tensor_scalar(h[:, t, :], T.x[:, t, :], stat[:, 1, t:t + 1], None, ALU.mult).then_inc(rows.sem, rows.adds(1))
                if t == 0:
                    dve.wait_ge(loads.sem, loads.at(6 * 16))
                    dve.wait_ge(squares.sem, squares.at(NT))
                else:
                    modulated.copy_out(dve, turns, hT, modulated.vector, 1, 2 * (t - 1), 2 * t)
            modulated.copy_out(dve, turns, hT, modulated.vector, 1, 2 * NT - 2)
            dve.wait_ge(product.sem, product.at(1))
            v.tensor_tensor(logit[:, :, :], T.ps[:, 4, 0:NT * R].rearrange("p (t n) -> p t n", t=NT),
                               bias[:, :].unsqueeze(1).broadcast_to([P, NT, R]), ALU.add).then_inc(steps.sem, steps.adds(1))
            dve.wait_ge(steps.sem, steps.now())

            def first_largest(x, n, k, out):
                c = cand[:, :, 0:n]
                v.reduce_max(top[:, k, :], x, AX).then_inc(steps.sem, steps.adds(1))
                dve.wait_ge(steps.sem, steps.now())
                v.tensor_tensor(c, x, wide(top[:, k, :], n), ALU.is_equal).then_inc(steps.sem, steps.adds(1))
                dve.wait_ge(steps.sem, steps.now())
                v.scalar_tensor_tensor(out=c, in0=c, scalar=-64.0,
                                          in1=T.c("iota")[:, 0:n].unsqueeze(1).broadcast_to([P, NT, n]),
                                          op0=ALU.mult, op1=ALU.add).then_inc(steps.sem, steps.adds(1))
                dve.wait_ge(steps.sem, steps.now())
                v.tensor_reduce(least[:, k, :], c, AX, ALU.min).then_inc(steps.sem, steps.adds(1))
                dve.wait_ge(steps.sem, steps.now())
                v.tensor_tensor(out, c, wide(least[:, k, :], n), ALU.is_equal).then_inc(steps.sem, steps.adds(1))
                dve.wait_ge(steps.sem, steps.now())

            group, expert = logit[:, :, 0:N_GRP], logit[:, :, N_GRP:]
            first_largest(group, N_GRP, 0, chosen_g[:, :, :])
            v.tensor_tensor(g_exp[:, :, :], group, wide(top[:, 0, :], N_GRP), ALU.subtract).then_inc(shifted.sem, shifted.adds(1))
            dve.wait_ge(shifted.sem, shifted.now())
            v.tensor_scalar(chosen_g[:, :, :], chosen_g[:, :, :], -1.0, BIG, ALU.add, ALU.mult).then_inc(steps.sem, steps.adds(1))
            dve.wait_ge(steps.sem, steps.now())
            by_group = lambda a: a.rearrange("p t (g e) -> p t g e", g=N_GRP)
            v.tensor_tensor(by_group(left[:, :, :]), by_group(expert), wide(chosen_g[:, :, :], PER_GRP), ALU.add).then_inc(steps.sem, steps.adds(1))
            dve.wait_ge(steps.sem, steps.now())
            first_largest(left[:, :, :], N_EXP, 1, chosen[:, 0])
            v.scalar_tensor_tensor(out=left[:, :, :], in0=chosen[:, 0], scalar=-3.0 * BIG, in1=left[:, :, :],
                                      op0=ALU.mult, op1=ALU.add).then_inc(steps.sem, steps.adds(1))
            dve.wait_ge(steps.sem, steps.now())
            first_largest(left[:, :, :], N_EXP, 2, chosen[:, 1])
            v.tensor_tensor(ratio[:, 0, :], top[:, 2, :], top[:, 1, :], ALU.subtract).then_inc(shifted.sem, shifted.adds(1))
            dve.wait_ge(shifted.sem, shifted.now())
            v.tensor_tensor(both[:, :, :], chosen[:, 0], chosen[:, 1], ALU.add).then_inc(marked.sem, marked.adds(1))
            dve.wait_ge(marked.sem, marked.now())
            dve.wait_ge(exps.sem, exps.at(2))
            v.reduce_sum(p_top[:, :], g_exp[:, :, :], AX).then_inc(steps.sem, steps.adds(1))
            dve.wait_ge(steps.sem, steps.now())
            v.tensor_scalar(ratio[:, 1, :], ratio[:, 0, :], 1.0, None, ALU.add).then_inc(steps.sem, steps.adds(1))
            dve.wait_ge(steps.sem, steps.now())
            v.tensor_tensor(p_top[:, :], p_top[:, :], ratio[:, 1, :], ALU.mult).then_inc(steps.sem, steps.adds(1))
            dve.wait_ge(steps.sem, steps.now())
            v.reciprocal(plan.weight[:, 0, :], p_top[:, :]).then_inc(steps.sem, steps.adds(1))
            dve.wait_ge(steps.sem, steps.now())
            v.tensor_tensor(plan.weight[:, 1, :], plan.weight[:, 0, :], ratio[:, 0, :], ALU.mult).then_inc(steps.sem, steps.adds(1))
            dve.wait_ge(steps.sem, steps.now())
            dve.wait_ge(product.sem, product.at(2))
            v.tensor_copy(rank[:, :, :], T.ps[:, 5, 0:(NT + 1) * N_EXP].rearrange("p (t n) -> p t n", n=N_EXP)).then_inc(steps.sem, steps.adds(1))
            dve.wait_ge(steps.sem, steps.now())
            count = rank[:, NT, :]
            n_thr = MAX_BLK - 1
            by_expert = above[:, :].rearrange("p (e m) -> p e m", m=n_thr)
            v.tensor_tensor(by_expert, wide(count, n_thr), T.c("thr").rearrange("p (e m) -> p e m", m=n_thr), ALU.is_gt).then_inc(steps.sem, steps.adds(1))
            dve.wait_ge(steps.sem, steps.now())
            v.reduce_sum(extra[:, :], by_expert, AX).then_inc(steps.sem, steps.adds(1))
            dve.wait_ge(steps.sem, steps.now())
            v.tensor_tensor_scan(upto[:, :], T.c("ones")[:, 0:N_EXP], extra[:, :], 0.0, ALU.mult, ALU.add).then_inc(steps.sem, steps.adds(1))
            dve.wait_ge(steps.sem, steps.now())
            v.tensor_tensor(start[:, :], upto[:, :], extra[:, :], ALU.subtract).then_inc(steps.sem, steps.adds(1))
            dve.wait_ge(steps.sem, steps.now())
            for k in range(2):
                part = slice(k * NT, (k + 1) * NT)
                v.tensor_tensor(picked[:, :, :], chosen[:, k], rank[:, 0:NT, :], ALU.mult).then_inc(steps.sem, steps.adds(1))
                dve.wait_ge(steps.sem, steps.now())
                v.reduce_sum(r[:, part], picked[:, :, :], AX).then_inc(steps.sem, steps.adds(1))
                dve.wait_ge(steps.sem, steps.now())
                v.tensor_tensor(picked[:, :, :], chosen[:, k], start[:, :].unsqueeze(1).broadcast_to([P, NT, N_EXP]),
                                   ALU.mult).then_inc(steps.sem, steps.adds(1))
                dve.wait_ge(steps.sem, steps.now())
                v.reduce_sum(base[:, part], picked[:, :, :], AX).then_inc(steps.sem, steps.adds(1))
                dve.wait_ge(steps.sem, steps.now())
            quot = above[:, 0:2 * NT * n_thr].rearrange("p (n m) -> p n m", m=n_thr)
            v.tensor_tensor(quot, wide(r[:, :], n_thr), T.c("thr")[:, 0:n_thr].unsqueeze(1).broadcast_to([P, 2 * NT, n_thr]),
                               ALU.is_ge).then_inc(steps.sem, steps.adds(1))
            dve.wait_ge(steps.sem, steps.now())
            v.reduce_sum(q[:, :], quot, AX).then_inc(steps.sem, steps.adds(1))
            dve.wait_ge(steps.sem, steps.now())
            v.scalar_tensor_tensor(out=row[:, :], in0=q[:, :], scalar=-float(BLK), in1=r[:, :], op0=ALU.mult, op1=ALU.add).then_inc(steps.sem, steps.adds(1))
            dve.wait_ge(steps.sem, steps.now())
            e = least[:, 1:3, :].rearrange("p k t -> p (k t)")
            v.tensor_scalar(e, e, 64.0, None, ALU.add).then_inc(steps.sem, steps.adds(1))
            dve.wait_ge(steps.sem, steps.now())
            v.tensor_tensor(base[:, :], base[:, :], q[:, :], ALU.add).then_inc(steps.sem, steps.adds(1))
            dve.wait_ge(steps.sem, steps.now())
            v.scalar_tensor_tensor(out=tmp[:, :], in0=base[:, :], scalar=N_EXP - 1.0, in1=e, op0=ALU.add, op1=ALU.subtract).then_inc(steps.sem, steps.adds(1))
            dve.wait_ge(steps.sem, steps.now())
            v.tensor_scalar(q[:, :], q[:, :], 1.0, None, ALU.min).then_inc(steps.sem, steps.adds(1))
            dve.wait_ge(steps.sem, steps.now())
            v.tensor_tensor(tmp[:, :], tmp[:, :], q[:, :], ALU.mult).then_inc(steps.sem, steps.adds(1))
            dve.wait_ge(steps.sem, steps.now())
            v.tensor_tensor(blk[:, :], tmp[:, :], e, ALU.add).then_inc(steps.sem, steps.adds(1))
            dve.wait_ge(steps.sem, steps.now())
            iota = T.c("iota")
            v.tensor_tensor(row_hot[:, :, :], iota.unsqueeze(1).broadcast_to([P, 2 * NT, BLK]), wide(row[:, :], BLK),
                               ALU.is_equal).then_inc(steps.sem, steps.adds(1))
            dve.wait_ge(steps.sem, steps.now())
            v.tensor_tensor(blk_hot[:, :, :], iota[:, 0:N_BLK].unsqueeze(1).broadcast_to([P, 2 * NT, N_BLK]),
                               wide(blk[:, :], N_BLK), ALU.is_equal).then_inc(steps.sem, steps.adds(1))
            dve.wait_ge(steps.sem, steps.now())
            v.tensor_tensor(marks[:, :, :, :], blk_hot[:, :, :].unsqueeze(2).broadcast_to([P, 2 * NT, 2, N_BLK]),
                            wide(T.c("token").rearrange("p (n c) -> p n c", c=2), N_BLK), ALU.mult).then_inc(
                                marked.sem, marked.adds(1))
            v.tensor_tensor(before[:, :, :], wide(iota[0:1, 0:OVER], N_EXP),
                               upto[0:1, :].unsqueeze(1).broadcast_to([1, OVER, N_EXP]), ALU.is_ge).then_inc(steps.sem, steps.adds(1))
            dve.wait_ge(steps.sem, steps.now())
            v.reduce_sum(over[:, 0:OVER], before[:, :, :], AX).then_inc(steps.sem, steps.adds(1))
            dve.wait_ge(steps.sem, steps.now())
            v.tensor_scalar(over[:, 0:OVER], over[:, 0:OVER], N_EXP - 1.0, None, ALU.min).then_inc(steps.sem, steps.adds(1))
            dve.wait_ge(steps.sem, steps.now())
            v.tensor_copy(over[:, OVER:], upto[0:1, N_EXP - 1:N_EXP]).then_inc(steps.sem, steps.adds(1))
            dve.wait_ge(steps.sem, steps.now())
            v.tensor_copy(plan.over[:, :], over[:, :]).then_inc(steps.sem, steps.adds(1))
            dve.wait_ge(steps.sem, steps.now())
            dve.wait_ge(product.sem, product.at(3))
            v.tensor_scalar(table[:, :], T.ps[0:BLK, 6, 0:2 * N_BLK], float(NO_ROW), None, ALU.add).then_inc(
                steps.sem, steps.adds(1))
            dve.wait_ge(steps.sem, steps.now())
            v.tensor_copy(plan.table[:, :], table[:, :]).then_inc(steps.sem, steps.adds(1))

        @block.tensor
        def _(pe):
            turns.tensor(pe)
            turns.wait_all(pe)
            pe.wait_ge(loads.sem, loads.at(6 * 16))
            for t in range(NT):
                for c in range(KC):
                    ins = nc.tensor.matmul(T.ps[:, 4, t * R:(t + 1) * R], hT[:, c, t * P:(t + 1) * P], w[:, c, :],
                                           start=(c == 0), stop=(c == KC - 1))
            ins.then_inc(product.sem, product.adds(1))
            pe.wait_ge(marked.sem, marked.at(1))
            for t in range(NT + 1):
                out = T.ps[:, 5, t * N_EXP:(t + 1) * N_EXP]
                earlier = list(range(t))
                for n, s in enumerate(earlier):
                    ins = nc.tensor.matmul(out, T.c("ones"), both[:, s, :], start=(n == 0), stop=(t == NT and n == NT - 1))
                if t < NT:
                    ins = nc.tensor.matmul(out, T.c("tri"), both[:, t, :], start=(t == 0), stop=True)
            ins.then_inc(product.sem, product.adds(1))
            pe.wait_ge(marked.sem, marked.at(2))
            for n in range(2 * NT):
                ins = nc.tensor.matmul(T.ps[0:BLK, 6, 0:2 * N_BLK], row_hot[:, n, :],
                                       marks[:, n, :, :].rearrange("p c b -> p (c b)"),
                                       start=(n == 0), stop=(n == 2 * NT - 1))
            ins.then_inc(product.sem, product.adds(1))
    T.end_stage()


def stage_experts(T, l, first, plan):
    nc = T.nc
    pairs = N_EXP // 2
    FC = FF // P
    tag = f"e{l}_"
    with ExitStack() as ctx:
        sb = lambda name, shape: T.sb(ctx, tag + name, shape)
        x_in, xT = plan.x_in, sb("xT", [P, 2, KC * BLK])
        sig, hid = sb("sig", [P, FC * BLK]), sb("hid", [P, FC * BLK])
        y = sb("y", [BLK, 2, D])
        over_w = sb("over_w", [P, 2, UNIT])
        over_x = x_in[:, 2, :]
        over_idx = T.sb(ctx, tag + "over_idx", [BLK, 2], U32)
        if l == 0:
            odd_rows = FinishModulation(T, ctx)
        gathered = [T.counter(f"gathered{i}") for i in range(2)]
        stored = [T.counter(f"y_stored{i}") for i in range(2)]
        turned, turned_out, sigmoid = T.counter("x_turned"), T.counter("x_turned_out"), T.counter("sigmoid")
        half_up, half_hidden = T.counter("half_up"), T.counter("half_hidden")
        silu, hidden, y_act, y_dve = T.counter("silu"), T.counter("hidden"), T.counter("y_act"), T.counter("y_dve")
        o = {n: T.counter(f"o{l}_{n}") for n in ("turn", "x", "idx", "index_read", "y_seen", "x_seen", "w", "down_w", "turned", "xT", "gate", "up",
                                                "sig", "silu", "hidden", "down", "y", "stored")}
        block = ctx.enter_context(nc.Block())

        def each_pair(engine, step):
            for s in range(2):
                step(0, s)
            with T.loop(engine, 1, pairs) as i:
                for s in range(2):
                    step(i, s)

        def each_extra(engine, step):
            n = engine.value_load(plan.over[0:1, OVER:OVER + 1], min_val=0, max_val=OVER)
            with engine.If(n > 0):
                with engine.Fori(0, OVER) as i:
                    with engine.If(i < n):
                        step(i)

        def count(i, s, k=0):
            return i * 2 + (s + k)

        def turn(pe, x, bank):
            for c in range(KC):
                ins = nc.tensor.transpose(bank[:, c * BLK:(c + 1) * BLK], x[:, c::KC], T.c("ident", BLK)[:, 0:BLK])
            return ins

        def up(pe, weights, xt, bank, chunks=range(FC)):
            for k, j in enumerate(chunks):
                for c in range(KC):
                    ins = nc.tensor.matmul(bank[:, k * BLK:(k + 1) * BLK], weights[:, c, j * P:(j + 1) * P],
                                           xt[:, c * BLK:(c + 1) * BLK], start=(c == 0), stop=(c == KC - 1))
            return ins

        def down(pe, weights, n, chunks):
            for j in chunks:
                ins = nc.tensor.matmul(T.ps[0:BLK, 3 + n, :], hid[:, j * BLK:(j + 1) * BLK],
                                       weights[:, j, n * 512:(n + 1) * 512], start=(j == 0), stop=(j == FC - 1))
            return ins

        def as_up(w):
            return w.rearrange("p (c n) -> p c n", c=KC)

        def as_down(w):
            return w.rearrange("p (j n) -> p j n", j=FC)

        def slot(u):
            return T.ring[:, u % RING, :]

        gate_ps = T.ps[:, 1, 0:FC * BLK]
        halves = [slice(0, FC // 2 * BLK), slice(FC // 2 * BLK, FC * BLK)]
        up_ps = [T.ps[:, 2, halves[0]], T.ps[:, 5, halves[0]]]

        @block.sync
        def _(sp):
            with sp.Fori(0, pairs - 1) as i:
                for k in range(RING):
                    T.load_unit(sp, first + RING + k, i)
            T.load_ahead(sp, first + 3 * N_EXP - RING, first + 3 * N_EXP)

            def extra(i):
                e = sp.value_load(plan.over[0:1, bass.ds(i, 1)], min_val=0, max_val=N_EXP - 1)
                sp.wait_ge(o["turn"].sem, i + 1)
                for part in range(2):
                    sp.dma_start(over_w[:, part, :].rearrange("p (c n) -> p c n", c=KC),
                                 T.expert_source(l, e, part)).then_inc(o["w"].sem, 16)
                sp.wait_ge(o["gate"].sem, i + 1)
                sp.dma_start(over_w[:, 0, :].rearrange("p (j n) -> p j n", j=FC),
                             T.expert_source(l, e, 2)).then_inc(o["down_w"].sem, 16)

            each_extra(sp, extra)

        @block.gpsimd
        def _(pool):
            for b in range(N_EXP + 3):
                if b <= N_EXP:
                    if b >= 2:
                        pool.wait_ge(turned.sem, turned.at(b - 1))
                    nc.gpsimd.indirect_dma_start(
                        out=x_in[:, b % 2, :], out_offset=None, in_=T.h_dram, in_offset=plan.tokens(b),
                        bounds_check=TOK - 1, oob_is_err=False).then_inc(gathered[b % 2].sem, gathered[b % 2].adds(16))
                if b >= 3:
                    done = b - 3
                    pool.wait_ge(y_act.sem, y_act.at(done + 1))
                    pool.wait_ge(y_dve.sem, y_dve.at(done + 1))
                    nc.gpsimd.indirect_dma_start(
                        out=T.y_dram, out_offset=plan.targets(done), in_=y[:, done % 2, :], in_offset=None,
                        bounds_check=2 * TOK - 1, oob_is_err=False).then_inc(stored[done % 2].sem, stored[done % 2].adds(16))
                if l == 0 and b in (4, 16):
                    odd_rows.load(pool, b // 16)
                if l == 0 and b in (8, 20):
                    odd_rows.finish(pool, b // 20)
            pool.wait_ge(gathered[N_EXP % 2].sem, gathered[N_EXP % 2].at(16 * (N_EXP // 2 + 1)))

            if l == 0:
                pool.wait_ge(odd_rows.stored.sem, odd_rows.stored.at(32))

            def extra(i):
                pool.wait_ge(o["turn"].sem, i + 1)
                both = plan.table[:, :].rearrange("p (c b) -> p c b", c=2)
                nc.gpsimd.tensor_copy(over_idx[:, :], both[:, :, bass.ds(i + N_EXP, 1)]).then_inc(o["idx"].sem, 1)
                pool.wait_ge(o["idx"].sem, i + 1)
                pool.sem_inc(o["index_read"].sem, 1)
                nc.gpsimd.indirect_dma_start(
                    out=over_x, out_offset=None, in_=T.h_dram,
                    in_offset=bass.IndirectOffsetOnAxis(ap=over_idx[:, 0:1], axis=0),
                    bounds_check=TOK - 1, oob_is_err=False).then_inc(o["x"].sem, 16)
                pool.wait_ge(o["y"].sem, i * 2 + 2)
                pool.sem_inc(o["y_seen"].sem, 1)
                nc.gpsimd.indirect_dma_start(
                    out=T.y_dram, out_offset=bass.IndirectOffsetOnAxis(ap=over_idx[:, 1:2], axis=0),
                    in_=y[:, 0, :], in_offset=None, bounds_check=2 * TOK - 1,
                    oob_is_err=False).then_inc(o["stored"].sem, 16)

            each_extra(pool, extra)

        @block.tensor
        def _(pe):
            def turn_next(s):
                turn(pe, x_in[:, s, :], T.ps[:, 0, :]).then_inc(turned.sem, turned.adds(1))

            def step(i, s):
                u = first + 3 * s
                peeled = isinstance(i, int)
                pe.wait_ge(turned_out.sem, turned_out.at(count(i, s, 1)))
                pe.wait_ge(T.landing(u), T.landed_at(u, i))
                up(pe, as_up(slot(u)), xT[:, s, :], gate_ps).then_inc(T.unit_used.sem, T.unit_used.adds(1))
                pe.wait_ge(gathered[1 - s].sem, gathered[1 - s].at((i + s) * 16 + 16))
                pe.wait_ge(T.landing(u + 1), T.landed_at(u + 1, i))
                up(pe, as_up(slot(u + 1)), xT[:, s, :], up_ps[0], range(0, FC // 2)).then_inc(
                    half_up.sem, half_up.adds(1))
                up(pe, as_up(slot(u + 1)), xT[:, s, :], up_ps[1], range(FC // 2, FC)).then_inc(
                    T.unit_used.sem, T.unit_used.adds(1))
                turn_next(1 - s)
                pe.wait_ge(half_hidden.sem, half_hidden.at(count(i, s, 1)))
                if not (peeled and s == 0):
                    pe.wait_ge(y_act.sem, y_act.at(count(i, s)))
                    pe.wait_ge(y_dve.sem, y_dve.at(count(i, s)))
                pe.wait_ge(T.landing(u + 2), T.landed_at(u + 2, i))
                w_down = as_down(slot(u + 2))
                down(pe, w_down, 0, range(0, FC // 2))
                pe.wait_ge(hidden.sem, hidden.at(count(i, s, 1)))
                down(pe, w_down, 0, range(FC // 2, FC))
                down(pe, w_down, 1, range(FC)).then_inc(T.unit_used.sem, T.unit_used.adds(1))

            pe.wait_ge(gathered[0].sem, gathered[0].at(16))
            turn_next(0)
            each_pair(pe, step)
            pe.wait_ge(y_act.sem, y_act.at(N_EXP))
            pe.wait_ge(y_dve.sem, y_dve.at(N_EXP))
            pe.wait_ge(turned_out.sem, turned_out.at(N_EXP + 1))

            def extra(i):
                pe.wait_ge(o["x"].sem, i * 16 + 16)
                pe.sem_inc(o["x_seen"].sem, 1)
                turn(pe, over_x, T.ps[:, 0, :]).then_inc(o["turned"].sem, 1)
                pe.wait_ge(o["xT"].sem, i + 1)
                pe.wait_ge(o["w"].sem, i * 32 + 32)
                up(pe, as_up(over_w[:, 0, :]), xT[:, 0, :], gate_ps).then_inc(o["gate"].sem, 1)
                up(pe, as_up(over_w[:, 1, :]), xT[:, 0, :], up_ps[0], range(0, FC // 2)).then_inc(o["up"].sem, 1)
                up(pe, as_up(over_w[:, 1, :]), xT[:, 0, :], up_ps[1], range(FC // 2, FC)).then_inc(o["up"].sem, 1)
                pe.wait_ge(o["hidden"].sem, i * 2 + 2)
                pe.wait_ge(o["down_w"].sem, i * 16 + 16)
                down(pe, as_down(over_w[:, 0, :]), 0, range(FC))
                down(pe, as_down(over_w[:, 0, :]), 1, range(FC)).then_inc(o["down"].sem, 1)

            each_extra(pe, extra)

        @block.scalar
        def _(act):
            def copy_turned(i, s):
                act.wait_ge(turned.sem, turned.at(count(i, s, 1)))
                nc.scalar.copy(xT[:, s, :], T.ps[:, 0, :]).then_inc(turned_out.sem, turned_out.adds(1))

            def step(i, s):
                u = first + 3 * s
                peeled = isinstance(i, int)
                act.wait_ge(T.unit_used.sem, T.used_at(u, i))
                if not (peeled and s == 0):
                    act.wait_ge(hidden.sem, hidden.at(count(i, s)))
                nc.scalar.activation(sig[:, :], gate_ps, ACT.Exp, scale=-1.0).then_inc(sigmoid.sem, sigmoid.adds(1))
                copy_turned(i + s, 1 - s)
                act.wait_ge(T.unit_used.sem, T.used_at(u + 2, i))
                if not peeled:
                    act.wait_ge(stored[s].sem, stored[s].at(i * 16))
                nc.scalar.copy(y[:, s, 0:512], T.ps[0:BLK, 3, :]).then_inc(y_act.sem, y_act.adds(1))

            copy_turned(0, 0)
            each_pair(act, step)
            for s in range(2):
                act.wait_ge(stored[s].sem, stored[s].at(16 * pairs))
            act.sem_inc(o["turn"].sem, 1)

            def extra(i):
                act.wait_ge(o["turned"].sem, i + 1)
                nc.scalar.copy(xT[:, 0, :], T.ps[:, 0, :]).then_inc(o["xT"].sem, 1)
                act.wait_ge(o["gate"].sem, i + 1)
                nc.scalar.activation(sig[:, :], gate_ps, ACT.Exp, scale=-1.0).then_inc(o["sig"].sem, 1)
                act.wait_ge(o["down"].sem, i + 1)
                for n in range(2):
                    nc.scalar.copy(y[:, 0, n * 512:(n + 1) * 512], T.ps[0:BLK, 3 + n, :]).then_inc(o["y"].sem, 1)
                act.wait_ge(o["stored"].sem, i * 16 + 16)
                act.sem_inc(o["turn"].sem, 1)

            each_extra(act, extra)

        @block.vector
        def _(dve):
            v = nc.vector

            def step(i, s):
                u = first + 3 * s
                n = count(i, s) * 3
                dve.wait_ge(sigmoid.sem, sigmoid.at(count(i, s, 1)))
                v.tensor_scalar(sig[:, :], sig[:, :], 1.0, None, ALU.add).then_inc(silu.sem, silu.adds(1))
                dve.wait_ge(silu.sem, silu.at(n + 1))
                v.reciprocal(sig[:, :], sig[:, :]).then_inc(silu.sem, silu.adds(1))
                dve.wait_ge(silu.sem, silu.at(n + 2))
                v.tensor_tensor(sig[:, :], sig[:, :], gate_ps, ALU.mult).then_inc(silu.sem, silu.adds(1))
                dve.wait_ge(silu.sem, silu.at(n + 3))
                dve.wait_ge(half_up.sem, half_up.at(count(i, s, 1)))
                v.tensor_tensor(hid[:, halves[0]], sig[:, halves[0]], up_ps[0], ALU.mult).then_inc(
                    half_hidden.sem, half_hidden.adds(1))
                dve.wait_ge(T.unit_used.sem, T.used_at(u + 1, i))
                v.tensor_tensor(hid[:, halves[1]], sig[:, halves[1]], up_ps[1], ALU.mult).then_inc(
                    hidden.sem, hidden.adds(1))
                dve.wait_ge(T.unit_used.sem, T.used_at(u + 2, i))
                if not isinstance(i, int):
                    dve.wait_ge(stored[s].sem, stored[s].at(i * 16))
                v.tensor_copy(y[:, s, 512:D], T.ps[0:BLK, 4, :]).then_inc(y_dve.sem, y_dve.adds(1))

            each_pair(dve, step)

            def extra(i):
                silu_n = i * 3
                dve.wait_ge(o["sig"].sem, i + 1)
                v.tensor_scalar(sig[:, :], sig[:, :], 1.0, None, ALU.add).then_inc(o["silu"].sem, 1)
                dve.wait_ge(o["silu"].sem, silu_n + 1)
                v.reciprocal(sig[:, :], sig[:, :]).then_inc(o["silu"].sem, 1)
                dve.wait_ge(o["silu"].sem, silu_n + 2)
                v.tensor_tensor(sig[:, :], sig[:, :], gate_ps, ALU.mult).then_inc(o["silu"].sem, 1)
                dve.wait_ge(o["silu"].sem, silu_n + 3)
                dve.wait_ge(o["up"].sem, i * 2 + 2)
                for half in range(2):
                    v.tensor_tensor(hid[:, halves[half]], sig[:, halves[half]], up_ps[half], ALU.mult).then_inc(
                        o["hidden"].sem, 1)

            each_extra(dve, extra)
    T.end_stage()


def stage_combine(T, l, plan):
    nc, O = T.nc, T.O
    with ExitStack() as ctx:
        gate = T.sb(ctx, f"gate2_{l}", [P, 2, D])
        rows = T.sb(ctx, f"rows{l}", [P, 2 * NT, D])
        steps, added, weighted, gated = (T.counter("dve_done"), T.counter("rows"), T.counter("act_done"),
                                         T.counter("normed"))
        gate_in = [T.counter("loads_act"), T.counter("rows_in")]
        fetched = [T.counter(f"fetched{t}") for t in range(NT)]
        stored = T.counter("stored_act")
        block = ctx.enter_context(nc.Block())

        @block.sync
        def _(sp):
            by_tile = T.y_dram.rearrange("(k t p) d -> p k t d", k=2, p=P)
            for t in range(NT):
                sp.dma_start(rows[:, t::NT, :], by_tile[:, :, t, :]).then_inc(fetched[t].sem, fetched[t].adds(16))
                if t < 2:
                    sp.dma_start(gate[:, t, :], spread(T.mod_dram[l, t, 5 * D:6 * D])).then_inc(gate_in[t].sem, gate_in[t].adds(16))

        @block.scalar
        def _(act):
            for t in range(NT):
                act.wait_ge(fetched[t].sem, fetched[t].at(16))
                act.mul(rows[:, t, :], rows[:, t, :], plan.weight[:, 0, t:t + 1]).then_inc(weighted.sem, weighted.adds(1))
            if l == 1:
                for t in range(NT):
                    act.wait_ge(added.sem, added.at(t + 1))
                    out = O["y_sample"][0, (t - 1) * P:t * P, :] if t else O["y_prompt"][0]
                    act.dma_start(out, T.x[:, t, :]).then_inc(stored.sem, stored.adds(16))
                act.wait_ge(stored.sem, stored.at(16 * NT))

        @block.gpsimd
        def _(pool):
            for t in range(NT):
                pool.wait_ge(gated.sem, gated.at(t + 1))
                nc.gpsimd.tensor_tensor(T.x[:, t, :], T.x[:, t, :], rows[:, t, :], ALU.add).then_inc(added.sem, added.adds(1))

        @block.vector
        def _(dve):
            v = nc.vector
            for t in range(NT):
                a, b = rows[:, t, :], rows[:, NT + t, :]
                dve.wait_ge(weighted.sem, weighted.at(t + 1))
                v.scalar_tensor_tensor(out=a, in0=b, scalar=plan.weight[:, 1, t:t + 1], in1=a,
                                       op0=ALU.mult, op1=ALU.add).then_inc(steps.sem, steps.adds(1))
                dve.wait_ge(steps.sem, steps.now())
                if t < 2:
                    dve.wait_ge(gate_in[t].sem, gate_in[t].at(16))
                v.tensor_tensor(a, a, gate[:, min(t, 1), :], ALU.mult).then_inc(gated.sem, gated.adds(1))
    T.end_stage()


class Plan:

    def __init__(self, T, ctx, l):
        self.table = T.sb(ctx, f"table{l}", [BLK, 2 * N_BLK], U32)
        self.x_in = T.sb(ctx, f"x_in{l}", [BLK, 3, D])
        self.over = T.sb(ctx, f"over{l}", [1, OVER + 1], I32)
        self.weight = T.sb(ctx, f"weight{l}", [P, 2, NT])

    def tokens(self, b):
        return bass.IndirectOffsetOnAxis(ap=self.table[:, b:b + 1], axis=0)

    def targets(self, b):
        return bass.IndirectOffsetOnAxis(ap=self.table[:, N_BLK + b:N_BLK + b + 1], axis=0)


def program(nc, I, O):
    with ExitStack() as ctx:
        T = Trunk(nc, ctx, I, O)
        first = 0
        for l in range(2):
            total = ODD_COLS if l else EVEN_COLS
            n_in = -(-total // 512)
            if l == 0:
                stage_modulation(T, first)
                first += MOD_UNITS
            with ExitStack() as mixer:
                z = T.sb(mixer, f"z{l}", [P, NT, total])
                stage_projection(T, l, first, z)
                first += n_in
                mix = T.sb(mixer, f"mix{l}", [P, NT, D])
                if l == 0:
                    stage_window(T, first, z, mix)
                    stage_mlstm(T, first, z, mix)
                    first += MOD_UNITS
                else:
                    with ExitStack() as heads:
                        qT = T.sb(heads, "mla_qT", [P, HEADS, TOK])
                        kT = T.sb(heads, "mla_kT", [P, HEADS, 4 * P])
                        v = T.sb(heads, "mla_v", [P, 4, HEADS * HD])
                        stage_mla_heads(T, z, mix, qT[:, :, :], kT[:, :, :], v[:, :, :])
                        stage_mla_attention(T, mix, qT, kT, v)
                    stage_neighbourhood(T, z, mix)
                stage_output(T, l, first, mix)
                first += 2
            with ExitStack() as moe:
                plan = Plan(T, moe, l)
                stage_router(T, l, plan)
                stage_experts(T, l, first, plan)
                first += 3 * N_EXP
                stage_combine(T, l, plan)


OUTPUTS = (("y_prompt", (1, SEQ, D)), ("y_sample", (1, LAT, D)), ("ml_c", (1, 1, 2, ML_H, ML_D, ML_D)),
           ("ml_n", (1, 1, 2, ML_H, ML_D)), ("ml_m", (1, 1, 2, ML_H)),
           ("win_k", (1, 1, SEQ, 2, HD)), ("win_v", (1, 1, SEQ, 2, HD)), ("mla_ckv", (1, 1, SEQ, P)),
           ("mla_kpe", (1, 1, SEQ, MLA_ROPE)), ("nat_k", (1, 1, SEQ, HEADS, HD)),
           ("nat_v", (1, 1, SEQ, HEADS, HD)))
INPUTS = ("x_prompt", "x_sample", "state_ml_c", "state_ml_n", "state_ml_m", "cache_win_k", "cache_win_v",
          "cache_mla_ckv", "cache_mla_kpe", "cache_nat_k", "cache_nat_v", "c", "c_ctx", "ada_w", "ada_b",
          "norm1_g", "norm2_g", "even_w_in", "ml_gate_b", "ml_out_g", "win_q_g", "win_k_g", "win_sink",
          "even_w_out", "odd_w_in", "mla_q_a_g", "mla_kv_a_g", "mla_w_q_up", "mla_w_kv_up", "mla_q_g",
          "mla_k_g", "nat_q_g", "nat_k_g", "nat_rpb", "odd_w_out", "moe_w_group", "moe_b_group",
          "moe_w_expert", "moe_b_expert", "moe_w_gate", "moe_w_up", "moe_w_down")


def kernel(**inputs):
    import concourse.bacc as bacc
    from concourse.bass_utils import run_bass_kernel_spmd

    nc = bacc.Bacc("TRN2", target_bir_lowering=False, num_devices=1)
    arrays = {name: np.ascontiguousarray(inputs[name]) for name in INPUTS}
    arrays["const"] = constants()
    I = {name: nc.dram_tensor("in_" + name, a.shape, mybir.dt.from_np(a.dtype), kind="ExternalInput").ap()
         for name, a in arrays.items()}
    O = {name: nc.dram_tensor("out_" + name, shape, F32, kind="ExternalOutput").ap() for name, shape in OUTPUTS}
    program(nc, I, O)
    got = run_bass_kernel_spmd(nc, [{"in_" + name: a for name, a in arrays.items()}], core_ids=[0]).results[0]
    return tuple(got["out_" + name] for name, _ in OUTPUTS)
```

```python
from contextlib import ExitStack, contextmanager

import numpy as np

import concourse.bass as bass
from concourse import mybir

F32 = mybir.dt.float32
I32 = mybir.dt.int32
U32 = mybir.dt.uint32
ALU = mybir.AluOpType
ACT = mybir.ActivationFunctionType
AX = mybir.AxisListType.X

P = 128
D = 1024
KC = D // P
NT = 3
SEQ, LAT = 128, 256
TOK = SEQ + LAT
GRID_W = 64
EPS = 1e-6
BIG = 1e30
N_EXP, N_GRP, PER_GRP, FF = 32, 4, 8, 512
HEADS, HD = 8, 64
ML_H, ML_D = 4, 128
MLA_QK, MLA_NOPE, MLA_ROPE = 96, 64, 32

RING = 6
UNIT = 4096
BLK = 64
MAX_BLK = -(-TOK // BLK)
OVER = (2 * TOK - 2) // BLK
N_BLK = N_EXP + OVER
NO_ROW = 1024

EVEN_COLS, ODD_COLS = 2832, 1952
WQ0, WK0, WV0, ZG0 = 2064, 2576, 2704, 2048
ZKV0, ZPE0, NQ0, NK0, NV0 = 256, 384, 416, 928, 1440

CONST = {}
_at = 0
for _name, _width in (("ident", P), ("flip", P), ("tri", P), ("ones", P), ("win", 2 * 384), ("nat", 2 * 256),
                      ("ml_f", P), ("ml_b", P), ("cos64", 2 * 64), ("sin64", 2 * 64),
                      ("cos32", 2 * 32), ("sin32", 2 * 32), ("token", 4 * NT), ("iota", 64),
                      ("sel", 4 * P), ("half", 64), ("thr", N_EXP * (MAX_BLK - 1))):
    CONST[_name] = (_at, _width)
    _at += _width
N_CONST = _at


def constants():
    c = np.zeros((P, N_CONST), np.float32)

    def put(name, a):
        at, w = CONST[name]
        c[:, at:at + w] = np.asarray(a, np.float32).reshape(-1, w)

    r = np.arange(P)
    put("ident", np.eye(P))
    put("flip", r[:, None] // GRID_W * GRID_W + GRID_W - 1 - r[:, None] % GRID_W == r[None, :])
    put("tri", r[:, None] < r[None, :])
    put("ones", np.ones((P, P)))
    t = np.arange(LAT)
    near = np.abs(t[:, None] - t[None, :]) <= 128
    win = np.concatenate([np.zeros((LAT, P)), np.where(near, 0, -BIG)], 1)
    put("win", win.reshape(2, P, 384).transpose(1, 0, 2))
    col = t % GRID_W
    start = np.clip(col - 8, 0, GRID_W - 16)
    ok = (col[None, :] >= start[:, None]) & (col[None, :] < start[:, None] + 16)
    put("nat", np.where(ok, 0, -BIG).reshape(2, P, 256).transpose(1, 0, 2))
    put("ml_f", np.where(r[:, None] <= r[None, :], 0, BIG))
    put("ml_b", np.where(r[:, None] >= r[None, :], 0, BIG))
    for width in (64, 32):
        nf = width // 4
        inv = 10000.0 ** (-np.arange(nf, dtype=np.float32) / nf)
        cos, sin = [], []
        for pos in (t // GRID_W, t % GRID_W):
            ang = pos.astype(np.float32)[:, None] * inv[None, :].astype(np.float32)
            cos += [np.cos(ang), np.cos(ang)]
            sin += [-np.sin(ang), np.sin(ang)]
        put(f"cos{width}", np.concatenate(cos, 1).reshape(2, P, width).transpose(1, 0, 2))
        put(f"sin{width}", np.concatenate(sin, 1).reshape(2, P, width).transpose(1, 0, 2))
    token = np.broadcast_to(r[:, None, None] + P * np.arange(NT), (P, 2, NT))
    put("token", np.stack([token, token + TOK * np.arange(2)[:, None]], -1) - NO_ROW)
    put("iota", np.broadcast_to(np.arange(64), (P, 64)))
    sel = np.zeros((P, 4, P))
    for h in range(4):
        sel[h, h] = 1
    put("sel", sel)
    put("half", np.full((P, 64), -0.5))
    over = BLK * (1 + np.arange(MAX_BLK - 1))
    put("thr", np.broadcast_to(over, (P, N_EXP, MAX_BLK - 1)))
    return c


class Counter:

    def __init__(self, nc, ctx, name):
        self.sem = ctx.enter_context(nc.semaphore(name))
        self.base = self.made = 0

    def adds(self, n):
        self.made += n
        return n

    def at(self, n):
        return self.base + n

    def now(self):
        return self.base + self.made


def weight_units(I):
    units = []

    def modulation(l):
        w = I["ada_w"][l].rearrange("(p c) n -> p c n", c=KC)
        return [(w[:, :, n:n + 512], 512) for n in range(0, 6 * D, 512)]

    units += modulation(0)
    for l in range(2):
        w_in = I["odd_w_in" if l else "even_w_in"][0].rearrange("(p c) n -> p c n", c=KC)
        total = ODD_COLS if l else EVEN_COLS
        units += [(w_in[:, :, n:min(n + 512, total)], min(512, total - n)) for n in range(0, total, 512)]
        if l == 0:
            units += modulation(1)
        w_out = I["odd_w_out" if l else "even_w_out"][0].rearrange("(p c) n -> p c n", c=KC)
        units += [(w_out[:, :, n:n + 512], 512) for n in (0, 512)]
        units += [("experts", l)] * (3 * N_EXP)
    return units


class Trunk:

    def __init__(self, nc, ctx, I, O):
        self.nc, self.ctx, self.I, self.O = nc, ctx, I, O
        self.counters = {}
        sb = self.sb
        self.const = sb(ctx, "const", [P, N_CONST])
        self.x = sb(ctx, "x", [P, NT, D])
        self.cond = sb(ctx, "cond", [P, 2, KC])
        self.ring = sb(ctx, "ring", [P, RING, UNIT])
        self.ps = ctx.enter_context(nc.psum_tensor("ps", [P, 8, 512], F32))
        self.units = weight_units(I)
        self.landed = [self.counter(f"landed{i}") for i in range(RING)]
        self.unit_used = self.counter("unit_used")
        dram = lambda name, shape: nc.dram_tensor(name, shape, F32, kind="Internal").ap()
        self.mod_dram = dram("mod_rows", (2, 2, 6 * D))
        self.raw_dram = dram("raw_mod_rows", (2, 6 * D))
        self.h_dram = dram("h_rows", (TOK, D))
        self.y_dram = dram("expert_rows", (2 * TOK, D))

    def sb(self, ctx, name, shape, dt=F32):
        return ctx.enter_context(self.nc.sbuf_tensor(name, shape, dt))

    def counter(self, name):
        if name not in self.counters:
            self.counters[name] = Counter(self.nc, self.ctx, name)
        return self.counters[name]

    def c(self, name, parts=P):
        at, w = CONST[name]
        return self.const[0:parts, at:at + w]

    @contextmanager
    def loop(self, engine, start, end):
        before = {name: s.made for name, s in self.counters.items()}
        with engine.Fori(start, end) as i:
            yield i
        for name, s in self.counters.items():
            s.made += (s.made - before.get(name, 0)) * (end - start - 1)

    def end_stage(self):
        for s in self.counters.values():
            s.base += s.made
            s.made = 0

    def unit(self, u):
        n = self.units[u][1]
        return self.ring[:, u % RING, 0:KC * n].rearrange("p (c n) -> p c n", c=KC)

    def load_unit(self, sp, u, i=0):
        slot = u % RING
        if u >= RING:
            sp.wait_ge(self.unit_used.sem, u - RING + 1 + i * RING)
        if self.units[u][0] == "experts":
            l = self.units[u][1]
            first = self.units.index(("experts", l))
            e, part = divmod(u - first, 3)
            src = self.expert_source(l, e + 2 * i, part)
            dst = self.ring[:, slot, :].rearrange("p (c n) -> p c n", c=KC if part < 2 else FF // P)
        else:
            src, _ = self.units[u]
            dst = self.unit(u)
        sp.dma_start(dst, src).then_inc(self.landed[slot].sem, 16)

    def expert_source(self, l, e, part):
        w = self.I[("moe_w_gate", "moe_w_up", "moe_w_down")[part]][l]
        one = w[bass.ds(e, 1)]
        if part < 2:
            return one.rearrange("o (p c) n -> p (o c) n", c=KC)
        return one.rearrange("o (j p) n -> p (o j) n", p=P)

    def load_ahead(self, sp, first, end):
        if first == 0:
            for u in range(min(RING, len(self.units))):
                self.load_unit(sp, u)
        for u in range(first + RING, min(end + RING, len(self.units))):
            self.load_unit(sp, u)

    def used_at(self, u, i=0):
        return u + 1 + i * RING

    def landing(self, u):
        return self.landed[u % RING].sem

    def landed_at(self, u, i=0):
        return (u // RING + 1 + i) * 16


def spread(ap, parts=P):
    return ap.partition_broadcast(parts)


class Modulated:

    def __init__(self, T, columns):
        self.T, self.columns = T, columns

    def scalars(self, c, t):
        g = min(t, 1)
        return self.columns[:, 1, g, c:c + 1], self.columns[:, 0, g, c:c + 1]

    def scalar(self, out, src, c, t):
        scale, shift = self.scalars(c, t)
        return self.T.nc.scalar.activation(out, src, ACT.Identity, bias=shift, scale=scale)

    def vector(self, out, src, c, t):
        scale, shift = self.scalars(c, t)
        return self.T.nc.vector.tensor_scalar(out, src, scale, shift, ALU.mult, ALU.add)

    def copy_out(self, engine, turns, hT, modulate, parity, first=0, end=None):
        for g in range(first, len(turns.groups) if end is None else end):
            if g % 2 == parity:
                t, half = divmod(g, 2)
                engine.wait_ge(turns.done.sem, turns.done.at(g + 1))
                for k in range(4):
                    c = 4 * half + k
                    ins = modulate(hT[:, c, t * P:(t + 1) * P], turns.bank(g)[:, k * P:(k + 1) * P], c, t)
                ins.then_inc(turns.copied[parity].sem, turns.copied[parity].adds(1))


class Turns:

    BANKS = 2

    def __init__(self, T, groups):
        self.T, self.groups = T, groups
        self.done = T.counter("turned")
        self.copied = (T.counter("turned_act"), T.counter("turned_dve"))

    def bank(self, g):
        return self.T.ps[:, g % self.BANKS, :]

    def tensor(self, pe, first=0, end=None):
        T = self.T
        for g in range(first, len(self.groups) if end is None else end):
            sources, _, ready = self.groups[g]
            if ready is not None:
                producer, n = ready
                pe.wait_ge(producer.sem, producer.at(n))
            if g >= self.BANKS:
                self.wait_copied(pe, g - self.BANKS)
            for k, s in enumerate(sources):
                rows, cols = s.shape[0], int(np.prod(s.shape[1:]))
                ins = T.nc.tensor.transpose(self.bank(g)[0:cols, k * rows:(k + 1) * rows], s,
                                            T.c("ident")[0:rows, 0:rows])
            ins.then_inc(self.done.sem, self.done.adds(1))

    def wait_copied(self, engine, g):
        engine.wait_ge(self.copied[g % 2].sem, self.copied[g % 2].at(g // 2 + 1))

    def wait_all(self, engine):
        n = len(self.groups)
        for g in (n - 2, n - 1):
            if g >= 0:
                self.wait_copied(engine, g)

    def copy_out(self, engine, copy, parity, first=0, end=None):
        for g in range(first, len(self.groups) if end is None else end):
            if g % 2 == parity:
                sources, out, _ = self.groups[g]
                rows, cols = sources[0].shape[0], int(np.prod(sources[0].shape[1:]))
                engine.wait_ge(self.done.sem, self.done.at(g + 1))
                src = self.bank(g)[0:cols, 0:rows * len(sources)]
                if len(out.shape) == 3:
                    src = src.rearrange("p (k r) -> p k r", k=len(sources))
                copy(out, src).then_inc(self.copied[parity].sem, self.copied[parity].adds(1))


MOD_UNITS = 6 * D // 512


WIN_MOD = 5


class Modulation:

    BUFFERS = 4

    def __init__(self, T, ctx, first, start, end, banks):
        self.T, self.first, self.start, self.end, self.banks = T, first, start, end, banks
        self.rows = T.sb(ctx, f"mod{start}_rows", [2, self.BUFFERS, 512])
        self.copied = T.counter("mod_copied")
        self.stored = [T.counter(f"mod_stored{i}") for i in range(self.BUFFERS)]

    def tensor(self, pe, n, chunks=range(KC)):
        T, u = self.T, self.first + n
        if chunks[0] == 0:
            pe.wait_ge(T.landing(u), T.landed_at(u))
            k = n - self.start
            last = [j for j in range(k) if self.banks[j] == self.banks[k]]
            if last:
                pe.wait_ge(self.copied.sem, self.copied.at(last[-1] + 1))
        for c in chunks:
            ins = T.nc.tensor.matmul(T.ps[0:2, self.banks[n - self.start], :], T.cond[:, :, c], T.unit(u)[:, c, :],
                                     start=(c == 0), stop=(c == KC - 1))
        if chunks[-1] == KC - 1:
            ins.then_inc(T.unit_used.sem, T.unit_used.adds(1))

    def scalar(self, act, n):
        T, k = self.T, n - self.start
        stored, row = self.stored[k % self.BUFFERS], self.rows[:, k % self.BUFFERS, :]
        act.wait_ge(T.unit_used.sem, T.used_at(self.first + n))
        if k >= self.BUFFERS:
            act.wait_ge(stored.sem, stored.now())
        act.copy(row, T.ps[0:2, self.banks[k], :]).then_inc(self.copied.sem, self.copied.adds(1))
        act.wait_ge(self.copied.sem, self.copied.now())
        act.dma_start(T.raw_dram[:, n * 512:(n + 1) * 512], row).then_inc(stored.sem, stored.adds(16))

    def finish(self, act):
        for stored in self.stored:
            act.wait_ge(stored.sem, stored.now())


class FinishModulation:

    HALF = 3 * D

    def __init__(self, T, ctx):
        self.T = T
        self.rows, self.bias, self.gain = (T.sb(ctx, "finish_" + n, [2, w])
                                           for n, w in (("rows", self.HALF), ("bias", self.HALF), ("gain", D)))
        self.loaded, self.done, self.stored = (T.counter("finish_" + n) for n in ("loaded", "done", "stored"))

    def load(self, pool, half):
        T, I = self.T, self.T.I
        cols = slice(half * self.HALF, (half + 1) * self.HALF)
        if half:
            pool.wait_ge(self.stored.sem, self.stored.at(16))
        for dst, src in ((self.rows, T.raw_dram[:, cols]), (self.bias, spread(I["ada_b"][1, cols], 2)),
                         (self.gain, spread(I[("norm1_g", "norm2_g")[half]][1], 2))):
            pool.dma_start(dst[:, :], src).then_inc(self.loaded.sem, self.loaded.adds(16))

    def finish(self, pool, half):
        T, nc = self.T, self.T.nc
        rows, bias, gain = self.rows[:, :], self.bias[:, :], self.gain[:, :]
        pool.wait_ge(self.loaded.sem, self.loaded.at(48 * (half + 1)))
        nc.gpsimd.tensor_tensor(rows, rows, bias, ALU.add).then_inc(self.done.sem, self.done.adds(1))
        pool.wait_ge(self.done.sem, self.done.now())
        scale = rows[:, D:2 * D]
        nc.gpsimd.tensor_scalar(scale, scale, 1.0, None, ALU.add).then_inc(self.done.sem, self.done.adds(1))
        pool.wait_ge(self.done.sem, self.done.now())
        nc.gpsimd.tensor_tensor(scale, scale, gain, ALU.mult).then_inc(self.done.sem, self.done.adds(1))
        pool.wait_ge(self.done.sem, self.done.now())
        pool.dma_start(T.mod_dram[1, :, half * self.HALF:(half + 1) * self.HALF], rows).then_inc(
            self.stored.sem, self.stored.adds(16))


def stage_modulation(T, first):
    nc, I = T.nc, T.I
    with ExitStack() as ctx:
        ce = T.sb(ctx, "ce", [P, 2, KC])
        rows = T.sb(ctx, "even_rows", [2, 6 * D])
        bias = T.sb(ctx, "even_bias", [2, 6 * D])
        gain = T.sb(ctx, "even_gain", [2, 2, D])
        loads, exp, silu = T.counter("loads"), T.counter("act_done"), T.counter("dve_done")
        bias_in, row_done, stored = T.counter("bias_in"), T.counter("row_done"), T.counter("stored_act")
        const_in = T.counter("const_in")
        block = ctx.enter_context(nc.Block())

        @block.sync
        def _(sp):
            sp.wait_ge(loads.sem, loads.at(32))
            T.load_ahead(sp, first, first + MOD_UNITS - RING + 2)

        @block.scalar
        def _(act):
            act.dma_start(T.cond[:, 0, :], I["c_ctx"].rearrange("(p c) -> p c", c=KC)).then_inc(
                loads.sem, loads.adds(16))
            act.dma_start(T.cond[:, 1, :], I["c"][0].rearrange("(p c) -> p c", c=KC)).then_inc(
                loads.sem, loads.adds(16))
            act.dma_start(bias[:, :], spread(I["ada_b"][0], 2)).then_inc(bias_in.sem, bias_in.adds(16))
            for k, name in enumerate(("norm1_g", "norm2_g")):
                act.dma_start(gain[:, k, :], spread(I[name][0], 2)).then_inc(bias_in.sem, bias_in.adds(16))
            act.wait_ge(loads.sem, loads.at(32))
            act.activation(ce[:, :, :], T.cond[:, :, :], ACT.Exp, scale=-1.0).then_inc(exp.sem, exp.adds(1))
            act.wait_ge(T.unit_used.sem, T.used_at(first))
            act.dma_start(T.const[:, :], I["const"]).then_inc(const_in.sem, const_in.adds(16))
            act.dma_start(T.x[:, 0, :], I["x_prompt"][0]).then_inc(const_in.sem, const_in.adds(16))
            act.dma_start(T.x[:, 1:3, :], I["x_sample"][0].rearrange("(t p) d -> p t d", p=P)).then_inc(
                const_in.sem, const_in.adds(16))
            act.wait_ge(row_done.sem, row_done.at(MOD_UNITS + 2))
            act.dma_start(T.mod_dram[0], rows[:, :]).then_inc(stored.sem, stored.adds(16))
            act.wait_ge(stored.sem, stored.at(16))
            act.wait_ge(const_in.sem, const_in.at(48))

        @block.vector
        def _(dve):
            cond = T.cond[:, :, :]
            dve.wait_ge(exp.sem, exp.at(1))
            nc.vector.tensor_scalar(ce[:, :, :], ce[:, :, :], 1.0, None, ALU.add).then_inc(silu.sem, silu.adds(1))
            dve.wait_ge(silu.sem, silu.now())
            nc.vector.reciprocal(ce[:, :, :], ce[:, :, :]).then_inc(silu.sem, silu.adds(1))
            dve.wait_ge(silu.sem, silu.now())
            nc.vector.tensor_tensor(cond, cond, ce[:, :, :], ALU.mult).then_inc(silu.sem, silu.adds(1))
            dve.wait_ge(bias_in.sem, bias_in.at(48))
            for n in range(MOD_UNITS):
                dve.wait_ge(T.unit_used.sem, T.used_at(first + n))
                cols = slice(n * 512, n * 512 + 512)
                nc.vector.tensor_tensor(rows[:, cols], T.ps[0:2, n % 2, :], bias[:, cols], ALU.add).then_inc(
                    row_done.sem, row_done.adds(1))
            dve.wait_ge(row_done.sem, row_done.at(MOD_UNITS))
            for k, at in ((0, D), (1, 4 * D)):
                r = rows[:, at:at + D]
                nc.vector.scalar_tensor_tensor(out=r, in0=r, scalar=1.0, in1=gain[:, k, :], op0=ALU.add,
                                               op1=ALU.mult).then_inc(row_done.sem, row_done.adds(1))

        @block.tensor
        def _(pe):
            pe.wait_ge(silu.sem, silu.at(3))
            for n in range(MOD_UNITS):
                u = first + n
                pe.wait_ge(T.landing(u), T.landed_at(u))
                if n >= 2:
                    pe.wait_ge(row_done.sem, row_done.at(n - 1))
                for c in range(KC):
                    ins = nc.tensor.matmul(T.ps[0:2, n % 2, :], T.cond[:, :, c], T.unit(u)[:, c, :],
                                           start=(c == 0), stop=(c == KC - 1))
                ins.then_inc(T.unit_used.sem, T.unit_used.adds(1))
    T.end_stage()


class OddNorms:

    def __init__(self, T, ctx, z, mix, tables):
        self.T, self.tables = T, tables
        gains = T.sb(ctx, "nat_gains", [P, 2, HD])
        jobs = [(0, 0, 256, 1, tables.g_qa), (0, ZKV0, P, 1, tables.g_kv),
                (1, NQ0, 512, HEADS, gains[:, 0, :]), (2, NK0, 512, HEADS, gains[:, 1, :])]
        self.jobs = []
        for n, (unit, at, width, heads, gain) in enumerate(jobs):
            by_head = lambda a, heads=heads: a.rearrange("p t (h d) -> p t h d", h=heads)
            x, room = z[:, :, at:at + width], mix[:, :, (at if n < 2 else 0):(at if n < 2 else 0) + width]
            stat = T.sb(ctx, f"odd_stat{n}", [P, 2, NT * heads])
            self.jobs.append((unit, x, by_head(x), room, by_head(room), stat, heads, width // heads, gain))
        self.gains = gains
        self.loaded, self.squares, self.sums, self.rstd, self.normed = (
            T.counter("odd_" + n) for n in ("loaded", "squares", "sums", "rstd", "normed"))

    def load(self, act):
        I, loads = self.T.I, self.tables.loads()
        loads += [(self.gains[:, 0, :], spread(I["nat_q_g"][0])), (self.gains[:, 1, :], spread(I["nat_k_g"][0]))]
        for dst, src in loads:
            act.dma_start(dst, src).then_inc(self.loaded.sem, self.loaded.adds(16))

    def scalar(self, act, unit, out):
        for n, (after, x, _, room, _, _, _, _, _) in enumerate(self.jobs):
            if after == unit:
                done = 3 * unit + 3
                act.wait_ge(out[0].sem, out[0].at(-(-done // 2)))
                act.wait_ge(out[1].sem, out[1].at(done // 2))
                if n >= 2:
                    act.wait_ge(self.sums.sem, self.sums.at(n))
                act.activation(room, x, ACT.Square).then_inc(self.squares.sem, self.squares.adds(1))

    def vector(self, dve, unit):
        nc = self.T.nc
        for n, (after, _, x, _, room, stat, heads, width, gain) in enumerate(self.jobs):
            if after == unit:
                dve.wait_ge(self.squares.sem, self.squares.at(n + 1))
                nc.vector.reduce_sum(stat[:, 0, :].rearrange("p (t h) -> p t h", t=NT), room, AX).then_inc(
                    self.sums.sem, self.sums.adds(1))
                dve.wait_ge(self.loaded.sem, self.loaded.now())
                dve.wait_ge(self.rstd.sem, self.rstd.at(2 * n + 2))
                each = stat[:, 1, :].rearrange("p (t h) -> p t h", t=NT).unsqueeze(3).broadcast_to([P, NT, heads, width])
                nc.vector.tensor_tensor(x, x, each, ALU.mult).then_inc(self.normed.sem, self.normed.adds(1))
                dve.wait_ge(self.normed.sem, self.normed.now())
                gain = gain.unsqueeze(1).unsqueeze(1).broadcast_to([P, NT, heads, width])
                nc.vector.tensor_tensor(x, x, gain, ALU.mult).then_inc(self.normed.sem, self.normed.adds(1))

    def pool(self, pool):
        nc = self.T.nc
        for n, (_, _, _, _, _, stat, heads, width, _) in enumerate(self.jobs):
            pool.wait_ge(self.sums.sem, self.sums.at(n + 1))
            nc.gpsimd.tensor_scalar(stat[:, 0, :], stat[:, 0, :], 1.0 / width, EPS, ALU.mult, ALU.add).then_inc(
                self.rstd.sem, self.rstd.adds(1))
            pool.wait_ge(self.rstd.sem, self.rstd.now())
            nc.gpsimd.tensor_tensor(stat[:, 1, :], stat[:, 0, :], self.T.c("half")[:, 0:NT * heads], ALU.pow).then_inc(
                self.rstd.sem, self.rstd.adds(1))


class MlaTables:

    QW, KVW = HEADS * MLA_QK, HEADS * 2 * HD

    def __init__(self, T, mix, kT):
        QW, KVW = self.QW, self.KVW
        self.T, self.k_room = T, kT.rearrange("p h t -> p (h t)")
        room = self.k_room
        self.w_q = room[:, 0:2 * QW].rearrange("p (c n) -> p c n", c=2)
        self.qaT = room[:, 2 * QW:2 * QW + 2 * TOK].rearrange("p (c t) -> p c t", c=2)
        self.ckvT = room[:, 2 * QW + 2 * TOK:2 * QW + 2 * TOK + 4 * P]
        self.w_kv = room[:, 4 * QW:4 * QW + KVW]
        self.g_qa, self.g_kv, self.ckv_c = mix[:, 0, QW:D], mix[:, 1, QW:QW + P], mix[:, 1, QW + P:D]
        self.g_heads = mix[:, 2, QW:QW + 2 * MLA_QK].rearrange("p (a d) -> p a d", a=2)
        self.kpe_c = mix[:, 2, QW + 2 * MLA_QK:QW + 2 * MLA_QK + MLA_ROPE]

    def loads(self):
        I = self.T.I
        return [(self.g_qa, spread(I["mla_q_a_g"][0])), (self.g_kv, spread(I["mla_kv_a_g"][0])),
                (self.ckv_c, I["cache_mla_ckv"][0, 0]), (self.kpe_c, I["cache_mla_kpe"][0, 0]),
                (self.w_q, I["mla_w_q_up"][0].rearrange("(p c) n -> p c n", c=2)), (self.w_kv, I["mla_w_kv_up"][0]),
                (self.g_heads[:, 0, :], spread(I["mla_q_g"][0])), (self.g_heads[:, 1, :], spread(I["mla_k_g"][0]))]


def stage_projection(T, l, first, z, mix=None, tables=None):
    nc = T.nc
    total = ODD_COLS if l else EVEN_COLS
    n_units = -(-total // 512)
    with ExitStack() as ctx:
        columns = T.sb(ctx, f"columns{l}", [P, 2, 2, KC])
        h = T.sb(ctx, f"h{l}", [P, 2, D])
        hT = T.sb(ctx, f"hT{l}", [P, KC, TOK])
        stat = T.sb(ctx, f"stat{l}", [P, 2, NT])
        loads, squares, rstd, row = T.counter("loads"), T.counter("squares"), T.counter("rstd"), T.counter("rows")
        product, out = T.counter("product"), (T.counter("z_act"), T.counter("z_dve"))
        groups = []
        for t in range(NT):
            for k in range(2):
                src = [h[:, t % 2, c::KC] for c in range(4 * k, 4 * k + 4)]
                ready = (row, t + 1) if k == 0 else None
                groups.append((src, hT[:, 4 * k:4 * k + 4, t * P:(t + 1) * P], ready))
        turns = Turns(T, groups)
        modulated = Modulated(T, columns)
        odd = OddNorms(T, ctx, z, mix, tables) if l else None
        block = ctx.enter_context(nc.Block())

        def z_out(engine, copy, parity, after_unit):
            for e in range(n_units * NT):
                n, t = divmod(e, NT)
                if e % 2 != parity:
                    if t == NT - 1:
                        after_unit(n)
                    continue
                cols = min(512, total - n * 512)
                if t < NT - 1:
                    engine.wait_ge(product.sem, product.at(n * (NT - 1) + t + 1))
                else:
                    engine.wait_ge(T.unit_used.sem, T.used_at(first + n))
                copy(z[:, t, n * 512:n * 512 + cols], T.ps[:, 4 + e % 4, 0:cols]).then_inc(
                    out[parity].sem, out[parity].adds(1))
                if t == NT - 1:
                    after_unit(n)

        @block.sync
        def _(sp):
            for g in range(2):
                sp.dma_start(columns[:, :, g, :],
                              T.mod_dram[l, g, 0:2 * D].rearrange("(k p c) -> p k c", k=2, c=KC)).then_inc(
                                  loads.sem, loads.adds(16))
            if l == 0:
                sp.wait_ge(loads.sem, loads.at(32))
                T.load_ahead(sp, first + 2 - RING, first)
            T.load_ahead(sp, first, first + n_units)

        @block.scalar
        def _(act):
            for t in range(NT):
                if t >= 1:
                    act.wait_ge(squares.sem, squares.at(t))
                act.activation(hT[:, 0:KC, 0:P], T.x[:, t, :].rearrange("p (c n) -> p c n", c=KC),
                                          ACT.Square, accum_out=stat[:, 0, t:t + 1]).then_inc(
                                              squares.sem, squares.adds(1))
            act.wait_ge(squares.sem, squares.at(NT))
            act.wait_ge(loads.sem, loads.at(32))
            if odd:
                odd.load(act)
            modulated.copy_out(act, turns, hT, modulated.scalar, 0)
            z_out(act, nc.scalar.copy, 0, lambda n: odd.scalar(act, n, out) if odd else None)

        @block.gpsimd
        def _(pool):
            for t in range(NT):
                one = slice(t, t + 1)
                pool.wait_ge(squares.sem, squares.at(t + 1))
                nc.gpsimd.tensor_scalar(stat[:, 0, one], stat[:, 0, one], 1.0 / D, EPS, ALU.mult, ALU.add).then_inc(
                    rstd.sem, rstd.adds(1))
                pool.wait_ge(rstd.sem, rstd.now())
                nc.gpsimd.tensor_tensor(stat[:, 1, one], stat[:, 0, one], T.c("half")[:, 0:1], ALU.pow).then_inc(
                    rstd.sem, rstd.adds(1))
            if odd:
                odd.pool(pool)

        @block.vector
        def _(dve):
            for t in range(NT):
                dve.wait_ge(rstd.sem, rstd.at(2 * t + 2))
                if t >= 2:
                    dve.wait_ge(turns.done.sem, turns.done.at(2 * (t - 1)))
                nc.vector.tensor_scalar(h[:, t % 2, :], T.x[:, t, :], stat[:, 1, t:t + 1], None, ALU.mult).then_inc(
                    row.sem, row.adds(1))
                if t == 0:
                    dve.wait_ge(loads.sem, loads.at(32))
                    dve.wait_ge(squares.sem, squares.at(NT))
                else:
                    modulated.copy_out(dve, turns, hT, modulated.vector, 1, 2 * (t - 1), 2 * t)
            modulated.copy_out(dve, turns, hT, modulated.vector, 1, 2 * NT - 2)
            z_out(dve, nc.vector.tensor_copy, 1, lambda n: odd.vector(dve, n) if odd else None)

        @block.tensor
        def _(pe):
            turns.tensor(pe)
            turns.wait_all(pe)
            for n in range(n_units):
                cols = min(512, total - n * 512)
                pe.wait_ge(T.landing(first + n), T.landed_at(first + n))
                for t in range(NT):
                    e = n * NT + t
                    if e >= 4:
                        pe.wait_ge(out[(e - 4) % 2].sem, out[(e - 4) % 2].at((e - 4) // 2 + 1))
                    for c in range(KC):
                        ins = nc.tensor.matmul(T.ps[:, 4 + e % 4, 0:cols], hT[:, c, t * P:(t + 1) * P],
                                               T.unit(first + n)[:, c, :], start=(c == 0), stop=(c == KC - 1))
                    if t < NT - 1:
                        ins.then_inc(product.sem, product.adds(1))
                    else:
                        ins.then_inc(T.unit_used.sem, T.unit_used.adds(1))
    T.end_stage()


def stage_output(T, l, first, mix):
    nc = T.nc
    with ExitStack() as ctx:
        mixT = T.sb(ctx, f"mixT{l}", [P, KC, TOK])
        part = T.sb(ctx, f"part{l}", [P, 2, 512])
        gate = T.sb(ctx, f"gate{l}", [P, 2, D])
        loads = T.counter("loads")
        product, used, steps = T.counter("product"), T.counter("row_done"), T.counter("dve_done")
        groups = [([mix[:, t, c::KC] for c in range(4 * k, 4 * k + 4)],
                   mixT[:, 4 * k:4 * k + 4, t * P:(t + 1) * P], None) for t in range(NT) for k in range(2)]
        turns = Turns(T, groups)
        block = ctx.enter_context(nc.Block())

        @block.sync
        def _(sp):
            sp.dma_start(gate[:, :, :], spread(T.mod_dram[l, :, 2 * D:3 * D])).then_inc(loads.sem, loads.adds(16))
            T.load_ahead(sp, first, first + 2)

        @block.scalar
        def _(act):
            turns.copy_out(act, nc.scalar.copy, 0)

        @block.vector
        def _(dve):
            turns.copy_out(dve, nc.vector.tensor_copy, 1)
            dve.wait_ge(loads.sem, loads.at(16))
            for e in range(2 * NT):
                n, t = divmod(e, NT)
                if t < NT - 1:
                    dve.wait_ge(product.sem, product.at(n * (NT - 1) + t + 1))
                else:
                    dve.wait_ge(T.unit_used.sem, T.used_at(first + n))
                cols = slice(n * 512, n * 512 + 512)
                nc.vector.tensor_tensor(part[:, e % 2, :], T.ps[:, 4 + e % 4, :],
                                                       gate[:, min(t, 1), cols], ALU.mult).then_inc(
                                                           used.sem, used.adds(1))
                dve.wait_ge(used.sem, used.now())
                nc.vector.tensor_tensor(T.x[:, t, cols], T.x[:, t, cols], part[:, e % 2, :], ALU.add).then_inc(
                    steps.sem, steps.adds(1))
                if e >= 1:
                    dve.wait_ge(steps.sem, steps.at(e))

        @block.tensor
        def _(pe):
            turns.tensor(pe)
            turns.wait_all(pe)
            for n in range(2):
                pe.wait_ge(T.landing(first + n), T.landed_at(first + n))
                for t in range(NT):
                    e = n * NT + t
                    if e >= 4:
                        pe.wait_ge(used.sem, used.at(e - 3))
                    for c in range(KC):
                        ins = nc.tensor.matmul(T.ps[:, 4 + e % 4, :], mixT[:, c, t * P:(t + 1) * P],
                                               T.unit(first + n)[:, c, :], start=(c == 0), stop=(c == KC - 1))
                    if t < NT - 1:
                        ins.then_inc(product.sem, product.adds(1))
                    else:
                        ins.then_inc(T.unit_used.sem, T.unit_used.adds(1))
    T.end_stage()


class Attention:

    def __init__(self, T, ctx, name, groups):
        self.T, self.groups = T, groups
        self.units = [u for g in groups for u in g[0]]
        n = len(self.units)
        self.masked = T.sb(ctx, name + "_masked", [P, 2, 384])
        self.prob = T.sb(ctx, name + "_prob", [P, 2, 384])
        self.probT = T.sb(ctx, name + "_probT", [P, 2, 384])
        self.top = T.sb(ctx, name + "_top", [P, n])
        self.shift = T.sb(ctx, name + "_shift", [P, n])
        self.sum = T.sb(ctx, name + "_sum", [P, n])
        if self.sinks():
            self.sink = T.sb(ctx, name + "_sink_exp", [P, n])
        names = ("score", "shift", "prob", "turn", "out", "sink_in", "sink_out", "group")
        (self.s_score, self.s_shift, self.s_prob, self.s_turn, self.s_out, self.s_sink_in, self.s_sink_out,
         self.s_group) = (T.counter("att_" + s) for s in names)
        self.copied = (T.counter("att_copied_act"), T.counter("att_copied_dve"))

    def tensor(self, pe, between=None):
        T, nc, n = self.T, self.T.nc, len(self.units)
        for i in range(n + 2):
            if i < n:
                q, k = self.units[i][:2]
                if i >= 2:
                    pe.wait_ge(self.s_prob.sem, self.s_prob.at(i - 1))
                nc.tensor.matmul(T.ps[:, i % 2, 0:k.shape[1]], q, k, start=True, stop=True).then_inc(
                    self.s_score.sem, self.s_score.adds(1))
            if 1 <= i < n + 1:
                u = i - 1
                keys = self.units[u][1].shape[1]
                pe.wait_ge(self.s_prob.sem, self.s_prob.at(u + 1))
                if u >= 2:
                    pe.wait_ge(self.copied[u % 2].sem, self.copied[u % 2].at(u // 2))
                for j in range(keys // P):
                    ins = nc.tensor.transpose(T.ps[:, 2 + u % 2, j * P:(j + 1) * P],
                                              self.prob[:, u % 2, j * P:(j + 1) * P], T.c("ident"))
                ins.then_inc(self.s_turn.sem, self.s_turn.adds(1))
            if i >= 2:
                u = i - 2
                g, h = self.place(u)
                values = self.units[u][2]
                pe.wait_ge(self.copied[u % 2].sem, self.copied[u % 2].at(u // 2 + 1))
                if h == 0 and g >= 2:
                    pe.wait_ge(self.s_group.sem, self.s_group.at(g - 1))
                for j, v in enumerate(values):
                    ins = nc.tensor.matmul(T.ps[:, 4 + g % 2, h * HD:(h + 1) * HD],
                                           self.probT[:, u % 2, j * P:(j + 1) * P], v,
                                           start=(j == 0), stop=(j == len(values) - 1))
                ins.then_inc(self.s_out.sem, self.s_out.adds(1))
            if between is not None:
                between(i)

    def place(self, u):
        return u // HEADS, u % HEADS

    def copy_out(self, engine, copy, u):
        if 0 <= u < len(self.units):
            keys = self.units[u][1].shape[1]
            engine.wait_ge(self.s_turn.sem, self.s_turn.at(u + 1))
            if u >= 2:
                engine.wait_ge(self.s_out.sem, self.s_out.at(u - 1))
            copy(self.probT[:, u % 2, 0:keys], self.T.ps[:, 2 + u % 2, 0:keys]).then_inc(
                self.copied[u % 2].sem, self.copied[u % 2].adds(1))

    def sinks(self):
        return [g for g in range(len(self.groups)) if self.groups[g][2] is not None]

    def scalar(self, act):
        nc, n = self.T.nc, len(self.units)
        for i in range(n + 3):
            if i < n:
                q, k, _, mask, scale = self.units[i]
                keys = k.shape[1]
                act.wait_ge(self.s_shift.sem, self.s_shift.at(i + 1))
                if i >= 2:
                    act.wait_ge(self.s_turn.sem, self.s_turn.at(i - 1))
                src = self.T.ps[:, i % 2, 0:keys] if mask is None else self.masked[:, i % 2, 0:keys]
                act.activation(self.prob[:, i % 2, 0:keys], src, ACT.Exp, bias=self.shift[:, i:i + 1],
                                              scale=scale, accum_out=self.sum[:, i:i + 1]).then_inc(
                                                  self.s_prob.sem, self.s_prob.adds(1))
            if i >= 1 and (i - 1) % 2 == 0:
                self.copy_out(act, nc.scalar.copy, i - 1)
            g = (i - 2) // HEADS
            if i >= 2 and (i - 2) % HEADS == HEADS - 1 and self.groups[g][2] is not None:
                act.wait_ge(self.s_sink_in.sem, self.s_sink_in.at(self.sinks().index(g) + 1))
                cols = self.sink[:, g * HEADS:(g + 1) * HEADS]
                act.activation(cols, cols, ACT.Exp).then_inc(self.s_sink_out.sem, self.s_sink_out.adds(1))

    def vector(self, dve, between=None):
        nc, T, n = self.T.nc, self.T, len(self.units)
        steps = T.counter("dve_done")
        for i in range(n + 3):
            if i < n:
                g, h = self.place(i)
                q, k, _, mask, scale = self.units[i]
                keys = k.shape[1]
                dve.wait_ge(self.s_score.sem, self.s_score.at(i + 1))
                scores = T.ps[:, i % 2, 0:keys]
                top = self.top[:, i:i + 1]
                if mask is None:
                    nc.vector.reduce_max(top, scores, AX).then_inc(steps.sem, steps.adds(1))
                    dve.wait_ge(steps.sem, steps.now())
                else:
                    if i >= 2:
                        dve.wait_ge(self.s_prob.sem, self.s_prob.at(i - 1))
                    nc.vector.tensor_tensor_reduce(
                        out=self.masked[:, i % 2, 0:keys], in0=scores, in1=mask, scale=1.0, scalar=-3e38,
                        op0=ALU.add, op1=ALU.max, accum_out=top).then_inc(steps.sem, steps.adds(1))
                    dve.wait_ge(steps.sem, steps.now())
                sink = self.groups[g][2]
                if sink is None:
                    nc.vector.tensor_scalar(self.shift[:, i:i + 1], top, -scale, None, ALU.mult).then_inc(
                        self.s_shift.sem, self.s_shift.adds(1))
                else:
                    nc.vector.tensor_scalar(self.shift[:, i:i + 1], top, -scale,
                                                            sink[:, HEADS + h:HEADS + h + 1], ALU.mult, ALU.min).then_inc(
                                                                self.s_shift.sem, self.s_shift.adds(1))
            if i >= 1 and (i - 1) % 2 == 1:
                self.copy_out(dve, nc.vector.tensor_copy, i - 1)
            if between is not None:
                between(i)
            if i >= 2 and (i - 2) % HEADS == HEADS - 1:
                g = (i - 2) // HEADS
                _, out, sink = self.groups[g]
                cols = slice(g * HEADS, (g + 1) * HEADS)
                dve.wait_ge(self.s_prob.sem, self.s_prob.at((g + 1) * HEADS))
                if sink is not None:
                    nc.vector.tensor_tensor(self.sink[:, cols], self.shift[:, cols],
                                                              sink[:, 0:HEADS], ALU.add).then_inc(
                                                                  self.s_sink_in.sem, self.s_sink_in.adds(1))
                    dve.wait_ge(self.s_sink_out.sem, self.s_sink_out.at(self.sinks().index(g) + 1))
                    nc.vector.tensor_tensor(self.sum[:, cols], self.sum[:, cols],
                                                            self.sink[:, cols], ALU.add).then_inc(
                                                                steps.sem, steps.adds(1))
                    dve.wait_ge(steps.sem, steps.now())
                nc.vector.reciprocal(self.sum[:, cols], self.sum[:, cols]).then_inc(steps.sem, steps.adds(1))
                dve.wait_ge(steps.sem, steps.now())
                dve.wait_ge(self.s_out.sem, self.s_out.at((g + 1) * HEADS))
                each = self.sum[:, cols].unsqueeze(2).broadcast_to([P, HEADS, HD])
                nc.vector.tensor_tensor(
                    out, T.ps[:, 4 + g % 2, 0:HEADS * HD].rearrange("p (h d) -> p h d", h=HEADS), each, ALU.mult).then_inc(
                        self.s_group.sem, self.s_group.adds(1))


def key_order(kT):
    return kT[..., 0:P], kT[..., P:4 * P]


def stage_window(T, first, z, mix):
    nc, I, O = T.nc, T.I, T.O
    qk_heads = 10
    with ExitStack() as ctx:
        sq = mix[:, :, 0:qk_heads * HD]
        rot = z[:, 1:3, WQ0:WQ0 + qk_heads * HD]
        stat = T.sb(ctx, "win_stat", [P, 2, NT * qk_heads])
        gains = T.sb(ctx, "win_gain", [P, 2, HD])
        sink = T.sb(ctx, "win_sink", [P, 2 * HEADS])
        kc = T.sb(ctx, "win_kc", [P, P])
        vc = T.sb(ctx, "win_vc", [P, P])
        qT = T.sb(ctx, "win_qT", [P, 4, TOK])
        kT = T.sb(ctx, "win_kT", [P, 4 * P])
        loads, squares, sums, rstd = T.counter("loads"), T.counter("squares"), T.counter("sums"), T.counter("rstd")
        steps, ready, rotated, stored = (T.counter("dve_done"), T.counter("rows"), T.counter("pool_done"),
                                         T.counter("stored_act"))
        normed = T.counter("normed")
        qk = z[:, :, WQ0:WQ0 + qk_heads * HD]
        by_head = qk.rearrange("p t (h d) -> p t h d", d=HD)
        paired = T.sb(ctx, "win_paired", [P, NT, qk_heads * HD])
        paired_heads = paired[:, :, :].rearrange("p t (h d) -> p t h d", d=HD)
        groups = [([paired[:, t, 2 * j * HD:2 * (j + 1) * HD] for t in range(NT)], qT[:, j, :],
                   (ready, 1) if j == 0 else None) for j in range(4)]
        keys = paired[:, :, HEADS * HD:]
        groups.append(([keys[:, 0, :], kc[:, :], keys[:, 1, :], keys[:, 2, :]],
                       kT[:, :], (loads, 5 * 16)))
        turns = Turns(T, groups)

        att_groups = []
        for t in range(NT):
            units = []
            for h in range(HEADS):
                kv = h // 4
                rows = slice(kv * HD, kv * HD + HD)
                k = key_order(kT[rows, :])[min(t, 1)]
                own = [z[:, s, WV0 + kv * HD:WV0 + (kv + 1) * HD] for s in range(NT)]
                values = own[0:1] if t == 0 else [vc[:, kv * HD:(kv + 1) * HD]] + own[1:]
                mask = None if t == 0 else T.c("win")[:, (t - 1) * 384:t * 384]
                units.append((qT[rows, h % 4, t * P:(t + 1) * P], k, values, mask, HD ** -0.5))
            out = mix[:, t, 512:1024].rearrange("p (h d) -> p h d", d=HD)
            att_groups.append((units, out, sink))
        att = Attention(T, ctx, "win", att_groups)
        mod = Modulation(T, ctx, first, 0, WIN_MOD, [6, 7] * WIN_MOD)
        early = range(WIN_MOD - 1)
        block = ctx.enter_context(nc.Block())

        @block.sync
        def _(sp):
            for dst, src in ((gains[:, 0, :], spread(I["win_q_g"][0])), (gains[:, 1, :], spread(I["win_k_g"][0])),
                             (sink[:, 0:HEADS], spread(I["win_sink"][0])),
                             (kc[:, :], I["cache_win_k"][0, 0].rearrange("s h d -> s (h d)")),
                             (vc[:, :], I["cache_win_v"][0, 0].rearrange("s h d -> s (h d)"))):
                sp.dma_start(dst, src).then_inc(loads.sem, loads.adds(16))
            T.load_ahead(sp, first, first + WIN_MOD)

        @block.scalar
        def _(act):
            act.activation(sq[:, :, :], qk, ACT.Square).then_inc(squares.sem, squares.adds(1))
            for n in early:
                mod.scalar(act, n)
            turns.copy_out(act, nc.scalar.copy, 0)
            att.scalar(act)
            mod.scalar(act, WIN_MOD - 1)
            mod.finish(act)
            act.wait_ge(normed.sem, normed.at(1))
            act.dma_start(O["win_k"][0, 0].rearrange("s h d -> s (h d)"), keys[:, 0, :]).then_inc(
                stored.sem, stored.adds(16))
            act.dma_start(O["win_v"][0, 0].rearrange("s h d -> s (h d)"), z[:, 0, WV0:WV0 + P]).then_inc(
                stored.sem, stored.adds(16))
            act.wait_ge(stored.sem, stored.at(32))

        @block.gpsimd
        def _(pool):
            pool.wait_ge(sums.sem, sums.at(1))
            nc.gpsimd.tensor_scalar(stat[:, 0, :], stat[:, 0, :], 1.0 / HD, EPS, ALU.mult, ALU.add).then_inc(
                rstd.sem, rstd.adds(1))
            pool.wait_ge(rstd.sem, rstd.now())
            nc.gpsimd.tensor_tensor(stat[:, 1, :], stat[:, 0, :], T.c("half")[:, 0:NT * qk_heads], ALU.pow).then_inc(
                rstd.sem, rstd.adds(1))
            pool.wait_ge(normed.sem, normed.at(1))
            for t in range(2):
                cos = T.c("cos64")[:, t * HD:(t + 1) * HD].unsqueeze(1).broadcast_to([P, qk_heads, HD])
                nc.gpsimd.tensor_tensor(rot[:, t, :].rearrange("p (h d) -> p h d", d=HD),
                                                   paired_heads[:, t + 1], cos, ALU.mult).then_inc(
                                                       rotated.sem, rotated.adds(1))

        @block.vector
        def _(dve):
            dve.wait_ge(squares.sem, squares.at(1))
            nc.vector.reduce_sum(stat[:, 0, :].rearrange("p (t h) -> p t h", t=NT),
                                         sq[:, :, :].rearrange("p t (h d) -> p t h d", d=HD), AX).then_inc(
                                             sums.sem, sums.adds(1))
            dve.wait_ge(loads.sem, loads.at(5 * 16))
            nc.vector.tensor_scalar(sink[:, HEADS:], sink[:, 0:HEADS], -1.0, None, ALU.mult).then_inc(
                steps.sem, steps.adds(1))
            dve.wait_ge(steps.sem, steps.now())
            dve.wait_ge(rstd.sem, rstd.at(2))
            each = stat[:, 1, :].rearrange("p (t h) -> p t h", t=NT).unsqueeze(3).broadcast_to([P, NT, qk_heads, HD])
            nc.vector.tensor_tensor(by_head, by_head, each, ALU.mult).then_inc(steps.sem, steps.adds(1))
            dve.wait_ge(steps.sem, steps.now())
            for t in range(NT):
                gain = gains[:, 0, :].unsqueeze(1).unsqueeze(1).broadcast_to([P, 2, 4, HD])
                nc.vector.tensor_tensor(
                    paired[:, t, 0:512].rearrange("p (j a d) -> p a j d", a=2, d=HD),
                    z[:, t, WQ0:WQ0 + 512].rearrange("p (a j d) -> p a j d", a=2, d=HD), gain, ALU.mult).then_inc(
                        steps.sem, steps.adds(1))
            gain = gains[:, 1, :].unsqueeze(1).unsqueeze(1).broadcast_to([P, NT, 2, HD])
            dve.wait_ge(steps.sem, steps.now())
            nc.vector.tensor_tensor(paired_heads[:, :, 8:10, :], by_head[:, :, 8:10, :], gain, ALU.mult).then_inc(
                normed.sem, normed.adds(1))
            dve.wait_ge(normed.sem, normed.now())
            rope(T, dve, paired_heads[:, 1:3], sq, rot, (rotated, 2), qk_heads, HD, ready)
            turns.copy_out(dve, nc.vector.tensor_copy, 1)
            att.vector(dve)

        @block.tensor
        def _(pe):
            for n in early:
                mod.tensor(pe, n)
            turns.tensor(pe)
            turns.wait_all(pe)

            def between(i):
                if i % 3 == 2 and i // 3 < KC:
                    mod.tensor(pe, WIN_MOD - 1, range(i // 3, i // 3 + 1))

            att.tensor(pe, between)
    T.end_stage()


def rope(T, dve, x, swapped, straight, straight_ready, heads, width, done):
    nc, steps = T.nc, T.counter("dve_done")
    q = width // 4
    for t in range(2):
        src = x[:, t].rearrange("p h (a b d) -> p h a b d", a=2, b=2)
        dst = swapped[:, t, 0:heads * width].rearrange("p (h a b d) -> p h a b d", h=heads, a=2, b=2)
        sin = T.c(f"sin{width}")[:, t * width:(t + 1) * width].rearrange("p (a b d) -> p a b d", a=2, b=2)
        for b in range(2):
            s = sin[:, :, b, :].unsqueeze(1).broadcast_to([P, heads, 2, q])
            ins = nc.vector.tensor_tensor(dst[:, :, :, b, :], src[:, :, :, 1 - b, :], s, ALU.mult)
            ins.then_inc(steps.sem, steps.adds(1))
    dve.wait_ge(steps.sem, steps.now())
    dve.wait_ge(straight_ready[0].sem, straight_ready[0].at(straight_ready[1]))
    ins = nc.vector.tensor_tensor(x, straight[:, :, 0:heads * width].rearrange("p t (h d) -> p t h d", d=width),
                                  swapped[:, 0:2, 0:heads * width].rearrange("p t (h d) -> p t h d", d=width), ALU.add)
    ins.then_inc(done.sem, done.adds(1))


def stage_mlstm(T, first, z, mix):
    nc, I, O = T.nc, T.I, T.O
    pairs = [(h, d) for h in range(ML_H) for d in range(2)]
    W = ML_D + 1
    k_scale = ML_D ** -0.5
    with ExitStack() as ctx:
        sb = lambda name, shape: T.sb(ctx, "ml_" + name, shape)
        area = sb("area", [P, 4 * TOK])
        gates = area[0:4, :].rearrange("p (k t) -> p k t", k=4)
        decay = area[:, 0:1024].rearrange("p (b n) -> p b n", b=2)
        run = sb("run", [4, 2, 2, TOK])
        gate_b = sb("gate_b", [4, 4])
        m0_row, m0_all = sb("m0_row", [4, 2]), sb("m0_all", [P, 2 * ML_H])
        cols = sb("cols", [P, NT, 3, 2 * ML_H])
        w_prev = sb("w_prev", [P, 2, 2 * ML_H])
        floor = sb("floor", [P, NT, 2 * ML_H])
        qT, kT = sb("qT", [P, 2, TOK]), sb("kT", [P, 2, TOK])
        v1 = z[:, :, WQ0:WQ0 + ML_H * W].rearrange("p t (h n) -> p t h n", h=ML_H)
        c0 = sb("c0", [P, 2 * ML_H, W])
        prob = sb("prob", [P, 2, 512])
        kw = sb("kw", [P, 2, P])
        own = sb("own", [P, 2, NT, W])
        state = sb("state", [P, 2, W])
        den = sb("den", [P, 2, NT])
        stat = sb("stat", [P, 2, NT * ML_H])
        gain = sb("gain", [P, ML_D])
        squares_at = z[:, :, 0:512]

        loads, steps, act_steps = T.counter("loads"), T.counter("dve_done"), T.counter("act_done")
        gates_turned, gates_in, logs, rows = (T.counter("ml_" + n) for n in ("gates_turned", "gates_in", "logs", "rows"))
        cols_turned, cols_in, factors = (T.counter("ml_" + n) for n in ("cols_turned", "cols_in", "factors"))
        score, spread_m, log_d, exp_d, prob_in, kw_in = (
            T.counter("ml_" + n) for n in ("score", "spread", "log_d", "exp_d", "prob", "kw"))
        num, num_out, c_out, combined = (T.counter("ml_" + n) for n in ("num", "num_out", "c_out", "combined"))
        stored, v_in, squares, sums, rstd = (T.counter("stored_act"), T.counter("ml_v"), T.counter("squares"),
                                             T.counter("sums"), T.counter("rstd"))
        state_stored = [T.counter(f"ml_state_stored{i}") for i in range(2)]
        groups = []
        for h in range(ML_H):
            for base, buf in ((0, qT), (512, kT)):
                groups.append(([z[:, t, base + h * P:base + (h + 1) * P] for t in range(NT)], buf[:, h % 2, :], None))
        turns = Turns(T, groups)
        tiles = [(0, 0), (1, 1), (2, 2), (1, 2), (2, 1)]
        gates_ps = T.ps[0:4, 4:7, :].rearrange("p a b -> p (a b)")
        cols_ps = T.ps[:, 7, 0:NT * 24].rearrange("p (t w n) -> p t w n", t=NT, w=3)
        c_ps = T.ps[:, 7, 2 * W:3 * W]
        mod = Modulation(T, ctx, first, WIN_MOD, MOD_UNITS, [3, 2] + [3] * MOD_UNITS)
        early, late = range(WIN_MOD, MOD_UNITS - 4), range(MOD_UNITS - 4, MOD_UNITS)
        block = ctx.enter_context(nc.Block())

        @block.sync
        def _(sp):
            with nc.allow_non_contiguous_dma(reason="small vectors"):
                for dst, src in ((gate_b[:, :], I["ml_gate_b"][0].rearrange("(k h) -> h k", k=4)),
                                 (m0_row[:, :], I["state_ml_m"][0, 0].rearrange("d h -> h d")),
                                 (m0_all[:, :], spread(I["state_ml_m"][0, 0].rearrange("d h -> (d h)"))),
                                 (gain[:, :], spread(I["ml_out_g"][0])),
                                 (c0[:, :, 0:ML_D], I["state_ml_c"][0, 0].rearrange("d h k v -> k (d h) v")),
                                 (c0[:, :, ML_D], I["state_ml_n"][0, 0].rearrange("d h k -> k (d h)"))):
                    sp.dma_start(dst, src).then_inc(loads.sem, loads.adds(16))
            T.load_ahead(sp, first + WIN_MOD, first + MOD_UNITS)

        def tile(a, t):
            return a[:, t * P:(t + 1) * P]

        @block.scalar
        def _(act):
            turns.copy_out(act, nc.scalar.copy, 0, 0, 2)
            act.wait_ge(gates_in.sem, gates_in.at(4))
            f = gates[:, 1::2, :]
            tmp = run[:, 1, :, :]
            act.activation(tmp, f, ACT.Abs).then_inc(act_steps.sem, act_steps.adds(1))
            act.wait_ge(act_steps.sem, act_steps.now())
            act.activation(tmp, tmp, ACT.Exp, scale=-1.0).then_inc(act_steps.sem, act_steps.adds(1))
            act.wait_ge(act_steps.sem, act_steps.now())
            act.activation(tmp, tmp, ACT.Ln, bias=1.0).then_inc(logs.sem, logs.adds(1))
            for n in early:
                mod.scalar(act, n)
            zo = z[:, :, 1536:2048]
            act.activation(zo, zo, ACT.Exp, scale=-1.0).then_inc(act_steps.sem, act_steps.adds(1))
            act.wait_ge(rows.sem, rows.at(1))
            with nc.allow_non_contiguous_dma(reason="four numbers"):
                for d in range(2):
                    last = SEQ - 1 if d == 0 else 0
                    act.dma_start(O["ml_m"][0, 0, d].rearrange("(h o) -> h o", o=1),
                                            gates[:, 2 * d + 1, last:last + 1]).then_inc(stored.sem, stored.adds(16))
            act.wait_ge(cols_in.sem, cols_in.at(2))
            act.activation(w_prev[:, :, :], w_prev[:, :, :], ACT.Exp).then_inc(factors.sem, factors.adds(1))
            act.activation(floor[:, :, :], cols[:, :, 2, :], ACT.Exp, scale=-1.0).then_inc(
                factors.sem, factors.adds(1))
            for i in range(len(pairs) + 1):
                if i % 2 == 0 and i >= 2:
                    mod.scalar(act, late[i // 2 - 1])
                if i < len(pairs):
                    act.wait_ge(log_d.sem, log_d.at(i + 1))
                    act.activation(decay[:, i % 2, :], decay[:, i % 2, :], ACT.Exp, scale=-1.0).then_inc(
                        exp_d.sem, exp_d.adds(1))
                if i >= 1:
                    w = i - 1
                    h, d = pairs[w]
                    act.wait_ge(num.sem, num.at(w + 1))
                    if w >= 2:
                        act.wait_ge(combined.sem, combined.at(w - 1))
                    nc.scalar.copy(own[:, w % 2, :, :], T.ps[:, 6, 0:NT * W].rearrange("p (t n) -> p t n", t=NT)).then_inc(
                        num_out.sem, num_out.adds(1))
                    act.wait_ge(c_out.sem, c_out.at(w + 1))
                    with nc.allow_non_contiguous_dma(reason="n, one number per partition"):
                        act.dma_start(O["ml_c"][0, 0, d, h], state[:, w % 2, 0:ML_D]).then_inc(
                            state_stored[w % 2].sem, state_stored[w % 2].adds(16))
                        act.dma_start(O["ml_n"][0, 0, d, h].rearrange("(k o) -> k o", o=1),
                                                            state[:, w % 2, ML_D:W]).then_inc(
                                                                state_stored[w % 2].sem, state_stored[w % 2].adds(16))
                if i % 2 == 1 and i + 1 < len(pairs):
                    turns.copy_out(act, nc.scalar.copy, 0, i + 1, i + 3)
            act.wait_ge(combined.sem, combined.at(len(pairs)))
            act.activation(squares_at, mix[:, :, 0:512], ACT.Square).then_inc(squares.sem, squares.adds(1))
            mod.finish(act)
            for half in range(2):
                act.wait_ge(state_stored[half].sem, state_stored[half].at(32 * len(pairs) // 2))

        @block.gpsimd
        def _(pool):
            for h in range(ML_H):
                nc.gpsimd.tensor_copy(v1[:, :, h, 0:ML_D], z[:, :, 1024 + h * P:1024 + (h + 1) * P]).then_inc(
                    v_in.sem, v_in.adds(1))
            nc.gpsimd.memset(v1[:, :, :, ML_D:W], 1.0).then_inc(v_in.sem, v_in.adds(1))
            pool.wait_ge(sums.sem, sums.at(1))
            nc.gpsimd.tensor_scalar(stat[:, 0, :], stat[:, 0, :], 1.0 / ML_D, EPS, ALU.mult, ALU.add).then_inc(
                rstd.sem, rstd.adds(1))
            pool.wait_ge(rstd.sem, rstd.now())
            nc.gpsimd.tensor_tensor(stat[:, 1, :], stat[:, 0, :], T.c("half")[:, 0:NT * ML_H], ALU.pow).then_inc(
                rstd.sem, rstd.adds(1))

        @block.vector
        def _(dve):
            turns.copy_out(dve, nc.vector.tensor_copy, 1, 0, 2)
            dve.wait_ge(loads.sem, loads.at(6 * 16))
            dve.wait_ge(gates_turned.sem, gates_turned.at(1))
            for k in range(4):
                nc.vector.tensor_scalar(gates[:, k, :], gates_ps[:, k * TOK:(k + 1) * TOK],
                                                    gate_b[:, k:k + 1], None, ALU.add).then_inc(
                                                        gates_in.sem, gates_in.adds(1))
            dve.wait_ge(logs.sem, logs.at(1))
            f, i_gate = gates[:, 1::2, :], gates[:, 0::2, :]
            nc.vector.scalar_tensor_tensor(out=f, in0=f, scalar=0.0, in1=run[:, 1, :, :],
                                                           op0=ALU.min, op1=ALU.subtract).then_inc(
                                                               steps.sem, steps.adds(1))
            dve.wait_ge(steps.sem, steps.now())
            spans = (slice(0, SEQ), slice(SEQ, TOK))
            ones = T.c("ones", 4)[:, 0:1]

            def scan(out, src, first, op):
                for d in range(2):
                    for n, span in enumerate(spans):
                        o, s = out[:, d, span], src(d)[:, span]
                        width = span.stop - span.start
                        if d:
                            o, s = o[:, ::-1], s[:, ::-1]
                        nc.vector.tensor_tensor_scan(o, ones.broadcast_to([4, width]), s, first(d, n), ALU.mult, op).then_inc(
                            steps.sem, steps.adds(1))
                dve.wait_ge(steps.sem, steps.now())

            scan(run[:, 0], lambda d: gates[:, 2 * d + 1, :], lambda d, n: 0.0, ALU.add)
            nc.vector.tensor_tensor(i_gate, i_gate, run[:, 0], ALU.subtract).then_inc(steps.sem, steps.adds(1))
            dve.wait_ge(steps.sem, steps.now())
            scan(run[:, 1], lambda d: gates[:, 2 * d, :], lambda d, n: m0_row[:, d:d + 1] if n else 0.0, ALU.max)
            nc.vector.tensor_tensor(f, run[:, 0], run[:, 1], ALU.add).then_inc(rows.sem, rows.adds(1))
            dve.wait_ge(cols_turned.sem, cols_turned.at(1))
            nc.vector.tensor_copy(cols[:, :, :, :], cols_ps).then_inc(cols_in.sem, cols_in.adds(1))
            dve.wait_ge(cols_in.sem, cols_in.now())
            heads = lambda a: a.rearrange("p t (h d) -> p t h d", h=ML_H)
            zo = z[:, :, 1536:2048]

            def output_gate(step):
                dve.wait_ge(act_steps.sem, act_steps.at(3))
                if step == 0:
                    ins = nc.vector.tensor_scalar(zo, zo, 1.0, None, ALU.add)
                elif step == 1:
                    ins = nc.vector.reciprocal(zo, zo)
                else:
                    g = gain[:, :].unsqueeze(1).unsqueeze(1).broadcast_to([P, NT, ML_H, ML_D])
                    ins = nc.vector.tensor_tensor(heads(zo), heads(zo), g, ALU.mult)
                ins.then_inc(steps.sem, steps.adds(1))
                dve.wait_ge(steps.sem, steps.now())

            m0 = m0_all[:, :].unsqueeze(1).broadcast_to([P, 2, 2 * ML_H])
            nc.vector.tensor_tensor(w_prev[:, :, :], m0, cols[:, 1:3, 1, :], ALU.subtract).then_inc(
                cols_in.sem, cols_in.adds(1))
            dve.wait_ge(stored.sem, stored.at(32))

            def combine(w):
                h, d = pairs[w]
                o = own[:, w % 2]
                dve.wait_ge(num.sem, num.at(w + 1))
                if w >= 2:
                    dve.wait_ge(state_stored[w % 2].sem, state_stored[w % 2].at(32 * (w // 2)))
                nc.vector.tensor_copy(state[:, w % 2, :], c_ps).then_inc(c_out.sem, c_out.adds(1))
                dve.wait_ge(num_out.sem, num_out.at(w + 1))
                dve.wait_ge(factors.sem, factors.at(2))
                for t in (1, 2):
                    nc.vector.scalar_tensor_tensor(
                        out=o[:, t, :], in0=T.ps[:, 7, (t - 1) * W:t * W], scalar=w_prev[:, t - 1, d * ML_H + h:d * ML_H + h + 1],
                        in1=o[:, t, :], op0=ALU.mult, op1=ALU.add).then_inc(steps.sem, steps.adds(1))
                dve.wait_ge(steps.sem, steps.now())
                n = den[:, w % 2, :]
                nc.vector.scalar_tensor_tensor(out=n, in0=o[:, :, ML_D], scalar=-1.0,
                                                               in1=floor[:, :, d * ML_H + h], op0=ALU.mult, op1=ALU.max).then_inc(
                                                                   steps.sem, steps.adds(1))
                dve.wait_ge(steps.sem, steps.now())
                nc.vector.tensor_tensor(n, n, o[:, :, ML_D], ALU.max).then_inc(steps.sem, steps.adds(1))
                dve.wait_ge(steps.sem, steps.now())
                nc.vector.reciprocal(n, n).then_inc(steps.sem, steps.adds(1))
                dve.wait_ge(steps.sem, steps.now())
                each = n.unsqueeze(2).broadcast_to([P, NT, ML_D])
                out = mix[:, :, h * P:(h + 1) * P]
                if d == 0:
                    nc.vector.tensor_tensor(out, o[:, :, 0:ML_D], each, ALU.mult).then_inc(
                        combined.sem, combined.adds(1))
                    dve.wait_ge(combined.sem, combined.now())
                else:
                    nc.vector.tensor_tensor(o[:, :, 0:ML_D], o[:, :, 0:ML_D], each, ALU.mult).then_inc(
                        steps.sem, steps.adds(1))
                    dve.wait_ge(steps.sem, steps.now())
                    nc.vector.tensor_tensor(out, out, o[:, :, 0:ML_D], ALU.add).then_inc(
                        combined.sem, combined.adds(1))
                    dve.wait_ge(combined.sem, combined.now())

            for i in range(len(pairs) + 2):
                if i < len(pairs):
                    h, d = pairs[i]
                    m_all = T.ps[:, 4 + i % 2, 0:TOK]
                    mask = T.c("ml_b" if d else "ml_f")
                    dve.wait_ge(spread_m.sem, spread_m.at(i + 1))
                    if i >= 2:
                        dve.wait_ge(kw_in.sem, kw_in.at(i - 1))
                        dve.wait_ge(prob_in.sem, prob_in.at(i - 1))
                    dec = decay[:, i % 2, :]
                    for slot, (s, t) in enumerate(tiles[0:3] + [tiles[3 + d]]):
                        a = cols[:, s, 0, d * ML_H + h:d * ML_H + h + 1]
                        if slot < 3:
                            ins = nc.vector.scalar_tensor_tensor(out=tile(dec, slot), in0=tile(m_all, t), scalar=a,
                                                                 in1=mask, op0=ALU.subtract, op1=ALU.max)
                        else:
                            ins = nc.vector.tensor_scalar(tile(dec, slot), tile(m_all, t), a, 0.0, ALU.subtract, ALU.max)
                        done = log_d if slot == 3 else steps
                        ins.then_inc(done.sem, done.adds(1))
                if i >= 2:
                    combine(i - 2)
                if i < len(pairs):
                    dve.wait_ge(exp_d.sem, exp_d.at(i + 1))
                    dve.wait_ge(score.sem, score.at(h + 1))
                    pr = prob[:, i % 2, :]
                    if i >= 2:
                        dve.wait_ge(num.sem, num.at(i - 1))
                    same = 4 if d == 0 else 3
                    ins = nc.vector.scalar_tensor_tensor(out=pr[:, 0:same * P], in0=dec[:, 0:same * P], scalar=k_scale,
                                                         in1=T.ps[:, 2, 0:same * P], op0=ALU.mult, op1=ALU.mult)
                    if d:
                        ins.then_inc(steps.sem, steps.adds(1))
                        dve.wait_ge(steps.sem, steps.now())
                        ins = nc.vector.scalar_tensor_tensor(out=pr[:, 3 * P:], in0=dec[:, 3 * P:], scalar=k_scale,
                                                             in1=T.ps[:, 5, TOK:], op0=ALU.mult, op1=ALU.mult)
                    ins.then_inc(prob_in.sem, prob_in.adds(1))
                    last = SEQ - 1 if d == 0 else 0
                    nc.vector.tensor_scalar(kw[:, i % 2, :], z[:, 0, 512 + h * P:512 + (h + 1) * P],
                                                     dec[:, last:last + 1], k_scale, ALU.mult, ALU.mult).then_inc(
                                                         kw_in.sem, kw_in.adds(1))
                if i % 2 == 1 and i + 1 < len(pairs):
                    turns.copy_out(dve, nc.vector.tensor_copy, 1, i + 1, i + 3)
                if i in (2, 4, 6):
                    output_gate(i // 2 - 1)
            dve.wait_ge(squares.sem, squares.at(1))
            nc.vector.reduce_sum(stat[:, 0, :].rearrange("p (t h) -> p t h", t=NT), heads(squares_at), AX).then_inc(
                sums.sem, sums.adds(1))
            out = mix[:, :, 0:512]
            nc.vector.tensor_tensor(out, out, zo, ALU.mult).then_inc(steps.sem, steps.adds(1))
            dve.wait_ge(steps.sem, steps.now())
            dve.wait_ge(rstd.sem, rstd.at(2))
            each = stat[:, 1, :].rearrange("p (t h) -> p t h", t=NT).unsqueeze(3).broadcast_to([P, NT, ML_H, ML_D])
            nc.vector.tensor_tensor(heads(out), heads(out), each, ALU.mult).then_inc(steps.sem, steps.adds(1))

        @block.tensor
        def _(pe):
            for k in range(4):
                for t in range(NT):
                    ins = nc.tensor.transpose(gates_ps[:, k * TOK + t * P:k * TOK + (t + 1) * P],
                                              z[:, t, ZG0 + 4 * k:ZG0 + 4 * k + 4], T.c("ident"))
            ins.then_inc(gates_turned.sem, gates_turned.adds(1))
            turns.tensor(pe, 0, 2)
            for n in early:
                mod.tensor(pe, n)
            pe.wait_ge(rows.sem, rows.at(1))
            for t in range(NT):
                for w, of in enumerate((lambda d: gates[:, 2 * d, :], lambda d: run[:, 1, d, :],
                                        lambda d: gates[:, 2 * d + 1, :])):
                    for d in range(2):
                        ins = nc.tensor.transpose(cols_ps[:, t, w, d * ML_H:(d + 1) * ML_H],
                                                  of(d)[:, t * P:(t + 1) * P], T.c("ident", 4)[:, 0:4])
            ins.then_inc(cols_turned.sem, cols_turned.adds(1))
            pe.wait_ge(cols_in.sem, cols_in.at(1))
            pe.wait_ge(loads.sem, loads.at(6 * 16))
            pe.wait_ge(v_in.sem, v_in.at(5))
            pe.wait_ge(mod.copied.sem, mod.copied.at(len(early)))
            for i in range(len(pairs) + 1):
                if i < len(pairs):
                    h, d = pairs[i]
                    if i >= 2:
                        pe.wait_ge(log_d.sem, log_d.at(i - 1))
                        pe.wait_ge(prob_in.sem, prob_in.at(i - 1))
                    ins = nc.tensor.matmul(T.ps[:, 4 + i % 2, 0:TOK], T.c("sel", 4)[:, h * P:(h + 1) * P],
                                           run[:, 1, d, :], start=True, stop=True)
                    if d:
                        s, t = tiles[4]
                        ins = nc.tensor.matmul(T.ps[:, 5, TOK:], tile(kT[:, h % 2, :], s), tile(qT[:, h % 2, :], t),
                                               start=True, stop=True)
                    ins.then_inc(spread_m.sem, spread_m.adds(1))
                    if d == 0:
                        turns.wait_copied(pe, 2 * h)
                        turns.wait_copied(pe, 2 * h + 1)
                        if i:
                            pe.wait_ge(prob_in.sem, prob_in.at(i))
                        for slot, (s, t) in enumerate(tiles[0:4]):
                            ins = nc.tensor.matmul(T.ps[:, 2, slot * P:(slot + 1) * P], tile(kT[:, h % 2, :], s),
                                                   tile(qT[:, h % 2, :], t), start=True, stop=True)
                        ins.then_inc(score.sem, score.adds(1))
                    mod.tensor(pe, late[i // 2], range(i % 2 * KC // 2, (i % 2 + 1) * KC // 2))
                if i >= 1:
                    w = i - 1
                    h, d = pairs[w]
                    if w >= 1:
                        pe.wait_ge(combined.sem, combined.at(w))
                        pe.wait_ge(num_out.sem, num_out.at(w))
                        pe.wait_ge(c_out.sem, c_out.at(w))
                    for t in (1, 2):
                        nc.tensor.matmul(T.ps[:, 7, (t - 1) * W:t * W], tile(qT[:, h % 2, :], t), c0[:, d * ML_H + h, :],
                                         start=True, stop=True)
                    pe.wait_ge(kw_in.sem, kw_in.at(w + 1))
                    nc.tensor.matmul(c_ps, kw[:, w % 2, :], v1[:, 0, h, :], start=True, stop=True)
                    for t in range(NT):
                        own_slots = [slot for slot in (0, 1, 2, 3) if (tiles[0:3] + [tiles[3 + d]])[slot][1] == t]
                        for n, slot in enumerate(own_slots):
                            s = (tiles[0:3] + [tiles[3 + d]])[slot][0]
                            ins = nc.tensor.matmul(T.ps[:, 6, t * W:(t + 1) * W], tile(prob[:, w % 2, :], slot),
                                                   v1[:, s, h, :], start=(n == 0), stop=(n == len(own_slots) - 1))
                    ins.then_inc(num.sem, num.adds(1))
                if i % 2 == 1 and i + 1 < len(pairs):
                    turns.tensor(pe, i + 1, i + 3)
    T.end_stage()


def stage_mla_heads(T, z, mix, tables, qT, v):
    nc, O = T.nc, T.O
    QW = HEADS * MLA_QK
    with ExitStack() as ctx:
        sb = lambda name, shape: T.sb(ctx, "mla_" + name, shape)
        k = sb("k", [P, 4, QW])
        stat_q, stat_k = sb("stat_q", [P, 2, NT * HEADS]), sb("stat_k", [P, 2, 4 * HEADS])
        q = mix[:, :, 0:QW]
        q_heads = q.rearrange("p t (h d) -> p t h d", h=HEADS)
        k_heads = k[:, :, :].rearrange("p t (h d) -> p t h d", h=HEADS)
        q_room, k_room = qT.rearrange("p h t -> p (h t)"), tables.k_room
        kT = k_room.rearrange("p (h t) -> p h t", h=HEADS)
        w_q, qaT, ckvT, w_kv = tables.w_q, tables.qaT, tables.ckvT, tables.w_kv
        ckv_c, kpe_c, g_heads = tables.ckv_c, tables.kpe_c, tables.g_heads
        steps, pool_steps = T.counter("dve_done"), T.counter("pool_done")
        squares, sums, rstd, normed = T.counter("squares"), T.counter("sums"), T.counter("rstd"), T.counter("normed")
        straight, ready, product = T.counter("straight"), T.counter("rows"), T.counter("product")
        out = (T.counter("z_act"), T.counter("z_dve"))
        stored, k_out = T.counter("stored_act"), T.counter("k_out")
        groups = [([z[:, t, c:256:2] for t in range(NT)], qaT[:, c, :],
                   None) for c in range(2)]
        groups.append(([z[:, 0, ZKV0:ZKV0 + P], ckv_c, z[:, 1, ZKV0:ZKV0 + P], z[:, 2, ZKV0:ZKV0 + P]],
                       ckvT, None))
        for h in range(HEADS):
            groups.append(([q[:, t, h * MLA_QK:(h + 1) * MLA_QK] for t in range(NT)], qT[0:MLA_QK, h, :],
                           (ready, 1) if h == 0 else None))
        for h in range(HEADS):
            groups.append(([k[:, t, h * MLA_QK:(h + 1) * MLA_QK] for t in range(4)], kT[0:MLA_QK, h, :],
                           (ready, 2) if h == 0 else None))
        turns = Turns(T, groups)
        jobs = [("q", t, half) for t in range(NT) for half in range(2)]
        jobs += [("kv", t, half) for t in range(4) for half in range(2)]
        block = ctx.enter_context(nc.Block())

        def products_out(engine, copy, parity, first, end):
            for e in range(first, end):
                what, t, half = jobs[e]
                if e % 2 != parity:
                    continue
                engine.wait_ge(product.sem, product.at(e + 1))
                bank = T.ps[:, 4 + e % 4, :]
                if what == "q":
                    copy(q[:, t, half * 384:(half + 1) * 384], bank[:, 0:384]).then_inc(
                        out[parity].sem, out[parity].adds(1))
                else:
                    both = bank.rearrange("p (h n) -> p h n", h=4)
                    heads = slice(4 * half, 4 * half + 4)
                    copy(k_heads[:, t, heads, 0:HD], both[:, :, 0:HD]).then_inc(k_out.sem, k_out.adds(1))
                    copy(v[:, t, half * 256:(half + 1) * 256].rearrange("p (h n) -> p h n", h=4),
                                        both[:, :, HD:2 * HD]).then_inc(out[parity].sem, out[parity].adds(1))

        @block.scalar
        def _(act):
            turns.copy_out(act, nc.scalar.copy, 0, 0, 3)
            products_out(act, nc.scalar.copy, 0, 0, 6)
            for parity in range(2):
                act.wait_ge(out[parity].sem, out[parity].at(3))
            act.activation(q_room[:, 0:NT * QW].rearrange("p (t n) -> p t n", t=NT), q, ACT.Square).then_inc(
                squares.sem, squares.adds(1))
            products_out(act, nc.scalar.copy, 0, 6, len(jobs))
            for parity in range(2):
                act.wait_ge(out[parity].sem, out[parity].at(7))
            act.wait_ge(pool_steps.sem, pool_steps.at(4))
            act.activation(k_room[:, 0:4 * QW].rearrange("p (t n) -> p t n", t=4), k[:, :, :], ACT.Square).then_inc(
                squares.sem, squares.adds(1))
            turns.copy_out(act, nc.scalar.copy, 0, 3)
            act.dma_start(O["mla_ckv"][0, 0], z[:, 0, ZKV0:ZKV0 + P]).then_inc(stored.sem, stored.adds(16))
            act.dma_start(O["mla_kpe"][0, 0], z[:, 0, ZPE0:ZPE0 + MLA_ROPE]).then_inc(stored.sem, stored.adds(16))
            act.wait_ge(stored.sem, stored.at(32))

        def rotate(pool, n, heads, room):
            pool.wait_ge(normed.sem, normed.at(n))
            for t in range(2):
                cos = T.c("cos32")[:, t * 32:(t + 1) * 32].unsqueeze(1).broadcast_to([P, HEADS, 32])
                nc.gpsimd.tensor_tensor(room[:, t].rearrange("p (h d) -> p h d", h=HEADS),
                                                    heads[:, t, :, MLA_NOPE:], cos, ALU.mult).then_inc(
                                                        straight.sem, straight.adds(1))

        def power(pool, s, ready_at, scales):
            pool.wait_ge(sums.sem, sums.at(ready_at))
            for cols, n in scales:
                nc.gpsimd.tensor_scalar(s[:, 0, cols], s[:, 0, cols], 1.0 / n, EPS, ALU.mult, ALU.add).then_inc(
                    rstd.sem, rstd.adds(1))
                pool.wait_ge(rstd.sem, rstd.now())
            width = s.shape[2]
            nc.gpsimd.tensor_tensor(s[:, 1, :], s[:, 0, :], T.c("half")[:, 0:width], ALU.pow).then_inc(
                rstd.sem, rstd.adds(1))

        @block.gpsimd
        def _(pool):
            for t, pe_row in enumerate((z[:, 0, ZPE0:ZPE0 + MLA_ROPE], kpe_c, z[:, 1, ZPE0:ZPE0 + MLA_ROPE],
                                        z[:, 2, ZPE0:ZPE0 + MLA_ROPE])):
                nc.gpsimd.tensor_copy(k_heads[:, t, :, MLA_NOPE:],
                                                    pe_row.unsqueeze(1).broadcast_to([P, HEADS, MLA_ROPE])).then_inc(
                                                        pool_steps.sem, pool_steps.adds(1))
            power(pool, stat_q, 1, ((slice(0, NT * HEADS), MLA_QK),))
            power(pool, stat_k, 2, ((slice(0, 4 * HEADS), MLA_QK),))
            rotate(pool, 1, q_heads[:, 1:3], z[:, 0:2, 0:256])
            rotate(pool, 2, k_heads[:, 2:4], k_room[:, 0:512].rearrange("p (t n) -> p t n", t=2))

        @block.vector
        def _(dve):
            turns.copy_out(dve, nc.vector.tensor_copy, 1, 0, 3)
            products_out(dve, nc.vector.tensor_copy, 1, 0, 10)
            parts = ((q_heads, NT, stat_q, q_room), (k_heads, 4, stat_k, k_room))
            for n, (x, tiles, s, room) in enumerate(parts):
                if n == 1:
                    products_out(dve, nc.vector.tensor_copy, 1, 10, len(jobs))
                dve.wait_ge(squares.sem, squares.at(1 + n))
                nc.vector.reduce_sum(s[:, 0, :].rearrange("p (t h) -> p t h", t=tiles),
                                     room[:, 0:tiles * QW].rearrange("p (t h d) -> p t h d", t=tiles, h=HEADS),
                                     AX).then_inc(sums.sem, sums.adds(1))
            for n, (x, tiles, s, room) in enumerate(parts):
                dve.wait_ge(rstd.sem, rstd.at(2 + 2 * n))
                each = s[:, 1, :].rearrange("p (t h) -> p t h", t=tiles).unsqueeze(3).broadcast_to([P, tiles, HEADS, MLA_QK])
                nc.vector.tensor_tensor(x, x, each, ALU.mult).then_inc(steps.sem, steps.adds(1))
                dve.wait_ge(steps.sem, steps.now())
                gain = g_heads[:, n, :].unsqueeze(1).unsqueeze(1).broadcast_to([P, tiles, HEADS, MLA_QK])
                nc.vector.tensor_tensor(x, x, gain, ALU.mult).then_inc(normed.sem, normed.adds(1))
                dve.wait_ge(normed.sem, normed.now())
                turned = x[:, tiles - 2:tiles, :, MLA_NOPE:]
                plain = z[:, 0:2, 0:256] if n == 0 else room[:, 0:512].rearrange("p (t n) -> p t n", t=2)
                spare = room[:, 1024:1536].rearrange("p (t n) -> p t n", t=2)
                rope(T, dve, turned, spare, plain, (straight, 2 * (n + 1)), HEADS, MLA_ROPE, ready)
            turns.copy_out(dve, nc.vector.tensor_copy, 1, 3)

        @block.tensor
        def _(pe):
            turns.tensor(pe, 0, 3)
            for g in range(3):
                turns.wait_copied(pe, g)
            for e, (what, t, half) in enumerate(jobs):
                if e >= 4:
                    pe.wait_ge(out[e % 2].sem, out[e % 2].at((e - 4) // 2 + 1))
                bank = T.ps[:, 4 + e % 4, :]
                if what == "q":
                    for c in range(2):
                        ins = nc.tensor.matmul(bank[:, 0:384], qaT[:, c, t * P:(t + 1) * P],
                                               w_q[:, c, half * 384:(half + 1) * 384], start=(c == 0), stop=(c == 1))
                else:
                    ins = nc.tensor.matmul(bank, ckvT[:, t * P:(t + 1) * P], w_kv[:, half * 512:(half + 1) * 512],
                                           start=True, stop=True)
                ins.then_inc(product.sem, product.adds(1))
            turns.tensor(pe, 3)
    T.end_stage()


def stage_mla_attention(T, mix, qT, kT, v):
    nc = T.nc
    with ExitStack() as ctx:
        groups = []
        for t in range(NT):
            units = []
            for h in range(HEADS):
                k = key_order(kT[0:MLA_QK, h, :])[min(t, 1)]
                tiles = (0,) if t == 0 else (1, 2, 3)
                values = [v[:, s, h * HD:(h + 1) * HD] for s in tiles]
                units.append((qT[0:MLA_QK, h, t * P:(t + 1) * P], k, values, None, MLA_QK ** -0.5))
            groups.append((units, mix[:, t, 0:512].rearrange("p (h d) -> p h d", d=HD), None))
        att = Attention(T, ctx, "mla", groups)
        block = ctx.enter_context(nc.Block())

        @block.scalar
        def _(act):
            att.scalar(act)

        @block.vector
        def _(dve):
            att.vector(dve)

        @block.tensor
        def _(pe):
            att.tensor(pe)
    T.end_stage()


def stage_neighbourhood(T, z, mix):
    nc, I, O = T.nc, T.I, T.O
    ROWS, RPB_COLS = LAT // GRID_W, 31
    SP_HEADS = 5
    with ExitStack() as ctx:
        sb = lambda name, shape: T.sb(ctx, "nat_" + name, shape)
        qT, kT = sb("qT", [P, 4, TOK]), sb("kT", [P, 4, 4 * P])
        kc, vc = sb("kc", [P, 512]), sb("vc", [P, 512])
        bias = sb("bias", [P, 2, HEADS, 384])
        loads, tables, pool_tables = T.counter("loads"), T.counter("bias_sp"), T.counter("bias_pool")
        zeroed, stored = T.counter("pool_done"), T.counter("stored_act")
        flipped, biased = T.counter("nat_flipped"), T.counter("nat_biased")
        groups = [([z[:, t, NQ0 + j * P:NQ0 + (j + 1) * P] for t in range(NT)], qT[:, j, :],
                   None) for j in range(4)]
        for j in range(4):
            at = slice(NK0 + j * P, NK0 + (j + 1) * P)
            groups.append(([z[:, 0, at], kc[:, j * P:(j + 1) * P], z[:, 1, at], z[:, 2, at]], kT[:, j, :],
                           (loads, 2 * 16) if j == 0 else None))
        turns = Turns(T, groups)
        att_groups = []
        for t in range(NT):
            units = []
            for h in range(HEADS):
                rows = slice((h % 2) * HD, (h % 2) * HD + HD)
                k = key_order(kT[rows, h // 2, :])[min(t, 1)]
                own = [z[:, s, NV0 + h * HD:NV0 + (h + 1) * HD] for s in range(NT)]
                values = own[0:1] if t == 0 else [vc[:, h * HD:(h + 1) * HD]] + own[1:]
                mask = None if t == 0 else bias[:, t - 1, h, :]
                units.append((qT[rows, h // 2, t * P:(t + 1) * P], k, values, mask, HD ** -0.5))
            att_groups.append((units, mix[:, t, 512:1024].rearrange("p (h d) -> p h d", d=HD), None))
        att = Attention(T, ctx, "nat", att_groups)
        block = ctx.enter_context(nc.Block())

        @block.scalar
        def _(act):
            for dst, src in ((kc[:, :], I["cache_nat_k"][0, 0].rearrange("s h d -> s (h d)")),
                             (vc[:, :], I["cache_nat_v"][0, 0].rearrange("s h d -> s (h d)"))):
                act.dma_start(dst, src).then_inc(loads.sem, loads.adds(16))
            turns.copy_out(act, nc.scalar.copy, 0)
            att.scalar(act)
            act.dma_start(O["nat_k"][0, 0].rearrange("s h d -> s (h d)"), z[:, 0, NK0:NK0 + 512]).then_inc(
                stored.sem, stored.adds(16))
            act.dma_start(O["nat_v"][0, 0].rearrange("s h d -> s (h d)"), z[:, 0, NV0:NV0 + 512]).then_inc(
                stored.sem, stored.adds(16))
            act.wait_ge(stored.sem, stored.at(32))

        def bias_load(queue, h, r):
            first = (h * 15 + 7 - r) * RPB_COLS + 15 - (GRID_W - 1)
            src = bass.AP(tensor=I["nat_rpb"].tensor, offset=I["nat_rpb"].offset + first,
                          ap=[[1, GRID_W], [RPB_COLS, ROWS], [1, GRID_W]])
            part = slice((r % 2) * GRID_W, (r % 2 + 1) * GRID_W)
            dst = bias[part, r // 2, h, P:].rearrange("p (k c) -> p k c", k=ROWS)
            return queue.dma_start(dst, src)

        @block.sync
        def _(sp):
            for h in range(SP_HEADS):
                for r in range(ROWS):
                    bias_load(sp, h, r).then_inc(tables.sem, tables.adds(16))

        @block.gpsimd
        def _(pool):
            for h in range(SP_HEADS, HEADS):
                for r in range(ROWS):
                    bias_load(pool, h, r).then_inc(pool_tables.sem, pool_tables.adds(16))
            nc.gpsimd.memset(bias[:, :, :, 0:P], 0.0).then_inc(zeroed.sem, zeroed.adds(1))
            pool.wait_ge(pool_tables.sem, pool_tables.now())

        @block.vector
        def _(dve):
            turns.copy_out(dve, nc.vector.tensor_copy, 1)
            def between(n):
                if n >= HEADS:
                    return
                t, h = divmod(2 * n, HEADS)
                dve.wait_ge(flipped.sem, flipped.at(n + 1))
                mask = T.c("nat")[:, t * LAT:(t + 1) * LAT].unsqueeze(1).broadcast_to([P, 2, LAT])
                nc.vector.scalar_tensor_tensor(
                    out=bias[:, t, h:h + 2, P:], in0=T.ps[:, 6 + n % 2, :].rearrange("p (h k) -> p h k", h=2),
                    scalar=HD ** 0.5, in1=mask, op0=ALU.mult, op1=ALU.add).then_inc(biased.sem, biased.adds(1))
                if n == HEADS - 1:
                    dve.wait_ge(biased.sem, biased.at(HEADS))
                    dve.wait_ge(zeroed.sem, zeroed.at(1))

            att.vector(dve, between)

        @block.tensor
        def _(pe):
            turns.tensor(pe)
            turns.wait_all(pe)

            def between(n):
                if n >= HEADS:
                    return
                t, h = divmod(2 * n, HEADS)
                if n == 0:
                    pe.wait_ge(tables.sem, tables.at(16 * SP_HEADS * ROWS))
                    pe.wait_ge(pool_tables.sem, pool_tables.at(16 * (HEADS - SP_HEADS) * ROWS))
                if n >= 2:
                    pe.wait_ge(biased.sem, biased.at(n - 1))
                nc.tensor.matmul(T.ps[:, 6 + n % 2, :], T.c("flip"), bias[:, t, h:h + 2, P:],
                                 start=True, stop=True).then_inc(flipped.sem, flipped.adds(1))

            att.tensor(pe, between)
    T.end_stage()


def stage_router(T, l, plan):
    nc, I = T.nc, T.I
    R = N_GRP + N_EXP
    with ExitStack() as ctx:
        sb = lambda name, shape: T.sb(ctx, f"r{l}_" + name, shape)
        scale, shift = sb("scale", [P, 2, D]), sb("shift", [P, 2, D])
        h, hT = sb("h", [P, NT, D]), sb("hT", [P, KC, TOK])
        w, bias = sb("w", [P, KC, R]), sb("bias", [P, R])
        stat = sb("stat", [P, 2, NT])
        logit_by_expert = sb("logit_by_expert", [R, TOK])
        by_expert_out, by_expert_in = T.counter("r_by_expert_out"), T.counter("r_by_expert_in")
        logit = sb("logit", [P, NT, R])
        top, least = sb("top", [P, 3, NT]), sb("least", [P, 3, NT])
        cand, chosen_g = sb("cand", [P, NT, N_EXP]), sb("chosen_g", [P, NT, N_GRP])
        g_exp, p_top, ratio = sb("g_exp", [P, NT, N_GRP]), sb("p_top", [P, NT]), sb("ratio", [P, 2, NT])
        left = sb("left", [P, NT, N_EXP])
        chosen, both = sb("chosen", [P, 2, NT, N_EXP]), sb("both", [P, NT, N_EXP])
        rank = sb("rank", [P, NT + 1, N_EXP])
        above = sb("above", [P, N_EXP * (MAX_BLK - 1)])
        extra, upto, start = sb("extra", [P, N_EXP]), sb("upto", [P, N_EXP]), sb("start", [P, N_EXP])
        picked = sb("picked", [P, NT, N_EXP])
        r, base, q, row, blk, tmp = (sb(n, [P, 2 * NT]) for n in ("rk", "base", "q", "row", "blk", "tmp"))
        row_hot, blk_hot = sb("row_hot", [P, 2 * NT, BLK]), sb("blk_hot", [P, 2 * NT, N_BLK])
        marks = sb("marks", [P, 2 * NT, 2, N_BLK])
        table = sb("table", [BLK, 2 * N_BLK])
        before, over = sb("before", [1, OVER, N_EXP]), sb("over", [1, OVER + 1])
        columns = sb("columns", [P, 2, 2, KC])
        rows_in, columns_in = T.counter("rows_in"), T.counter("columns_in")
        loads, squares, rstd, rows = T.counter("loads"), T.counter("squares"), T.counter("rstd"), T.counter("rows")
        steps, stored, product = T.counter("dve_done"), T.counter("stored_act"), T.counter("product")
        blank = T.counter("blank")
        shifted, exps, marked = T.counter("r_shifted"), T.counter("r_exps"), T.counter("r_marked")
        groups = [([h[:, t, c::KC] for c in range(4 * k, 4 * k + 4)], hT[:, 4 * k:4 * k + 4, t * P:(t + 1) * P],
                   (rows, t + 1) if k == 0 else None) for t in range(NT) for k in range(2)]
        turns = Turns(T, groups)
        modulated = Modulated(T, columns)
        modulated_rows = T.counter("modulated_rows")
        block = ctx.enter_context(nc.Block())

        @block.sync
        def _(sp):
            with nc.allow_non_contiguous_dma(reason="the router's narrow weights"):
                by_feature = T.mod_dram[l, :, 3 * D:5 * D].rearrange("g (k p c) -> g p k c", k=2, c=KC)
                for g in range(2):
                    sp.dma_start(columns[:, :, g, :], by_feature[g]).then_inc(columns_in.sem, columns_in.adds(16))
                for dst, src in ((w[:, :, 0:N_GRP], I["moe_w_group"][l].rearrange("(p c) n -> p c n", c=KC)),
                                 (w[:, :, N_GRP:], I["moe_w_expert"][l].rearrange("(p c) n -> p c n", c=KC)),
                                 (bias[:, 0:N_GRP], spread(I["moe_b_group"][l])),
                                 (bias[:, N_GRP:], spread(I["moe_b_expert"][l]))):
                    sp.dma_start(dst, src).then_inc(loads.sem, loads.adds(16))
                for dst, src in ((scale[:, :, :], spread(T.mod_dram[l, :, 4 * D:5 * D])),
                                 (shift[:, :, :], spread(T.mod_dram[l, :, 3 * D:4 * D]))):
                    sp.dma_start(dst, src).then_inc(rows_in.sem, rows_in.adds(16))

        @block.scalar
        def _(act):
            for t in range(NT):
                if t >= 1:
                    act.wait_ge(squares.sem, squares.at(t))
                act.activation(hT[:, 0:KC, 0:P], T.x[:, t, :].rearrange("p (c n) -> p c n", c=KC),
                                          ACT.Square, accum_out=stat[:, 0, t:t + 1]).then_inc(
                                              squares.sem, squares.adds(1))
            act.wait_ge(squares.sem, squares.at(NT))
            act.wait_ge(columns_in.sem, columns_in.at(32))
            modulated.copy_out(act, turns, hT, modulated.scalar, 0)
            act.wait_ge(by_expert_out.sem, by_expert_out.at(1))
            nc.scalar.copy(logit_by_expert[:, :], T.ps[0:R, 7, 0:TOK]).then_inc(
                by_expert_in.sem, by_expert_in.adds(1))
            act.wait_ge(shifted.sem, shifted.at(1))
            act.activation(g_exp[:, :, :], g_exp[:, :, :], ACT.Exp).then_inc(exps.sem, exps.adds(1))
            act.wait_ge(shifted.sem, shifted.at(2))
            act.activation(ratio[:, 0, :], ratio[:, 0, :], ACT.Exp).then_inc(exps.sem, exps.adds(1))
            act.wait_ge(modulated_rows.sem, modulated_rows.at(2 * NT))
            act.dma_start(T.h_dram.rearrange("(t p) d -> p t d", p=P), h[:, :, :]).then_inc(
                stored.sem, stored.adds(16))
            act.wait_ge(stored.sem, stored.at(16))

        @block.gpsimd
        def _(pool):
            nc.gpsimd.memset(plan.x_in[:, :, :], 0.0).then_inc(blank.sem, blank.adds(1))
            for t in range(NT):
                one = slice(t, t + 1)
                pool.wait_ge(squares.sem, squares.at(t + 1))
                nc.gpsimd.tensor_scalar(stat[:, 0, one], stat[:, 0, one], 1.0 / D, EPS, ALU.mult, ALU.add).then_inc(
                    rstd.sem, rstd.adds(1))
                pool.wait_ge(rstd.sem, rstd.now())
                nc.gpsimd.tensor_tensor(stat[:, 1, one], stat[:, 0, one], T.c("half")[:, 0:1], ALU.pow).then_inc(
                    rstd.sem, rstd.adds(1))
            pool.wait_ge(rows_in.sem, rows_in.at(32))
            for t in range(NT):
                g = min(t, 1)
                pool.wait_ge(turns.done.sem, turns.done.at(2 * t + 2))
                nc.gpsimd.tensor_tensor(h[:, t, :], h[:, t, :], scale[:, g, :], ALU.mult).then_inc(
                    modulated_rows.sem, modulated_rows.adds(1))
                pool.wait_ge(modulated_rows.sem, modulated_rows.now())
                nc.gpsimd.tensor_tensor(h[:, t, :], h[:, t, :], shift[:, g, :], ALU.add).then_inc(
                    modulated_rows.sem, modulated_rows.adds(1))

        @block.vector
        def _(dve):
            v = nc.vector

            def wide(a, n):
                return a.unsqueeze(len(a.shape)).broadcast_to(list(a.shape) + [n])

            for t in range(NT):
                dve.wait_ge(rstd.sem, rstd.at(2 * t + 2))
                v.tensor_scalar(h[:, t, :], T.x[:, t, :], stat[:, 1, t:t + 1], None, ALU.mult).then_inc(
                    rows.sem, rows.adds(1))
                if t == 0:
                    dve.wait_ge(columns_in.sem, columns_in.at(32))
                    dve.wait_ge(squares.sem, squares.at(NT))
                else:
                    modulated.copy_out(dve, turns, hT, modulated.vector, 1, 2 * (t - 1), 2 * t)
            modulated.copy_out(dve, turns, hT, modulated.vector, 1, 2 * NT - 2)
            dve.wait_ge(loads.sem, loads.at(4 * 16))
            dve.wait_ge(product.sem, product.at(1))
            v.tensor_tensor(logit[:, :, :], T.ps[:, 4, 0:NT * R].rearrange("p (t n) -> p t n", t=NT),
                               bias[:, :].unsqueeze(1).broadcast_to([P, NT, R]), ALU.add).then_inc(
                                   steps.sem, steps.adds(1))
            dve.wait_ge(steps.sem, steps.now())

            def first_largest(x, n, k, out):
                c = cand[:, :, 0:n]
                v.reduce_max(top[:, k, :], x, AX).then_inc(steps.sem, steps.adds(1))
                dve.wait_ge(steps.sem, steps.now())
                v.tensor_tensor(c, x, wide(top[:, k, :], n), ALU.is_equal).then_inc(steps.sem, steps.adds(1))
                dve.wait_ge(steps.sem, steps.now())
                v.scalar_tensor_tensor(out=c, in0=c, scalar=-64.0,
                                          in1=T.c("iota")[:, 0:n].unsqueeze(1).broadcast_to([P, NT, n]),
                                          op0=ALU.mult, op1=ALU.add).then_inc(steps.sem, steps.adds(1))
                dve.wait_ge(steps.sem, steps.now())
                v.tensor_reduce(least[:, k, :], c, AX, ALU.min).then_inc(steps.sem, steps.adds(1))
                dve.wait_ge(steps.sem, steps.now())
                v.tensor_tensor(out, c, wide(least[:, k, :], n), ALU.is_equal).then_inc(steps.sem, steps.adds(1))
                dve.wait_ge(steps.sem, steps.now())

            group, expert = logit[:, :, 0:N_GRP], logit[:, :, N_GRP:]
            first_largest(group, N_GRP, 0, chosen_g[:, :, :])
            v.tensor_tensor(g_exp[:, :, :], group, wide(top[:, 0, :], N_GRP), ALU.subtract).then_inc(
                shifted.sem, shifted.adds(1))
            dve.wait_ge(shifted.sem, shifted.now())
            v.tensor_scalar(chosen_g[:, :, :], chosen_g[:, :, :], -1.0, BIG, ALU.add, ALU.mult).then_inc(
                steps.sem, steps.adds(1))
            dve.wait_ge(steps.sem, steps.now())
            by_group = lambda a: a.rearrange("p t (g e) -> p t g e", g=N_GRP)
            v.tensor_tensor(by_group(left[:, :, :]), by_group(expert), wide(chosen_g[:, :, :], PER_GRP), ALU.add).then_inc(
                steps.sem, steps.adds(1))
            dve.wait_ge(steps.sem, steps.now())
            first_largest(left[:, :, :], N_EXP, 1, chosen[:, 0])
            v.scalar_tensor_tensor(out=left[:, :, :], in0=chosen[:, 0], scalar=-3.0 * BIG, in1=left[:, :, :],
                                      op0=ALU.mult, op1=ALU.add).then_inc(steps.sem, steps.adds(1))
            dve.wait_ge(steps.sem, steps.now())
            first_largest(left[:, :, :], N_EXP, 2, chosen[:, 1])
            v.tensor_tensor(ratio[:, 0, :], top[:, 2, :], top[:, 1, :], ALU.subtract).then_inc(
                shifted.sem, shifted.adds(1))
            dve.wait_ge(shifted.sem, shifted.now())
            v.tensor_tensor(both[:, :, :], chosen[:, 0], chosen[:, 1], ALU.add).then_inc(marked.sem, marked.adds(1))
            dve.wait_ge(marked.sem, marked.now())
            dve.wait_ge(exps.sem, exps.at(2))
            v.reduce_sum(p_top[:, :], g_exp[:, :, :], AX).then_inc(steps.sem, steps.adds(1))
            dve.wait_ge(steps.sem, steps.now())
            v.tensor_scalar(ratio[:, 1, :], ratio[:, 0, :], 1.0, None, ALU.add).then_inc(steps.sem, steps.adds(1))
            dve.wait_ge(steps.sem, steps.now())
            v.tensor_tensor(p_top[:, :], p_top[:, :], ratio[:, 1, :], ALU.mult).then_inc(steps.sem, steps.adds(1))
            dve.wait_ge(steps.sem, steps.now())
            v.reciprocal(plan.weight[:, 0, :], p_top[:, :]).then_inc(steps.sem, steps.adds(1))
            dve.wait_ge(steps.sem, steps.now())
            v.tensor_tensor(plan.weight[:, 1, :], plan.weight[:, 0, :], ratio[:, 0, :], ALU.mult).then_inc(
                steps.sem, steps.adds(1))
            dve.wait_ge(steps.sem, steps.now())
            dve.wait_ge(product.sem, product.at(2))
            v.tensor_copy(rank[:, :, :], T.ps[:, 5, 0:(NT + 1) * N_EXP].rearrange("p (t n) -> p t n", n=N_EXP)).then_inc(
                steps.sem, steps.adds(1))
            dve.wait_ge(steps.sem, steps.now())
            count = rank[:, NT, :]
            n_thr = MAX_BLK - 1
            by_expert = above[:, :].rearrange("p (e m) -> p e m", m=n_thr)
            v.tensor_tensor(by_expert, wide(count, n_thr), T.c("thr").rearrange("p (e m) -> p e m", m=n_thr), ALU.is_gt).then_inc(
                steps.sem, steps.adds(1))
            dve.wait_ge(steps.sem, steps.now())
            v.reduce_sum(extra[:, :], by_expert, AX).then_inc(steps.sem, steps.adds(1))
            dve.wait_ge(steps.sem, steps.now())
            v.tensor_tensor_scan(upto[:, :], T.c("ones")[:, 0:N_EXP], extra[:, :], 0.0, ALU.mult, ALU.add).then_inc(
                steps.sem, steps.adds(1))
            dve.wait_ge(steps.sem, steps.now())
            v.tensor_tensor(start[:, :], upto[:, :], extra[:, :], ALU.subtract).then_inc(steps.sem, steps.adds(1))
            dve.wait_ge(steps.sem, steps.now())
            for k in range(2):
                part = slice(k * NT, (k + 1) * NT)
                v.tensor_tensor(picked[:, :, :], chosen[:, k], rank[:, 0:NT, :], ALU.mult).then_inc(
                    steps.sem, steps.adds(1))
                dve.wait_ge(steps.sem, steps.now())
                v.reduce_sum(r[:, part], picked[:, :, :], AX).then_inc(steps.sem, steps.adds(1))
                dve.wait_ge(steps.sem, steps.now())
                v.tensor_tensor(picked[:, :, :], chosen[:, k], start[:, :].unsqueeze(1).broadcast_to([P, NT, N_EXP]),
                                   ALU.mult).then_inc(steps.sem, steps.adds(1))
                dve.wait_ge(steps.sem, steps.now())
                v.reduce_sum(base[:, part], picked[:, :, :], AX).then_inc(steps.sem, steps.adds(1))
                dve.wait_ge(steps.sem, steps.now())
            quot = above[:, 0:2 * NT * n_thr].rearrange("p (n m) -> p n m", m=n_thr)
            v.tensor_tensor(quot, wide(r[:, :], n_thr), T.c("thr")[:, 0:n_thr].unsqueeze(1).broadcast_to([P, 2 * NT, n_thr]),
                               ALU.is_ge).then_inc(steps.sem, steps.adds(1))
            dve.wait_ge(steps.sem, steps.now())
            v.reduce_sum(q[:, :], quot, AX).then_inc(steps.sem, steps.adds(1))
            dve.wait_ge(steps.sem, steps.now())
            v.scalar_tensor_tensor(out=row[:, :], in0=q[:, :], scalar=-float(BLK), in1=r[:, :], op0=ALU.mult, op1=ALU.add).then_inc(
                steps.sem, steps.adds(1))
            dve.wait_ge(steps.sem, steps.now())
            e = least[:, 1:3, :].rearrange("p k t -> p (k t)")
            v.tensor_scalar(e, e, 64.0, None, ALU.add).then_inc(steps.sem, steps.adds(1))
            dve.wait_ge(steps.sem, steps.now())
            v.tensor_tensor(base[:, :], base[:, :], q[:, :], ALU.add).then_inc(steps.sem, steps.adds(1))
            dve.wait_ge(steps.sem, steps.now())
            v.scalar_tensor_tensor(out=tmp[:, :], in0=base[:, :], scalar=N_EXP - 1.0, in1=e, op0=ALU.add, op1=ALU.subtract).then_inc(
                steps.sem, steps.adds(1))
            dve.wait_ge(steps.sem, steps.now())
            v.tensor_scalar(q[:, :], q[:, :], 1.0, None, ALU.min).then_inc(steps.sem, steps.adds(1))
            dve.wait_ge(steps.sem, steps.now())
            v.tensor_tensor(tmp[:, :], tmp[:, :], q[:, :], ALU.mult).then_inc(steps.sem, steps.adds(1))
            dve.wait_ge(steps.sem, steps.now())
            v.tensor_tensor(blk[:, :], tmp[:, :], e, ALU.add).then_inc(steps.sem, steps.adds(1))
            dve.wait_ge(steps.sem, steps.now())
            iota = T.c("iota")
            v.tensor_tensor(row_hot[:, :, :], iota.unsqueeze(1).broadcast_to([P, 2 * NT, BLK]), wide(row[:, :], BLK),
                               ALU.is_equal).then_inc(steps.sem, steps.adds(1))
            dve.wait_ge(steps.sem, steps.now())
            v.tensor_tensor(blk_hot[:, :, :], iota[:, 0:N_BLK].unsqueeze(1).broadcast_to([P, 2 * NT, N_BLK]),
                               wide(blk[:, :], N_BLK), ALU.is_equal).then_inc(steps.sem, steps.adds(1))
            dve.wait_ge(steps.sem, steps.now())
            v.tensor_tensor(marks[:, :, :, :], blk_hot[:, :, :].unsqueeze(2).broadcast_to([P, 2 * NT, 2, N_BLK]),
                            wide(T.c("token").rearrange("p (n c) -> p n c", c=2), N_BLK), ALU.mult).then_inc(
                                marked.sem, marked.adds(1))
            v.tensor_tensor(before[:, :, :], wide(iota[0:1, 0:OVER], N_EXP),
                               upto[0:1, :].unsqueeze(1).broadcast_to([1, OVER, N_EXP]), ALU.is_ge).then_inc(
                                   steps.sem, steps.adds(1))
            dve.wait_ge(steps.sem, steps.now())
            v.reduce_sum(over[:, 0:OVER], before[:, :, :], AX).then_inc(steps.sem, steps.adds(1))
            dve.wait_ge(steps.sem, steps.now())
            v.tensor_scalar(over[:, 0:OVER], over[:, 0:OVER], N_EXP - 1.0, None, ALU.min).then_inc(
                steps.sem, steps.adds(1))
            dve.wait_ge(steps.sem, steps.now())
            v.tensor_copy(over[:, OVER:], upto[0:1, N_EXP - 1:N_EXP]).then_inc(steps.sem, steps.adds(1))
            dve.wait_ge(steps.sem, steps.now())
            v.tensor_copy(plan.over[:, :], over[:, :]).then_inc(steps.sem, steps.adds(1))
            dve.wait_ge(steps.sem, steps.now())
            dve.wait_ge(product.sem, product.at(3))
            v.tensor_scalar(table[:, :], T.ps[0:BLK, 6, 0:2 * N_BLK], float(NO_ROW), None, ALU.add).then_inc(
                steps.sem, steps.adds(1))
            dve.wait_ge(steps.sem, steps.now())
            v.tensor_copy(plan.table[:, :], table[:, :]).then_inc(steps.sem, steps.adds(1))

        @block.tensor
        def _(pe):
            turns.tensor(pe)
            turns.wait_all(pe)
            pe.wait_ge(loads.sem, loads.at(4 * 16))
            for c in range(KC):
                ins = nc.tensor.matmul(T.ps[0:R, 7, 0:TOK], w[:, c, :], hT[:, c, :], start=(c == 0), stop=(c == KC - 1))
            ins.then_inc(by_expert_out.sem, by_expert_out.adds(1))
            pe.wait_ge(by_expert_in.sem, by_expert_in.at(1))
            for t in range(NT):
                ins = nc.tensor.transpose(T.ps[:, 4, t * R:(t + 1) * R], logit_by_expert[:, t * P:(t + 1) * P],
                                          T.c("ident", R)[:, 0:R])
            ins.then_inc(product.sem, product.adds(1))
            pe.wait_ge(marked.sem, marked.at(1))
            for t in range(NT + 1):
                out = T.ps[:, 5, t * N_EXP:(t + 1) * N_EXP]
                earlier = list(range(t))
                for n, s in enumerate(earlier):
                    ins = nc.tensor.matmul(out, T.c("ones"), both[:, s, :], start=(n == 0), stop=(t == NT and n == NT - 1))
                if t < NT:
                    ins = nc.tensor.matmul(out, T.c("tri"), both[:, t, :], start=(t == 0), stop=True)
            ins.then_inc(product.sem, product.adds(1))
            pe.wait_ge(marked.sem, marked.at(2))
            for n in range(2 * NT):
                ins = nc.tensor.matmul(T.ps[0:BLK, 6, 0:2 * N_BLK], row_hot[:, n, :],
                                       marks[:, n, :, :].rearrange("p c b -> p (c b)"),
                                       start=(n == 0), stop=(n == 2 * NT - 1))
            ins.then_inc(product.sem, product.adds(1))
    T.end_stage()


def stage_experts(T, l, first, plan):
    nc = T.nc
    pairs = N_EXP // 2
    FC = FF // P
    tag = f"e{l}_"
    with ExitStack() as ctx:
        sb = lambda name, shape: T.sb(ctx, tag + name, shape)
        x_in, xT = plan.x_in, sb("xT", [P, 2, KC * BLK])
        sig, hid = sb("sig", [P, FC * BLK]), sb("hid", [P, FC * BLK])
        y = sb("y", [BLK, 2, D])
        over_w = sb("over_w", [P, 2, UNIT])
        over_x = x_in[:, 2, :]
        over_idx = T.sb(ctx, tag + "over_idx", [BLK, 2], U32)
        if l == 0:
            odd_rows = FinishModulation(T, ctx)
        gathered = [T.counter(f"gathered{i}") for i in range(2)]
        stored = [T.counter(f"y_stored{i}") for i in range(2)]
        turned, turned_out, sigmoid = T.counter("x_turned"), T.counter("x_turned_out"), T.counter("sigmoid")
        half_up, half_hidden = T.counter("half_up"), T.counter("half_hidden")
        silu, hidden, y_act, y_dve = T.counter("silu"), T.counter("hidden"), T.counter("y_act"), T.counter("y_dve")
        o = {n: T.counter(f"o{l}_{n}") for n in ("turn", "x", "idx", "index_read", "y_seen", "x_seen", "w", "down_w", "turned", "xT", "gate", "up",
                                                "sig", "silu", "hidden", "down", "y", "stored")}
        block = ctx.enter_context(nc.Block())

        def each_pair(engine, step):
            for s in range(2):
                step(0, s)
            with T.loop(engine, 1, pairs) as i:
                for s in range(2):
                    step(i, s)

        def each_extra(engine, step):
            n = engine.value_load(plan.over[0:1, OVER:OVER + 1], min_val=0, max_val=OVER)
            with engine.If(n > 0):
                with engine.Fori(0, OVER) as i:
                    with engine.If(i < n):
                        step(i)

        def count(i, s, k=0):
            return i * 2 + (s + k)

        def turn(pe, x, bank):
            for c in range(KC):
                ins = nc.tensor.transpose(bank[:, c * BLK:(c + 1) * BLK], x[:, c::KC], T.c("ident", BLK)[:, 0:BLK])
            return ins

        def up(pe, weights, xt, bank, chunks=range(FC)):
            for k, j in enumerate(chunks):
                for c in range(KC):
                    ins = nc.tensor.matmul(bank[:, k * BLK:(k + 1) * BLK], weights[:, c, j * P:(j + 1) * P],
                                           xt[:, c * BLK:(c + 1) * BLK], start=(c == 0), stop=(c == KC - 1))
            return ins

        def down(pe, weights, n, chunks):
            for j in chunks:
                ins = nc.tensor.matmul(T.ps[0:BLK, 3 + n, :], hid[:, j * BLK:(j + 1) * BLK],
                                       weights[:, j, n * 512:(n + 1) * 512], start=(j == 0), stop=(j == FC - 1))
            return ins

        def as_up(w):
            return w.rearrange("p (c n) -> p c n", c=KC)

        def as_down(w):
            return w.rearrange("p (j n) -> p j n", j=FC)

        def slot(u):
            return T.ring[:, u % RING, :]

        gate_ps = T.ps[:, 1, 0:FC * BLK]
        halves = [slice(0, FC // 2 * BLK), slice(FC // 2 * BLK, FC * BLK)]
        up_ps = [T.ps[:, 2, halves[0]], T.ps[:, 5, halves[0]]]

        @block.sync
        def _(sp):
            with sp.Fori(0, pairs - 1) as i:
                for k in range(RING):
                    T.load_unit(sp, first + RING + k, i)
            T.load_ahead(sp, first + 3 * N_EXP - RING, first + 3 * N_EXP)

            def extra(i):
                e = sp.value_load(plan.over[0:1, bass.ds(i, 1)], min_val=0, max_val=N_EXP - 1)
                sp.wait_ge(o["turn"].sem, i + 1)
                for part in range(2):
                    sp.dma_start(over_w[:, part, :].rearrange("p (c n) -> p c n", c=KC),
                                 T.expert_source(l, e, part)).then_inc(o["w"].sem, 16)
                sp.wait_ge(o["gate"].sem, i + 1)
                sp.dma_start(over_w[:, 0, :].rearrange("p (j n) -> p j n", j=FC),
                             T.expert_source(l, e, 2)).then_inc(o["down_w"].sem, 16)

            each_extra(sp, extra)

        @block.gpsimd
        def _(pool):
            for b in range(N_EXP + 3):
                if b <= N_EXP:
                    if b >= 2:
                        pool.wait_ge(turned.sem, turned.at(b - 1))
                    nc.gpsimd.indirect_dma_start(
                        out=x_in[:, b % 2, :], out_offset=None, in_=T.h_dram, in_offset=plan.tokens(b),
                        bounds_check=TOK - 1, oob_is_err=False).then_inc(
                            gathered[b % 2].sem, gathered[b % 2].adds(16))
                if b >= 3:
                    done = b - 3
                    pool.wait_ge(y_act.sem, y_act.at(done + 1))
                    pool.wait_ge(y_dve.sem, y_dve.at(done + 1))
                    nc.gpsimd.indirect_dma_start(
                        out=T.y_dram, out_offset=plan.targets(done), in_=y[:, done % 2, :], in_offset=None,
                        bounds_check=2 * TOK - 1, oob_is_err=False).then_inc(
                            stored[done % 2].sem, stored[done % 2].adds(16))
                if l == 0 and b in (4, 16):
                    odd_rows.load(pool, b // 16)
                if l == 0 and b in (8, 20):
                    odd_rows.finish(pool, b // 20)
            pool.wait_ge(gathered[N_EXP % 2].sem, gathered[N_EXP % 2].at(16 * (N_EXP // 2 + 1)))

            if l == 0:
                pool.wait_ge(odd_rows.stored.sem, odd_rows.stored.at(32))

            def extra(i):
                pool.wait_ge(o["turn"].sem, i + 1)
                both = plan.table[:, :].rearrange("p (c b) -> p c b", c=2)
                nc.gpsimd.tensor_copy(over_idx[:, :], both[:, :, bass.ds(i + N_EXP, 1)]).then_inc(o["idx"].sem, 1)
                pool.wait_ge(o["idx"].sem, i + 1)
                pool.sem_inc(o["index_read"].sem, 1)
                nc.gpsimd.indirect_dma_start(
                    out=over_x, out_offset=None, in_=T.h_dram,
                    in_offset=bass.IndirectOffsetOnAxis(ap=over_idx[:, 0:1], axis=0),
                    bounds_check=TOK - 1, oob_is_err=False).then_inc(o["x"].sem, 16)
                pool.wait_ge(o["y"].sem, i * 2 + 2)
                pool.sem_inc(o["y_seen"].sem, 1)
                nc.gpsimd.indirect_dma_start(
                    out=T.y_dram, out_offset=bass.IndirectOffsetOnAxis(ap=over_idx[:, 1:2], axis=0),
                    in_=y[:, 0, :], in_offset=None, bounds_check=2 * TOK - 1,
                    oob_is_err=False).then_inc(o["stored"].sem, 16)

            each_extra(pool, extra)

        @block.tensor
        def _(pe):
            def turn_next(s):
                turn(pe, x_in[:, s, :], T.ps[:, 0, :]).then_inc(turned.sem, turned.adds(1))

            def step(i, s):
                u = first + 3 * s
                peeled = isinstance(i, int)
                pe.wait_ge(turned_out.sem, turned_out.at(count(i, s, 1)))
                pe.wait_ge(T.landing(u), T.landed_at(u, i))
                up(pe, as_up(slot(u)), xT[:, s, :], gate_ps).then_inc(T.unit_used.sem, T.unit_used.adds(1))
                pe.wait_ge(gathered[1 - s].sem, gathered[1 - s].at((i + s) * 16 + 16))
                pe.wait_ge(T.landing(u + 1), T.landed_at(u + 1, i))
                up(pe, as_up(slot(u + 1)), xT[:, s, :], up_ps[0], range(0, FC // 2)).then_inc(
                    half_up.sem, half_up.adds(1))
                up(pe, as_up(slot(u + 1)), xT[:, s, :], up_ps[1], range(FC // 2, FC)).then_inc(
                    T.unit_used.sem, T.unit_used.adds(1))
                turn_next(1 - s)
                pe.wait_ge(half_hidden.sem, half_hidden.at(count(i, s, 1)))
                if not (peeled and s == 0):
                    pe.wait_ge(y_act.sem, y_act.at(count(i, s)))
                    pe.wait_ge(y_dve.sem, y_dve.at(count(i, s)))
                pe.wait_ge(T.landing(u + 2), T.landed_at(u + 2, i))
                w_down = as_down(slot(u + 2))
                down(pe, w_down, 0, range(0, FC // 2))
                pe.wait_ge(hidden.sem, hidden.at(count(i, s, 1)))
                down(pe, w_down, 0, range(FC // 2, FC))
                down(pe, w_down, 1, range(FC)).then_inc(T.unit_used.sem, T.unit_used.adds(1))

            pe.wait_ge(gathered[0].sem, gathered[0].at(16))
            turn_next(0)
            each_pair(pe, step)
            pe.wait_ge(y_act.sem, y_act.at(N_EXP))
            pe.wait_ge(y_dve.sem, y_dve.at(N_EXP))
            pe.wait_ge(turned_out.sem, turned_out.at(N_EXP + 1))

            def extra(i):
                pe.wait_ge(o["x"].sem, i * 16 + 16)
                pe.sem_inc(o["x_seen"].sem, 1)
                turn(pe, over_x, T.ps[:, 0, :]).then_inc(o["turned"].sem, 1)
                pe.wait_ge(o["xT"].sem, i + 1)
                pe.wait_ge(o["w"].sem, i * 32 + 32)
                up(pe, as_up(over_w[:, 0, :]), xT[:, 0, :], gate_ps).then_inc(o["gate"].sem, 1)
                up(pe, as_up(over_w[:, 1, :]), xT[:, 0, :], up_ps[0], range(0, FC // 2)).then_inc(o["up"].sem, 1)
                up(pe, as_up(over_w[:, 1, :]), xT[:, 0, :], up_ps[1], range(FC // 2, FC)).then_inc(o["up"].sem, 1)
                pe.wait_ge(o["hidden"].sem, i * 2 + 2)
                pe.wait_ge(o["down_w"].sem, i * 16 + 16)
                down(pe, as_down(over_w[:, 0, :]), 0, range(FC))
                down(pe, as_down(over_w[:, 0, :]), 1, range(FC)).then_inc(o["down"].sem, 1)

            each_extra(pe, extra)

        @block.scalar
        def _(act):
            def copy_turned(i, s):
                act.wait_ge(turned.sem, turned.at(count(i, s, 1)))
                nc.scalar.copy(xT[:, s, :], T.ps[:, 0, :]).then_inc(turned_out.sem, turned_out.adds(1))

            def step(i, s):
                u = first + 3 * s
                peeled = isinstance(i, int)
                act.wait_ge(T.unit_used.sem, T.used_at(u, i))
                if not (peeled and s == 0):
                    act.wait_ge(hidden.sem, hidden.at(count(i, s)))
                nc.scalar.activation(sig[:, :], gate_ps, ACT.Exp, scale=-1.0).then_inc(sigmoid.sem, sigmoid.adds(1))
                copy_turned(i + s, 1 - s)
                act.wait_ge(T.unit_used.sem, T.used_at(u + 2, i))
                if not peeled:
                    act.wait_ge(stored[s].sem, stored[s].at(i * 16))
                nc.scalar.copy(y[:, s, 0:512], T.ps[0:BLK, 3, :]).then_inc(y_act.sem, y_act.adds(1))

            copy_turned(0, 0)
            each_pair(act, step)
            for s in range(2):
                act.wait_ge(stored[s].sem, stored[s].at(16 * pairs))
            act.sem_inc(o["turn"].sem, 1)

            def extra(i):
                act.wait_ge(o["turned"].sem, i + 1)
                nc.scalar.copy(xT[:, 0, :], T.ps[:, 0, :]).then_inc(o["xT"].sem, 1)
                act.wait_ge(o["gate"].sem, i + 1)
                nc.scalar.activation(sig[:, :], gate_ps, ACT.Exp, scale=-1.0).then_inc(o["sig"].sem, 1)
                act.wait_ge(o["down"].sem, i + 1)
                for n in range(2):
                    nc.scalar.copy(y[:, 0, n * 512:(n + 1) * 512], T.ps[0:BLK, 3 + n, :]).then_inc(o["y"].sem, 1)
                act.wait_ge(o["stored"].sem, i * 16 + 16)
                act.sem_inc(o["turn"].sem, 1)

            each_extra(act, extra)

        @block.vector
        def _(dve):
            v = nc.vector

            def step(i, s):
                u = first + 3 * s
                n = count(i, s) * 3
                dve.wait_ge(sigmoid.sem, sigmoid.at(count(i, s, 1)))
                v.tensor_scalar(sig[:, :], sig[:, :], 1.0, None, ALU.add).then_inc(silu.sem, silu.adds(1))
                dve.wait_ge(silu.sem, silu.at(n + 1))
                v.reciprocal(sig[:, :], sig[:, :]).then_inc(silu.sem, silu.adds(1))
                dve.wait_ge(silu.sem, silu.at(n + 2))
                v.tensor_tensor(sig[:, :], sig[:, :], gate_ps, ALU.mult).then_inc(silu.sem, silu.adds(1))
                dve.wait_ge(silu.sem, silu.at(n + 3))
                dve.wait_ge(half_up.sem, half_up.at(count(i, s, 1)))
                v.tensor_tensor(hid[:, halves[0]], sig[:, halves[0]], up_ps[0], ALU.mult).then_inc(
                    half_hidden.sem, half_hidden.adds(1))
                dve.wait_ge(T.unit_used.sem, T.used_at(u + 1, i))
                v.tensor_tensor(hid[:, halves[1]], sig[:, halves[1]], up_ps[1], ALU.mult).then_inc(
                    hidden.sem, hidden.adds(1))
                dve.wait_ge(T.unit_used.sem, T.used_at(u + 2, i))
                if not isinstance(i, int):
                    dve.wait_ge(stored[s].sem, stored[s].at(i * 16))
                v.tensor_copy(y[:, s, 512:D], T.ps[0:BLK, 4, :]).then_inc(y_dve.sem, y_dve.adds(1))

            each_pair(dve, step)

            def extra(i):
                silu_n = i * 3
                dve.wait_ge(o["sig"].sem, i + 1)
                v.tensor_scalar(sig[:, :], sig[:, :], 1.0, None, ALU.add).then_inc(o["silu"].sem, 1)
                dve.wait_ge(o["silu"].sem, silu_n + 1)
                v.reciprocal(sig[:, :], sig[:, :]).then_inc(o["silu"].sem, 1)
                dve.wait_ge(o["silu"].sem, silu_n + 2)
                v.tensor_tensor(sig[:, :], sig[:, :], gate_ps, ALU.mult).then_inc(o["silu"].sem, 1)
                dve.wait_ge(o["silu"].sem, silu_n + 3)
                dve.wait_ge(o["up"].sem, i * 2 + 2)
                for half in range(2):
                    v.tensor_tensor(hid[:, halves[half]], sig[:, halves[half]], up_ps[half], ALU.mult).then_inc(
                        o["hidden"].sem, 1)

            each_extra(dve, extra)
    T.end_stage()


def stage_combine(T, l, plan):
    nc, O = T.nc, T.O
    with ExitStack() as ctx:
        gate = T.sb(ctx, f"gate2_{l}", [P, 2, D])
        rows = T.sb(ctx, f"rows{l}", [P, 2 * NT, D])
        steps, added, weighted, gated = (T.counter("dve_done"), T.counter("rows"), T.counter("act_done"),
                                         T.counter("normed"))
        gate_in = [T.counter("loads"), T.counter("rows_in")]
        fetched = [T.counter(f"fetched{t}") for t in range(NT)]
        stored = T.counter("stored_act")
        block = ctx.enter_context(nc.Block())

        @block.sync
        def _(sp):
            by_tile = T.y_dram.rearrange("(k t p) d -> p k t d", k=2, p=P)
            for t in range(NT):
                sp.dma_start(rows[:, t::NT, :], by_tile[:, :, t, :]).then_inc(fetched[t].sem, fetched[t].adds(16))
                if t < 2:
                    sp.dma_start(gate[:, t, :], spread(T.mod_dram[l, t, 5 * D:6 * D])).then_inc(
                        gate_in[t].sem, gate_in[t].adds(16))

        @block.scalar
        def _(act):
            for t in range(NT):
                act.wait_ge(fetched[t].sem, fetched[t].at(16))
                act.mul(rows[:, t, :], rows[:, t, :], plan.weight[:, 0, t:t + 1]).then_inc(
                    weighted.sem, weighted.adds(1))
            if l == 1:
                for t in range(NT):
                    act.wait_ge(added.sem, added.at(t + 1))
                    out = O["y_sample"][0, (t - 1) * P:t * P, :] if t else O["y_prompt"][0]
                    act.dma_start(out, T.x[:, t, :]).then_inc(stored.sem, stored.adds(16))
                act.wait_ge(stored.sem, stored.at(16 * NT))

        @block.gpsimd
        def _(pool):
            for t in range(NT):
                pool.wait_ge(gated.sem, gated.at(t + 1))
                nc.gpsimd.tensor_tensor(T.x[:, t, :], T.x[:, t, :], rows[:, t, :], ALU.add).then_inc(
                    added.sem, added.adds(1))

        @block.vector
        def _(dve):
            v = nc.vector
            for t in range(NT):
                a, b = rows[:, t, :], rows[:, NT + t, :]
                dve.wait_ge(weighted.sem, weighted.at(t + 1))
                v.scalar_tensor_tensor(out=a, in0=b, scalar=plan.weight[:, 1, t:t + 1], in1=a,
                                       op0=ALU.mult, op1=ALU.add).then_inc(steps.sem, steps.adds(1))
                dve.wait_ge(steps.sem, steps.now())
                if t < 2:
                    dve.wait_ge(gate_in[t].sem, gate_in[t].at(16))
                v.tensor_tensor(a, a, gate[:, min(t, 1), :], ALU.mult).then_inc(gated.sem, gated.adds(1))
    T.end_stage()


class Plan:

    def __init__(self, T, ctx, l):
        self.table = T.sb(ctx, f"table{l}", [BLK, 2 * N_BLK], U32)
        self.x_in = T.sb(ctx, f"x_in{l}", [BLK, 3, D])
        self.over = T.sb(ctx, f"over{l}", [1, OVER + 1], I32)
        self.weight = T.sb(ctx, f"weight{l}", [P, 2, NT])

    def tokens(self, b):
        return bass.IndirectOffsetOnAxis(ap=self.table[:, b:b + 1], axis=0)

    def targets(self, b):
        return bass.IndirectOffsetOnAxis(ap=self.table[:, N_BLK + b:N_BLK + b + 1], axis=0)


def program(nc, I, O):
    with ExitStack() as ctx:
        T = Trunk(nc, ctx, I, O)
        first = 0
        for l in range(2):
            total = ODD_COLS if l else EVEN_COLS
            n_in = -(-total // 512)
            if l == 0:
                stage_modulation(T, first)
                first += MOD_UNITS
            with ExitStack() as mixer:
                z = T.sb(mixer, f"z{l}", [P, NT, total])
                mix = T.sb(mixer, f"mix{l}", [P, NT, D])
                if l == 0:
                    stage_projection(T, l, first, z)
                    first += n_in
                    stage_window(T, first, z, mix)
                    stage_mlstm(T, first, z, mix)
                    first += MOD_UNITS
                else:
                    with ExitStack() as heads:
                        kT = T.sb(heads, "mla_kT", [P, HEADS, 4 * P])
                        tables = MlaTables(T, mix, kT[:, :, :])
                        stage_projection(T, l, first, z, mix, tables)
                        first += n_in
                        qT = T.sb(heads, "mla_qT", [P, HEADS, TOK])
                        v = T.sb(heads, "mla_v", [P, 4, HEADS * HD])
                        stage_mla_heads(T, z, mix, tables, qT[:, :, :], v[:, :, :])
                        stage_mla_attention(T, mix, qT, kT, v)
                    stage_neighbourhood(T, z, mix)
                stage_output(T, l, first, mix)
                first += 2
            with ExitStack() as moe:
                plan = Plan(T, moe, l)
                stage_router(T, l, plan)
                stage_experts(T, l, first, plan)
                first += 3 * N_EXP
                stage_combine(T, l, plan)


OUTPUTS = (("y_prompt", (1, SEQ, D)), ("y_sample", (1, LAT, D)), ("ml_c", (1, 1, 2, ML_H, ML_D, ML_D)),
           ("ml_n", (1, 1, 2, ML_H, ML_D)), ("ml_m", (1, 1, 2, ML_H)),
           ("win_k", (1, 1, SEQ, 2, HD)), ("win_v", (1, 1, SEQ, 2, HD)), ("mla_ckv", (1, 1, SEQ, P)),
           ("mla_kpe", (1, 1, SEQ, MLA_ROPE)), ("nat_k", (1, 1, SEQ, HEADS, HD)),
           ("nat_v", (1, 1, SEQ, HEADS, HD)))
INPUTS = ("x_prompt", "x_sample", "state_ml_c", "state_ml_n", "state_ml_m", "cache_win_k", "cache_win_v",
          "cache_mla_ckv", "cache_mla_kpe", "cache_nat_k", "cache_nat_v", "c", "c_ctx", "ada_w", "ada_b",
          "norm1_g", "norm2_g", "even_w_in", "ml_gate_b", "ml_out_g", "win_q_g", "win_k_g", "win_sink",
          "even_w_out", "odd_w_in", "mla_q_a_g", "mla_kv_a_g", "mla_w_q_up", "mla_w_kv_up", "mla_q_g",
          "mla_k_g", "nat_q_g", "nat_k_g", "nat_rpb", "odd_w_out", "moe_w_group", "moe_b_group",
          "moe_w_expert", "moe_b_expert", "moe_w_gate", "moe_w_up", "moe_w_down")


def kernel(**inputs):
    import concourse.bacc as bacc
    from concourse.bass_utils import run_bass_kernel_spmd

    nc = bacc.Bacc("TRN2", target_bir_lowering=False, num_devices=1)
    arrays = {name: np.ascontiguousarray(inputs[name]) for name in INPUTS}
    arrays["const"] = constants()
    I = {name: nc.dram_tensor("in_" + name, a.shape, mybir.dt.from_np(a.dtype), kind="ExternalInput").ap()
         for name, a in arrays.items()}
    O = {name: nc.dram_tensor("out_" + name, shape, F32, kind="ExternalOutput").ap() for name, shape in OUTPUTS}
    program(nc, I, O)
    got = run_bass_kernel_spmd(nc, [{"in_" + name: a for name, a in arrays.items()}], core_ids=[0]).results[0]
    return tuple(got["out_" + name] for name, _ in OUTPUTS)
```
